# Optimizing a Trainium2 kernel written in Bass

```python
import math
import jax, jax.numpy as jnp
from jax import lax
import numpy as np
import functools
import jax
import jax.numpy as jnp

D_MODEL = 1024
BATCH = 1
SEQ = 512
DEPTH = 1

D_MIX = D_MODEL
HEAD_DIM = 64
RWKV_WIDTH = D_MIX // 2
SB_WIDTH = D_MIX - RWKV_WIDTH
RWKV_HEADS = RWKV_WIDTH // HEAD_DIM
SB_HEADS = SB_WIDTH // HEAD_DIM
DECAY_LORA = 64
ICLR_LORA = 64
SHIFT_COLS = 3 * RWKV_WIDTH + DECAY_LORA + ICLR_LORA
RWKV_COLS = SHIFT_COLS + RWKV_WIDTH
SB_COLS = 4 * SB_WIDTH
IN_COLS = RWKV_COLS + SB_COLS
Q_BLOCK = 128
NORM_EPS = 1e-6
GN_EPS = 64e-5


def rmsnorm(x, g):
    xf = x.astype(jnp.float32)
    y = xf * lax.rsqrt(jnp.mean(xf * xf, axis=-1, keepdims=True) + NORM_EPS)
    return (y * g.astype(jnp.float32)).astype(x.dtype)

def rwkv7_group(p, mu, w0, w2, a0, a2, k_k, k_a, r_k, ln_w, ln_b):
    B, S, _ = p.shape
    H, N = RWKV_HEADS, HEAD_DIM
    ps, g = p[..., :SHIFT_COLS], p[..., SHIFT_COLS:]
    prev = jnp.pad(ps, ((0, 0), (1, 0), (0, 0)))[:, :-1]
    ps = ps + (prev - ps) * mu
    r, k, v, zw, za = jnp.split(
        ps, [RWKV_WIDTH, 2 * RWKV_WIDTH, 3 * RWKV_WIDTH, 3 * RWKV_WIDTH + DECAY_LORA], axis=-1)
    w_log = -jax.nn.softplus(-(w0 + jnp.tanh(zw) @ w2)) - 0.5
    decay = jnp.exp(-jnp.exp(w_log.astype(jnp.float32)))
    a = jax.nn.sigmoid(a0 + za @ a2)
    hd = lambda t: t.reshape(B, S, H, N)
    r, k, v, decay, a = hd(r), hd(k), hd(v), hd(decay), hd(a)
    kk = hd(ps[..., RWKV_WIDTH:2 * RWKV_WIDTH] * k_k)
    kkf = kk.astype(jnp.float32)
    kk = kkf * lax.rsqrt(jnp.maximum(jnp.sum(kkf * kkf, axis=-1, keepdims=True), 1e-24))
    k = k * (1.0 + (a - 1.0) * k_a.reshape(H, N))

    def step(state, inp):
        r_t, w_t, k_t, v_t, kk_t, b_t = inp
        sa = jnp.einsum('bhij,bhj->bhi', state, -kk_t)
        state = (state * w_t[:, :, None, :]
                 + sa[..., None] * b_t[:, :, None, :]
                 + v_t[..., None] * k_t[:, :, None, :])
        y_t = jnp.einsum('bhij,bhj->bhi', state, r_t)
        return state, y_t

    tm = lambda t: jnp.moveaxis(t.astype(jnp.float32), 1, 0)
    state0 = jnp.zeros((B, H, N, N), jnp.float32)
    _, y = lax.scan(step, state0, (tm(r), tm(decay), tm(k), tm(v), tm(kk), tm(kk * a)))
    y = jnp.moveaxis(y, 0, 1)
    mean = jnp.mean(y, axis=-1, keepdims=True)
    var = jnp.mean(jnp.square(y - mean), axis=-1, keepdims=True)
    y = (y - mean) * lax.rsqrt(var + GN_EPS)
    y = y * ln_w.reshape(H, N) + ln_b.reshape(H, N)
    rf, kf, vf = r.astype(jnp.float32), k.astype(jnp.float32), v.astype(jnp.float32)
    y = y + jnp.sum(rf * kf * r_k, axis=-1, keepdims=True) * vf
    y = y.reshape(B, S, RWKV_WIDTH).astype(p.dtype)
    return y * jax.nn.silu(g)

def stick_breaking_group(p, sb_g):
    B, S, _ = p.shape
    H, N = SB_HEADS, HEAD_DIM
    n_blocks = S // Q_BLOCK
    q, k, v, g = jnp.split(p, 4, axis=-1)
    hd = lambda t: t.reshape(B, S, H, N).transpose(0, 2, 1, 3)
    q, k, v = hd(q), hd(k), hd(v)
    scale = 1.0 / math.sqrt(N)
    k_pos = jnp.arange(S)
    q_blocks = q.reshape(B, H, n_blocks, Q_BLOCK, N).transpose(2, 0, 1, 3, 4)

    def block(args):
        q_blk, idx = args
        q_pos = idx * Q_BLOCK + jnp.arange(Q_BLOCK)
        z = jnp.einsum('bhqd,bhkd->bhqk', q_blk, k).astype(jnp.float32) * scale
        mask = k_pos[None, :] < q_pos[:, None]
        log_1m = jnp.where(mask, jax.nn.log_sigmoid(-z), 0.0)
        after = lax.cumsum(log_1m, axis=3, reverse=True) - log_1m
        attn = jnp.where(mask, jnp.exp(jax.nn.log_sigmoid(z) + after), 0.0)
        return jnp.einsum('bhqk,bhkd->bhqd', attn.astype(v.dtype), v)

    o = lax.map(block, (q_blocks, jnp.arange(n_blocks)))
    o = o.transpose(1, 3, 0, 2, 4).reshape(B, S, H, N)
    o = rmsnorm(o, sb_g.reshape(H, N)).reshape(B, S, SB_WIDTH)
    return o * jax.nn.silu(g)

def first_inputs(seed: int = 0) -> dict:
    key = jax.random.key(seed)
    ks = jax.random.split(key, 20)
    nrm = lambda k, shape, s: s * jax.random.normal(k, shape, jnp.float32)
    return {
        "x": nrm(ks[0], (BATCH, SEQ, D_MODEL), 1.0),
        "c": nrm(ks[1], (BATCH, D_MODEL), 1.0),
        "norm_g": 1.0 + nrm(ks[2], (DEPTH, D_MODEL), 0.05),
        "ada_w": nrm(ks[3], (DEPTH, D_MODEL, 3 * D_MODEL), 0.5 * D_MODEL ** -0.5),
        "ada_b": nrm(ks[4], (DEPTH, 3 * D_MODEL), 0.02),
        "w_in": nrm(ks[5], (DEPTH, D_MODEL, IN_COLS), D_MODEL ** -0.5),
        "w_out": nrm(ks[6], (DEPTH, D_MIX, D_MODEL), D_MIX ** -0.5),
        "tshift_mu": jax.random.uniform(ks[7], (DEPTH, SHIFT_COLS), jnp.float32),
        "decay_w0": jax.random.uniform(ks[8], (DEPTH, RWKV_WIDTH), jnp.float32, minval=-4.0, maxval=1.0),
        "decay_w2": nrm(ks[9], (DEPTH, DECAY_LORA, RWKV_WIDTH), 0.5 * DECAY_LORA ** -0.5),
        "iclr_a0": nrm(ks[10], (DEPTH, RWKV_WIDTH), 0.5),
        "iclr_a2": nrm(ks[11], (DEPTH, ICLR_LORA, RWKV_WIDTH), 0.5 * ICLR_LORA ** -0.5),
        "k_k": 0.85 + nrm(ks[12], (DEPTH, RWKV_WIDTH), 0.05),
        "k_a": 1.0 + nrm(ks[13], (DEPTH, RWKV_WIDTH), 0.05),
        "r_k": nrm(ks[14], (DEPTH, RWKV_HEADS, HEAD_DIM), 0.1),
        "rwkv_ln_w": 1.0 + nrm(ks[15], (DEPTH, RWKV_WIDTH), 0.05),
        "rwkv_ln_b": nrm(ks[16], (DEPTH, RWKV_WIDTH), 0.02),
        "sb_norm_g": 1.0 + nrm(ks[17], (DEPTH, SB_WIDTH), 0.05),
        "final_g": 1.0 + nrm(ks[18], (D_MODEL,), 0.05),
    }

def first_block(x, c, norm_g, ada_w, ada_b, w_in, w_out, tshift_mu, decay_w0, decay_w2,
              iclr_a0, iclr_a2, k_k, k_a, r_k, rwkv_ln_w, rwkv_ln_b, sb_norm_g, final_g):
    c_act = jax.nn.silu(c)
    for l in range(DEPTH):
        mod = c_act @ ada_w[l] + ada_b[l]
        shift, scale, gate = jnp.split(mod, 3, axis=-1)
        h = rmsnorm(x, norm_g[l]) * (1.0 + scale[:, None, :]) + shift[:, None, :]
        p = h @ w_in[l]
        y_rwkv = rwkv7_group(p[..., :RWKV_COLS], tshift_mu[l], decay_w0[l], decay_w2[l],
                             iclr_a0[l], iclr_a2[l], k_k[l], k_a[l], r_k[l],
                             rwkv_ln_w[l], rwkv_ln_b[l])
        y_sb = stick_breaking_group(p[..., RWKV_COLS:], sb_norm_g[l])
        y = jnp.concatenate([y_rwkv, y_sb], axis=-1) @ w_out[l]
        x = x + gate[:, None, :] * y
    return rmsnorm(x, final_g)


N_MIXERS = 4
CHUNK = 64
CONV_K = 5
PLE_DIM = 256

GDN_QK_HEADS = 8
GDN_V_HEADS = 16
GDN_HEAD_DIM = 128
GDN_KEY_WIDTH = GDN_QK_HEADS * GDN_HEAD_DIM
GDN_VAL_WIDTH = GDN_V_HEADS * GDN_HEAD_DIM
GDN_CONV_CH = 2 * GDN_KEY_WIDTH + GDN_VAL_WIDTH
GDN_IN = GDN_CONV_CH + GDN_VAL_WIDTH + 4 * GDN_V_HEADS

M2_D_INNER = 2 * D_MODEL
M2_HEAD_DIM = 64
M2_HEADS = M2_D_INNER // M2_HEAD_DIM
M2_GROUPS = 4
M2_HEADS_PER_GROUP = M2_HEADS // M2_GROUPS
M2_STATE = 128
M2_CONV_CH = M2_D_INNER + 2 * M2_GROUPS * M2_STATE
M2_IN = M2_D_INNER + M2_CONV_CH + 2 * M2_HEADS

HG_EXPAND = 128
HG_HEADS = D_MODEL // HG_EXPAND
HG_WIDTH = HG_HEADS * HG_EXPAND
HG_IN = 5 * HG_WIDTH

GLA_HEADS = 4
GLA_KEY_WIDTH = D_MODEL // 2
GLA_VAL_WIDTH = D_MODEL
GLA_K = GLA_KEY_WIDTH // GLA_HEADS
GLA_V = GLA_VAL_WIDTH // GLA_HEADS
GLA_GATE_RANK = 16
GLA_GATE_TEMP = 16.0
GLA_IN = 2 * GLA_KEY_WIDTH + 2 * GLA_VAL_WIDTH + 2 * GLA_GATE_RANK

MOE_GROUPS = 4
MOE_EXPERTS_PER_GROUP = 8
MOE_EXPERTS = MOE_GROUPS * MOE_EXPERTS_PER_GROUP
MOE_TOPK = 2
MOE_HIDDEN = 256

DEEPNORM_ALPHA = (2 * DEPTH) ** 0.25
DEEPNORM_BETA = (8 * DEPTH) ** -0.25
LN_EPS = 1e-5
F32 = jnp.float32


def _n_uses(m):
    return (DEPTH - m + N_MIXERS - 1) // N_MIXERS

def _layernorm(t, g, b):
    tf = t.astype(F32)
    mu = jnp.mean(tf, axis=-1, keepdims=True)
    var = jnp.mean(jnp.square(tf - mu), axis=-1, keepdims=True)
    return ((tf - mu) * lax.rsqrt(var + LN_EPS) * g.astype(F32) + b.astype(F32)).astype(t.dtype)

def _rms(t):
    tf = t.astype(F32)
    return tf * lax.rsqrt(jnp.mean(tf * tf, axis=-1, keepdims=True) + NORM_EPS)

def _l2norm(t):
    tf = t.astype(F32)
    return tf * lax.rsqrt(jnp.sum(tf * tf, axis=-1, keepdims=True) + NORM_EPS)

def _dwconv(t, w):
    return lax.conv_general_dilated(
        t, w[:, None, :].astype(t.dtype), window_strides=(1,),
        padding=[(CONV_K // 2, CONV_K // 2)],
        dimension_numbers=("NWC", "WIO", "NWC"),
        feature_group_count=t.shape[-1])

def _rev(t):
    return jnp.flip(t, axis=1)

def _chunks(t):
    bsz, seq = t.shape[:2]
    t = t.reshape(bsz, seq // CHUNK, CHUNK, *t.shape[2:])
    return jnp.swapaxes(jnp.swapaxes(t, 0, 1), 2, 3)

def _unchunks(t):
    t = jnp.swapaxes(jnp.swapaxes(t, 2, 3), 0, 1)
    return t.reshape(t.shape[0], t.shape[1] * t.shape[2], *t.shape[3:])

def _gated_delta_rule(q, k, v, beta, g):
    q, k, v, beta, g = (_chunks(t.astype(F32)) for t in (q, k, v, beta, g))
    gc = jnp.cumsum(g, axis=-1)
    incl = jnp.tril(jnp.ones((CHUNK, CHUNK), dtype=bool))
    decay = jnp.exp(jnp.where(incl, gc[..., :, None] - gc[..., None, :], -jnp.inf))
    eye = jnp.eye(CHUNK, dtype=F32)
    kb = k * beta[..., None]
    lhs = eye + jnp.einsum("nbhik,nbhjk->nbhij", kb, k) * decay * (1.0 - eye)
    solve = functools.partial(lax.linalg.triangular_solve, left_side=True, lower=True,
                              unit_diagonal=True)
    u = solve(lhs, v * beta[..., None])
    w = solve(lhs, kb * jnp.exp(gc)[..., None])
    attn = jnp.einsum("nbhik,nbhjk->nbhij", q, k) * decay
    q_dec = q * jnp.exp(gc)[..., None]
    k_dec = k * jnp.exp(gc[..., -1:] - gc)[..., None]
    g_last = jnp.exp(gc[..., -1])

    def step(state, inp):
        attn_c, q_c, k_c, u_c, w_c, gl = inp
        v_new = u_c - jnp.einsum("bhck,bhkv->bhcv", w_c, state)
        o = jnp.einsum("bhck,bhkv->bhcv", q_c, state) + jnp.einsum("bhij,bhjv->bhiv", attn_c, v_new)
        state = state * gl[..., None, None] + jnp.einsum("bhck,bhcv->bhkv", k_c, v_new)
        return state, o

    s0 = jnp.zeros(q.shape[1:3] + (q.shape[-1], v.shape[-1]), F32)
    _, o = lax.scan(step, s0, (attn, q_dec, k_dec, u, w, g_last))
    return _unchunks(o)

def _ssd_grouped(c, b, u, g):
    c, b, u, g = (_chunks(t.astype(F32)) for t in (c, b, u, g))
    gc = jnp.cumsum(g, axis=3)
    tril = jnp.tril(jnp.ones((CHUNK, CHUNK), dtype=bool))[:, :, None]
    seg = gc[:, :, :, :, None, :] - gc[:, :, :, None, :, :]
    decay = jnp.exp(jnp.where(tril, seg, -jnp.inf))
    scores = jnp.einsum("nbgis,nbgjs->nbgij", c, b)[..., None] * decay
    y_intra = jnp.einsum("nbgijr,nbgjrp->nbgirp", scores, u)

    def step(state, inp):
        c_c, b_c, u_c, gc_c = inp
        y = jnp.exp(gc_c)[..., None] * jnp.einsum("bgis,bgrsp->bgirp", c_c, state)
        g_last = gc_c[:, :, -1]
        u_dec = u_c * jnp.exp(g_last[:, :, None] - gc_c)[..., None]
        state = state * jnp.exp(g_last)[..., None, None] + jnp.einsum("bgjs,bgjrp->bgrsp", b_c, u_dec)
        return state, y

    s0 = jnp.zeros((c.shape[1], c.shape[2], u.shape[4], c.shape[4], u.shape[5]), F32)
    _, y_inter = lax.scan(step, s0, (c, b, u, gc))
    return _unchunks(y_intra + y_inter)

def _gla_chunked(q, k, v, g):
    q, k, v, g = (_chunks(t.astype(F32)) for t in (q, k, v, g))
    gc = jnp.cumsum(g, axis=3)
    tril = jnp.tril(jnp.ones((CHUNK, CHUNK), dtype=bool))[:, :, None]

    def step(state, inp):
        q_c, k_c, v_c, gc_c = inp
        seg = gc_c[:, :, :, None, :] - gc_c[:, :, None, :, :]
        decay = jnp.exp(jnp.where(tril, seg, -jnp.inf))
        attn = jnp.einsum("bhijk,bhjk->bhij", decay * q_c[:, :, :, None, :], k_c)
        g_last = gc_c[:, :, -1]
        o = (jnp.einsum("bhij,bhjv->bhiv", attn, v_c)
             + jnp.einsum("bhik,bhkv->bhiv", q_c * jnp.exp(gc_c), state))
        state = (state * jnp.exp(g_last)[..., None]
                 + jnp.einsum("bhjk,bhjv->bhkv", k_c * jnp.exp(g_last[:, :, None] - gc_c), v_c))
        return state, o

    s0 = jnp.zeros(q.shape[1:3] + (q.shape[-1], v.shape[-1]), F32)
    _, o = lax.scan(step, s0, (q, k, v, gc))
    return _unchunks(o)

def _gdn_mixer(x, w_in, conv_w, a_log, dt_bias, norm_w, w_out):
    bsz, seq, _ = x.shape
    qkv, z, ab = jnp.split(x @ w_in, [GDN_CONV_CH, GDN_CONV_CH + GDN_VAL_WIDTH], axis=-1)
    qkv = jax.nn.silu(_dwconv(qkv, conv_w))
    q, k, v = jnp.split(qkv, [GDN_KEY_WIDTH, 2 * GDN_KEY_WIDTH], axis=-1)
    rep = GDN_V_HEADS // GDN_QK_HEADS
    qk_shape = (bsz, seq, GDN_QK_HEADS, GDN_HEAD_DIM)
    q = jnp.repeat(_l2norm(q.reshape(qk_shape)), rep, axis=2) * GDN_HEAD_DIM ** -0.5
    k = jnp.repeat(_l2norm(k.reshape(qk_shape)), rep, axis=2)
    v = v.reshape(bsz, seq, GDN_V_HEADS, GDN_HEAD_DIM).astype(F32)
    ab = ab.astype(F32).reshape(bsz, seq, 2, 2, GDN_V_HEADS)
    g = -jnp.exp(a_log.astype(F32)) * jax.nn.softplus(ab[:, :, 0] + dt_bias.astype(F32))
    beta = jax.nn.sigmoid(ab[:, :, 1])
    o = (_gated_delta_rule(q, k, v, beta[:, :, 0], g[:, :, 0])
         + _rev(_gated_delta_rule(_rev(q), _rev(k), _rev(v), _rev(beta[:, :, 1]), _rev(g[:, :, 1]))))
    o = _rms(o) * norm_w.astype(F32) * jax.nn.silu(
        z.astype(F32).reshape(bsz, seq, GDN_V_HEADS, GDN_HEAD_DIM))
    return o.reshape(bsz, seq, GDN_VAL_WIDTH).astype(x.dtype) @ w_out

def _mamba2_mixer(x, w_in, conv_w, conv_b, a_log, dt_bias, d_skip, norm_w, w_out):
    bsz, seq, _ = x.shape
    z, xbc, dt = jnp.split(x @ w_in, [M2_D_INNER, M2_D_INNER + M2_CONV_CH], axis=-1)
    xbc = jax.nn.silu(_dwconv(xbc, conv_w) + conv_b).astype(F32)
    xs, b_in, c_out = jnp.split(xbc, [M2_D_INNER, M2_D_INNER + M2_GROUPS * M2_STATE], axis=-1)
    xs = xs.reshape(bsz, seq, M2_GROUPS, M2_HEADS_PER_GROUP, M2_HEAD_DIM)
    b_in = b_in.reshape(bsz, seq, M2_GROUPS, M2_STATE)
    c_out = c_out.reshape(bsz, seq, M2_GROUPS, M2_STATE)
    hshape = (2, M2_GROUPS, M2_HEADS_PER_GROUP)
    dt = jax.nn.softplus(dt.astype(F32).reshape(bsz, seq, *hshape) + dt_bias.astype(F32).reshape(hshape))
    g = -jnp.exp(a_log.astype(F32)).reshape(hshape) * dt
    u_f = xs * dt[:, :, 0, :, :, None]
    u_b = xs * dt[:, :, 1, :, :, None]
    y = (_ssd_grouped(c_out, b_in, u_f, g[:, :, 0])
         + _rev(_ssd_grouped(_rev(c_out), _rev(b_in), _rev(u_b), _rev(g[:, :, 1]))))
    y = y + d_skip.astype(F32).reshape(M2_GROUPS, M2_HEADS_PER_GROUP, 1) * xs
    y = y.reshape(bsz, seq, M2_GROUPS, -1) * jax.nn.silu(z.astype(F32).reshape(bsz, seq, M2_GROUPS, -1))
    y = _rms(y) * norm_w.astype(F32).reshape(M2_GROUPS, -1)
    return y.reshape(bsz, seq, M2_D_INNER).astype(x.dtype) @ w_out

def _hgrn2_mixer(x, w_in, lb, norm_w, w_out):
    bsz, seq, _ = x.shape
    hs = (bsz, seq, HG_HEADS, HG_EXPAND)
    q, f_fwd, f_bwd, i_in, gate = jnp.split((x @ w_in).astype(F32), 5, axis=-1)
    q = jax.nn.silu(q).reshape(hs)
    i_in = i_in.reshape(hs)
    lb = lb.reshape(HG_HEADS, HG_EXPAND)

    def forget(f):
        f = f.reshape(hs)
        log_f = jnp.logaddexp(jnp.log(lb), jnp.log1p(-lb) + jax.nn.log_sigmoid(f))
        return (1.0 - lb) * jax.nn.sigmoid(-f), log_f

    k_f, g_f = forget(f_fwd)
    k_b, g_b = forget(f_bwd)
    o = (_gla_chunked(q, k_f, i_in, g_f)
         + _rev(_gla_chunked(_rev(q), _rev(k_b), _rev(i_in), _rev(g_b))))
    o = _rms(o) * norm_w.astype(F32) * jax.nn.silu(gate.reshape(hs))
    return o.reshape(bsz, seq, HG_WIDTH).astype(x.dtype) @ w_out

def _gla_mixer(x, w_in, w_gk, b_gk, norm_w, w_out):
    bsz, seq, _ = x.shape
    splits = [GLA_KEY_WIDTH, 2 * GLA_KEY_WIDTH, 2 * GLA_KEY_WIDTH + GLA_VAL_WIDTH,
              2 * GLA_KEY_WIDTH + 2 * GLA_VAL_WIDTH]
    q, k, v, gate, r = jnp.split((x @ w_in).astype(F32), splits, axis=-1)
    ks = (bsz, seq, GLA_HEADS, GLA_K)
    vs = (bsz, seq, GLA_HEADS, GLA_V)
    q = q.reshape(ks) * GLA_K ** -0.5
    k = k.reshape(ks)
    v = v.reshape(vs)
    r = r.reshape(bsz, seq, 2, GLA_GATE_RANK)
    gk = jax.nn.log_sigmoid(jnp.einsum("blzr,zrk->blzk", r, w_gk.astype(F32))
                            + b_gk.astype(F32)) / GLA_GATE_TEMP
    g_f = gk[:, :, 0].reshape(ks)
    g_b = gk[:, :, 1].reshape(ks)
    o = (_gla_chunked(q, k, v, g_f)
         + _rev(_gla_chunked(_rev(q), _rev(k), _rev(v), _rev(g_b))))
    o = _rms(o) * norm_w.astype(F32) * jax.nn.silu(gate.reshape(vs))
    return o.reshape(bsz, seq, GLA_VAL_WIDTH).astype(x.dtype) @ w_out

def _hier_moe(x, w_group, b_group, w_router, b_router, w_gate, w_up, w_down):
    bsz, seq, d = x.shape
    xt = x.reshape(bsz * seq, d)
    g_logits = (xt @ w_group).astype(F32) + b_group.astype(F32)
    g_onehot = jax.nn.one_hot(jnp.argmax(g_logits, axis=-1), MOE_GROUPS, dtype=F32)
    g_prob = jnp.sum(jax.nn.softmax(g_logits, axis=-1) * g_onehot, axis=-1)
    e_logits = ((xt @ w_router).astype(F32) + b_router.astype(F32)).reshape(
        -1, MOE_GROUPS, MOE_EXPERTS_PER_GROUP)
    e_logits = jnp.einsum("tge,tg->te", e_logits, g_onehot)
    top_val, top_idx = lax.top_k(e_logits, MOE_TOPK)
    top_w = jax.nn.softmax(top_val, axis=-1) * g_prob[:, None]
    within = jnp.einsum("tk,tke->te", top_w,
                        jax.nn.one_hot(top_idx, MOE_EXPERTS_PER_GROUP, dtype=F32))
    comb = (g_onehot[:, :, None] * within[:, None, :]).astype(x.dtype)
    out = jnp.zeros_like(xt)
    for grp in range(MOE_GROUPS):
        h = (jax.nn.silu(jnp.einsum("td,edf->tef", xt, w_gate[grp]))
             * jnp.einsum("td,edf->tef", xt, w_up[grp]))
        out = out + jnp.einsum("tef,efd->td", h * comb[:, grp, :, None], w_down[grp])
    return out.reshape(bsz, seq, d)

def second_inputs(seed: int = 0) -> dict:
    key = jax.random.key(seed)
    ks = iter(jax.random.split(key, 48))

    def nrm(shape, scale):
        return jax.random.normal(next(ks), shape, F32) * scale

    def a_log(shape):
        return jnp.log(jax.random.uniform(next(ks), shape, F32, 1.0, 16.0))

    def dt_bias(shape):
        dt = jnp.exp(jax.random.uniform(next(ks), shape, F32, math.log(1e-3), math.log(1e-1)))
        return dt + jnp.log(-jnp.expm1(-dt))

    na, nb, nc, nd = (_n_uses(m) for m in range(N_MIXERS))
    D = D_MODEL
    sd = D ** -0.5
    beta = DEEPNORM_BETA
    return {
        "x": nrm((BATCH, SEQ, D), 1.0),
        "p": nrm((DEPTH, BATCH, SEQ, PLE_DIM), 1.0),
        "gdn_w_in": nrm((na, D, GDN_IN), sd),
        "gdn_conv_w": nrm((na, CONV_K, GDN_CONV_CH), CONV_K ** -0.5),
        "gdn_a_log": a_log((na, 2, GDN_V_HEADS)),
        "gdn_dt_bias": dt_bias((na, 2, GDN_V_HEADS)),
        "gdn_norm_w": 1.0 + nrm((na, GDN_HEAD_DIM), 0.02),
        "gdn_w_out": nrm((na, GDN_VAL_WIDTH, D), GDN_VAL_WIDTH ** -0.5 * beta),
        "m2_w_in": nrm((nb, D, M2_IN), sd),
        "m2_conv_w": nrm((nb, CONV_K, M2_CONV_CH), CONV_K ** -0.5),
        "m2_conv_b": nrm((nb, M2_CONV_CH), 0.02),
        "m2_a_log": a_log((nb, 2, M2_HEADS)),
        "m2_dt_bias": dt_bias((nb, 2, M2_HEADS)),
        "m2_d": 1.0 + nrm((nb, M2_HEADS), 0.1),
        "m2_norm_w": 1.0 + nrm((nb, M2_D_INNER), 0.02),
        "m2_w_out": nrm((nb, M2_D_INNER, D), M2_D_INNER ** -0.5 * beta),
        "hg_w_in": nrm((nc, D, HG_IN), sd),
        "hg_lb_logits": nrm((DEPTH, HG_WIDTH), 0.1),
        "hg_norm_w": 1.0 + nrm((nc, HG_EXPAND), 0.02),
        "hg_w_out": nrm((nc, HG_WIDTH, D), HG_WIDTH ** -0.5 * beta),
        "gla_w_in": nrm((nd, D, GLA_IN), sd),
        "gla_w_gk": nrm((nd, 2, GLA_GATE_RANK, GLA_KEY_WIDTH), GLA_GATE_RANK ** -0.5),
        "gla_b_gk": nrm((nd, 2, GLA_KEY_WIDTH), 0.1),
        "gla_norm_w": 1.0 + nrm((nd, GLA_V), 0.02),
        "gla_w_out": nrm((nd, GLA_VAL_WIDTH, D), GLA_VAL_WIDTH ** -0.5 * beta),
        "ln_g": 1.0 + nrm((DEPTH, 2, D), 0.02),
        "ln_b": nrm((DEPTH, 2, D), 0.02),
        "moe_w_group": nrm((DEPTH, D, MOE_GROUPS), sd),
        "moe_b_group": nrm((DEPTH, MOE_GROUPS), 0.01),
        "moe_w_router": nrm((DEPTH, D, MOE_EXPERTS), sd),
        "moe_b_router": nrm((DEPTH, MOE_EXPERTS), 0.01),
        "moe_w_gate": nrm((DEPTH, MOE_GROUPS, MOE_EXPERTS_PER_GROUP, D, MOE_HIDDEN), sd),
        "moe_w_up": nrm((DEPTH, MOE_GROUPS, MOE_EXPERTS_PER_GROUP, D, MOE_HIDDEN), sd),
        "moe_w_down": nrm((DEPTH, MOE_GROUPS, MOE_EXPERTS_PER_GROUP, MOE_HIDDEN, D),
                          MOE_HIDDEN ** -0.5 * beta),
        "pe_w_gate": nrm((DEPTH, D, D), sd),
        "pe_w_proj": nrm((DEPTH, PLE_DIM, D), PLE_DIM ** -0.5 * beta),
    }

def second_block(x, p, gdn_w_in, gdn_conv_w, gdn_a_log, gdn_dt_bias, gdn_norm_w, gdn_w_out,
              m2_w_in, m2_conv_w, m2_conv_b, m2_a_log, m2_dt_bias, m2_d, m2_norm_w, m2_w_out,
              hg_w_in, hg_lb_logits, hg_norm_w, hg_w_out,
              gla_w_in, gla_w_gk, gla_b_gk, gla_norm_w, gla_w_out,
              ln_g, ln_b, moe_w_group, moe_b_group, moe_w_router, moe_b_router,
              moe_w_gate, moe_w_up, moe_w_down, pe_w_gate, pe_w_proj):
    lb_all = jnp.cumsum(jax.nn.softmax(hg_lb_logits.astype(F32), axis=0), axis=0)
    lb_all = lb_all - lb_all[0]
    for i in range(DEPTH):
        m, j = i % N_MIXERS, i // N_MIXERS
        if m == 0:
            h = _gdn_mixer(x, gdn_w_in[j], gdn_conv_w[j], gdn_a_log[j], gdn_dt_bias[j],
                           gdn_norm_w[j], gdn_w_out[j])
        elif m == 1:
            h = _mamba2_mixer(x, m2_w_in[j], m2_conv_w[j], m2_conv_b[j], m2_a_log[j],
                              m2_dt_bias[j], m2_d[j], m2_norm_w[j], m2_w_out[j])
        elif m == 2:
            h = _hgrn2_mixer(x, hg_w_in[j], lb_all[i], hg_norm_w[j], hg_w_out[j])
        else:
            h = _gla_mixer(x, gla_w_in[j], gla_w_gk[j], gla_b_gk[j], gla_norm_w[j], gla_w_out[j])
        x = _layernorm(DEEPNORM_ALPHA * x + h, ln_g[i, 0], ln_b[i, 0])
        h = _hier_moe(x, moe_w_group[i], moe_b_group[i], moe_w_router[i], moe_b_router[i],
                      moe_w_gate[i], moe_w_up[i], moe_w_down[i])
        x = _layernorm(DEEPNORM_ALPHA * x + h, ln_g[i, 1], ln_b[i, 1])
        x = x + jax.nn.sigmoid(x @ pe_w_gate[i]) * (p[i].astype(x.dtype) @ pe_w_proj[i])
    return x


def setup_inputs(seed=0):
    out = dict(first_inputs(seed))
    for name, value in second_inputs(seed + 1).items():
        if name != "x":
            out[name + "_2"] = value
    return out


def reference(
    x, c, norm_g, ada_w, ada_b, w_in, w_out, tshift_mu, decay_w0, decay_w2, iclr_a0, iclr_a2,
    k_k, k_a, r_k, rwkv_ln_w, rwkv_ln_b, sb_norm_g, final_g, p_2, gdn_w_in_2, gdn_conv_w_2,
    gdn_a_log_2, gdn_dt_bias_2, gdn_norm_w_2, gdn_w_out_2, m2_w_in_2, m2_conv_w_2, m2_conv_b_2,
    m2_a_log_2, m2_dt_bias_2, m2_d_2, m2_norm_w_2, m2_w_out_2, hg_w_in_2, hg_lb_logits_2,
    hg_norm_w_2, hg_w_out_2, gla_w_in_2, gla_w_gk_2, gla_b_gk_2, gla_norm_w_2, gla_w_out_2,
    ln_g_2, ln_b_2, moe_w_group_2, moe_b_group_2, moe_w_router_2, moe_b_router_2, moe_w_gate_2,
    moe_w_up_2, moe_w_down_2, pe_w_gate_2, pe_w_proj_2,
):
    x = first_block(
        x, c, norm_g, ada_w, ada_b, w_in, w_out, tshift_mu, decay_w0, decay_w2, iclr_a0,
        iclr_a2, k_k, k_a, r_k, rwkv_ln_w, rwkv_ln_b, sb_norm_g, final_g,
    )
    return second_block(
        x, p_2, gdn_w_in_2, gdn_conv_w_2, gdn_a_log_2, gdn_dt_bias_2, gdn_norm_w_2, gdn_w_out_2,
        m2_w_in_2, m2_conv_w_2, m2_conv_b_2, m2_a_log_2, m2_dt_bias_2, m2_d_2, m2_norm_w_2,
        m2_w_out_2, hg_w_in_2, hg_lb_logits_2, hg_norm_w_2, hg_w_out_2, gla_w_in_2, gla_w_gk_2,
        gla_b_gk_2, gla_norm_w_2, gla_w_out_2, ln_g_2, ln_b_2, moe_w_group_2, moe_b_group_2,
        moe_w_router_2, moe_b_router_2, moe_w_gate_2, moe_w_up_2, moe_w_down_2, pe_w_gate_2,
        pe_w_proj_2,
    )


_drawn_inputs = setup_inputs


def setup_inputs(seed=0):
    import zlib

    import numpy as np

    out = dict(_drawn_inputs(seed))
    spreads = {}
    factors = {'decay_w2': 3.48,
     'k_k': 6.434,
     'k_a': 4.229,
     'rwkv_ln_w': 4.797,
     'rwkv_ln_b': 7.968,
     'sb_norm_g': 4.571,
     'gdn_norm_w_2': 5.218,
     'moe_b_group_2': 140.477,
     'moe_b_router_2': 18.805}
    for name, (base, spread) in spreads.items():
        noise = np.random.default_rng([zlib.crc32(name.encode()), seed]).standard_normal(out[name].shape)
        drawn = base * np.exp(spread * noise) if base else spread * noise
        out[name] = jnp.asarray(drawn.astype(out[name].dtype))
    for name, factor in factors.items():
        out[name] = (out[name] * factor).astype(out[name].dtype)
    return out
```

```python
from contextlib import ExitStack
import math

import numpy as np
import concourse.bass as bass
from concourse import mybir

F32 = mybir.dt.float32
U8 = mybir.dt.uint8
ALU = mybir.AluOpType
ACT = mybir.ActivationFunctionType
X_AXIS = mybir.AxisListType.X

P = 128
SEQ, D = 512, 1024
NT = SEQ // P
ND = D // P
HD = 64
RW = D // 2
NPAIR = RW // P
SHIFT = 3 * RW + 2 * HD
SB0 = SHIFT + RW
NORM_EPS, GN_EPS, LN_EPS = 1e-6, 64e-5, 1e-5
DECAY = math.exp(-0.5)
QKH, VH = 8, 16
TAPS = 5
GDN_CONV = 4096
ALPHA = 2.0 ** 0.25
NEXP, NGRP, EPG, HID = 32, 4, 8, 256
PLE = 256
LEVELS = 7
CLAMP = 80.0
LNCLAMP = 44.0


class Steps:

    def __init__(self, book, sem, name, unit=1):
        self.names = book.setdefault(name, {})
        self.sem, self.unit, self.k, self.i = sem, unit, 0, None
        self.per = self.names.get("per iteration")

    def step(self, name=None):
        self.k += 1
        if name is not None:
            self.names[name] = self.k
        return self.sem, self.unit

    def value(self, k, i):
        k = k * self.unit
        return k if i is None else (i + 1) * (self.unit * (self.per or 1)) + k

    def at(self, name, i=None):
        return self.sem, self.value(self.names.get(name, 1), i)

    def last(self):
        return self.sem, self.value(self.k, self.i)

    def end(self, i=None):
        if i is None:
            return self.sem, self.unit * self.names.get("steps", 1)
        return self.sem, (i + 2) * (self.unit * (self.per or 1))

    def final(self, n):
        return self.end(n - 1)

    def credit(self, eng):
        eng.nop().then_inc(self.sem, self.unit * (self.per or 1))

    def begin(self, i):
        self.k, self.i = 0, i

    def close(self):
        self.names["per iteration" if self.i is not None else "steps"] = self.k


def bcast(ap, n):
    return ap.unsqueeze(2).to_broadcast([ap.shape[0], ap.shape[1], n])


def repeat(ap, n):
    return ap.unsqueeze(1).to_broadcast([ap.shape[0], n, ap.shape[1]])


def build(nc, a, out, book):
    ctx = ExitStack()

    def sb(name, shape, dt=F32):
        return ctx.enter_context(nc.sbuf_tensor(name, shape, dt))

    def sem(name):
        return ctx.enter_context(nc.semaphore(name))

    def steps(name, unit=1):
        return Steps(book, sem(name), name, unit)

    xtok = sb("xtok", [P, NT, D])
    hT = sb("hT", [P, ND, SEQ])
    yT = sb("yT", [P, 2 * ND, SEQ])
    W = sb("W", [P, 2, 6 * D])
    ident = sb("ident", [P, P])
    ones = sb("ones", [P, P])
    pairs = sb("pairs", [P, P])
    LE = sb("LE", [P, P])
    GE = sb("GE", [P, P])
    LT = sb("LT", [P, P])
    GT = sb("GT", [P, P])
    quad = sb("quad", [P, LEVELS, 6, P], U8)
    par = sb("par", [P, 61])
    conv = sb("conv", [P, 160])
    small = sb("small", [P, 64])
    lnshift = sb("lnshift", [P, 1])
    spare = sb("spare", [P, 32])
    arena = sb("arena", [P, 20480])
    ps = ctx.enter_context(nc.psum_tensor("ps", [P, 8, 512], F32))
    cut = [0]

    def take(*shape):
        n = math.prod(shape)
        ap = arena[:, cut[0]:cut[0] + n]
        cut[0] += n
        assert cut[0] <= arena.shape[1], cut[0]
        if len(shape) == 2:
            return ap.rearrange("p (a b) -> p a b", a=shape[0])
        if len(shape) == 3:
            return ap.rearrange("p (a b c) -> p a b c", a=shape[0], b=shape[1])
        if len(shape) == 4:
            return ap.rearrange("p (a b c d) -> p a b c d", a=shape[0], b=shape[1], c=shape[2])
        return ap

    held = [0]

    def hold(dve):
        held[0] += 1
        k = held[0] % 32
        return dve.tensor_copy(spare[:, k:k + 1], ones[:, 0:1])

    def rows(name):
        return a[name].flatten().rearrange("(r c) -> r c", c=P)

    def flat(name):
        return a[name].flatten().rearrange("(a n) -> a n", a=1)

    stores = sem("stores")
    progs = {"sync": [], "tensor": [], "vector": [], "scalar": [], "gpsimd": []}

    def runs(engine):
        return progs[engine].append

    PAR_G, PAR_C, PAR_MU, PAR_PAIR, PAR_SBG, PAR_MULORA = 0, 8, 16, 16, 56, 60
    PARAMS = [("norm_g", PAR_G, 8), ("c", PAR_C, 8), ("decay_w0", 28, 4), ("iclr_a0", 32, 4), ("k_k", 36, 4),
              ("k_a", 40, 4), ("r_k", 44, 4), ("rwkv_ln_w", 48, 4), ("rwkv_ln_b", 52, 4), ("sb_norm_g", 56, 4)]

    cut[0] = 0
    prm = take(P)
    cnv = take(2, P)
    adab = take(3 * D)
    acc = take(3 * D)
    xs = take(NT, D)
    gate = sb("gate", [P, D])
    modc = take(24)
    ct = take(4, 8)
    gs = take(8)
    sq = take(D)
    qtmp = take(2 * P)
    ssum = take(4)
    rstd = take(4)

    su_pe, su_dve, su_act, su_pool = steps("setup_products"), steps("setup_vector"), steps("setup_scalar"), steps("setup_pool")
    x_in, par_in, ada_in = sem("x_in"), sem("par_in"), [sem("ada_in0"), sem("ada_in1")]
    adab_in = sem("adab_in")
    CH = 3 * D // 4

    @runs("sync")
    def _(sp):
        sp.dma_start(xtok[:], a["x"][0].rearrange("(t p) d -> p t d", p=P)).then_inc(x_in, 16)
        for q in range(4):
            if q >= 2:
                sp.wait_ge(*su_dve.at(f"ada {q - 2}"))
            src = a["ada_w"][0].rearrange("(k p) n -> p k n", p=P)[:, :, q * CH:(q + 1) * CH]
            sp.dma_start(W[:, q % 2, :].rearrange("p (k n) -> p k n", k=ND), src).then_inc(ada_in[q % 2], 16)

    @runs("scalar")
    def _(act):
        act.preload_act_table_set("natural_log_exp_and_others")
        for name, at, n in PARAMS:
            act.dma_start(prm[at:at + n, :], rows(name)).then_inc(par_in, 16)
        act.dma_start(prm[16:28, :], rows("tshift_mu")[0:12, :]).then_inc(par_in, 16)
        act.dma_start(prm[60:61, :], rows("tshift_mu")[12:13, :]).then_inc(par_in, 16)
        for h in range(2):
            act.dma_start(cnv[0:80, h, :], rows("gdn_conv_w_2")[80 * h:80 * h + 80, :]).then_inc(par_in, 16)
        act.wait_ge(*su_pool.at("ada_b zeros"))
        act.dma_start(adab[0:1, :], flat("ada_b")).then_inc(adab_in, 16)
        act.wait_ge(*su_dve.at("c clamped"))
        act.activation(ct[:, 1, :], ct[:, 0, :], ACT.Exp, scale=-1.0).then_inc(*su_act.step("exp c"))
        act.wait_ge(x_in, 16)
        for t in range(NT):
            act.wait_ge(*su_act.last())
            act.activation(sq, xtok[:, t, :], ACT.Square, accum_out=ssum[:, t:t + 1]).then_inc(*su_act.step())
        act.wait_ge(*su_dve.at("ssum eps"))
        act.activation(rstd, rstd, ACT.Ln).then_inc(*su_act.step())
        act.wait_ge(*su_act.last())
        act.activation(rstd, rstd, ACT.Exp, scale=-0.5).then_inc(*su_act.step("rstd"))
        act.wait_ge(*su_dve.at("scales"))
        for k in range(ND):
            act.wait_ge(*su_pe.at(f"x^T {k}"))
            act.activation(hT[:, k, :], ps[:, k, :], ACT.Identity, scale=gs[:, k:k + 1],
                           bias=modc[:, k:k + 1]).then_inc(*su_act.step(f"h {k}"))
        su_act.close()

    @runs("gpsimd")
    def _(pool):
        def link(ins, name=None):
            ins.then_inc(*su_pool.step(name))
            pool.wait_ge(*su_pool.last())

        def keep(out_, in_, pattern, op, base, mult):
            link(pool.affine_select(out=out_, in_=in_, pattern=pattern, compare_op=op, fill=0.0, base=base,
                                    channel_multiplier=mult))

        link(pool.memset(ones[:], 1.0))
        keep(GE[:], ones[:], [[-1, P]], ALU.is_ge, 0, 1)
        keep(ident[:], GE[:], [[1, P]], ALU.is_ge, 0, -1)
        pool.nop().then_inc(*su_pool.step("ident"))
        link(pool.memset(adab, 0.0), "ada_b zeros")
        keep(LE[:], ones[:], [[1, P]], ALU.is_ge, 0, -1)
        keep(LT[:], ones[:], [[1, P]], ALU.is_gt, 0, -1)
        keep(GT[:], ones[:], [[-1, P]], ALU.is_gt, 0, 1)
        keep(pairs[:, 0:HD], ones[:, 0:HD], [[0, HD]], ALU.is_gt, HD, -1)
        keep(pairs[:, HD:P], ones[:, HD:P], [[0, HD]], ALU.is_ge, -HD, 1)
        q0, q1 = qtmp[:, 0:P], qtmp[:, P:2 * P]
        for lv in range(LEVELS):
            half = 1 << lv
            blocks = P // (2 * half)
            pool.memset(q0, 0.0).then_inc(*su_pool.step())
            link(pool.memset(q1, 0.0))
            low = q0.rearrange("p (b h r) -> p b h r", h=2, r=half)[:, :, 0, :]
            up = q1.rearrange("p (b h r) -> p b h r", h=2, r=half)[:, :, 1, :]
            src = ones[:].rearrange("p (b h r) -> p b h r", h=2, r=half)[:, :, 0, :]
            pat = [[-2 * half, blocks], [0, half]]
            neg = [[2 * half, blocks], [0, half]]
            keep(low, src, pat, ALU.is_ge, -half, 1)
            keep(low, low, neg, ALU.is_gt, 2 * half, -1)
            keep(up, src, pat, ALU.is_ge, 0, 1)
            keep(up, up, neg, ALU.is_gt, half, -1)
            for s, q in ((0, q0), (1, q0), (2, q1), (3, q1), (4, q0), (5, q0)):
                pool.tensor_copy(quad[:, lv, s, :], q).then_inc(*su_pool.step())
            pool.wait_ge(*su_pool.last())
        su_pool.close()

    @runs("tensor")
    def _(pe):
        pe.wait_ge(*su_pool.at("ident"))
        pe.wait_ge(par_in, 16 * (len(PARAMS) + 4))
        pe.transpose(ps[:, 0, 0:61], prm[0:61, :], ident[0:61, 0:61])
        for h in range(2):
            pe.transpose(ps[:, 0, P + 80 * h:P + 80 * h + 80], cnv[0:80, h, :], ident[0:80, 0:80])\
              .then_inc(*su_pe.step("columns"))
        pe.wait_ge(*su_dve.at("ada_b"))
        for j in range(24):
            mm = pe.matmul(ps[:, 1, j:j + 1], acc[:, j * P:(j + 1) * P], ones[:, 0:1], start=True, stop=True)
        mm.then_inc(*su_pe.step("mod columns"))
        for h in range(2):
            pe.matmul(ps[:, 2 + h, :], ones[:], acc[:, 2 * D + 512 * h:2 * D + 512 * h + 512], start=True, stop=True)\
              .then_inc(*su_pe.step("gate rows"))
        pe.wait_ge(*su_dve.at("gate"))
        pe.wait_ge(*su_dve.at("xs"))
        for k in range(ND):
            for t in range(NT):
                mm = pe.transpose(ps[:, k, t * P:(t + 1) * P], xs[:, t, k * P:(k + 1) * P], ident[:])
            mm.then_inc(*su_pe.step(f"x^T {k}"))
        su_pe.close()

    @runs("vector")
    def _(dve):
        def link(ins, name=None):
            ins.then_inc(*su_dve.step(name))
            dve.wait_ge(*su_dve.last())

        dve.wait_ge(*su_pe.at("columns"))
        dve.tensor_copy(par[:], ps[:, 0, 0:61]).then_inc(*su_dve.step())
        link(dve.tensor_copy(conv[:], ps[:, 0, P:P + 160]))
        link(dve.tensor_scalar(ct[:, 0, :], par[:, PAR_C:PAR_C + 8], -CLAMP, None, ALU.max), "c clamped")
        dve.wait_ge(*su_act.at("exp c"))
        link(dve.tensor_scalar(ct[:, 1, :], ct[:, 1, :], 1.0, None, ALU.add))
        link(dve.reciprocal(ct[:, 2, :], ct[:, 1, :]))
        link(dve.tensor_tensor(ct[:, 3, :], ct[:, 2, :], par[:, PAR_C:PAR_C + 8], ALU.mult))
        dve.wait_ge(adab_in, 16)
        for q in range(4):
            dve.wait_ge(ada_in[q % 2], 16 * (q // 2 + 1))
            w = W[:, q % 2, :].rearrange("p (k n) -> p k n", k=ND)
            part = acc[:, q * CH:(q + 1) * CH]
            for k in range(ND):
                link(dve.scalar_tensor_tensor(out=part, in0=w[:, k, :], scalar=ct[:, 3, k:k + 1],
                                              in1=adab[:, q * CH:(q + 1) * CH] if k == 0 else part,
                                              op0=ALU.mult, op1=ALU.add), f"ada {q}" if k == ND - 1 else None)
        dve.nop().then_inc(*su_dve.step("ada_b"))
        dve.wait_ge(x_in, 16)
        dve.wait_ge(*su_act.at("exp c"))
        dve.wait_ge(*su_act_sums())
        link(dve.tensor_scalar(rstd, ssum, 1.0 / D, NORM_EPS, ALU.mult, ALU.add), "ssum eps")
        dve.wait_ge(*su_pe.at("mod columns"))
        link(dve.tensor_copy(modc, ps[:, 1, 0:24]))
        link(dve.scalar_tensor_tensor(out=gs, in0=modc[:, 8:16], scalar=1.0, in1=par[:, PAR_G:PAR_G + 8],
                                      op0=ALU.add, op1=ALU.mult), "scales")
        dve.wait_ge(*su_pe.at("gate rows"))
        dve.tensor_copy(gate[:, 0:512], ps[:, 2, :]).then_inc(*su_dve.step())
        link(dve.tensor_copy(gate[:, 512:D], ps[:, 3, :]), "gate")
        dve.wait_ge(*su_act.at("rstd"))
        for t in range(NT):
            dve.tensor_scalar(xs[:, t, :], xtok[:, t, :], rstd[:, t:t + 1], None, ALU.mult)\
               .then_inc(*su_dve.step("xs"))
        su_dve.close()

    def su_act_sums():
        return su_act.sem, su_act.names.get("exp c", 1) + NT

    SETUP = [su_pe, su_dve, su_act, su_pool]
    SETUP = [(s, None) for s in SETUP]

    def after(eng, done):
        for s, n in done:
            eng.wait_ge(*(s.end() if n is None else s.final(n)))

    cut[0] = 0
    mixraw = take(3, SEQ + 1)
    loraraw = take(SEQ + 1)
    lora = take(SEQ)
    rkv = take(3, SEQ)
    sg = take(SEQ)
    sig = take(2, SEQ)
    tmp2 = take(2, SEQ)
    gsum = take(SEQ)
    E1 = take(SEQ)
    E2 = take(SEQ)
    E3 = take(SEQ)
    kk = take(SEQ)
    AR = take(NT, 2, P)
    BK = take(2, SEQ)
    tok = take(NT, 3, P)
    pc = take(16)
    mid = take(4)
    fac = take(2, 4)
    S0 = take(HD)
    S1 = take(HD)
    RU = take(P)
    U = take(P)
    bonus = take(SEQ)
    maskQ = take(4, P)
    pairTS = cut[0]
    N_ = take(2, NT, P)
    T_ = take(2, NT, P)
    TT_ = take(2, NT, P)
    wq = W[:, 0, 0:4096].rearrange("p (k j c) -> p k j c", k=ND, j=4)
    w2a2 = W[:, 0, 4096:4224]
    wlora = W[:, 0, 5120:6144].rearrange("p (k c) -> p k c", k=ND)
    Vs = W[:, 1, 4096:5120].rearrange("p (h c t) -> p h c t", h=2, c=NT)
    ysb, ysq = W[:, 1, 5120:5632], W[:, 1, 5632:6144]
    Q = yT[:, ND:2 * ND, :].rearrange("p k n -> p (k n)").rearrange("p (h c j t) -> p h c j t", h=2, c=NT, j=4)

    lo_pe, lo_dve, lo_act, lo_pool = steps("lora_products"), steps("lora_vector"), steps("lora_scalar"), steps("lora_pool")
    rw_pe, rw_dve, rw_act, rw_pool = steps("rwkv_products"), steps("rwkv_vector"), steps("rwkv_scalar"), steps("rwkv_pool")
    lora_in, rw_in = sem("lora_in"), steps("rwkv_weights_in", 16)
    w_in = a["w_in"][0].rearrange("(k p) n -> p k n", p=P)

    @runs("sync")
    def _(sp):
        after(sp, SETUP)
        sp.dma_start(wlora, w_in[:, :, 3 * RW:SHIFT]).then_inc(lora_in, 16)
        rw_in.credit(sp)
        with sp.Fori(0, NPAIR) as n:
            rw_in.begin(n)
            sp.wait_ge(*rw_pe.at("projected", n - 1))
            for j, c0 in enumerate((0, RW, 2 * RW, SHIFT)):
                sp.dma_start(wq[:, :, j, :], w_in[:, :, bass.ds(n * P + c0, P)]).then_inc(*rw_in.step())
            sp.dma_start(w2a2[0:HD, :], a["decay_w2"][0][:, bass.ds(n * P, P)]).then_inc(*rw_in.step())
            sp.dma_start(w2a2[HD:P, :], a["iclr_a2"][0][:, bass.ds(n * P, P)]).then_inc(*rw_in.step("in"))
            rw_in.close()

    @runs("tensor")
    def _(pe):
        after(pe, SETUP)
        pe.wait_ge(lora_in, 16)
        for k in range(ND):
            mm = pe.matmul(ps[:, 0, :], wlora[:, k, :], hT[:, k, :], start=(k == 0), stop=(k == ND - 1))
        mm.then_inc(*lo_pe.step("z"))
        lo_pe.close()
        rw_pe.credit(pe)
        with pe.Fori(0, NPAIR) as n:
            rw_pe.begin(n)
            for s in (rw_dve, rw_act, rw_pool):
                pe.wait_ge(*s.end(n - 1))
            pe.wait_ge(*lo_act.end())
            pe.wait_ge(*rw_in.at("in", n))
            for j in range(4):
                for k in range(ND):
                    mm = pe.matmul(ps[:, j, :], wq[:, k, j, :], hT[:, k, :], start=(k == 0), stop=(k == ND - 1))
                mm.then_inc(*rw_pe.step(f"proj {j}"))
            for j in range(2):
                r = slice(j * HD, j * HD + HD)
                mm = pe.matmul(ps[:, 4 + j, :], w2a2[r, :], lora[r, :], start=True, stop=True)
                mm.then_inc(*rw_pe.step("projected"))
            pe.wait_ge(*rw_act.at("kk^2", n))
            pe.matmul(ps[:, 6, :], pairs[:], tmp2[:, 0, :], start=True, stop=True).then_inc(*rw_pe.step("kk sums"))
            pe.wait_ge(*rw_dve.at("rkr", n))
            pe.matmul(ps[:, 7, :], pairs[:], tmp2[:, 1, :], start=True, stop=True).then_inc(*rw_pe.step("bonus sums"))
            pe.wait_ge(*rw_dve.at("factors", n))
            pe.wait_ge(*rw_pool.at("factors", n))
            for c in range(NT):
                cs = slice(c * P, c * P + P)
                if c:
                    pe.wait_ge(*rw_act.at(f"tok {c - 1}", n))
                for j, src in enumerate((BK[:, 0, cs], BK[:, 1, cs], rkv[:, 2, cs])):
                    mm = pe.transpose(ps[:, 0, j * P:(j + 1) * P], src, ident[:])
                mm.then_inc(*rw_pe.step(f"tok {c}"))
            pe.wait_ge(*rw_dve.at("bonus", n))
            pe.wait_ge(*rw_act.at(f"tok {NT - 1}", n))
            for h in range(2):
                r = slice(h * HD, h * HD + HD)
                for c in range(NT):
                    cs = slice(c * P, c * P + P)
                    if h:
                        pe.wait_ge(*rw_dve.at(f"Q 0 {c}", n))
                    ar = AR[r, c, :, :].rearrange("p j t -> p (j t)")
                    pe.matmul(ps[:, 1 + c, 0:256], BK[r, 0, cs], ar, start=True, stop=True)
                    pe.matmul(ps[:, 1 + c, 256:512], BK[r, 1, cs], ar, start=True, stop=True)\
                      .then_inc(*rw_pe.step(f"Q {h} {c}"))
                    mm = pe.matmul(ps[:, 5 + h, cs], AR[r, c, 0, :], BK[r, 0, cs], start=True, stop=True)
                mm.then_inc(*rw_pe.step(f"A {h}"))
            pe.wait_ge(*rw_dve.at(f"Q 1 {NT - 1}", n))
            for lv in range(1, LEVELS):
                for h in range(2):
                    pe.wait_ge(*rw_dve.at(f"T {h} {lv - 1}", n))
                    for c in range(NT):
                        mm = pe.matmul(ps[:, 1 + 3 * h, c * P:(c + 1) * P], N_[:, h, c, :], TT_[:, h, c, :], start=True, stop=True)
                    mm.then_inc(*rw_pe.step(f"V {h} {lv}"))
                for h in range(2):
                    pe.wait_ge(*rw_act.at(f"V {h} {lv}", n))
                    if lv < LEVELS - 1:
                        for c in range(NT):
                            mm = pe.matmul(ps[:, 2 + 3 * h, c * P:(c + 1) * P], Vs[:, h, c, :], T_[:, h, c, :], start=True, stop=True)
                        mm.then_inc(*rw_pe.step(f"T {h} {lv}"))
                    for c in range(NT):
                        mm = pe.matmul(ps[:, 3 + 3 * h, c * P:(c + 1) * P], T_[:, h, c, :], Vs[:, h, c, :], start=True, stop=True)
                    mm.then_inc(*rw_pe.step(f"TT {h} {lv}"))
            for h in range(2):
                pe.wait_ge(*rw_dve.at(f"T {h} {LEVELS - 1}", n))
            for c in range(NT):
                cs = slice(c * P, c * P + P)
                pe.wait_ge(*rw_dve.at(f"S0 {c}", n))
                for h in range(2):
                    r = slice(h * HD, h * HD + HD)
                    pe.matmul(ps[:, 4 * h, 0:HD], AR[r, c, 0, :], S0[r, :], start=True, stop=False)
                    mm = pe.matmul(ps[:, 4 * h, 0:HD], Q[:, h, c, 2, :], tok[:, c, 2, r], start=False, stop=True)
                mm.then_inc(*rw_pe.step(f"RU {c}"))
                pe.wait_ge(*rw_act.at(f"RU {c}", n))
                for h in range(2):
                    r = slice(h * HD, h * HD + HD)
                    mm = pe.matmul(ps[:, 1, r], TT_[:, h, c, :], RU[:, r], start=True, stop=True)
                mm.then_inc(*rw_pe.step(f"U {c}"))
                pe.wait_ge(*rw_act.at(f"U {c}", n))
                for h in range(2):
                    r = slice(h * HD, h * HD + HD)
                    pe.matmul(ps[r, 2, 0:HD], tok[:, c, 0, r], U[:, r], start=True, stop=False)
                    mm = pe.matmul(ps[r, 2, 0:HD], tok[:, c, 1, r], tok[:, c, 2, r], start=False, stop=True)
                mm.then_inc(*rw_pe.step(f"S1 {c}"))
                for h in range(2):
                    r = slice(h * HD, h * HD + HD)
                    pe.matmul(ps[r, 7, cs], U[:, r], Q[:, h, c, 1, :], start=True, stop=False)
                    pe.matmul(ps[r, 7, cs], tok[:, c, 2, r], Q[:, h, c, 3, :], start=False, stop=False)
                    mm = pe.matmul(ps[r, 7, cs], S0[r, :], AR[r, c, 1, :], start=False, stop=True)
                mm.then_inc(*rw_pe.step(f"Y {c}"))
            pe.wait_ge(*rw_act.at("Y", n))
            pe.matmul(ps[:, 3, :], pairs[:], ysb, start=True, stop=True).then_inc(*rw_pe.step("mean"))
            pe.wait_ge(*rw_act.at("Y dev^2", n))
            pe.matmul(ps[:, 4, :], pairs[:], ysq, start=True, stop=True).then_inc(*rw_pe.step("var"))
            rw_pe.close()

    @runs("scalar")
    def _(act):
        def link(ins, name=None):
            ins.then_inc(*S.step(name))
            act.wait_ge(*S.last())

        after(act, SETUP)
        S = lo_act
        act.wait_ge(*lo_pool.end())
        act.wait_ge(*lo_pe.at("z"))
        link(act.activation(loraraw[:, 1:SEQ + 1], ps[:, 0, :], ACT.Copy), "z")
        act.wait_ge(*lo_dve.at("clamped"))
        link(act.activation(tmp2[0:HD, 0, :], tmp2[0:HD, 0, :], ACT.Exp, scale=-2.0), "exp")
        lo_act.close()
        S = rw_act
        rw_act.credit(act)
        with act.Fori(0, NPAIR) as n:
            rw_act.begin(n)
            act.wait_ge(*lo_dve.end())
            for s in (rw_pe, rw_dve, rw_pool):
                act.wait_ge(*s.end(n - 1))
            for j in range(3):
                act.wait_ge(*rw_pe.at(f"proj {j}", n))
                act.activation(mixraw[:, j, 1:SEQ + 1], ps[:, j, :], ACT.Copy).then_inc(*rw_act.step(f"raw {j}"))
            act.wait_ge(*rw_dve.at("g clamped", n))
            act.activation(sg, sg, ACT.Exp, scale=-1.0).then_inc(*rw_act.step("exp g"))
            act.wait_ge(*rw_dve.at("sig clamped", n))
            act.activation(sig, sig, ACT.Exp, scale=-1.0).then_inc(*rw_act.step("exp sig"))
            act.wait_ge(*rw_dve.at("k", n))
            act.activation(tmp2[:, 0, :], rkv[:, 1, :], ACT.Square, scale=pc[:, 5:6]).then_inc(*rw_act.step("kk^2"))
            act.wait_ge(*rw_dve.at("kk clamped", n))
            link(act.activation(kk, kk, ACT.Ln, scale=2.0 ** 24))
            act.activation(kk, kk, ACT.Exp, scale=-0.5, bias=lnshift[:, 0:1]).then_inc(*rw_act.step("kk rsqrt"))
            act.wait_ge(*rw_dve.at("centred", n))
            act.activation(fac[:, 0, :], mid, ACT.Exp, scale=-DECAY).then_inc(*rw_act.step())
            act.activation(E1, gsum, ACT.Exp, scale=-DECAY).then_inc(*rw_act.step())
            act.activation(E2, gsum, ACT.Exp, scale=DECAY).then_inc(*rw_act.step())
            act.activation(E3, E3, ACT.Exp, scale=-DECAY).then_inc(*rw_act.step("decays"))
            for c in range(NT):
                act.wait_ge(*rw_pe.at(f"tok {c}", n))
                act.activation(tok[:, c, :, :].rearrange("p j t -> p (j t)"), ps[:, 0, 0:3 * P], ACT.Copy)\
                   .then_inc(*rw_act.step(f"tok {c}"))
            for h in range(2):
                act.wait_ge(*rw_pe.at(f"A {h}", n))
                act.activation(N_[:, h, :, :].rearrange("p c t -> p (c t)"), ps[:, 5 + h, :], ACT.Copy)\
                   .then_inc(*rw_act.step(f"N {h}"))
            for lv in range(1, LEVELS):
                for h in range(2):
                    act.wait_ge(*rw_pe.at(f"V {h} {lv}", n))
                    act.activation(Vs[:, h, :, :].rearrange("p c t -> p (c t)"), ps[:, 1 + 3 * h, :], ACT.Copy)\
                       .then_inc(*rw_act.step(f"V {h} {lv}"))
            for c in range(NT):
                act.wait_ge(*rw_pe.at(f"RU {c}", n))
                act.activation(RU.rearrange("p (h t) -> p h t", h=2), ps[:, 0:5:4, 0:HD], ACT.Copy).then_inc(*rw_act.step(f"RU {c}"))
                act.wait_ge(*rw_pe.at(f"U {c}", n))
                if c:
                    act.wait_ge(*rw_pe.at(f"Y {c - 1}", n))
                act.activation(U, ps[:, 1, 0:P], ACT.Copy).then_inc(*rw_act.step(f"U {c}"))
            act.wait_ge(*rw_pe.at(f"Y {NT - 1}", n))
            act.activation(ysb, ps[:, 7, :], ACT.Copy).then_inc(*rw_act.step("Y"))
            act.wait_ge(*rw_dve.at("Y dev", n))
            act.activation(ysq, ysb, ACT.Square).then_inc(*rw_act.step("Y dev^2"))
            act.wait_ge(*rw_dve.at("var eps", n))
            link(act.activation(ysq, ysq, ACT.Ln))
            act.activation(ysq, ysq, ACT.Exp, scale=-0.5).then_inc(*rw_act.step("rstd"))
            rw_act.close()

    @runs("gpsimd")
    def _(pool):
        def link(ins, name=None):
            ins.then_inc(*S.step(name))
            pool.wait_ge(*S.last())

        after(pool, SETUP)
        S = lo_pool
        pool.memset(mixraw[:, :, 0:1], 0.0).then_inc(*lo_pool.step())
        pool.memset(loraraw[:, 0:1], 0.0).then_inc(*lo_pool.step())
        pool.memset(lnshift[:], 12.0 * math.log(2.0)).then_inc(*lo_pool.step())
        for j, m in enumerate((LT, LE, LT, LE)):
            pool.tensor_copy(maskQ[:, j, :], m[:]).then_inc(*lo_pool.step())
        lo_pool.close()
        S = rw_pool
        rw_pool.credit(pool)
        with pool.Fori(0, NPAIR) as n:
            rw_pool.begin(n)
            pool.wait_ge(*lo_pool.last())
            for s in (rw_pe, rw_dve, rw_act):
                pool.wait_ge(*s.end(n - 1))
            for h in range(2):
                for t in (T_, TT_):
                    pool.tensor_tensor(t[:, h, :, :], repeat(ident[:], NT), repeat(ones[:], NT), ALU.mult)\
                        .then_inc(*rw_pool.step("identity"))
            pool.wait_ge(*rw_dve.at("k'", n))
            pool.wait_ge(*rw_act.at("decays", n))
            pool.tensor_tensor(BK[:, 1, :], rkv[:, 1, :], E2, ALU.mult).then_inc(*rw_pool.step())
            pool.tensor_tensor(AR[:, :, 1, :], rkv[:, 0, :].rearrange("p (c t) -> p c t", c=NT),
                               E1.rearrange("p (c t) -> p c t", c=NT), ALU.mult).then_inc(*rw_pool.step("factors"))
            rw_pool.close()

    @runs("vector")
    def _(dve):
        def link(ins, name=None):
            ins.then_inc(*S.step(name))
            dve.wait_ge(*S.last())

        def chunks(ap):
            return ap.rearrange("p (c t) -> p c t", c=NT)

        def sigmoid_of_exp(x):
            link(dve.tensor_scalar(x, x, 1.0, None, ALU.add))
            link(dve.reciprocal(x, x))

        after(dve, SETUP)
        S = lo_dve
        dve.wait_ge(*lo_act.at("z"))
        mu = par[:, PAR_MULORA:PAR_MULORA + 1]
        link(dve.tensor_tensor(lora, loraraw[:, 0:SEQ], loraraw[:, 1:SEQ + 1], ALU.subtract))
        link(dve.scalar_tensor_tensor(out=lora, in0=lora, scalar=mu, in1=loraraw[:, 1:SEQ + 1], op0=ALU.mult, op1=ALU.add))
        link(dve.tensor_scalar(tmp2[0:HD, 0, :], lora[0:HD, :], -CLAMP / 2, None, ALU.max), "clamped")
        dve.wait_ge(*lo_act.at("exp"))
        sigmoid_of_exp(tmp2[0:HD, 0, :])
        link(dve.tensor_scalar(lora[0:HD, :], tmp2[0:HD, 0, :], 2.0, -1.0, ALU.mult, ALU.add))
        lo_dve.close()
        S = rw_dve
        rw_dve.credit(dve)
        with dve.Fori(0, NPAIR) as n:
            rw_dve.begin(n)
            for s in (rw_pe, rw_act, rw_pool):
                dve.wait_ge(*s.end(n - 1))
            dve.wait_ge(*lo_pool.end())
            link(dve.tensor_scalar(pc[:, 0:10], par[:, bass.ds(n + PAR_PAIR, 10, 4)], 1.0, None, ALU.mult))
            dve.wait_ge(*rw_pe.at("proj 3", n))
            dve.tensor_scalar(sg, ps[:, 3, :], -CLAMP, None, ALU.max).then_inc(*rw_dve.step("g clamped"))
            dve.wait_ge(*rw_pe.at("projected", n))
            for j in range(2):
                dve.tensor_scalar(sig[:, j, :], ps[:, 4 + j, :], pc[:, 3 + j:4 + j], -CLAMP, ALU.add, ALU.max)\
                   .then_inc(*rw_dve.step("sig clamped"))
            for j in (1, 0, 2):
                dve.wait_ge(*rw_act.at(f"raw {j}", n))
                link(dve.tensor_tensor(rkv[:, j, :], mixraw[:, j, 0:SEQ], mixraw[:, j, 1:SEQ + 1], ALU.subtract))
                link(dve.scalar_tensor_tensor(out=rkv[:, j, :], in0=rkv[:, j, :], scalar=pc[:, j:j + 1],
                                              in1=mixraw[:, j, 1:SEQ + 1], op0=ALU.mult, op1=ALU.add),
                     "k" if j == 1 else None)
            dve.wait_ge(*rw_act.at("exp sig", n))
            sigmoid_of_exp(sig)
            for c in range(NT):
                cs = slice(c * P, c * P + P)
                dve.tensor_tensor_scan(gsum[:, cs], ones[:], sig[:, 0, cs], 0.0, ALU.mult, ALU.add).then_inc(*rw_dve.step())
            dve.wait_ge(*rw_dve.last())
            link(dve.tensor_copy(mid, chunks(gsum)[:, :, HD - 1]))
            link(dve.tensor_tensor(chunks(gsum), chunks(gsum), bcast(mid, P), ALU.subtract))
            link(dve.tensor_tensor(E3, gsum, sig[:, 0, :], ALU.subtract), "centred")
            dve.wait_ge(*rw_act.at("exp g", n))
            sigmoid_of_exp(sg)
            link(dve.tensor_tensor(sg, sg, ps[:, 3, :], ALU.mult))
            dve.wait_ge(*rw_pe.at("kk sums", n))
            link(dve.tensor_scalar(kk, ps[:, 6, :], 1e-24, None, ALU.max), "kk clamped")
            dve.wait_ge(*rw_act.at("kk rsqrt", n))
            link(dve.scalar_tensor_tensor(out=kk, in0=rkv[:, 1, :], scalar=pc[:, 5:6], in1=kk, op0=ALU.mult, op1=ALU.mult))
            link(dve.tensor_scalar(tmp2[:, 0, :], sig[:, 1, :], -1.0, pc[:, 6:7], ALU.add, ALU.mult))
            link(dve.scalar_tensor_tensor(out=rkv[:, 1, :], in0=tmp2[:, 0, :], scalar=1.0, in1=rkv[:, 1, :],
                                          op0=ALU.add, op1=ALU.mult), "k'")
            link(dve.scalar_tensor_tensor(out=tmp2[:, 1, :], in0=rkv[:, 0, :], scalar=pc[:, 7:8], in1=rkv[:, 1, :],
                                          op0=ALU.mult, op1=ALU.mult), "rkr")
            dve.wait_ge(*rw_act.at("decays", n))
            dve.scalar_tensor_tensor(out=AR[:, :, 0, :], in0=chunks(kk), scalar=-1.0, in1=chunks(E3),
                                     op0=ALU.mult, op1=ALU.mult).then_inc(*rw_dve.step())
            link(dve.tensor_tensor(BK[:, 0, :], kk, sig[:, 1, :], ALU.mult))
            dve.tensor_tensor(BK[:, 0, :], BK[:, 0, :], E2, ALU.mult).then_inc(*rw_dve.step("factors"))
            link(dve.tensor_tensor(fac[:, 1, 0:3], chunks(E1)[:, 0:3, P - 1], fac[:, 0, 1:4], ALU.mult))
            dve.wait_ge(*rw_pe.at("bonus sums", n))
            link(dve.tensor_tensor(bonus, ps[:, 7, :], rkv[:, 2, :], ALU.mult), "bonus")
            for h in range(2):
                for c in range(NT):
                    dve.wait_ge(*rw_pe.at(f"Q {h} {c}", n))
                    dve.tensor_tensor(Q[:, h, c, :, :].rearrange("p j t -> p (j t)"), ps[:, 1 + c, :],
                                      maskQ.rearrange("p j t -> p (j t)"), ALU.mult).then_inc(*rw_dve.step(f"Q {h} {c}"))
            dve.wait_ge(*rw_pool.at("identity", n))
            dve.wait_ge(*rw_dve.last())
            for h in range(2):
                dve.wait_ge(*rw_act.at(f"N {h}", n))
                hold(dve).then_inc(*rw_dve.step())
                dve.copy_predicated(T_[:, h, :, :], repeat(quad[:, 0, 0, :], NT), N_[:, h, :, :]).then_inc(*rw_dve.step())
                dve.copy_predicated(TT_[:, h, :, :], repeat(quad[:, 0, 2, :], NT), Q[:, h, :, 0, :])\
                   .then_inc(*rw_dve.step(f"T {h} 0"))
            for lv in range(1, LEVELS):
                for h in range(2):
                    dve.wait_ge(*rw_pe.at(f"TT {h} {lv}", n))
                    hold(dve).then_inc(*rw_dve.step())
                    if lv < LEVELS - 1:
                        dve.copy_predicated(T_[:, h, :, :], repeat(quad[:, lv, 0, :], NT), chunks(ps[:, 2 + 3 * h, :]))\
                           .then_inc(*rw_dve.step())
                    dve.copy_predicated(TT_[:, h, :, :], repeat(quad[:, lv, 2, :], NT), chunks(ps[:, 3 + 3 * h, :]))\
                       .then_inc(*rw_dve.step(f"T {h} {lv}"))
            link(dve.memset(S0, 0.0), "S0 0")
            for c in range(NT - 1):
                dve.wait_ge(*rw_pe.at(f"S1 {c}", n))
                link(dve.tensor_tensor(S1, ps[:, 2, 0:HD], S0, ALU.add))
                dve.wait_ge(*rw_pe.at(f"Y {c}", n))
                link(dve.tensor_scalar(S0, S1, fac[:, 1, c:c + 1], None, ALU.mult), f"S0 {c + 1}")
            dve.wait_ge(*rw_pe.at("mean", n))
            link(dve.scalar_tensor_tensor(out=ysb, in0=ps[:, 3, :], scalar=-1.0 / HD, in1=ysb, op0=ALU.mult, op1=ALU.add),
                 "Y dev")
            dve.wait_ge(*rw_pe.at("var", n))
            link(dve.tensor_scalar(ysq, ps[:, 4, :], 1.0 / HD, GN_EPS, ALU.mult, ALU.add), "var eps")
            dve.wait_ge(*rw_act.at("rstd", n))
            link(dve.tensor_tensor(ysb, ysb, ysq, ALU.mult))
            link(dve.tensor_scalar(ysb, ysb, pc[:, 8:9], pc[:, 9:10], ALU.mult, ALU.add))
            link(dve.tensor_tensor(ysb, ysb, bonus, ALU.add))
            dve.tensor_tensor(yT[:, bass.ds(n, 1), :].rearrange("p a t -> p (a t)"), ysb, sg, ALU.mult).then_inc(*rw_dve.step())
            rw_dve.close()

    RWKV = [(s, None) for s in (lo_pe, lo_dve, lo_act, lo_pool)] + [(s, NPAIR) for s in (rw_pe, rw_dve, rw_act, rw_pool)]

    cut[0] = 0
    qk = take(2, SEQ)
    vtok = take(NT, P)
    graw = take(SEQ)
    sgs = take(SEQ)
    WID = [SEQ - j * P for j in range(NT)]
    OFF = [sum(WID[:j]) for j in range(NT)]
    TRI = sum(WID)
    zs = take(2, TRI)
    spl = take(2, TRI)
    wt = take(2, TRI)
    osb, osq = take(SEQ), take(SEQ)
    sbg = take(1)
    wsb = W[:, 0, 0:4096].rearrange("p (k j c) -> p k j c", k=ND, j=4)
    sb_pe, sb_dve, sb_act = steps("stick_products"), steps("stick_vector"), steps("stick_scalar")
    sb_in = steps("stick_weights_in", 16)
    ZB = [[(4, 0), (5, 0), (6, 0), (6, WID[2])], [(0, 0), (1, 0), (2, 0), (2, WID[2])]]
    SPANS = [(0, 0, WID[0]), (1, OFF[1], WID[1]), (2, OFF[2], WID[2] + WID[3])]

    @runs("sync")
    def _(sp):
        after(sp, RWKV)
        sb_in.credit(sp)
        with sp.Fori(0, NPAIR) as n:
            sb_in.begin(n)
            sp.wait_ge(*sb_pe.at("projected", n - 1))
            for j in range(4):
                sp.dma_start(wsb[:, :, j, :], w_in[:, :, bass.ds(n * P + (SB0 + j * RW), P)]).then_inc(*sb_in.step("in"))
            sb_in.close()

    @runs("tensor")
    def _(pe):
        after(pe, RWKV)
        sb_pe.credit(pe)
        with pe.Fori(0, NPAIR) as n:
            sb_pe.begin(n)
            for s in (sb_dve, sb_act):
                pe.wait_ge(*s.end(n - 1))
            pe.wait_ge(*sb_in.at("in", n))
            for bank, j in ((0, 0), (1, 1), (2, 3)):
                for k in range(ND):
                    mm = pe.matmul(ps[:, bank, :], wsb[:, k, j, :], hT[:, k, :], start=(k == 0), stop=(k == ND - 1))
                mm.then_inc(*sb_pe.step(f"proj {bank}"))
            for t in range(NT):
                for k in range(ND):
                    mm = pe.matmul(ps[:, 3, t * P:(t + 1) * P], hT[:, k, t * P:(t + 1) * P], wsb[:, k, 2, :],
                                   start=(k == 0), stop=(k == ND - 1))
            mm.then_inc(*sb_pe.step("projected"))
            for h in range(2):
                r = slice(h * HD, h * HD + HD)
                pe.wait_ge(*sb_act.at("q k g v", n))
                for j in range(NT):
                    b, c = ZB[h][j]
                    pe.matmul(ps[:, b, c:c + WID[j]], qk[r, 1, j * P:(j + 1) * P], qk[r, 0, j * P:SEQ], start=True, stop=True)\
                      .then_inc(*sb_pe.step(f"z {h} {j}"))
            for h in range(2):
                pe.wait_ge(*sb_dve.at(f"sp {h}", n))
                for j in range(NT):
                    b, c = ZB[h][j]
                    mm = pe.matmul(ps[:, b, c:c + WID[j]], GE[:], spl[:, h, OFF[j]:OFF[j] + WID[j]], start=True,
                                   stop=(j == NT - 1))
                    for i in range(j + 1, NT):
                        mm = pe.matmul(ps[:, b, c + (i - j) * P:c + WID[j]], ones[:], spl[:, h, OFF[i]:OFF[i] + WID[i]],
                                       start=False, stop=(i == NT - 1))
                mm.then_inc(*sb_pe.step(f"R {h}"))
            for h in range(2):
                r = slice(h * HD, h * HD + HD)
                pe.wait_ge(*sb_dve.at(f"weights {h}", n))
                for j in range(NT):
                    mm = pe.matmul(ps[r, 3, j * P:SEQ], vtok[:, j, r], wt[:, h, OFF[j]:OFF[j] + WID[j]], start=(j == 0),
                                   stop=(j == NT - 1))
                mm.then_inc(*sb_pe.step("O"))
            pe.wait_ge(*sb_act.at("O^2", n))
            pe.matmul(ps[:, 7, :], pairs[:], osq, start=True, stop=True).then_inc(*sb_pe.step("O sums"))
            sb_pe.close()

    @runs("scalar")
    def _(act):
        after(act, RWKV)
        sb_act.credit(act)
        with act.Fori(0, NPAIR) as n:
            def link(ins, name=None):
                ins.then_inc(*sb_act.step(name))
                act.wait_ge(*sb_act.last())

            sb_act.begin(n)
            for s in (sb_pe, sb_dve):
                act.wait_ge(*s.end(n - 1))
            for bank, dst, scale in ((0, qk[:, 0, :], HD ** -0.5), (1, qk[:, 1, :], 1.0), (2, graw, 1.0)):
                act.wait_ge(*sb_pe.at(f"proj {bank}", n))
                act.activation(dst, ps[:, bank, :], ACT.Copy, scale=scale).then_inc(*sb_act.step())
            act.wait_ge(*sb_pe.at("projected", n))
            link(act.activation(vtok.rearrange("p t c -> p (t c)"), ps[:, 3, :], ACT.Copy), "q k g v")
            act.wait_ge(*sb_dve.at("g clamped", n))
            link(act.activation(sgs, sgs, ACT.Exp, scale=-1.0))
            link(act.activation(sgs, sgs, ACT.Ln, bias=1.0))
            link(act.activation(sgs, sgs, ACT.Exp, scale=-1.0), "sigmoid g")
            for h in range(2):
                act.wait_ge(*sb_pe.at(f"z {h} {NT - 1}", n))
                for b, c, w in SPANS:
                    act.activation(zs[:, h, c:c + w], ps[:, ZB[h][b][0], 0:w], ACT.Copy).then_inc(*sb_act.step())
                act.wait_ge(*sb_act.last())
                link(act.activation(wt[:, h, :], zs[:, h, :], ACT.Abs), f"zs {h}")
                link(act.activation(wt[:, h, :], wt[:, h, :], ACT.Exp, scale=-1.0))
                link(act.activation(wt[:, h, :], wt[:, h, :], ACT.Ln, bias=1.0), f"ln {h}")
            for h in range(2):
                act.wait_ge(*sb_dve.at(f"logs {h}", n))
                act.activation(wt[:, h, :], wt[:, h, :], ACT.Exp).then_inc(*sb_act.step(f"exp {h}"))
            act.wait_ge(*sb_pe.at("O", n))
            link(act.activation(osb, ps[:, 3, :], ACT.Copy))
            link(act.activation(osq, osb, ACT.Square), "O^2")
            act.wait_ge(*sb_dve.at("sums eps", n))
            link(act.activation(osq, osq, ACT.Ln))
            act.activation(osq, osq, ACT.Exp, scale=-0.5).then_inc(*sb_act.step("rstd"))
            sb_act.close()

    @runs("vector")
    def _(dve):
        after(dve, RWKV)
        sb_dve.credit(dve)
        with dve.Fori(0, NPAIR) as n:
            def link(ins, name=None):
                ins.then_inc(*sb_dve.step(name))
                dve.wait_ge(*sb_dve.last())

            sb_dve.begin(n)
            for s in (sb_pe, sb_act):
                dve.wait_ge(*s.end(n - 1))
            dve.tensor_scalar(sbg, par[:, bass.ds(n + PAR_SBG, 1)], 1.0, None, ALU.mult).then_inc(*sb_dve.step())
            dve.wait_ge(*sb_act.at("q k g v", n))
            link(dve.tensor_scalar(sgs, graw, -LNCLAMP, None, ALU.max), "g clamped")
            for h in range(2):
                dve.wait_ge(*sb_act.at(f"ln {h}", n))
                link(dve.scalar_tensor_tensor(out=spl[:, h, :], in0=zs[:, h, :], scalar=0.0, in1=wt[:, h, :],
                                              op0=ALU.max, op1=ALU.add))
                for j in range(NT):
                    d = spl[:, h, OFF[j]:OFF[j] + P]
                    dve.tensor_tensor(d, d, LT[:], ALU.mult).then_inc(*sb_dve.step(f"sp {h}"))
            dve.wait_ge(*sb_act.at("sigmoid g", n))
            dve.tensor_tensor(sgs, sgs, graw, ALU.mult).then_inc(*sb_dve.step())
            for h in range(2):
                dve.wait_ge(*sb_pe.at(f"R {h}", n))
                for b, c, w in SPANS:
                    dve.tensor_tensor(wt[:, h, c:c + w], zs[:, h, c:c + w], ps[:, ZB[h][b][0], 0:w], ALU.subtract)\
                       .then_inc(*sb_dve.step())
                dve.wait_ge(*sb_dve.last())
                for j in range(NT):
                    d = wt[:, h, OFF[j]:OFF[j] + P]
                    dve.tensor_scalar(d, d, 0.0, None, ALU.min).then_inc(*sb_dve.step(f"logs {h}"))
            for h in range(2):
                dve.wait_ge(*sb_act.at(f"exp {h}", n))
                for j in range(NT):
                    d = wt[:, h, OFF[j]:OFF[j] + P]
                    dve.tensor_tensor(d, d, LT[:], ALU.mult).then_inc(*sb_dve.step(f"weights {h}"))
            dve.wait_ge(*sb_pe.at("O sums", n))
            dve.wait_ge(*sb_act.at("O^2", n))
            link(dve.tensor_scalar(osq, ps[:, 7, :], 1.0 / HD, NORM_EPS, ALU.mult, ALU.add), "sums eps")
            dve.wait_ge(*sb_act.at("rstd", n))
            link(dve.scalar_tensor_tensor(out=osb, in0=osb, scalar=sbg, in1=osq, op0=ALU.mult, op1=ALU.mult))
            dve.tensor_tensor(yT[:, bass.ds(n + NPAIR, 1), :].rearrange("p a (i b) -> p (a i) b", b=NT),
                              osb.rearrange("p (b i) -> p i b", b=NT), sgs.rearrange("p (i b) -> p i b", b=NT), ALU.mult)\
               .then_inc(*sb_dve.step())
            sb_dve.close()

    STICK = [(s, NPAIR) for s in (sb_pe, sb_dve, sb_act)]

    cut[0] = 0
    grow = take(D)
    xsq = take(D)
    mixed = take(8, SEQ)
    fs = take(NT)
    wo1 = W[:].rearrange("p h n -> p (h n)")[:, 0:ND * D].rearrange("p (k n) -> p k n", k=ND)
    o1_pe, o1_dve, o1_act = steps("out1_products"), steps("out1_vector"), steps("out1_scalar")
    o1_in, o1_g = sem("out1_weights_in"), sem("out1_g_in")

    @runs("sync")
    def _(sp):
        after(sp, STICK)
        sp.dma_start(wo1, a["w_out"][0].rearrange("(k p) n -> p k n", p=P)).then_inc(o1_in, 16)
        sp.dma_start(grow, flat("final_g").to_broadcast([P, D])).then_inc(o1_g, 16)

    @runs("tensor")
    def _(pe):
        after(pe, STICK)
        pe.wait_ge(o1_in, 16)
        for t in range(NT):
            for h in range(2):
                for k in range(ND):
                    mm = pe.matmul(ps[:, 2 * t + h, :], yT[:, k, t * P:(t + 1) * P], wo1[:, k, 512 * h:512 * h + 512],
                                   start=(k == 0), stop=(k == ND - 1))
                mm.then_inc(*o1_pe.step(f"y {t} {h}"))
        for t in range(NT):
            pe.wait_ge(*o1_dve.at(f"x {t}"))
        for k in range(ND):
            for t in range(NT):
                mm = pe.transpose(ps[:, k, t * P:(t + 1) * P], xtok[:, t, k * P:(k + 1) * P], ident[:])
            mm.then_inc(*o1_pe.step(f"x^T {k}"))
        o1_pe.close()

    @runs("scalar")
    def _(act):
        after(act, STICK)
        for t in range(NT):
            act.wait_ge(*o1_dve.at(f"sum {t}"))
            act.wait_ge(*o1_act.last()) if t else None
            act.activation(xsq, xtok[:, t, :], ACT.Square, accum_out=fs[:, t:t + 1]).then_inc(*o1_act.step(f"ss {t}"))
            act.wait_ge(*o1_dve.at(f"eps {t}"))
            act.activation(fs[:, t:t + 1], fs[:, t:t + 1], ACT.Ln).then_inc(*o1_act.step())
            act.wait_ge(*o1_act.last())
            act.activation(fs[:, t:t + 1], fs[:, t:t + 1], ACT.Exp, scale=-0.5).then_inc(*o1_act.step(f"rstd {t}"))
        for k in range(ND):
            act.wait_ge(*o1_pe.at(f"x^T {k}"))
            act.activation(hT[:, k, :], ps[:, k, :], ACT.Copy).then_inc(*o1_act.step(f"hT {k}"))
        o1_act.close()

    @runs("vector")
    def _(dve):
        def link(ins, name=None):
            ins.then_inc(*o1_dve.step(name))
            dve.wait_ge(*o1_dve.last())

        after(dve, STICK)
        dve.wait_ge(o1_g, 16)
        for t in range(NT):
            for h in range(2):
                hs = slice(512 * h, 512 * h + 512)
                dve.wait_ge(*o1_pe.at(f"y {t} {h}"))
                link(dve.tensor_tensor(mixed[:, 2 * t + h, :], ps[:, 2 * t + h, :], gate[:, hs], ALU.mult))
                link(dve.tensor_tensor(xtok[:, t, hs], xtok[:, t, hs], mixed[:, 2 * t + h, :], ALU.add), f"sum {t}")
            dve.wait_ge(*o1_act.at(f"ss {t}"))
            link(dve.tensor_scalar(fs[:, t:t + 1], fs[:, t:t + 1], 1.0 / D, NORM_EPS, ALU.mult, ALU.add), f"eps {t}")
            dve.wait_ge(*o1_act.at(f"rstd {t}"))
            link(dve.scalar_tensor_tensor(out=xtok[:, t, :], in0=xtok[:, t, :], scalar=fs[:, t:t + 1], in1=grow,
                                          op0=ALU.mult, op1=ALU.mult), f"x {t}")
        o1_dve.close()

    OUT1 = [(s, None) for s in (o1_pe, o1_dve, o1_act)]

    cut[0] = 0
    raw = take(4, SEQ + TAPS - 1)
    cv = take(4, SEQ)
    Nn = take(NT, 4, P)
    zr, zg = take(NT, 2 * P), take(NT, 2 * P)
    ktok, vtk = take(NT, P), take(NT, 2, P)
    kkS, qkS, qkm = take(NT, P), take(NT, P), take(NT, 2, P)
    Gb = take(NT * 4, P)
    attnT = take(NT, 4, P)
    Tg = take(NT, 4, P)
    QUANT = 7
    pre = take(QUANT, NT, 32)
    pcg = take(QUANT, NT, 4)
    NLE, NGE = take(P), take(P)
    nw = take(P)
    ab = take(NT, 64)
    abt = take(NT, 64)
    alog, dtb = take(32), take(32)
    rsn = take(8)
    taps = take(TAPS, 4)
    half2 = W[:, 1, :]
    TTg = half2[:, 0:2048].rearrange("p (g b t) -> p g b t", g=NT, b=4)
    Vg = half2[:, 2048:3072].rearrange("p (s b t) -> p s b t", s=2, b=4)
    St = half2[:, 3072:3584].rearrange("p (b t) -> p b t", b=4)
    ob = half2[:, 3584:4096].rearrange("p (b t) -> p b t", b=4)
    oacc = half2[:, 4096:5120].rearrange("p (c e t) -> p c e t", c=NT, e=2)
    osqr = half2[:, 5120:6144].rearrange("p (c e t) -> p c e t", c=NT, e=2)
    ctmp = Nn.rearrange("p c b t -> p (c b t)").rearrange("p (j t) -> p j t", j=4)
    XD = [raw[:, k, 2:2 + SEQ] for k in range(4)]
    Rr, vn, vnd, qs = [Gb[:, 4 * k:4 * k + 4, :] for k in range(4)]
    wg = W[:, 0, :].rearrange("p (k n) -> p k n", k=ND)
    wab = W[:, 0, 0:512].rearrange("p (k n) -> p k n", k=ND)
    g_in = a["gdn_w_in_2"][0].rearrange("(k p) n -> p k n", p=P)
    GDN_AB = GDN_CONV + 2 * D

    ab_pe, ab_dve, ab_act, ab_pool = steps("gates_products"), steps("gates_vector"), steps("gates_scalar"), steps("gates_pool")
    gd_pe, gd_dve, gd_act, gd_pool = steps("gdn_products"), steps("gdn_vector"), steps("gdn_scalar"), steps("gdn_pool")
    ab_in, gd_in = sem("gates_in"), steps("gdn_weights_in", 16)

    def fl(ap):
        return ap.rearrange("p b t -> p (b t)")

    @runs("sync")
    def _(sp):
        after(sp, OUT1)
        sp.dma_start(wab, g_in[:, :, GDN_AB:GDN_AB + 64]).then_inc(ab_in, 16)
        sp.dma_start(alog, flat("gdn_a_log_2").to_broadcast([P, 32])).then_inc(ab_in, 16)
        sp.dma_start(dtb, flat("gdn_dt_bias_2").to_broadcast([P, 32])).then_inc(ab_in, 16)
        sp.dma_start(nw, flat("gdn_norm_w_2").to_broadcast([P, P])).then_inc(ab_in, 16)
        gd_in.credit(sp)
        sp.wait_ge(*ab_pe.at("ab"))
        with sp.Fori(0, QKH) as n:
            gd_in.begin(n)
            sp.wait_ge(*gd_pe.at("projected", n - 1))
            for dst, c0, each in ((0, 0, P), (P, D, P), (2 * P, 2 * D, 2 * P), (4 * P, GDN_CONV, 2 * P)):
                sp.dma_start(wg[:, :, dst:dst + each], g_in[:, :, bass.ds(n * each + c0, each)]).then_inc(*gd_in.step("in"))
            gd_in.close()

    @runs("tensor")
    def _(pe):
        after(pe, OUT1)
        pe.wait_ge(ab_in, 64)
        for t in range(NT):
            for k in range(ND):
                mm = pe.matmul(ps[:, 0, 64 * t:64 * t + 64], hT[:, k, t * P:(t + 1) * P], wab[:, k, :], start=(k == 0),
                               stop=(k == ND - 1))
        mm.then_inc(*ab_pe.step("ab"))
        pe.wait_ge(*ab_dve.at("g"))
        for t in range(NT):
            pe.matmul(ps[:, 1, 64 * t:64 * t + 16], LE[:], pre[:, 0, t, 0:16], start=True, stop=True)
            pe.matmul(ps[:, 1, 64 * t + 16:64 * t + 32], GE[:], pre[:, 0, t, 16:32], start=True, stop=True)
            mm = pe.matmul(ps[:, 1, 64 * t + 32:64 * t + 64], ones[:], pre[:, 0, t, :], start=True, stop=True)
        mm.then_inc(*ab_pe.step("sums"))
        ab_pe.close()
        gd_pe.credit(pe)
        with pe.Fori(0, QKH) as n:
            gd_pe.begin(n)
            for s in (gd_dve, gd_act, gd_pool):
                pe.wait_ge(*s.end(n - 1))
            pe.wait_ge(*ab_dve.end())
            pe.wait_ge(*ab_pool.end())
            pe.wait_ge(*gd_in.at("in", n))
            for j in range(4):
                for k in range(ND):
                    mm = pe.matmul(ps[:, j, :], wg[:, k, j * P:(j + 1) * P], hT[:, k, :], start=(k == 0), stop=(k == ND - 1))
                mm.then_inc(*gd_pe.step(f"proj {j}"))
            for t in range(NT):
                for k in range(ND):
                    mm = pe.matmul(ps[:, 4 + t // 2, 256 * (t % 2):256 * (t % 2) + 256], hT[:, k, t * P:(t + 1) * P],
                                   wg[:, k, 4 * P:6 * P], start=(k == 0), stop=(k == ND - 1))
            mm.then_inc(*gd_pe.step("projected"))
            pe.wait_ge(*gd_pool.at("G", n))
            pe.wait_ge(*gd_act.at("raw 1", n))
            for c in range(2):
                for d in range(2):
                    cols = ps[:, c % 2, 256 * d:256 * d + 256]
                    pe.matmul(cols, (NLE, NGE)[d], fl(Gb[:, 4 * c + 2 * d:4 * c + 2 * d + 2, :]), start=True, stop=False)
                    for e in range(2):
                        mm = pe.matmul(cols[:, P * e:P * e + P], Gb[:, 4 * c + 2 * d + e, :], (LE, GE)[d][:], start=False,
                                       stop=(e == 1))
                mm.then_inc(*gd_pe.step(f"X {c}"))
            for j in range(2):
                pe.wait_ge(*gd_act.at(f"square {j}", n))
                pe.matmul(ps[:, 6 + j, :], ones[:], ctmp[:, j, :], start=True, stop=True).then_inc(*gd_pe.step(f"norm {j}"))
            for c in range(2, NT):
                pe.wait_ge(*gd_dve.at(f"X {c - 2}", n))
                for d in range(2):
                    cols = ps[:, c % 2, 256 * d:256 * d + 256]
                    pe.matmul(cols, (NLE, NGE)[d], fl(Gb[:, 4 * c + 2 * d:4 * c + 2 * d + 2, :]), start=True, stop=False)
                    for e in range(2):
                        mm = pe.matmul(cols[:, P * e:P * e + P], Gb[:, 4 * c + 2 * d + e, :], (LE, GE)[d][:], start=False,
                                       stop=(e == 1))
                mm.then_inc(*gd_pe.step(f"X {c}"))
            pe.wait_ge(*gd_pool.at("silu 3", n))
            pe.wait_ge(*gd_dve.at("unit 1", n))
            pe.wait_ge(*gd_act.at("z raw", n))
            for c in range(NT):
                cs = slice(c * P, c * P + P)
                for e in range(2):
                    mm = pe.transpose(ps[:, 3 + c // 2, 256 * (c % 2) + P * e:256 * (c % 2) + P * e + P], cv[:, 2 + e, cs], ident[:])
            mm.then_inc(*gd_pe.step("v tokens"))
            for c in range(NT):
                cs = slice(c * P, c * P + P)
                mm = pe.transpose(ps[:, 2, cs], cv[:, 1, cs], ident[:])
            mm.then_inc(*gd_pe.step("k tokens"))
            for c in range(NT):
                cs = slice(c * P, c * P + P)
                mm = pe.matmul(ps[:, 5, cs], cv[:, 1, cs], cv[:, 1, cs], start=True, stop=True)
            mm.then_inc(*gd_pe.step("k k"))
            pe.wait_ge(*gd_dve.at("unit 0", n))
            for c in range(NT):
                cs = slice(c * P, c * P + P)
                mm = pe.matmul(ps[:, 6, cs], cv[:, 1, cs], cv[:, 0, cs], start=True, stop=True)
            mm.then_inc(*gd_pe.step("k q"))
            pe.wait_ge(*gd_act.at("tokens", n))
            for g in range(NT):
                s3 = 3 * (g % 2)
                pe.wait_ge(*gd_dve.at(f"N {g}", n))
                if g >= 2:
                    pe.wait_ge(*gd_dve.at(f"T {g - 2} 0", n))
                for b in range(4):
                    mm = pe.transpose(ps[:, s3 + 2, b * P:(b + 1) * P], Nn[:, g, b, :], ident[:])
                mm.then_inc(*gd_pe.step(f"N^T {g}"))
            for lv in range(1, LEVELS):
                for st in range(NT + 1):
                    if st < NT:
                        g, s3 = st, 3 * (st % 2)
                        pe.wait_ge(*gd_dve.at(f"T {g} {lv - 1}", n))
                        for b in range(4):
                            mm = pe.matmul(ps[:, s3, b * P:(b + 1) * P], Nn[:, g, b, :], TTg[:, g, b, :], start=True, stop=True)
                        mm.then_inc(*gd_pe.step(f"V {g} {lv}"))
                    if st:
                        g, s3 = st - 1, 3 * ((st - 1) % 2)
                        pe.wait_ge(*gd_act.at(f"V {g} {lv}", n))
                        if g >= 2:
                            pe.wait_ge(*gd_dve.at(f"T {g - 2} {lv}", n))
                        elif lv > 1:
                            pe.wait_ge(*gd_dve.at(f"T {g + 2} {lv - 1}", n))
                        else:
                            pe.wait_ge(*gd_dve.at(f"T {g + 2} 0", n))
                        if lv < LEVELS - 1:
                            for b in range(4):
                                pe.matmul(ps[:, s3 + 1, b * P:(b + 1) * P], Vg[:, g % 2, b, :], Tg[:, g, b, :], start=True, stop=True)
                        for b in range(4):
                            mm = pe.matmul(ps[:, s3 + 2, b * P:(b + 1) * P], Tg[:, g, b, :], Vg[:, g % 2, b, :], start=True, stop=True)
                        mm.then_inc(*gd_pe.step(f"T {g} {lv}"))
            for st in range(NT):
                cc = (st, NT - 1 - st)
                pe.wait_ge(*gd_dve.at(f"S {st}", n))
                if st == 0:
                    pe.wait_ge(*gd_pool.at("T beta", n))
                for d in range(2):
                    cs = slice(cc[d] * P, cc[d] * P + P)
                    mm = pe.matmul(ps[:, 0, 256 * d:256 * d + 256], cv[:, 1, cs], fl(St[:, 2 * d:2 * d + 2, :]), start=True, stop=True)
                mm.then_inc(*gd_pe.step(f"kS {st}"))
                for d in range(2):
                    cs = slice(cc[d] * P, cc[d] * P + P)
                    mm = pe.matmul(ps[:, 1, 256 * d:256 * d + 256], cv[:, 0, cs], fl(St[:, 2 * d:2 * d + 2, :]), start=True, stop=True)
                mm.then_inc(*gd_pe.step(f"qS {st}"))
                pe.wait_ge(*gd_dve.at(f"R {st}", n))
                for b in range(4):
                    mm = pe.matmul(ps[:, 2, b * P:(b + 1) * P], TTg[:, cc[b // 2], b, :], Rr[:, b, :], start=True, stop=True)
                mm.then_inc(*gd_pe.step(f"v' {st}"))
                pe.wait_ge(*gd_dve.at(f"v'd {st}", n))
                for d in range(2):
                    mm = pe.matmul(ps[:, 4, 256 * d:256 * d + 256], ktok[:, cc[d], :], fl(vnd[:, 2 * d:2 * d + 2, :]), start=True, stop=True)
                mm.then_inc(*gd_pe.step(f"dS {st}"))
                pe.wait_ge(*gd_act.at(f"v' {st}", n))
                for b in range(4):
                    mm = pe.matmul(ps[:, 3, b * P:(b + 1) * P], attnT[:, cc[b // 2], b, :], vn[:, b, :], start=True, stop=True)
                mm.then_inc(*gd_pe.step(f"o {st}"))
            pe.wait_ge(*gd_dve.at("gated", n))
            for e in range(2):
                for c in range(NT):
                    mm = pe.transpose(ps[:, 5 + e, c * P:(c + 1) * P], oacc[:, c, e, :], ident[:])
                mm.then_inc(*gd_pe.step(f"o^T {e}"))
            gd_pe.close()

    @runs("scalar")
    def _(act):
        def link(ins, name=None):
            ins.then_inc(*S.step(name))
            act.wait_ge(*S.last())

        after(act, OUT1)
        S = ab_act
        act.wait_ge(*ab_pe.at("ab"))
        link(act.activation(ab.rearrange("p t c -> p (t c)"), ps[:, 0, 0:256], ACT.Copy), "ab")
        act.wait_ge(*ab_dve.at("arguments"))
        link(act.activation(abt[:, :, 0:32], abt[:, :, 0:32], ACT.Abs))
        link(act.activation(abt, abt, ACT.Exp, scale=-1.0))
        link(act.activation(abt, abt, ACT.Ln, bias=1.0))
        link(act.activation(abt[:, :, 32:64], abt[:, :, 32:64], ACT.Exp, scale=-1.0))
        act.wait_ge(ab_in, 64)
        link(act.activation(alog, alog, ACT.Exp), "logs")
        act.wait_ge(*ab_dve.at("sums"))
        for q, src in ((3, pre[:, 3, :, :]), (5, pre[:, 5, :, :]), (6, pre[:, 6, :, :])):
            link(act.activation(src, src, ACT.Exp), "exps")
        ab_act.close()
        S = gd_act
        gd_act.credit(act)
        with act.Fori(0, QKH) as n:
            gd_act.begin(n)
            for s in (gd_pe, gd_dve, gd_pool):
                act.wait_ge(*s.end(n - 1))
            act.wait_ge(*ab_pool.end())
            for j in range(4):
                act.wait_ge(*gd_pe.at(f"proj {j}", n))
                act.activation(raw[:, j, 2:2 + SEQ], ps[:, j, :], ACT.Copy).then_inc(*gd_act.step(f"raw {j}"))
            act.wait_ge(*gd_pe.at("projected", n))
            act.activation(zr.rearrange("p t c -> p (t c)").rearrange("p (b c) -> p b c", b=2), ps[:, 4:6, :], ACT.Copy)\
               .then_inc(*gd_act.step("z raw"))
            for j in range(4):
                act.wait_ge(*gd_dve.at(f"clamped {j}", n))
                link(act.activation(ctmp[:, j, :], ctmp[:, j, :], ACT.Exp, scale=-1.0))
                link(act.activation(ctmp[:, j, :], ctmp[:, j, :], ACT.Ln, bias=1.0))
                link(act.activation(ctmp[:, j, :], ctmp[:, j, :], ACT.Exp, scale=-1.0), f"sigmoid {j}")
            for j in range(2):
                act.wait_ge(*gd_pool.at(f"silu {j}", n))
                act.activation(ctmp[:, j, :], cv[:, j, :], ACT.Square).then_inc(*gd_act.step(f"square {j}"))
            act.wait_ge(*gd_dve.at("z clamped", n))
            link(act.activation(zg, zg, ACT.Exp, scale=-1.0))
            link(act.activation(zg, zg, ACT.Ln, bias=1.0))
            link(act.activation(zg, zg, ACT.Exp, scale=-1.0), "sigmoid z")
            for j in (0, 1):
                act.wait_ge(*gd_dve.at(f"norm eps {j}", n))
                link(act.activation(ctmp[:, j, :], ctmp[:, j, :], ACT.Ln))
                act.activation(ctmp[:, j, :], ctmp[:, j, :], ACT.Exp, scale=-0.5).then_inc(*gd_act.step(f"rsqrt {j}"))
            act.wait_ge(*gd_pe.at("v tokens", n))
            act.activation(vtk.rearrange("p c e t -> p (c e t)").rearrange("p (b t) -> p b t", b=2), ps[:, 3:5, :], ACT.Copy)\
               .then_inc(*gd_act.step())
            act.wait_ge(*gd_pe.at("k k", n))
            act.activation(ktok.rearrange("p c t -> p (c t)"), ps[:, 2, :], ACT.Copy).then_inc(*gd_act.step())
            act.activation(kkS.rearrange("p c t -> p (c t)"), ps[:, 5, :], ACT.Copy).then_inc(*gd_act.step())
            act.wait_ge(*gd_pe.at("k q", n))
            act.activation(qkS.rearrange("p c t -> p (c t)"), ps[:, 6, :], ACT.Copy).then_inc(*gd_act.step("tokens"))
            for c in range(NT):
                act.wait_ge(*gd_dve.at(f"X {c}", n))
                for k in range(2):
                    buf = XD[2 * (c % 2) + k]
                    act.activation(buf, buf, ACT.Exp, scale=(1.0, -1.0)[k]).then_inc(*gd_act.step(f"D {c}"))
            for lv in range(1, LEVELS):
                for g in range(NT):
                    act.wait_ge(*gd_pe.at(f"V {g} {lv}", n))
                    if g >= 2:
                        act.wait_ge(*gd_pe.at(f"T {g - 2} {lv}", n))
                    elif lv > 1:
                        act.wait_ge(*gd_pe.at(f"T {g + 2} {lv - 1}", n))
                    act.activation(Vg[:, g % 2, :, :].rearrange("p b t -> p (b t)"), ps[:, 3 * (g % 2), :], ACT.Copy)\
                       .then_inc(*gd_act.step(f"V {g} {lv}"))
            for st in range(NT):
                cc = (st, NT - 1 - st)
                act.wait_ge(*gd_pe.at(f"qS {st}", n))
                if st:
                    act.wait_ge(*gd_dve.at(f"o {st - 1}", n))
                for b in range(4):
                    act.activation(qs[:, b, :], ps[:, 1, b * P:(b + 1) * P], ACT.Copy, scale=pcg[:, 3, cc[b // 2], b:b + 1])\
                       .then_inc(*gd_act.step(f"qS {st}"))
                act.wait_ge(*gd_pe.at(f"v' {st}", n))
                act.wait_ge(*gd_dve.at(f"v'd {st}", n))
                act.activation(fl(vn), ps[:, 2, :], ACT.Copy).then_inc(*gd_act.step(f"v' {st}"))
            act.wait_ge(*gd_dve.at(f"o {NT - 1}", n))
            act.activation(osqr, oacc, ACT.Square).then_inc(*gd_act.step("o^2"))
            act.wait_ge(*gd_dve.at("o eps", n))
            link(act.activation(rsn, rsn, ACT.Ln))
            act.activation(rsn, rsn, ACT.Exp, scale=-0.5).then_inc(*gd_act.step("o rstd"))
            gd_act.close()

    @runs("gpsimd")
    def _(pool):
        def link(ins, name=None):
            ins.then_inc(*S.step(name))
            pool.wait_ge(*S.last())

        after(pool, OUT1)
        S = ab_pool
        for c0 in (0, SEQ + 2):
            pool.memset(raw[:, :, c0:c0 + 2], 0.0).then_inc(*ab_pool.step())
        pool.tensor_scalar(NLE, LE[:], -1.0, None, ALU.mult).then_inc(*ab_pool.step())
        pool.tensor_scalar(NGE, GE[:], -1.0, None, ALU.mult).then_inc(*ab_pool.step())
        ab_pool.close()
        S = gd_pool
        gd_pool.credit(pool)
        with pool.Fori(0, QKH) as n:
            gd_pool.begin(n)
            pool.wait_ge(*ab_pool.end())
            for s in (gd_pe, gd_dve, gd_act):
                pool.wait_ge(*s.end(n - 1))
            pool.wait_ge(*gd_dve.at("columns", n))
            pool.tensor_tensor(Gb, bcast(pcg[:, 0, :, :].rearrange("p c b -> p (c b)"), P), repeat(ones[:], 16), ALU.mult)\
                .then_inc(*gd_pool.step("G"))
            for t in (Tg, TTg):
                for g in range(NT):
                    pool.tensor_tensor(t[:, g, :, :], repeat(ident[:], 4), repeat(ones[:], 4), ALU.mult)\
                        .then_inc(*gd_pool.step("identity"))
            for j in range(4):
                pool.wait_ge(*gd_act.at(f"sigmoid {j}", n))
                pool.tensor_tensor(cv[:, j, :], cv[:, j, :], ctmp[:, j, :], ALU.mult).then_inc(*gd_pool.step(f"silu {j}"))
            pool.wait_ge(*gd_act.at("sigmoid z", n))
            pool.tensor_tensor(zg, zg, zr, ALU.mult).then_inc(*gd_pool.step("silu z"))
            pool.wait_ge(*gd_act.at("tokens", n))
            for d, m in ((0, LE), (1, GE)):
                pool.tensor_tensor(qkm[:, :, d, :], qkS, repeat(m[:], NT), ALU.mult).then_inc(*gd_pool.step())
            pool.wait_ge(*gd_pool.last())
            for c in range(NT):
                pool.wait_ge(*gd_act.at(f"D {c}", n))
                for d in range(2):
                    pool.tensor_tensor(attnT[:, c, 2 * d:2 * d + 2, :], XD[2 * (c % 2)].rearrange("p (b t) -> p b t", b=4)[:, 2 * d:2 * d + 2, :],
                                       repeat(qkm[:, c, d, :], 2), ALU.mult).then_inc(*gd_pool.step(f"attention {c}"))
            for g in range(NT):
                pool.wait_ge(*gd_dve.at(f"T {g} {LEVELS - 1}", n))
                pool.tensor_tensor(TTg[:, g, :, :], TTg[:, g, :, :], bcast(pcg[:, 1, g, :], P), ALU.mult).then_inc(*gd_pool.step("T beta"))
            gd_pool.close()

    @runs("vector")
    def _(dve):
        def link(ins, name=None):
            ins.then_inc(*S.step(name))
            dve.wait_ge(*S.last())

        after(dve, OUT1)
        S = ab_dve
        dve.wait_ge(ab_in, 64)
        dve.wait_ge(*ab_act.at("ab"))
        link(dve.tensor_tensor(ab[:, :, 0:32], ab[:, :, 0:32], repeat(dtb, NT), ALU.add))
        dve.tensor_copy(abt[:, :, 0:32], ab[:, :, 0:32]).then_inc(*ab_dve.step())
        link(dve.tensor_scalar(abt[:, :, 32:64], ab[:, :, 32:64], -LNCLAMP, None, ALU.max), "arguments")
        dve.wait_ge(*ab_act.at("logs"))
        link(dve.scalar_tensor_tensor(out=pre[:, 0, :, :], in0=ab[:, :, 0:32], scalar=0.0, in1=abt[:, :, 0:32], op0=ALU.max, op1=ALU.add))
        link(dve.scalar_tensor_tensor(out=pre[:, 0, :, :], in0=pre[:, 0, :, :], scalar=-1.0, in1=repeat(alog, NT),
                                      op0=ALU.mult, op1=ALU.mult), "g")
        link(dve.tensor_copy(pre[:, 1, :, :], abt[:, :, 32:64]))
        link(dve.tensor_scalar(pre[:, 2, :, :], pre[:, 1, :, :], -1.0, None, ALU.mult))
        dve.wait_ge(*ab_pe.at("sums"))
        sums = ps[:, 1, 0:256].rearrange("p (t c) -> p t c", t=NT)
        link(dve.tensor_copy(pre[:, 3, :, :], sums[:, :, 0:32]))
        link(dve.tensor_copy(pre[:, 6, :, :], sums[:, :, 32:64]))
        link(dve.tensor_tensor(pre[:, 5, :, :], pre[:, 6, :, :], pre[:, 3, :, :], ALU.subtract), "sums")
        dve.wait_ge(*ab_act.at("exps"))
        link(dve.tensor_scalar(pre[:, 4, :, :], pre[:, 3, :, :], -1.0, None, ALU.mult))
        ab_dve.close()
        S = gd_dve
        gd_dve.credit(dve)
        with dve.Fori(0, QKH) as n:
            gd_dve.begin(n)
            for s in (gd_pe, gd_act, gd_pool):
                dve.wait_ge(*s.end(n - 1))
            src = pre.rearrange("p q t (d h) -> p (q t d) h", d=2)[:, :, bass.ds(n * 2, 2)]
            link(dve.tensor_scalar(pcg.rearrange("p q t (d e) -> p (q t d) e", d=2), src, 1.0, None, ALU.mult), "columns")
            tcol = conv[:].rearrange("p (w c) -> p w c", w=TAPS)
            for j, c0, step in ((0, 0, 1), (1, 8, 1), (2, 16, 2), (3, 17, 2)):
                dve.tensor_scalar(taps[:, :, j], tcol[:, :, bass.ds(n * step + c0, 1)].rearrange("p w c -> p (w c)"), 1.0, None, ALU.mult).then_inc(*gd_dve.step())
            dve.wait_ge(*gd_dve.last())
            for j in range(4):
                dve.wait_ge(*gd_act.at(f"raw {j}", n))
                link(dve.tensor_scalar(cv[:, j, :], raw[:, j, 0:SEQ], taps[:, 0, j:j + 1], None, ALU.mult))
                for w in range(1, TAPS):
                    link(dve.scalar_tensor_tensor(out=cv[:, j, :], in0=raw[:, j, w:w + SEQ], scalar=taps[:, w, j:j + 1],
                                                  in1=cv[:, j, :], op0=ALU.mult, op1=ALU.add), f"conv {j}" if w == TAPS - 1 else None)
                dve.tensor_scalar(ctmp[:, j, :], cv[:, j, :], -LNCLAMP, None, ALU.max).then_inc(*gd_dve.step(f"clamped {j}"))
            dve.wait_ge(*gd_act.at("z raw", n))
            dve.tensor_scalar(zg, zr, -LNCLAMP, None, ALU.max).then_inc(*gd_dve.step("z clamped"))
            for j in range(2):
                dve.wait_ge(*gd_pe.at(f"norm {j}", n))
                link(dve.tensor_scalar(ctmp[:, j, :], ps[:, 6 + j, :], NORM_EPS, None, ALU.add), f"norm eps {j}")
                dve.wait_ge(*gd_act.at(f"rsqrt {j}", n))
                link(dve.scalar_tensor_tensor(out=cv[:, j, :], in0=cv[:, j, :], scalar=(P ** -0.5, 1.0)[j], in1=ctmp[:, j, :],
                                              op0=ALU.mult, op1=ALU.mult), f"unit {j}")
            for c in range(NT):
                dve.wait_ge(*gd_pe.at(f"X {c}", n))
                if c >= 2:
                    dve.wait_ge(*gd_pool.at(f"attention {c - 2}", n))
                    dve.wait_ge(*gd_dve.last())
                dve.tensor_scalar(XD[2 * (c % 2)], ps[:, c % 2, :], 0.0, None, ALU.min).then_inc(*gd_dve.step())
                dve.tensor_scalar(XD[2 * (c % 2) + 1], ps[:, c % 2, :], 0.0, None, ALU.max).then_inc(*gd_dve.step(f"X {c}"))
                if c:
                    triangle(dve, c - 1, n)
            triangle(dve, NT - 1, n)
            dve.wait_ge(*gd_pool.at("identity", n))
            for g in range(NT):
                dve.wait_ge(*gd_pe.at(f"N^T {g}", n))
                hold(dve).then_inc(*gd_dve.step())
                dve.copy_predicated(Tg[:, g, :, :], quad[:, 0, 0:4, :], Nn[:, g, :, :]).then_inc(*gd_dve.step())
                dve.copy_predicated(TTg[:, g, :, :], quad[:, 0, 2:6, :], ps[:, 3 * (g % 2) + 2, :].rearrange("p (b t) -> p b t", b=4))\
                   .then_inc(*gd_dve.step(f"T {g} 0"))
            for lv in range(1, LEVELS):
                for g in range(NT):
                    dve.wait_ge(*gd_pe.at(f"T {g} {lv}", n))
                    hold(dve).then_inc(*gd_dve.step())
                    if lv < LEVELS - 1:
                        dve.copy_predicated(Tg[:, g, :, :], quad[:, lv, 0:4, :], ps[:, 3 * (g % 2) + 1, :].rearrange("p (b t) -> p b t", b=4))\
                           .then_inc(*gd_dve.step())
                    dve.copy_predicated(TTg[:, g, :, :], quad[:, lv, 2:6, :], ps[:, 3 * (g % 2) + 2, :].rearrange("p (b t) -> p b t", b=4))\
                       .then_inc(*gd_dve.step(f"T {g} {lv}"))
            link(dve.memset(St, 0.0), "S 0")
            for st in range(NT):
                cc = (st, NT - 1 - st)
                dve.wait_ge(*gd_pe.at(f"kS {st}", n))
                for b in range(4):
                    dve.scalar_tensor_tensor(out=Rr[:, b, :], in0=ps[:, 0, b * P:(b + 1) * P], scalar=pcg[:, 4, cc[b // 2], b:b + 1],
                                             in1=vtk[:, cc[b // 2], b % 2, :], op0=ALU.mult, op1=ALU.add).then_inc(*gd_dve.step(f"R {st}"))
                dve.wait_ge(*gd_pe.at(f"v' {st}", n))
                for d in range(2):
                    dve.tensor_tensor(vnd[:, 2 * d:2 * d + 2, :], ps[:, 2, 256 * d:256 * d + 256].rearrange("p (e t) -> p e t", e=2),
                                      bcast(pcg[:, 5, cc[d], 2 * d:2 * d + 2], P), ALU.mult).then_inc(*gd_dve.step(f"v'd {st}"))
                dve.wait_ge(*gd_pe.at(f"dS {st}", n))
                dve.wait_ge(*gd_pe.at(f"qS {st}", n))
                for b in range(4):
                    dve.scalar_tensor_tensor(out=St[:, b, :], in0=St[:, b, :], scalar=pcg[:, 6, cc[b // 2], b:b + 1],
                                             in1=ps[:, 4, b * P:(b + 1) * P], op0=ALU.mult, op1=ALU.add).then_inc(*gd_dve.step(f"S {st + 1}"))
                dve.wait_ge(*gd_pe.at(f"o {st}", n))
                dve.wait_ge(*gd_act.at(f"qS {st}", n))
                dve.wait_ge(*gd_dve.last())
                for d in range(2):
                    o, pso, q = oacc[:, cc[d], :, :], ps[:, 3, 256 * d:256 * d + 256].rearrange("p (e t) -> p e t", e=2), qs[:, 2 * d:2 * d + 2, :]
                    if st < NT // 2:
                        dve.tensor_tensor(o, pso, q, ALU.add).then_inc(*gd_dve.step(f"o {st}"))
                    else:
                        link(dve.tensor_tensor(ob[:, 2 * d:2 * d + 2, :], pso, q, ALU.add))
                        dve.tensor_tensor(o, o, ob[:, 2 * d:2 * d + 2, :], ALU.add).then_inc(*gd_dve.step(f"o {st}"))
            dve.wait_ge(*gd_act.at("o^2", n))
            link(dve.tensor_reduce(rsn, osqr.rearrange("p c e t -> p (c e) t"), X_AXIS, ALU.add))
            link(dve.tensor_scalar(rsn, rsn, 1.0 / P, NORM_EPS, ALU.mult, ALU.add), "o eps")
            flat8 = oacc.rearrange("p c e t -> p (c e) t")
            dve.wait_ge(*gd_act.at("o rstd", n))
            link(dve.tensor_tensor(flat8, flat8, bcast(rsn, P), ALU.mult))
            link(dve.tensor_tensor(flat8, flat8, repeat(nw, 8), ALU.mult))
            dve.wait_ge(*gd_pool.at("silu z", n))
            link(dve.tensor_tensor(flat8, flat8, zg.rearrange("p c (e t) -> p (c e) t", e=2), ALU.mult), "gated")
            for e in range(2):
                dve.wait_ge(*gd_pe.at(f"o^T {e}", n))
                dve.tensor_scalar(yT[:, bass.ds(n * 2 + e, 1), :].rearrange("p a t -> p (a t)"), ps[:, 5 + e, :], 1.0, None, ALU.mult)\
                   .then_inc(*gd_dve.step())
            gd_dve.close()

    def triangle(dve, c, n):
        dve.wait_ge(*gd_act.at("tokens", n))
        dve.wait_ge(*gd_act.at(f"D {c}", n))
        buf = XD[2 * (c % 2) + 1].rearrange("p (b t) -> p b t", b=4)
        dve.tensor_tensor(buf, buf, repeat(kkS[:, c, :], 4), ALU.mult).then_inc(*gd_dve.step())
        dve.wait_ge(*gd_dve.last())
        dve.tensor_tensor(Nn[:, c, :, :], buf, bcast(pcg[:, 2, c, :], P), ALU.mult).then_inc(*gd_dve.step(f"N {c}"))

    GDN = [(s, None) for s in (ab_pe, ab_dve, ab_act, ab_pool)] + [(s, QKH) for s in (gd_pe, gd_dve, gd_act, gd_pool)]

    cut[0] = 0
    lng, lnb = take(2, D), take(2, D)
    stats = take(NT, 2, 6)
    mv = take(NT, 2)
    lrs = take(NT)
    wr = take(ND, NGRP + NEXP)
    rb = take(NGRP + NEXP)
    lg = take(NT, NGRP + NEXP)
    comb = take(NT, NEXP)
    desc = take(EPG)
    ohg, gex, geq = take(NT, NGRP), take(NT, NGRP), take(NT, NGRP)
    prod = take(NT * NGRP, EPG)
    e8, e8b, eq8, oh1, oh2 = [take(NT, EPG) for _ in range(5)]
    gmax, gsum4, v1, v2, dd, wa, wb = [take(NT) for _ in range(7)]
    hsig = take(2, SEQ)
    hid = take(2, 2, SEQ)
    ccol = take(2, NT)
    xq = take(4, 512)
    ptok = take(NT, PLE)
    pT = take(2, SEQ)
    sgate = take(2, D)
    res = take(2, D)
    Wall = W[:].rearrange("p h n -> p (h n)")
    ring = [Wall[:, 4096 * s:4096 * s + 4096].rearrange("p (k n) -> p k n", k=4) for s in range(3)]
    w_out2 = a["gdn_w_out_2"][0].rearrange("(k p) n -> p k n", p=P)
    o2_pe, o2_dve, o2_act, o2_pool = steps("out2_products"), steps("out2_vector"), steps("out2_scalar"), steps("out2_pool")
    o2_in = [sem(f"out2_weights_in{s}") for s in range(3)]
    ln_in, rt_in = sem("layernorm_in"), sem("router_in")

    def layernorm(dve, act_steps, S, t, which, name):
        def link(ins, n=None):
            ins.then_inc(*S.step(n))
            dve.wait_ge(*S.last())
        for h in range(2):
            dve.bn_stats(stats[:, t, h, :], xtok[:, t, 512 * h:512 * h + 512]).then_inc(*S.step())
        dve.wait_ge(*S.last())
        link(dve.bn_aggr(mv[:, t, :], stats[:, t, :, :]))
        link(dve.tensor_scalar(lrs[:, t:t + 1], mv[:, t, 1:2], LN_EPS, None, ALU.add), f"{name} eps {t}")
        dve.wait_ge(*act_steps.at(f"{name} rstd {t}"))
        link(dve.tensor_scalar(xtok[:, t, :], xtok[:, t, :], mv[:, t, 0:1], lrs[:, t:t + 1], ALU.subtract, ALU.mult))
        link(dve.tensor_tensor(xtok[:, t, :], xtok[:, t, :], lng[:, which, :], ALU.mult))
        link(dve.tensor_tensor(xtok[:, t, :], xtok[:, t, :], lnb[:, which, :], ALU.add), f"{name} {t}")

    def rsqrt_of(act, dve_steps, S, t, name):
        act.wait_ge(*dve_steps.at(f"{name} eps {t}"))
        act.activation(lrs[:, t:t + 1], lrs[:, t:t + 1], ACT.Ln).then_inc(*S.step())
        act.wait_ge(*S.last())
        act.activation(lrs[:, t:t + 1], lrs[:, t:t + 1], ACT.Exp, scale=-0.5).then_inc(*S.step(f"{name} rstd {t}"))

    @runs("sync")
    def _(sp):
        after(sp, GDN)
        for c in range(4):
            if c == 3:
                sp.wait_ge(*o2_pe.at("y 0"))
            sp.dma_start(ring[c % 3], w_out2[:, 4 * c:4 * c + 4, :]).then_inc(o2_in[c % 3], 16)
        for w in range(2):
            for dst, name in ((lng, "ln_g_2"), (lnb, "ln_b_2")):
                sp.dma_start(dst[:, w, :], flat(name)[:, w * D:(w + 1) * D].to_broadcast([P, D])).then_inc(ln_in, 16)
        for dst, name, c0, n in ((wr, "moe_w_group_2", 0, NGRP), (wr, "moe_w_router_2", NGRP, NEXP)):
            sp.dma_start(dst[:, :, c0:c0 + n], a[name][0].rearrange("(k p) n -> p k n", p=P)).then_inc(rt_in, 16)
        for name, c0, n in (("moe_b_group_2", 0, NGRP), ("moe_b_router_2", NGRP, NEXP)):
            sp.dma_start(rb[:, c0:c0 + n], flat(name).to_broadcast([P, n])).then_inc(rt_in, 16)
        sp.dma_start(ptok, a["p_2"][0, 0].rearrange("(t p) c -> p t c", p=P)).then_inc(rt_in, 16)

    @runs("tensor")
    def _(pe):
        after(pe, GDN)
        for c in range(4):
            pe.wait_ge(o2_in[c % 3], 16 * (c // 3 + 1))
            for t in range(NT):
                for h in range(2):
                    for k in range(4):
                        mm = pe.matmul(ps[:, 2 * t + h, :], yT[:, 4 * c + k, t * P:(t + 1) * P],
                                       ring[c % 3][:, k, 512 * h:512 * h + 512], start=(c == 0 and k == 0),
                                       stop=(c == 3 and k == 3))
                if c == 3:
                    mm.then_inc(*o2_pe.step(f"h {t}"))
            if c < 3:
                mm.then_inc(*o2_pe.step(f"y {c}"))
        for t in range(NT):
            pe.wait_ge(*o2_dve.at(f"x2 {t}"))
        for k in range(ND):
            for t in range(NT):
                mm = pe.transpose(ps[:, k, t * P:(t + 1) * P], xtok[:, t, k * P:(k + 1) * P], ident[:])
            mm.then_inc(*o2_pe.step(f"x^T {k}"))
        pe.wait_ge(*o2_act.at(f"hT {ND - 1}"))
        pe.wait_ge(rt_in, 80)
        NL = NGRP + NEXP
        for t in range(NT):
            for k in range(ND):
                mm = pe.matmul(ps[:, 0, NL * t:NL * t + NL], hT[:, k, t * P:(t + 1) * P], wr[:, k, :], start=(k == 0), stop=(k == ND - 1))
        mm.then_inc(*o2_pe.step("logits"))
        for k in range(2):
            for t in range(NT):
                mm = pe.transpose(ps[:, 1 + k, t * P:(t + 1) * P], ptok[:, t, k * P:(k + 1) * P], ident[:])
        mm.then_inc(*o2_pe.step("p^T"))
        o2_pe.close()

    @runs("scalar")
    def _(act):
        after(act, GDN)
        for t in range(NT):
            rsqrt_of(act, o2_dve, o2_act, t, "x2")
        for k in range(ND):
            act.wait_ge(*o2_pe.at(f"x^T {k}"))
            act.activation(hT[:, k, :], ps[:, k, :], ACT.Copy).then_inc(*o2_act.step(f"hT {k}"))
        act.wait_ge(*o2_pe.at("p^T"))
        act.activation(pT, ps[:, 1:3, :], ACT.Copy).then_inc(*o2_act.step())
        act.wait_ge(*o2_dve.at("shifted groups"))
        act.activation(gex, gex, ACT.Exp).then_inc(*o2_act.step("exp groups"))
        act.wait_ge(*o2_dve.at("v2 - v1"))
        act.activation(dd, dd, ACT.Exp).then_inc(*o2_act.step("exp experts"))
        o2_act.close()

    @runs("gpsimd")
    def _(pool):
        after(pool, GDN)
        for j in range(EPG):
            pool.memset(desc[:, j:j + 1], float(EPG - j)).then_inc(*o2_pool.step())
        o2_pool.close()

    @runs("vector")
    def _(dve):
        def link(ins, name=None):
            ins.then_inc(*o2_dve.step(name))
            dve.wait_ge(*o2_dve.last())

        def first_max(onehot, x, m, eq, n):
            link(dve.tensor_reduce(m, x, X_AXIS, ALU.max))
            link(dve.tensor_tensor(eq, x, bcast(m, n), ALU.is_equal))
            link(dve.tensor_tensor(eq, eq, repeat(desc[:, 0:n], NT), ALU.mult))
            link(dve.tensor_reduce(wa, eq, X_AXIS, ALU.max))
            link(dve.tensor_tensor(onehot, eq, bcast(wa, n), ALU.is_equal))

        after(dve, GDN)
        dve.wait_ge(ln_in, 64)
        for t in range(NT):
            dve.wait_ge(*o2_pe.at(f"h {t}"))
            for h in range(2):
                hs = slice(512 * h, 512 * h + 512)
                dve.scalar_tensor_tensor(out=xtok[:, t, hs], in0=xtok[:, t, hs], scalar=ALPHA, in1=ps[:, 2 * t + h, :],
                                         op0=ALU.mult, op1=ALU.add).then_inc(*o2_dve.step())
            dve.wait_ge(*o2_dve.last())
            layernorm(dve, o2_act, o2_dve, t, 0, "x2")
        dve.wait_ge(*o2_pe.at("logits"))
        dve.wait_ge(rt_in, 80)
        dve.wait_ge(*o2_pool.end())
        link(dve.tensor_tensor(lg, ps[:, 0, 0:NT * (NGRP + NEXP)].rearrange("p (t c) -> p t c", t=NT), repeat(rb, NT), ALU.add))
        gl, el = lg[:, :, 0:NGRP], lg[:, :, NGRP:NGRP + NEXP]
        first_max(ohg, gl, gmax, geq, NGRP)
        link(dve.tensor_tensor(gex, gl, bcast(gmax, NGRP), ALU.subtract), "shifted groups")
        for t in range(NT):
            dve.tensor_tensor(prod[:, NGRP * t:NGRP * t + NGRP, :], el[:, t, :].rearrange("p (g j) -> p g j", g=NGRP),
                              bcast(ohg[:, t, :], EPG), ALU.mult).then_inc(*o2_dve.step())
        dve.wait_ge(*o2_dve.last())
        link(dve.tensor_reduce(e8, prod.rearrange("p (t g) j -> p t j g", t=NT), X_AXIS, ALU.add))
        first_max(oh1, e8, v1, eq8, EPG)
        link(dve.scalar_tensor_tensor(out=e8b, in0=oh1, scalar=-1e30, in1=e8, op0=ALU.mult, op1=ALU.add))
        first_max(oh2, e8b, v2, eq8, EPG)
        link(dve.tensor_tensor(dd, v2, v1, ALU.subtract), "v2 - v1")
        dve.wait_ge(*o2_act.at("exp groups"))
        link(dve.tensor_reduce(gsum4, gex, X_AXIS, ALU.add))
        dve.wait_ge(*o2_act.at("exp experts"))
        link(dve.tensor_scalar(wb, dd, 1.0, None, ALU.add))
        link(dve.tensor_tensor(wb, wb, gsum4, ALU.mult))
        link(dve.reciprocal(wa, wb))
        link(dve.tensor_tensor(wb, wa, dd, ALU.mult))
        link(dve.tensor_tensor(oh1, oh1, bcast(wa, EPG), ALU.mult))
        link(dve.tensor_tensor(oh2, oh2, bcast(wb, EPG), ALU.mult))
        link(dve.tensor_tensor(oh1, oh1, oh2, ALU.add))
        for t in range(NT):
            dve.tensor_tensor(comb[:, t, :].rearrange("p (g j) -> p g j", g=NGRP), bcast(ohg[:, t, :], EPG),
                              repeat(oh1[:, t, :], NGRP), ALU.mult).then_inc(*o2_dve.step())
        for t in range(NT):
            if t == 0:
                dve.wait_ge(*o2_pe.at(f"x^T {ND - 1}"))
            dve.tensor_scalar(xtok[:, t, :], xtok[:, t, :], ALPHA, None, ALU.mult).then_inc(*o2_dve.step())
        o2_dve.close()

    OUT2 = [(s, None) for s in (o2_pe, o2_dve, o2_act, o2_pool)]

    NIT = NEXP // 2
    KW = ND * HID
    mo_pe, mo_dve, mo_act = steps("experts_products"), steps("experts_vector"), steps("experts_scalar")
    mo_in = [steps(f"experts_weights_in{b}", 16) for b in range(2)]

    def wview(b, j):
        v = W[:, b, KW * j:KW * j + KW]
        return v.rearrange("p (k n) -> p k n", k=ND) if j < 2 else v.rearrange("p (k n) -> p k n", k=2)

    def expert_rows(name, i, b):
        return a[name][0].rearrange("g e (k p) n -> (g e) p k n", p=P)[bass.ds(2 * i + b, 1)].rearrange("a p k n -> p (a k) n")

    def before(i, b):
        return (i, 0) if b else (i - 1, 1)

    @runs("sync")
    def _(sp):
        after(sp, OUT2)
        for b in range(2):
            mo_in[b].credit(sp)
        with sp.Fori(0, NIT) as i:
            for b in range(2):
                mo_in[b].begin(i)
                sp.wait_ge(*mo_pe.at(f"up {b}", i - 1))
                for j, name in enumerate(("moe_w_gate_2", "moe_w_up_2")):
                    sp.dma_start(wview(b, j), expert_rows(name, i, b)).then_inc(*mo_in[b].step("in"))
                sp.wait_ge(*mo_pe.at(f"down {b}", i - 1))
                sp.dma_start(wview(b, 2), expert_rows("moe_w_down_2", i, b)).then_inc(*mo_in[b].step("all"))
                mo_in[b].close()

    @runs("tensor")
    def _(pe):
        after(pe, OUT2)
        mo_pe.credit(pe)
        with pe.Fori(0, NIT) as i:
            mo_pe.begin(i)
            for b in range(2):
                pi, pb = before(i, b)
                pe.wait_ge(*mo_in[b].at("all", i))
                pe.wait_ge(*mo_dve.at(f"hidden {pb}", pi))
                for j in range(2):
                    for f in range(2):
                        for k in range(ND):
                            mm = pe.matmul(ps[:, 2 * j + f, :], wview(b, j)[:, k, f * P:(f + 1) * P], hT[:, k, :], start=(k == 0),
                                           stop=(k == ND - 1))
                    mm.then_inc(*mo_pe.step(("gate", "up")[j] + f" {b}"))
                pe.wait_ge(*mo_dve.at(f"hidden {b}", i))
                for t in range(NT):
                    if t >= 2:
                        pe.wait_ge(*mo_dve.at(f"add {b} {t - 2}", i))
                    else:
                        pe.wait_ge(*mo_dve.at(f"add {pb} {t + 2}", pi))
                    for h in range(2):
                        for f in range(2):
                            mm = pe.matmul(ps[:, 4 + 2 * (t % 2) + h, :], hid[:, b, f, t * P:(t + 1) * P],
                                           wview(b, 2)[:, f, 512 * h:512 * h + 512], start=(f == 0), stop=(f == 1))
                    mm.then_inc(*mo_pe.step(f"down {b} {t}" if t < NT - 1 else f"down {b}"))
            mo_pe.close()

    @runs("scalar")
    def _(act):
        after(act, OUT2)
        mo_act.credit(act)
        with act.Fori(0, NIT) as i:
            def link(ins, name=None):
                ins.then_inc(*mo_act.step(name))
                act.wait_ge(*mo_act.last())

            mo_act.begin(i)
            for b in range(2):
                act.wait_ge(*mo_dve.at(f"clamped {b}", i))
                link(act.activation(hsig, hsig, ACT.Exp, scale=-1.0))
                link(act.activation(hsig, hsig, ACT.Ln, bias=1.0))
                link(act.activation(hsig, hsig, ACT.Exp, scale=-1.0), f"sigmoid {b}")
            mo_act.close()

    @runs("vector")
    def _(dve):
        after(dve, OUT2)
        mo_dve.credit(dve)
        with dve.Fori(0, NIT) as i:
            def link(ins, name=None):
                ins.then_inc(*mo_dve.step(name))
                dve.wait_ge(*mo_dve.last())

            mo_dve.begin(i)
            for b in range(2):
                pi, pb = before(i, b)
                dve.wait_ge(*mo_pe.at(f"gate {b}", i))
                dve.tensor_scalar(ccol[:, b, :], comb[:, :, bass.ds(2 * i + b, 1)].rearrange("p t a -> p (t a)"), 1.0, None, ALU.mult)\
                    .then_inc(*mo_dve.step())
                dve.wait_ge(*mo_dve.last())
                dve.tensor_scalar(hsig, ps[:, 0:2, :], -LNCLAMP, None, ALU.max).then_inc(*mo_dve.step(f"clamped {b}"))
                dve.wait_ge(*mo_act.at(f"sigmoid {b}", i))
                link(dve.tensor_tensor(hsig, hsig, ps[:, 0:2, :], ALU.mult))
                dve.wait_ge(*mo_pe.at(f"up {b}", i))
                dve.wait_ge(*mo_pe.at(f"down {b}", i - 1))
                link(dve.tensor_tensor(hid[:, b, :, :], hsig, ps[:, 2:4, :], ALU.mult), f"hidden {b}")
                for t in range(NT):
                    dve.wait_ge(*mo_pe.at(f"down {b} {t}" if t < NT - 1 else f"down {b}", i))
                    for h in range(2):
                        x = xtok[:, t, 512 * h:512 * h + 512]
                        dve.scalar_tensor_tensor(out=x, in0=ps[:, 4 + 2 * (t % 2) + h, :], scalar=ccol[:, b, t:t + 1], in1=x,
                                                 op0=ALU.mult, op1=ALU.add).then_inc(*mo_dve.step(f"add {b} {t}"))
            mo_dve.close()

    MOE = [(mo_pe, NIT), (mo_dve, NIT), (mo_act, NIT)]

    wpg = Wall[:, 0:ND * D].rearrange("p (k n) -> p k n", k=ND)
    wpp = Wall[:, ND * D:ND * D + 2 * D].rearrange("p (k n) -> p k n", k=2)
    fin_pe, fin_dve, fin_act = steps("last_products"), steps("last_vector"), steps("last_scalar")
    fin_in = sem("last_weights_in")

    @runs("sync")
    def _(sp):
        after(sp, MOE)
        sp.dma_start(wpg, a["pe_w_gate_2"][0].rearrange("(k p) n -> p k n", p=P)).then_inc(fin_in, 16)
        sp.dma_start(wpp, a["pe_w_proj_2"][0].rearrange("(k p) n -> p k n", p=P)).then_inc(fin_in, 16)
        for t in range(NT):
            sp.wait_ge(*fin_dve.at(f"out {t}"))
            sp.dma_start(out[0, t * P:(t + 1) * P, :], xtok[:, t, :]).then_inc(stores, 16)
        sp.wait_ge(stores, 16 * NT)

    @runs("tensor")
    def _(pe):
        after(pe, MOE)
        for t in range(NT):
            pe.wait_ge(*fin_dve.at(f"x3 {t}"))
        for k in range(ND):
            for t in range(NT):
                mm = pe.transpose(ps[:, k, t * P:(t + 1) * P], xtok[:, t, k * P:(k + 1) * P], ident[:])
            mm.then_inc(*fin_pe.step(f"x^T {k}"))
        pe.wait_ge(*fin_act.at(f"hT {ND - 1}"))
        pe.wait_ge(fin_in, 32)
        for t in range(NT):
            b0 = 4 * (t % 2)
            if t >= 2:
                pe.wait_ge(*fin_dve.at(f"out {t - 2}"))
            for h in range(2):
                for k in range(ND):
                    mm = pe.matmul(ps[:, b0 + h, :], hT[:, k, t * P:(t + 1) * P], wpg[:, k, 512 * h:512 * h + 512], start=(k == 0),
                                   stop=(k == ND - 1))
            mm.then_inc(*fin_pe.step(f"gate {t}"))
            for h in range(2):
                for k in range(2):
                    mm = pe.matmul(ps[:, b0 + 2 + h, :], pT[:, k, t * P:(t + 1) * P], wpp[:, k, 512 * h:512 * h + 512], start=(k == 0),
                                   stop=(k == 1))
            mm.then_inc(*fin_pe.step(f"proj {t}"))
        fin_pe.close()

    @runs("scalar")
    def _(act):
        def link(ins, name=None):
            ins.then_inc(*fin_act.step(name))
            act.wait_ge(*fin_act.last())

        after(act, MOE)
        for t in range(NT):
            rsqrt_of(act, fin_dve, fin_act, t, "x3")
        for k in range(ND):
            act.wait_ge(*fin_pe.at(f"x^T {k}"))
            act.activation(hT[:, k, :], ps[:, k, :], ACT.Copy).then_inc(*fin_act.step(f"hT {k}"))
        for t in range(NT):
            act.wait_ge(*fin_dve.at(f"clamped {t}"))
            s = sgate[:, t % 2, :]
            link(act.activation(s, s, ACT.Exp, scale=-1.0))
            link(act.activation(s, s, ACT.Ln, bias=1.0))
            link(act.activation(s, s, ACT.Exp, scale=-1.0), f"sigmoid {t}")
        fin_act.close()

    @runs("vector")
    def _(dve):
        def link(ins, name=None):
            ins.then_inc(*fin_dve.step(name))
            dve.wait_ge(*fin_dve.last())

        after(dve, MOE)
        for t in range(NT):
            layernorm(dve, fin_act, fin_dve, t, 1, "x3")
        for t in range(NT):
            b0 = 4 * (t % 2)
            s = sgate[:, t % 2, :]
            dve.wait_ge(*fin_pe.at(f"gate {t}"))
            link(dve.tensor_scalar(s.rearrange("p (h c) -> p h c", h=2), ps[:, b0:b0 + 2, :], -LNCLAMP, None, ALU.max), f"clamped {t}")
            dve.wait_ge(*fin_act.at(f"sigmoid {t}"))
            dve.wait_ge(*fin_pe.at(f"proj {t}"))
            link(dve.tensor_tensor(s.rearrange("p (h c) -> p h c", h=2), s.rearrange("p (h c) -> p h c", h=2), ps[:, b0 + 2:b0 + 4, :], ALU.mult))
            link(dve.tensor_tensor(xtok[:, t, :], xtok[:, t, :], s, ALU.add), f"out {t}")
        fin_dve.close()

    block = ctx.enter_context(nc.Block())

    @block.sync
    def _(sp):
        for part in progs["sync"]:
            part(sp)

    @block.tensor
    def _(pe):
        for part in progs["tensor"]:
            part(pe)

    @block.vector
    def _(dve):
        for part in progs["vector"]:
            part(dve)

    @block.scalar
    def _(act):
        for part in progs["scalar"]:
            part(act)

    @block.gpsimd
    def _(pool):
        for part in progs["gpsimd"]:
            part(pool)

    ctx.close()


def compose(nc, names, shapes, dtypes):
    args = {n: nc.dram_tensor(f"in_{n}_dram", s, d, kind="ExternalInput").ap() for n, s, d in zip(names, shapes, dtypes)}
    return args, nc.dram_tensor("out_0_dram", (1, SEQ, D), F32, kind="ExternalOutput").ap()


_INS = ["x", "c", "norm_g", "ada_w", "ada_b", "w_in", "w_out", "tshift_mu", "decay_w0", "decay_w2", "iclr_a0", "iclr_a2",
        "k_k", "k_a", "r_k", "rwkv_ln_w", "rwkv_ln_b", "sb_norm_g", "final_g", "p_2", "gdn_w_in_2", "gdn_conv_w_2",
        "gdn_a_log_2", "gdn_dt_bias_2", "gdn_norm_w_2", "gdn_w_out_2", "ln_g_2", "ln_b_2", "moe_w_group_2",
        "moe_b_group_2", "moe_w_router_2", "moe_b_router_2", "moe_w_gate_2", "moe_w_up_2", "moe_w_down_2",
        "pe_w_gate_2", "pe_w_proj_2"]


def kernel(**inputs):
    import numpy as _np
    import concourse.bacc as _bacc
    from concourse import mybir as _mybir
    from concourse.bass_utils import run_bass_kernel_spmd as _run

    arrays = {f"in_{n}_dram": _np.ascontiguousarray(inputs[n]) for n in _INS}
    shapes = [arrays[f"in_{n}_dram"].shape for n in _INS]
    dtypes = [_mybir.dt.from_np(arrays[f"in_{n}_dram"].dtype) for n in _INS]
    book = {}
    for _ in range(2):
        nc = _bacc.Bacc("TRN2", target_bir_lowering=False, num_devices=1)
        args, out = compose(nc, _INS, shapes, dtypes)
        build(nc, args, out, book)
    r = _run(nc, [arrays], core_ids=[0])
    return r.results[0]["out_0_dram"]
```

```python
from contextlib import ExitStack
import math

import numpy as np
import concourse.bass as bass
from concourse import mybir

F32 = mybir.dt.float32
U8 = mybir.dt.uint8
U32 = mybir.dt.uint32
I32 = mybir.dt.int32
ALU = mybir.AluOpType
ACT = mybir.ActivationFunctionType
X_AXIS = mybir.AxisListType.X

P = 128
SEQ, D = 512, 1024
NT = SEQ // P
ND = D // P
HD = 64
RW = D // 2
NPAIR = RW // P
SHIFT = 3 * RW + 2 * HD
SB0 = SHIFT + RW
NORM_EPS, GN_EPS, LN_EPS = 1e-6, 64e-5, 1e-5
DECAY = math.exp(-0.5)
QKH, VH = 8, 16
TAPS = 5
GDN_CONV = 4096
ALPHA = 2.0 ** 0.25
NEXP, NGRP, EPG, HID = 32, 4, 8, 256
PLE = 256
LEVELS = 7
CLAMP = 80.0
LNCLAMP = 44.0


class Steps:

    def __init__(self, book, sem, name, unit=1):
        self.names = book.setdefault(name, {})
        self.sem, self.unit, self.k, self.i = sem, unit, 0, None
        self.per = self.names.get("per iteration")

    def step(self, name=None):
        self.k += 1
        if name is not None:
            self.names[name] = self.k
        return self.sem, self.unit

    def value(self, k, i):
        k = k * self.unit
        return k if i is None else (i + 1) * (self.unit * (self.per or 1)) + k

    def at(self, name, i=None):
        return self.sem, self.value(self.names.get(name, 1), i)

    def last(self):
        return self.sem, self.value(self.k, self.i)

    def end(self, i=None):
        if i is None:
            return self.sem, self.unit * self.names.get("steps", 1)
        return self.sem, (i + 2) * (self.unit * (self.per or 1))

    def final(self, n):
        return self.end(n - 1)

    def credit(self, eng):
        eng.nop().then_inc(self.sem, self.unit * (self.per or 1))

    def begin(self, i):
        self.k, self.i = 0, i

    def close(self):
        self.names["per iteration" if self.i is not None else "steps"] = self.k


def bcast(ap, n):
    return ap.unsqueeze(2).to_broadcast([ap.shape[0], ap.shape[1], n])


def repeat(ap, n):
    return ap.unsqueeze(1).to_broadcast([ap.shape[0], n, ap.shape[1]])


def build(nc, a, out, book):
    ctx = ExitStack()

    def sb(name, shape, dt=F32):
        return ctx.enter_context(nc.sbuf_tensor(name, shape, dt))

    def sem(name):
        return ctx.enter_context(nc.semaphore(name))

    def steps(name, unit=1):
        return Steps(book, sem(name), name, unit)

    xtok = sb("xtok", [P, NT, D])
    hT = sb("hT", [P, ND, SEQ])
    yT = sb("yT", [P, 2 * ND, SEQ])
    W = sb("W", [P, 2, 6 * D])
    ident = sb("ident", [P, P])
    ones = sb("ones", [P, P])
    pairs = sb("pairs", [P, P])
    LE = sb("LE", [P, P])
    GE = sb("GE", [P, P])
    LT = sb("LT", [P, P])
    GT = sb("GT", [P, P])
    quad = sb("quad", [P, LEVELS, 6, P], U8)
    par = sb("par", [P, 61])
    conv = sb("conv", [P, 160])
    small = sb("small", [P, 64])
    lnshift = sb("lnshift", [P, 1])
    spare = sb("spare", [P, 32])
    arena = sb("arena", [P, 20480])
    zeros = sb("zeros", [P, 256])
    ps = ctx.enter_context(nc.psum_tensor("ps", [P, 8, 512], F32))
    MAXT = (2 * SEQ - NEXP) // P + NEXP
    NTAB = MAXT + MAXT % 2 + 1
    assert NTAB <= 64
    yd = nc.dram_tensor("expert_rows", (NTAB * P, D), F32, kind="Internal").ap()
    zeroed = sem("expert_rows_zeroed")
    cut = [0]

    def take(*shape):
        n = math.prod(shape)
        ap = arena[:, cut[0]:cut[0] + n]
        cut[0] += n
        assert cut[0] <= arena.shape[1], cut[0]
        if len(shape) == 2:
            return ap.rearrange("p (a b) -> p a b", a=shape[0])
        if len(shape) == 3:
            return ap.rearrange("p (a b c) -> p a b c", a=shape[0], b=shape[1])
        if len(shape) == 4:
            return ap.rearrange("p (a b c d) -> p a b c d", a=shape[0], b=shape[1], c=shape[2])
        return ap

    held = [0]

    def hold(dve):
        held[0] += 1
        k = held[0] % 32
        return dve.tensor_copy(spare[:, k:k + 1], ones[:, 0:1])

    def rows(name):
        return a[name].flatten().rearrange("(r c) -> r c", c=P)

    def flat(name):
        return a[name].flatten().rearrange("(a n) -> a n", a=1)

    stores = sem("stores")
    progs = {"sync": [], "tensor": [], "vector": [], "scalar": [], "gpsimd": []}

    def runs(engine):
        return progs[engine].append

    PAR_G, PAR_C, PAR_MU, PAR_PAIR, PAR_SBG, PAR_MULORA = 0, 8, 16, 16, 56, 60
    PARAMS = [("norm_g", PAR_G, 8), ("c", PAR_C, 8), ("decay_w0", 28, 4), ("iclr_a0", 32, 4), ("k_k", 36, 4),
              ("k_a", 40, 4), ("r_k", 44, 4), ("rwkv_ln_w", 48, 4), ("rwkv_ln_b", 52, 4), ("sb_norm_g", 56, 4)]

    cut[0] = 0
    prm = take(P)
    cnv = take(2, P)
    adab = take(3 * D)
    acc = take(3 * D)
    xs = take(NT, D)
    gate = sb("gate", [P, D])
    modc = take(24)
    ct = take(4, 8)
    gs = take(8)
    sq = take(D)
    qtmp = take(2 * P)
    ssum = take(4)
    rstd = take(4)

    su_pe, su_dve, su_act, su_pool = steps("setup_products"), steps("setup_vector"), steps("setup_scalar"), steps("setup_pool")
    x_in, par_in, ada_in = sem("x_in"), sem("par_in"), [sem("ada_in0"), sem("ada_in1")]
    adab_in = sem("adab_in")
    CH = 3 * D // 4

    @runs("sync")
    def _(sp):
        sp.dma_start(xtok[:], a["x"][0].rearrange("(t p) d -> p t d", p=P)).then_inc(x_in, 16)
        for q in range(4):
            if q >= 2:
                sp.wait_ge(*su_dve.at(f"ada {q - 2}"))
            src = a["ada_w"][0].rearrange("(k p) n -> p k n", p=P)[:, :, q * CH:(q + 1) * CH]
            sp.dma_start(W[:, q % 2, :].rearrange("p (k n) -> p k n", k=ND), src).then_inc(ada_in[q % 2], 16)

    @runs("scalar")
    def _(act):
        act.preload_act_table_set("natural_log_exp_and_others")
        for name, at, n in PARAMS:
            act.dma_start(prm[at:at + n, :], rows(name)).then_inc(par_in, 16)
        act.dma_start(prm[16:28, :], rows("tshift_mu")[0:12, :]).then_inc(par_in, 16)
        act.dma_start(prm[60:61, :], rows("tshift_mu")[12:13, :]).then_inc(par_in, 16)
        for h in range(2):
            act.dma_start(cnv[0:80, h, :], rows("gdn_conv_w_2")[80 * h:80 * h + 80, :]).then_inc(par_in, 16)
        act.wait_ge(*su_pool.at("ada_b zeros"))
        act.dma_start(adab[0:1, :], flat("ada_b")).then_inc(adab_in, 16)
        act.wait_ge(*su_dve.at("c clamped"))
        act.activation(ct[:, 1, :], ct[:, 0, :], ACT.Exp, scale=-1.0).then_inc(*su_act.step("exp c"))
        act.wait_ge(x_in, 16)
        for t in range(NT):
            act.wait_ge(*su_act.last())
            act.activation(sq, xtok[:, t, :], ACT.Square, accum_out=ssum[:, t:t + 1]).then_inc(*su_act.step())
        act.wait_ge(*su_dve.at("ssum eps"))
        act.activation(rstd, rstd, ACT.Ln).then_inc(*su_act.step())
        act.wait_ge(*su_act.last())
        act.activation(rstd, rstd, ACT.Exp, scale=-0.5).then_inc(*su_act.step("rstd"))
        act.wait_ge(*su_dve.at("scales"))
        for k in range(ND):
            act.wait_ge(*su_pe.at(f"x^T {k}"))
            act.activation(hT[:, k, :], ps[:, k, :], ACT.Identity, scale=gs[:, k:k + 1],
                           bias=modc[:, k:k + 1]).then_inc(*su_act.step(f"h {k}"))
        su_act.close()
        first = 2 * SEQ // P
        act.wait_ge(*su_pool.at("zeros"))
        act.dma_start(yd[first * P:, :].rearrange("(p n) (c d) -> p (n c) d", p=P, d=256),
                      zeros[:].unsqueeze(1).to_broadcast([P, (NTAB - first) * (D // 256), 256])).then_inc(zeroed, 16)

    @runs("gpsimd")
    def _(pool):
        def link(ins, name=None):
            ins.then_inc(*su_pool.step(name))
            pool.wait_ge(*su_pool.last())

        def keep(out_, in_, pattern, op, base, mult):
            link(pool.affine_select(out=out_, in_=in_, pattern=pattern, compare_op=op, fill=0.0, base=base,
                                    channel_multiplier=mult))

        link(pool.memset(ones[:], 1.0))
        keep(GE[:], ones[:], [[-1, P]], ALU.is_ge, 0, 1)
        keep(ident[:], GE[:], [[1, P]], ALU.is_ge, 0, -1)
        pool.nop().then_inc(*su_pool.step("ident"))
        link(pool.memset(adab, 0.0), "ada_b zeros")
        pool.memset(zeros[:], 0.0).then_inc(*su_pool.step("zeros"))
        keep(LE[:], ones[:], [[1, P]], ALU.is_ge, 0, -1)
        keep(LT[:], ones[:], [[1, P]], ALU.is_gt, 0, -1)
        keep(GT[:], ones[:], [[-1, P]], ALU.is_gt, 0, 1)
        keep(pairs[:, 0:HD], ones[:, 0:HD], [[0, HD]], ALU.is_gt, HD, -1)
        keep(pairs[:, HD:P], ones[:, HD:P], [[0, HD]], ALU.is_ge, -HD, 1)
        q0, q1 = qtmp[:, 0:P], qtmp[:, P:2 * P]
        for lv in range(LEVELS):
            half = 1 << lv
            blocks = P // (2 * half)
            pool.memset(q0, 0.0).then_inc(*su_pool.step())
            link(pool.memset(q1, 0.0))
            low = q0.rearrange("p (b h r) -> p b h r", h=2, r=half)[:, :, 0, :]
            up = q1.rearrange("p (b h r) -> p b h r", h=2, r=half)[:, :, 1, :]
            src = ones[:].rearrange("p (b h r) -> p b h r", h=2, r=half)[:, :, 0, :]
            pat = [[-2 * half, blocks], [0, half]]
            neg = [[2 * half, blocks], [0, half]]
            keep(low, src, pat, ALU.is_ge, -half, 1)
            keep(low, low, neg, ALU.is_gt, 2 * half, -1)
            keep(up, src, pat, ALU.is_ge, 0, 1)
            keep(up, up, neg, ALU.is_gt, half, -1)
            for s, q in ((0, q0), (1, q0), (2, q1), (3, q1), (4, q0), (5, q0)):
                pool.tensor_copy(quad[:, lv, s, :], q).then_inc(*su_pool.step())
            pool.wait_ge(*su_pool.last())
        su_pool.close()

    @runs("tensor")
    def _(pe):
        pe.wait_ge(*su_pool.at("ident"))
        pe.wait_ge(par_in, 16 * (len(PARAMS) + 4))
        pe.transpose(ps[:, 0, 0:61], prm[0:61, :], ident[0:61, 0:61])
        for h in range(2):
            pe.transpose(ps[:, 0, P + 80 * h:P + 80 * h + 80], cnv[0:80, h, :], ident[0:80, 0:80])\
              .then_inc(*su_pe.step("columns"))
        pe.wait_ge(*su_dve.at("ada_b"))
        for j in range(24):
            mm = pe.matmul(ps[:, 1, j:j + 1], acc[:, j * P:(j + 1) * P], ones[:, 0:1], start=True, stop=True)
        mm.then_inc(*su_pe.step("mod columns"))
        for h in range(2):
            pe.matmul(ps[:, 2 + h, :], ones[:], acc[:, 2 * D + 512 * h:2 * D + 512 * h + 512], start=True, stop=True)\
              .then_inc(*su_pe.step("gate rows"))
        pe.wait_ge(*su_dve.at("gate"))
        pe.wait_ge(*su_dve.at("xs"))
        for k in range(ND):
            for t in range(NT):
                mm = pe.transpose(ps[:, k, t * P:(t + 1) * P], xs[:, t, k * P:(k + 1) * P], ident[:])
            mm.then_inc(*su_pe.step(f"x^T {k}"))
        su_pe.close()

    @runs("vector")
    def _(dve):
        def link(ins, name=None):
            ins.then_inc(*su_dve.step(name))
            dve.wait_ge(*su_dve.last())

        dve.wait_ge(*su_pe.at("columns"))
        dve.tensor_copy(par[:], ps[:, 0, 0:61]).then_inc(*su_dve.step())
        link(dve.tensor_copy(conv[:], ps[:, 0, P:P + 160]))
        link(dve.tensor_scalar(ct[:, 0, :], par[:, PAR_C:PAR_C + 8], -CLAMP, None, ALU.max), "c clamped")
        dve.wait_ge(*su_act.at("exp c"))
        link(dve.tensor_scalar(ct[:, 1, :], ct[:, 1, :], 1.0, None, ALU.add))
        link(dve.reciprocal(ct[:, 2, :], ct[:, 1, :]))
        link(dve.tensor_tensor(ct[:, 3, :], ct[:, 2, :], par[:, PAR_C:PAR_C + 8], ALU.mult))
        dve.wait_ge(adab_in, 16)
        for q in range(4):
            dve.wait_ge(ada_in[q % 2], 16 * (q // 2 + 1))
            w = W[:, q % 2, :].rearrange("p (k n) -> p k n", k=ND)
            part = acc[:, q * CH:(q + 1) * CH]
            for k in range(ND):
                link(dve.scalar_tensor_tensor(out=part, in0=w[:, k, :], scalar=ct[:, 3, k:k + 1],
                                              in1=adab[:, q * CH:(q + 1) * CH] if k == 0 else part,
                                              op0=ALU.mult, op1=ALU.add), f"ada {q}" if k == ND - 1 else None)
        dve.nop().then_inc(*su_dve.step("ada_b"))
        dve.wait_ge(x_in, 16)
        dve.wait_ge(*su_act.at("exp c"))
        dve.wait_ge(*su_act_sums())
        link(dve.tensor_scalar(rstd, ssum, 1.0 / D, NORM_EPS, ALU.mult, ALU.add), "ssum eps")
        dve.wait_ge(*su_pe.at("mod columns"))
        link(dve.tensor_copy(modc, ps[:, 1, 0:24]))
        link(dve.scalar_tensor_tensor(out=gs, in0=modc[:, 8:16], scalar=1.0, in1=par[:, PAR_G:PAR_G + 8],
                                      op0=ALU.add, op1=ALU.mult), "scales")
        dve.wait_ge(*su_pe.at("gate rows"))
        dve.tensor_copy(gate[:, 0:512], ps[:, 2, :]).then_inc(*su_dve.step())
        link(dve.tensor_copy(gate[:, 512:D], ps[:, 3, :]), "gate")
        dve.wait_ge(*su_act.at("rstd"))
        for t in range(NT):
            dve.tensor_scalar(xs[:, t, :], xtok[:, t, :], rstd[:, t:t + 1], None, ALU.mult)\
               .then_inc(*su_dve.step("xs"))
        su_dve.close()

    def su_act_sums():
        return su_act.sem, su_act.names.get("exp c", 1) + NT

    SETUP = [su_pe, su_dve, su_act, su_pool]
    SETUP = [(s, None) for s in SETUP]

    def after(eng, done):
        for s, n in done:
            eng.wait_ge(*(s.end() if n is None else s.final(n)))

    cut[0] = 0
    mixraw = take(3, SEQ + 1)
    loraraw = take(SEQ + 1)
    lora = take(SEQ)
    rkv = take(3, SEQ)
    sg = take(SEQ)
    sig = take(2, SEQ)
    tmp2 = take(2, SEQ)
    gsum = take(SEQ)
    E1 = take(SEQ)
    E2 = take(SEQ)
    E3 = take(SEQ)
    kk = take(SEQ)
    AR = take(NT, 2, P)
    BK = take(2, SEQ)
    tok = take(NT, 3, P)
    pc = take(16)
    mid = take(4)
    fac = take(2, 4)
    S0 = take(HD)
    S1 = take(HD)
    RU = take(P)
    U = take(P)
    bonus = take(SEQ)
    maskQ = take(4, P)
    pairTS = cut[0]
    N_ = take(2, NT, P)
    T_ = take(2, NT, P)
    TT_ = take(2, NT, P)
    wq = W[:, 0, 0:4096].rearrange("p (k j c) -> p k j c", k=ND, j=4)
    w2a2 = W[:, 0, 4096:4224]
    wlora = W[:, 0, 5120:6144].rearrange("p (k c) -> p k c", k=ND)
    Vs = W[:, 1, 4096:5120].rearrange("p (h c t) -> p h c t", h=2, c=NT)
    ysb, ysq = W[:, 1, 5120:5632], W[:, 1, 5632:6144]
    Q = yT[:, ND:2 * ND, :].rearrange("p k n -> p (k n)").rearrange("p (h c j t) -> p h c j t", h=2, c=NT, j=4)

    lo_pe, lo_dve, lo_act, lo_pool = steps("lora_products"), steps("lora_vector"), steps("lora_scalar"), steps("lora_pool")
    rw_pe, rw_dve, rw_act, rw_pool = steps("rwkv_products"), steps("rwkv_vector"), steps("rwkv_scalar"), steps("rwkv_pool")
    lora_in, rw_in = sem("lora_in"), steps("rwkv_weights_in", 16)
    w_in = a["w_in"][0].rearrange("(k p) n -> p k n", p=P)

    @runs("sync")
    def _(sp):
        after(sp, SETUP)
        sp.dma_start(wlora, w_in[:, :, 3 * RW:SHIFT]).then_inc(lora_in, 16)
        rw_in.credit(sp)
        with sp.Fori(0, NPAIR) as n:
            rw_in.begin(n)
            sp.wait_ge(*rw_pe.at("projected", n - 1))
            for j, c0 in enumerate((0, RW, 2 * RW, SHIFT)):
                sp.dma_start(wq[:, :, j, :], w_in[:, :, bass.ds(n * P + c0, P)]).then_inc(*rw_in.step())
            sp.dma_start(w2a2[0:HD, :], a["decay_w2"][0][:, bass.ds(n * P, P)]).then_inc(*rw_in.step())
            sp.dma_start(w2a2[HD:P, :], a["iclr_a2"][0][:, bass.ds(n * P, P)]).then_inc(*rw_in.step("in"))
            rw_in.close()

    @runs("tensor")
    def _(pe):
        after(pe, SETUP)
        pe.wait_ge(lora_in, 16)
        for k in range(ND):
            mm = pe.matmul(ps[:, 0, :], wlora[:, k, :], hT[:, k, :], start=(k == 0), stop=(k == ND - 1))
        mm.then_inc(*lo_pe.step("z"))
        lo_pe.close()
        rw_pe.credit(pe)
        with pe.Fori(0, NPAIR) as n:
            rw_pe.begin(n)
            for s in (rw_dve, rw_act, rw_pool):
                pe.wait_ge(*s.end(n - 1))
            pe.wait_ge(*lo_act.end())
            pe.wait_ge(*rw_in.at("in", n))
            for j in range(4):
                for k in range(ND):
                    mm = pe.matmul(ps[:, j, :], wq[:, k, j, :], hT[:, k, :], start=(k == 0), stop=(k == ND - 1))
                mm.then_inc(*rw_pe.step(f"proj {j}"))
            for j in range(2):
                r = slice(j * HD, j * HD + HD)
                mm = pe.matmul(ps[:, 4 + j, :], w2a2[r, :], lora[r, :], start=True, stop=True)
                mm.then_inc(*rw_pe.step("projected"))
            pe.wait_ge(*rw_act.at("kk^2", n))
            pe.matmul(ps[:, 6, :], pairs[:], tmp2[:, 0, :], start=True, stop=True).then_inc(*rw_pe.step("kk sums"))
            pe.wait_ge(*rw_dve.at("rkr", n))
            pe.matmul(ps[:, 7, :], pairs[:], tmp2[:, 1, :], start=True, stop=True).then_inc(*rw_pe.step("bonus sums"))
            pe.wait_ge(*rw_dve.at("factors", n))
            pe.wait_ge(*rw_pool.at("factors", n))
            for c in range(NT):
                cs = slice(c * P, c * P + P)
                if c:
                    pe.wait_ge(*rw_act.at(f"tok {c - 1}", n))
                for j, src in enumerate((BK[:, 0, cs], BK[:, 1, cs], rkv[:, 2, cs])):
                    mm = pe.transpose(ps[:, 0, j * P:(j + 1) * P], src, ident[:])
                mm.then_inc(*rw_pe.step(f"tok {c}"))
            pe.wait_ge(*rw_dve.at("bonus", n))
            pe.wait_ge(*rw_act.at(f"tok {NT - 1}", n))
            for h in range(2):
                r = slice(h * HD, h * HD + HD)
                for c in range(NT):
                    cs = slice(c * P, c * P + P)
                    if h:
                        pe.wait_ge(*rw_dve.at(f"Q 0 {c}", n))
                    ar = AR[r, c, :, :].rearrange("p j t -> p (j t)")
                    pe.matmul(ps[:, 1 + c, 0:256], BK[r, 0, cs], ar, start=True, stop=True)
                    pe.matmul(ps[:, 1 + c, 256:512], BK[r, 1, cs], ar, start=True, stop=True)\
                      .then_inc(*rw_pe.step(f"Q {h} {c}"))
                    mm = pe.matmul(ps[:, 5 + h, cs], AR[r, c, 0, :], BK[r, 0, cs], start=True, stop=True)
                mm.then_inc(*rw_pe.step(f"A {h}"))
            pe.wait_ge(*rw_dve.at(f"Q 1 {NT - 1}", n))
            for lv in range(1, LEVELS):
                for h in range(2):
                    pe.wait_ge(*rw_dve.at(f"T {h} {lv - 1}", n))
                    for c in range(NT):
                        mm = pe.matmul(ps[:, 1 + 3 * h, c * P:(c + 1) * P], N_[:, h, c, :], TT_[:, h, c, :], start=True, stop=True)
                    mm.then_inc(*rw_pe.step(f"V {h} {lv}"))
                for h in range(2):
                    pe.wait_ge(*rw_act.at(f"V {h} {lv}", n))
                    if lv < LEVELS - 1:
                        for c in range(NT):
                            mm = pe.matmul(ps[:, 2 + 3 * h, c * P:(c + 1) * P], Vs[:, h, c, :], T_[:, h, c, :], start=True, stop=True)
                        mm.then_inc(*rw_pe.step(f"T {h} {lv}"))
                    for c in range(NT):
                        mm = pe.matmul(ps[:, 3 + 3 * h, c * P:(c + 1) * P], T_[:, h, c, :], Vs[:, h, c, :], start=True, stop=True)
                    mm.then_inc(*rw_pe.step(f"TT {h} {lv}"))
            for h in range(2):
                pe.wait_ge(*rw_dve.at(f"T {h} {LEVELS - 1}", n))
            for c in range(NT):
                cs = slice(c * P, c * P + P)
                pe.wait_ge(*rw_dve.at(f"S0 {c}", n))
                for h in range(2):
                    r = slice(h * HD, h * HD + HD)
                    pe.matmul(ps[:, 4 * h, 0:HD], AR[r, c, 0, :], S0[r, :], start=True, stop=False)
                    mm = pe.matmul(ps[:, 4 * h, 0:HD], Q[:, h, c, 2, :], tok[:, c, 2, r], start=False, stop=True)
                mm.then_inc(*rw_pe.step(f"RU {c}"))
                pe.wait_ge(*rw_act.at(f"RU {c}", n))
                for h in range(2):
                    r = slice(h * HD, h * HD + HD)
                    mm = pe.matmul(ps[:, 1, r], TT_[:, h, c, :], RU[:, r], start=True, stop=True)
                mm.then_inc(*rw_pe.step(f"U {c}"))
                pe.wait_ge(*rw_act.at(f"U {c}", n))
                for h in range(2):
                    r = slice(h * HD, h * HD + HD)
                    pe.matmul(ps[r, 2, 0:HD], tok[:, c, 0, r], U[:, r], start=True, stop=False)
                    mm = pe.matmul(ps[r, 2, 0:HD], tok[:, c, 1, r], tok[:, c, 2, r], start=False, stop=True)
                mm.then_inc(*rw_pe.step(f"S1 {c}"))
                for h in range(2):
                    r = slice(h * HD, h * HD + HD)
                    pe.matmul(ps[r, 7, cs], U[:, r], Q[:, h, c, 1, :], start=True, stop=False)
                    pe.matmul(ps[r, 7, cs], tok[:, c, 2, r], Q[:, h, c, 3, :], start=False, stop=False)
                    mm = pe.matmul(ps[r, 7, cs], S0[r, :], AR[r, c, 1, :], start=False, stop=True)
                mm.then_inc(*rw_pe.step(f"Y {c}"))
            pe.wait_ge(*rw_act.at("Y", n))
            pe.matmul(ps[:, 3, :], pairs[:], ysb, start=True, stop=True).then_inc(*rw_pe.step("mean"))
            pe.wait_ge(*rw_act.at("Y dev^2", n))
            pe.matmul(ps[:, 4, :], pairs[:], ysq, start=True, stop=True).then_inc(*rw_pe.step("var"))
            rw_pe.close()

    @runs("scalar")
    def _(act):
        def link(ins, name=None):
            ins.then_inc(*S.step(name))
            act.wait_ge(*S.last())

        after(act, SETUP)
        S = lo_act
        act.wait_ge(*lo_pool.end())
        act.wait_ge(*lo_pe.at("z"))
        link(act.activation(loraraw[:, 1:SEQ + 1], ps[:, 0, :], ACT.Copy), "z")
        act.wait_ge(*lo_dve.at("clamped"))
        link(act.activation(tmp2[0:HD, 0, :], tmp2[0:HD, 0, :], ACT.Exp, scale=-2.0), "exp")
        lo_act.close()
        S = rw_act
        rw_act.credit(act)
        with act.Fori(0, NPAIR) as n:
            rw_act.begin(n)
            act.wait_ge(*lo_dve.end())
            for s in (rw_pe, rw_dve, rw_pool):
                act.wait_ge(*s.end(n - 1))
            for j in range(3):
                act.wait_ge(*rw_pe.at(f"proj {j}", n))
                act.activation(mixraw[:, j, 1:SEQ + 1], ps[:, j, :], ACT.Copy).then_inc(*rw_act.step(f"raw {j}"))
            act.wait_ge(*rw_dve.at("g clamped", n))
            act.activation(sg, sg, ACT.Exp, scale=-1.0).then_inc(*rw_act.step("exp g"))
            act.wait_ge(*rw_dve.at("sig clamped", n))
            act.activation(sig, sig, ACT.Exp, scale=-1.0).then_inc(*rw_act.step("exp sig"))
            act.wait_ge(*rw_dve.at("k", n))
            act.activation(tmp2[:, 0, :], rkv[:, 1, :], ACT.Square, scale=pc[:, 5:6]).then_inc(*rw_act.step("kk^2"))
            act.wait_ge(*rw_dve.at("kk clamped", n))
            link(act.activation(kk, kk, ACT.Ln, scale=2.0 ** 24))
            act.activation(kk, kk, ACT.Exp, scale=-0.5, bias=lnshift[:, 0:1]).then_inc(*rw_act.step("kk rsqrt"))
            act.wait_ge(*rw_dve.at("centred", n))
            act.activation(fac[:, 0, :], mid, ACT.Exp, scale=-DECAY).then_inc(*rw_act.step())
            act.activation(E1, gsum, ACT.Exp, scale=-DECAY).then_inc(*rw_act.step())
            act.activation(E2, gsum, ACT.Exp, scale=DECAY).then_inc(*rw_act.step())
            act.activation(E3, E3, ACT.Exp, scale=-DECAY).then_inc(*rw_act.step("decays"))
            for c in range(NT):
                act.wait_ge(*rw_pe.at(f"tok {c}", n))
                act.activation(tok[:, c, :, :].rearrange("p j t -> p (j t)"), ps[:, 0, 0:3 * P], ACT.Copy)\
                   .then_inc(*rw_act.step(f"tok {c}"))
            for h in range(2):
                act.wait_ge(*rw_pe.at(f"A {h}", n))
                act.activation(N_[:, h, :, :].rearrange("p c t -> p (c t)"), ps[:, 5 + h, :], ACT.Copy)\
                   .then_inc(*rw_act.step(f"N {h}"))
            for lv in range(1, LEVELS):
                for h in range(2):
                    act.wait_ge(*rw_pe.at(f"V {h} {lv}", n))
                    act.activation(Vs[:, h, :, :].rearrange("p c t -> p (c t)"), ps[:, 1 + 3 * h, :], ACT.Copy)\
                       .then_inc(*rw_act.step(f"V {h} {lv}"))
            for c in range(NT):
                act.wait_ge(*rw_pe.at(f"RU {c}", n))
                act.activation(RU.rearrange("p (h t) -> p h t", h=2), ps[:, 0:5:4, 0:HD], ACT.Copy).then_inc(*rw_act.step(f"RU {c}"))
                act.wait_ge(*rw_pe.at(f"U {c}", n))
                if c:
                    act.wait_ge(*rw_pe.at(f"Y {c - 1}", n))
                act.activation(U, ps[:, 1, 0:P], ACT.Copy).then_inc(*rw_act.step(f"U {c}"))
            act.wait_ge(*rw_pe.at(f"Y {NT - 1}", n))
            act.activation(ysb, ps[:, 7, :], ACT.Copy).then_inc(*rw_act.step("Y"))
            act.wait_ge(*rw_dve.at("Y dev", n))
            act.activation(ysq, ysb, ACT.Square).then_inc(*rw_act.step("Y dev^2"))
            act.wait_ge(*rw_dve.at("var eps", n))
            link(act.activation(ysq, ysq, ACT.Ln))
            act.activation(ysq, ysq, ACT.Exp, scale=-0.5).then_inc(*rw_act.step("rstd"))
            rw_act.close()

    @runs("gpsimd")
    def _(pool):
        def link(ins, name=None):
            ins.then_inc(*S.step(name))
            pool.wait_ge(*S.last())

        after(pool, SETUP)
        S = lo_pool
        pool.memset(mixraw[:, :, 0:1], 0.0).then_inc(*lo_pool.step())
        pool.memset(loraraw[:, 0:1], 0.0).then_inc(*lo_pool.step())
        pool.memset(lnshift[:], 12.0 * math.log(2.0)).then_inc(*lo_pool.step())
        for j, m in enumerate((LT, LE, LT, LE)):
            pool.tensor_copy(maskQ[:, j, :], m[:]).then_inc(*lo_pool.step())
        lo_pool.close()
        S = rw_pool
        rw_pool.credit(pool)
        with pool.Fori(0, NPAIR) as n:
            rw_pool.begin(n)
            pool.wait_ge(*lo_pool.last())
            for s in (rw_pe, rw_dve, rw_act):
                pool.wait_ge(*s.end(n - 1))
            for h in range(2):
                for t in (T_, TT_):
                    pool.tensor_tensor(t[:, h, :, :], repeat(ident[:], NT), repeat(ones[:], NT), ALU.mult)\
                        .then_inc(*rw_pool.step("identity"))
            pool.wait_ge(*rw_dve.at("k'", n))
            pool.wait_ge(*rw_act.at("decays", n))
            pool.tensor_tensor(BK[:, 1, :], rkv[:, 1, :], E2, ALU.mult).then_inc(*rw_pool.step())
            pool.tensor_tensor(AR[:, :, 1, :], rkv[:, 0, :].rearrange("p (c t) -> p c t", c=NT),
                               E1.rearrange("p (c t) -> p c t", c=NT), ALU.mult).then_inc(*rw_pool.step("factors"))
            rw_pool.close()

    @runs("vector")
    def _(dve):
        def link(ins, name=None):
            ins.then_inc(*S.step(name))
            dve.wait_ge(*S.last())

        def chunks(ap):
            return ap.rearrange("p (c t) -> p c t", c=NT)

        def sigmoid_of_exp(x):
            link(dve.tensor_scalar(x, x, 1.0, None, ALU.add))
            link(dve.reciprocal(x, x))

        after(dve, SETUP)
        S = lo_dve
        dve.wait_ge(*lo_act.at("z"))
        mu = par[:, PAR_MULORA:PAR_MULORA + 1]
        link(dve.tensor_tensor(lora, loraraw[:, 0:SEQ], loraraw[:, 1:SEQ + 1], ALU.subtract))
        link(dve.scalar_tensor_tensor(out=lora, in0=lora, scalar=mu, in1=loraraw[:, 1:SEQ + 1], op0=ALU.mult, op1=ALU.add))
        link(dve.tensor_scalar(tmp2[0:HD, 0, :], lora[0:HD, :], -CLAMP / 2, None, ALU.max), "clamped")
        dve.wait_ge(*lo_act.at("exp"))
        sigmoid_of_exp(tmp2[0:HD, 0, :])
        link(dve.tensor_scalar(lora[0:HD, :], tmp2[0:HD, 0, :], 2.0, -1.0, ALU.mult, ALU.add))
        lo_dve.close()
        S = rw_dve
        rw_dve.credit(dve)
        with dve.Fori(0, NPAIR) as n:
            rw_dve.begin(n)
            for s in (rw_pe, rw_act, rw_pool):
                dve.wait_ge(*s.end(n - 1))
            dve.wait_ge(*lo_pool.end())
            link(dve.tensor_scalar(pc[:, 0:10], par[:, bass.ds(n + PAR_PAIR, 10, 4)], 1.0, None, ALU.mult))
            dve.wait_ge(*rw_pe.at("proj 3", n))
            dve.tensor_scalar(sg, ps[:, 3, :], -CLAMP, None, ALU.max).then_inc(*rw_dve.step("g clamped"))
            dve.wait_ge(*rw_pe.at("projected", n))
            for j in range(2):
                dve.tensor_scalar(sig[:, j, :], ps[:, 4 + j, :], pc[:, 3 + j:4 + j], -CLAMP, ALU.add, ALU.max)\
                   .then_inc(*rw_dve.step("sig clamped"))
            for j in (1, 0, 2):
                dve.wait_ge(*rw_act.at(f"raw {j}", n))
                link(dve.tensor_tensor(rkv[:, j, :], mixraw[:, j, 0:SEQ], mixraw[:, j, 1:SEQ + 1], ALU.subtract))
                link(dve.scalar_tensor_tensor(out=rkv[:, j, :], in0=rkv[:, j, :], scalar=pc[:, j:j + 1],
                                              in1=mixraw[:, j, 1:SEQ + 1], op0=ALU.mult, op1=ALU.add),
                     "k" if j == 1 else None)
            dve.wait_ge(*rw_act.at("exp sig", n))
            sigmoid_of_exp(sig)
            for c in range(NT):
                cs = slice(c * P, c * P + P)
                dve.tensor_tensor_scan(gsum[:, cs], ones[:], sig[:, 0, cs], 0.0, ALU.mult, ALU.add).then_inc(*rw_dve.step())
            dve.wait_ge(*rw_dve.last())
            link(dve.tensor_copy(mid, chunks(gsum)[:, :, HD - 1]))
            link(dve.tensor_tensor(chunks(gsum), chunks(gsum), bcast(mid, P), ALU.subtract))
            link(dve.tensor_tensor(E3, gsum, sig[:, 0, :], ALU.subtract), "centred")
            dve.wait_ge(*rw_act.at("exp g", n))
            sigmoid_of_exp(sg)
            link(dve.tensor_tensor(sg, sg, ps[:, 3, :], ALU.mult))
            dve.wait_ge(*rw_pe.at("kk sums", n))
            link(dve.tensor_scalar(kk, ps[:, 6, :], 1e-24, None, ALU.max), "kk clamped")
            dve.wait_ge(*rw_act.at("kk rsqrt", n))
            link(dve.scalar_tensor_tensor(out=kk, in0=rkv[:, 1, :], scalar=pc[:, 5:6], in1=kk, op0=ALU.mult, op1=ALU.mult))
            link(dve.tensor_scalar(tmp2[:, 0, :], sig[:, 1, :], -1.0, pc[:, 6:7], ALU.add, ALU.mult))
            link(dve.scalar_tensor_tensor(out=rkv[:, 1, :], in0=tmp2[:, 0, :], scalar=1.0, in1=rkv[:, 1, :],
                                          op0=ALU.add, op1=ALU.mult), "k'")
            link(dve.scalar_tensor_tensor(out=tmp2[:, 1, :], in0=rkv[:, 0, :], scalar=pc[:, 7:8], in1=rkv[:, 1, :],
                                          op0=ALU.mult, op1=ALU.mult), "rkr")
            dve.wait_ge(*rw_act.at("decays", n))
            dve.scalar_tensor_tensor(out=AR[:, :, 0, :], in0=chunks(kk), scalar=-1.0, in1=chunks(E3),
                                     op0=ALU.mult, op1=ALU.mult).then_inc(*rw_dve.step())
            link(dve.tensor_tensor(BK[:, 0, :], kk, sig[:, 1, :], ALU.mult))
            dve.tensor_tensor(BK[:, 0, :], BK[:, 0, :], E2, ALU.mult).then_inc(*rw_dve.step("factors"))
            link(dve.tensor_tensor(fac[:, 1, 0:3], chunks(E1)[:, 0:3, P - 1], fac[:, 0, 1:4], ALU.mult))
            dve.wait_ge(*rw_pe.at("bonus sums", n))
            link(dve.tensor_tensor(bonus, ps[:, 7, :], rkv[:, 2, :], ALU.mult), "bonus")
            for h in range(2):
                for c in range(NT):
                    dve.wait_ge(*rw_pe.at(f"Q {h} {c}", n))
                    dve.tensor_tensor(Q[:, h, c, :, :].rearrange("p j t -> p (j t)"), ps[:, 1 + c, :],
                                      maskQ.rearrange("p j t -> p (j t)"), ALU.mult).then_inc(*rw_dve.step(f"Q {h} {c}"))
            dve.wait_ge(*rw_pool.at("identity", n))
            dve.wait_ge(*rw_dve.last())
            for h in range(2):
                dve.wait_ge(*rw_act.at(f"N {h}", n))
                hold(dve).then_inc(*rw_dve.step())
                dve.copy_predicated(T_[:, h, :, :], repeat(quad[:, 0, 0, :], NT), N_[:, h, :, :]).then_inc(*rw_dve.step())
                dve.copy_predicated(TT_[:, h, :, :], repeat(quad[:, 0, 2, :], NT), Q[:, h, :, 0, :])\
                   .then_inc(*rw_dve.step(f"T {h} 0"))
            for lv in range(1, LEVELS):
                for h in range(2):
                    dve.wait_ge(*rw_pe.at(f"TT {h} {lv}", n))
                    hold(dve).then_inc(*rw_dve.step())
                    if lv < LEVELS - 1:
                        dve.copy_predicated(T_[:, h, :, :], repeat(quad[:, lv, 0, :], NT), chunks(ps[:, 2 + 3 * h, :]))\
                           .then_inc(*rw_dve.step())
                    dve.copy_predicated(TT_[:, h, :, :], repeat(quad[:, lv, 2, :], NT), chunks(ps[:, 3 + 3 * h, :]))\
                       .then_inc(*rw_dve.step(f"T {h} {lv}"))
            link(dve.memset(S0, 0.0), "S0 0")
            for c in range(NT - 1):
                dve.wait_ge(*rw_pe.at(f"S1 {c}", n))
                link(dve.tensor_tensor(S1, ps[:, 2, 0:HD], S0, ALU.add))
                dve.wait_ge(*rw_pe.at(f"Y {c}", n))
                link(dve.tensor_scalar(S0, S1, fac[:, 1, c:c + 1], None, ALU.mult), f"S0 {c + 1}")
            dve.wait_ge(*rw_pe.at("mean", n))
            link(dve.scalar_tensor_tensor(out=ysb, in0=ps[:, 3, :], scalar=-1.0 / HD, in1=ysb, op0=ALU.mult, op1=ALU.add),
                 "Y dev")
            dve.wait_ge(*rw_pe.at("var", n))
            link(dve.tensor_scalar(ysq, ps[:, 4, :], 1.0 / HD, GN_EPS, ALU.mult, ALU.add), "var eps")
            dve.wait_ge(*rw_act.at("rstd", n))
            link(dve.tensor_tensor(ysb, ysb, ysq, ALU.mult))
            link(dve.tensor_scalar(ysb, ysb, pc[:, 8:9], pc[:, 9:10], ALU.mult, ALU.add))
            link(dve.tensor_tensor(ysb, ysb, bonus, ALU.add))
            dve.tensor_tensor(yT[:, bass.ds(n, 1), :].rearrange("p a t -> p (a t)"), ysb, sg, ALU.mult).then_inc(*rw_dve.step())
            rw_dve.close()

    RWKV = [(s, None) for s in (lo_pe, lo_dve, lo_act, lo_pool)] + [(s, NPAIR) for s in (rw_pe, rw_dve, rw_act, rw_pool)]

    cut[0] = 0
    qk = take(2, SEQ)
    vtok = take(NT, P)
    graw = take(SEQ)
    sgs = take(SEQ)
    WID = [SEQ - j * P for j in range(NT)]
    OFF = [sum(WID[:j]) for j in range(NT)]
    TRI = sum(WID)
    zs = take(2, TRI)
    spl = take(2, TRI)
    wt = take(2, TRI)
    osb, osq = take(SEQ), take(SEQ)
    sbg = take(1)
    wsb = W[:, 0, 0:4096].rearrange("p (k j c) -> p k j c", k=ND, j=4)
    sb_pe, sb_dve, sb_act = steps("stick_products"), steps("stick_vector"), steps("stick_scalar")
    sb_in = steps("stick_weights_in", 16)
    ZB = [[(4, 0), (5, 0), (6, 0), (6, WID[2])], [(0, 0), (1, 0), (2, 0), (2, WID[2])]]
    SPANS = [(0, 0, WID[0]), (1, OFF[1], WID[1]), (2, OFF[2], WID[2] + WID[3])]

    @runs("sync")
    def _(sp):
        after(sp, RWKV)
        sb_in.credit(sp)
        with sp.Fori(0, NPAIR) as n:
            sb_in.begin(n)
            sp.wait_ge(*sb_pe.at("projected", n - 1))
            for j in range(4):
                sp.dma_start(wsb[:, :, j, :], w_in[:, :, bass.ds(n * P + (SB0 + j * RW), P)]).then_inc(*sb_in.step("in"))
            sb_in.close()

    @runs("tensor")
    def _(pe):
        after(pe, RWKV)
        sb_pe.credit(pe)
        with pe.Fori(0, NPAIR) as n:
            sb_pe.begin(n)
            for s in (sb_dve, sb_act):
                pe.wait_ge(*s.end(n - 1))
            pe.wait_ge(*sb_in.at("in", n))
            for bank, j in ((0, 0), (1, 1), (2, 3)):
                for k in range(ND):
                    mm = pe.matmul(ps[:, bank, :], wsb[:, k, j, :], hT[:, k, :], start=(k == 0), stop=(k == ND - 1))
                mm.then_inc(*sb_pe.step(f"proj {bank}"))
            for t in range(NT):
                for k in range(ND):
                    mm = pe.matmul(ps[:, 3, t * P:(t + 1) * P], hT[:, k, t * P:(t + 1) * P], wsb[:, k, 2, :],
                                   start=(k == 0), stop=(k == ND - 1))
            mm.then_inc(*sb_pe.step("projected"))
            for h in range(2):
                r = slice(h * HD, h * HD + HD)
                pe.wait_ge(*sb_act.at("q k g v", n))
                for j in range(NT):
                    b, c = ZB[h][j]
                    pe.matmul(ps[:, b, c:c + WID[j]], qk[r, 1, j * P:(j + 1) * P], qk[r, 0, j * P:SEQ], start=True, stop=True)\
                      .then_inc(*sb_pe.step(f"z {h} {j}"))
            for h in range(2):
                pe.wait_ge(*sb_dve.at(f"sp {h}", n))
                for j in range(NT):
                    b, c = ZB[h][j]
                    mm = pe.matmul(ps[:, b, c:c + WID[j]], GE[:], spl[:, h, OFF[j]:OFF[j] + WID[j]], start=True,
                                   stop=(j == NT - 1))
                    for i in range(j + 1, NT):
                        mm = pe.matmul(ps[:, b, c + (i - j) * P:c + WID[j]], ones[:], spl[:, h, OFF[i]:OFF[i] + WID[i]],
                                       start=False, stop=(i == NT - 1))
                mm.then_inc(*sb_pe.step(f"R {h}"))
            for h in range(2):
                r = slice(h * HD, h * HD + HD)
                pe.wait_ge(*sb_dve.at(f"weights {h}", n))
                for j in range(NT):
                    mm = pe.matmul(ps[r, 3, j * P:SEQ], vtok[:, j, r], wt[:, h, OFF[j]:OFF[j] + WID[j]], start=(j == 0),
                                   stop=(j == NT - 1))
                mm.then_inc(*sb_pe.step("O"))
            pe.wait_ge(*sb_act.at("O^2", n))
            pe.matmul(ps[:, 7, :], pairs[:], osq, start=True, stop=True).then_inc(*sb_pe.step("O sums"))
            sb_pe.close()

    @runs("scalar")
    def _(act):
        after(act, RWKV)
        sb_act.credit(act)
        with act.Fori(0, NPAIR) as n:
            def link(ins, name=None):
                ins.then_inc(*sb_act.step(name))
                act.wait_ge(*sb_act.last())

            sb_act.begin(n)
            for s in (sb_pe, sb_dve):
                act.wait_ge(*s.end(n - 1))
            for bank, dst, scale in ((0, qk[:, 0, :], HD ** -0.5), (1, qk[:, 1, :], 1.0), (2, graw, 1.0)):
                act.wait_ge(*sb_pe.at(f"proj {bank}", n))
                act.activation(dst, ps[:, bank, :], ACT.Copy, scale=scale).then_inc(*sb_act.step())
            act.wait_ge(*sb_pe.at("projected", n))
            link(act.activation(vtok.rearrange("p t c -> p (t c)"), ps[:, 3, :], ACT.Copy), "q k g v")
            act.wait_ge(*sb_dve.at("g clamped", n))
            link(act.activation(sgs, sgs, ACT.Exp, scale=-1.0))
            link(act.activation(sgs, sgs, ACT.Ln, bias=1.0))
            link(act.activation(sgs, sgs, ACT.Exp, scale=-1.0), "sigmoid g")
            for h in range(2):
                act.wait_ge(*sb_pe.at(f"z {h} {NT - 1}", n))
                for b, c, w in SPANS:
                    act.activation(zs[:, h, c:c + w], ps[:, ZB[h][b][0], 0:w], ACT.Copy).then_inc(*sb_act.step())
                act.wait_ge(*sb_act.last())
                link(act.activation(wt[:, h, :], zs[:, h, :], ACT.Abs), f"zs {h}")
                link(act.activation(wt[:, h, :], wt[:, h, :], ACT.Exp, scale=-1.0))
                link(act.activation(wt[:, h, :], wt[:, h, :], ACT.Ln, bias=1.0), f"ln {h}")
            for h in range(2):
                act.wait_ge(*sb_dve.at(f"logs {h}", n))
                act.activation(wt[:, h, :], wt[:, h, :], ACT.Exp).then_inc(*sb_act.step(f"exp {h}"))
            act.wait_ge(*sb_pe.at("O", n))
            link(act.activation(osb, ps[:, 3, :], ACT.Copy))
            link(act.activation(osq, osb, ACT.Square), "O^2")
            act.wait_ge(*sb_dve.at("sums eps", n))
            link(act.activation(osq, osq, ACT.Ln))
            act.activation(osq, osq, ACT.Exp, scale=-0.5).then_inc(*sb_act.step("rstd"))
            sb_act.close()

    @runs("vector")
    def _(dve):
        after(dve, RWKV)
        sb_dve.credit(dve)
        with dve.Fori(0, NPAIR) as n:
            def link(ins, name=None):
                ins.then_inc(*sb_dve.step(name))
                dve.wait_ge(*sb_dve.last())

            sb_dve.begin(n)
            for s in (sb_pe, sb_act):
                dve.wait_ge(*s.end(n - 1))
            dve.tensor_scalar(sbg, par[:, bass.ds(n + PAR_SBG, 1)], 1.0, None, ALU.mult).then_inc(*sb_dve.step())
            dve.wait_ge(*sb_act.at("q k g v", n))
            link(dve.tensor_scalar(sgs, graw, -LNCLAMP, None, ALU.max), "g clamped")
            for h in range(2):
                dve.wait_ge(*sb_act.at(f"ln {h}", n))
                link(dve.scalar_tensor_tensor(out=spl[:, h, :], in0=zs[:, h, :], scalar=0.0, in1=wt[:, h, :],
                                              op0=ALU.max, op1=ALU.add))
                for j in range(NT):
                    d = spl[:, h, OFF[j]:OFF[j] + P]
                    dve.tensor_tensor(d, d, LT[:], ALU.mult).then_inc(*sb_dve.step(f"sp {h}"))
            dve.wait_ge(*sb_act.at("sigmoid g", n))
            dve.tensor_tensor(sgs, sgs, graw, ALU.mult).then_inc(*sb_dve.step())
            for h in range(2):
                dve.wait_ge(*sb_pe.at(f"R {h}", n))
                for b, c, w in SPANS:
                    dve.tensor_tensor(wt[:, h, c:c + w], zs[:, h, c:c + w], ps[:, ZB[h][b][0], 0:w], ALU.subtract)\
                       .then_inc(*sb_dve.step())
                dve.wait_ge(*sb_dve.last())
                for j in range(NT):
                    d = wt[:, h, OFF[j]:OFF[j] + P]
                    dve.tensor_scalar(d, d, 0.0, None, ALU.min).then_inc(*sb_dve.step(f"logs {h}"))
            for h in range(2):
                dve.wait_ge(*sb_act.at(f"exp {h}", n))
                for j in range(NT):
                    d = wt[:, h, OFF[j]:OFF[j] + P]
                    dve.tensor_tensor(d, d, LT[:], ALU.mult).then_inc(*sb_dve.step(f"weights {h}"))
            dve.wait_ge(*sb_pe.at("O sums", n))
            dve.wait_ge(*sb_act.at("O^2", n))
            link(dve.tensor_scalar(osq, ps[:, 7, :], 1.0 / HD, NORM_EPS, ALU.mult, ALU.add), "sums eps")
            dve.wait_ge(*sb_act.at("rstd", n))
            link(dve.scalar_tensor_tensor(out=osb, in0=osb, scalar=sbg, in1=osq, op0=ALU.mult, op1=ALU.mult))
            dve.tensor_tensor(yT[:, bass.ds(n + NPAIR, 1), :].rearrange("p a (i b) -> p (a i) b", b=NT),
                              osb.rearrange("p (b i) -> p i b", b=NT), sgs.rearrange("p (i b) -> p i b", b=NT), ALU.mult)\
               .then_inc(*sb_dve.step())
            sb_dve.close()

    STICK = [(s, NPAIR) for s in (sb_pe, sb_dve, sb_act)]

    cut[0] = 0
    grow = take(D)
    xsq = take(D)
    mixed = take(8, SEQ)
    fs = take(NT)
    wo1 = W[:].rearrange("p h n -> p (h n)")[:, 0:ND * D].rearrange("p (k n) -> p k n", k=ND)
    o1_pe, o1_dve, o1_act = steps("out1_products"), steps("out1_vector"), steps("out1_scalar")
    o1_in, o1_g = sem("out1_weights_in"), sem("out1_g_in")

    @runs("sync")
    def _(sp):
        after(sp, STICK)
        sp.dma_start(wo1, a["w_out"][0].rearrange("(k p) n -> p k n", p=P)).then_inc(o1_in, 16)
        sp.dma_start(grow, flat("final_g").to_broadcast([P, D])).then_inc(o1_g, 16)

    @runs("tensor")
    def _(pe):
        after(pe, STICK)
        pe.wait_ge(o1_in, 16)
        for t in range(NT):
            for h in range(2):
                for k in range(ND):
                    mm = pe.matmul(ps[:, 2 * t + h, :], yT[:, k, t * P:(t + 1) * P], wo1[:, k, 512 * h:512 * h + 512],
                                   start=(k == 0), stop=(k == ND - 1))
                mm.then_inc(*o1_pe.step(f"y {t} {h}"))
        for t in range(NT):
            pe.wait_ge(*o1_dve.at(f"x {t}"))
        for k in range(ND):
            for t in range(NT):
                mm = pe.transpose(ps[:, k, t * P:(t + 1) * P], xtok[:, t, k * P:(k + 1) * P], ident[:])
            mm.then_inc(*o1_pe.step(f"x^T {k}"))
        o1_pe.close()

    @runs("scalar")
    def _(act):
        after(act, STICK)
        for t in range(NT):
            act.wait_ge(*o1_dve.at(f"sum {t}"))
            act.wait_ge(*o1_act.last()) if t else None
            act.activation(xsq, xtok[:, t, :], ACT.Square, accum_out=fs[:, t:t + 1]).then_inc(*o1_act.step(f"ss {t}"))
            act.wait_ge(*o1_dve.at(f"eps {t}"))
            act.activation(fs[:, t:t + 1], fs[:, t:t + 1], ACT.Ln).then_inc(*o1_act.step())
            act.wait_ge(*o1_act.last())
            act.activation(fs[:, t:t + 1], fs[:, t:t + 1], ACT.Exp, scale=-0.5).then_inc(*o1_act.step(f"rstd {t}"))
        for k in range(ND):
            act.wait_ge(*o1_pe.at(f"x^T {k}"))
            act.activation(hT[:, k, :], ps[:, k, :], ACT.Copy).then_inc(*o1_act.step(f"hT {k}"))
        o1_act.close()

    @runs("vector")
    def _(dve):
        def link(ins, name=None):
            ins.then_inc(*o1_dve.step(name))
            dve.wait_ge(*o1_dve.last())

        after(dve, STICK)
        dve.wait_ge(o1_g, 16)
        for t in range(NT):
            for h in range(2):
                hs = slice(512 * h, 512 * h + 512)
                dve.wait_ge(*o1_pe.at(f"y {t} {h}"))
                link(dve.tensor_tensor(mixed[:, 2 * t + h, :], ps[:, 2 * t + h, :], gate[:, hs], ALU.mult))
                link(dve.tensor_tensor(xtok[:, t, hs], xtok[:, t, hs], mixed[:, 2 * t + h, :], ALU.add), f"sum {t}")
            dve.wait_ge(*o1_act.at(f"ss {t}"))
            link(dve.tensor_scalar(fs[:, t:t + 1], fs[:, t:t + 1], 1.0 / D, NORM_EPS, ALU.mult, ALU.add), f"eps {t}")
            dve.wait_ge(*o1_act.at(f"rstd {t}"))
            link(dve.scalar_tensor_tensor(out=xtok[:, t, :], in0=xtok[:, t, :], scalar=fs[:, t:t + 1], in1=grow,
                                          op0=ALU.mult, op1=ALU.mult), f"x {t}")
        o1_dve.close()

    OUT1 = [(s, None) for s in (o1_pe, o1_dve, o1_act)]

    cut[0] = 0
    raw = take(4, SEQ + TAPS - 1)
    cv = take(4, SEQ)
    Nn = take(NT, 4, P)
    zr, zg = take(NT, 2 * P), take(NT, 2 * P)
    ktok, vtk = take(NT, P), take(NT, 2, P)
    kkS, qkS, qkm = take(NT, P), take(NT, P), take(NT, 2, P)
    Gb = take(NT * 4, P)
    attnT = take(NT, 4, P)
    Tg = take(NT, 4, P)
    QUANT = 7
    pre = take(QUANT, NT, 32)
    pcg = take(QUANT, NT, 4)
    NLE, NGE = take(P), take(P)
    nw = take(P)
    ab = take(NT, 64)
    abt = take(NT, 64)
    alog, dtb = take(32), take(32)
    rsn = take(8)
    taps = take(TAPS, 4)
    half2 = W[:, 1, :]
    TTg = half2[:, 0:2048].rearrange("p (g b t) -> p g b t", g=NT, b=4)
    Vg = half2[:, 2048:3072].rearrange("p (s b t) -> p s b t", s=2, b=4)
    St = half2[:, 3072:3584].rearrange("p (b t) -> p b t", b=4)
    ob = half2[:, 3584:4096].rearrange("p (b t) -> p b t", b=4)
    oacc = half2[:, 4096:5120].rearrange("p (c e t) -> p c e t", c=NT, e=2)
    osqr = half2[:, 5120:6144].rearrange("p (c e t) -> p c e t", c=NT, e=2)
    ctmp = Nn.rearrange("p c b t -> p (c b t)").rearrange("p (j t) -> p j t", j=4)
    XD = [raw[:, k, 2:2 + SEQ] for k in range(4)]
    Rr, vn, vnd, qs = [Gb[:, 4 * k:4 * k + 4, :] for k in range(4)]
    wg = W[:, 0, :].rearrange("p (k n) -> p k n", k=ND)
    wab = W[:, 0, 0:512].rearrange("p (k n) -> p k n", k=ND)
    g_in = a["gdn_w_in_2"][0].rearrange("(k p) n -> p k n", p=P)
    GDN_AB = GDN_CONV + 2 * D

    ab_pe, ab_dve, ab_act, ab_pool = steps("gates_products"), steps("gates_vector"), steps("gates_scalar"), steps("gates_pool")
    gd_pe, gd_dve, gd_act, gd_pool = steps("gdn_products"), steps("gdn_vector"), steps("gdn_scalar"), steps("gdn_pool")
    ab_in, gd_in = sem("gates_in"), steps("gdn_weights_in", 16)

    def fl(ap):
        return ap.rearrange("p b t -> p (b t)")

    @runs("sync")
    def _(sp):
        after(sp, OUT1)
        sp.dma_start(wab, g_in[:, :, GDN_AB:GDN_AB + 64]).then_inc(ab_in, 16)
        sp.dma_start(alog, flat("gdn_a_log_2").to_broadcast([P, 32])).then_inc(ab_in, 16)
        sp.dma_start(dtb, flat("gdn_dt_bias_2").to_broadcast([P, 32])).then_inc(ab_in, 16)
        sp.dma_start(nw, flat("gdn_norm_w_2").to_broadcast([P, P])).then_inc(ab_in, 16)
        gd_in.credit(sp)
        sp.wait_ge(*ab_pe.at("ab"))
        with sp.Fori(0, QKH) as n:
            gd_in.begin(n)
            sp.wait_ge(*gd_pe.at("projected", n - 1))
            for dst, c0, each in ((0, 0, P), (P, D, P), (2 * P, 2 * D, 2 * P), (4 * P, GDN_CONV, 2 * P)):
                sp.dma_start(wg[:, :, dst:dst + each], g_in[:, :, bass.ds(n * each + c0, each)]).then_inc(*gd_in.step("in"))
            gd_in.close()

    @runs("tensor")
    def _(pe):
        after(pe, OUT1)
        pe.wait_ge(ab_in, 64)
        for t in range(NT):
            for k in range(ND):
                mm = pe.matmul(ps[:, 0, 64 * t:64 * t + 64], hT[:, k, t * P:(t + 1) * P], wab[:, k, :], start=(k == 0),
                               stop=(k == ND - 1))
        mm.then_inc(*ab_pe.step("ab"))
        pe.wait_ge(*ab_dve.at("g"))
        for t in range(NT):
            pe.matmul(ps[:, 1, 64 * t:64 * t + 16], LE[:], pre[:, 0, t, 0:16], start=True, stop=True)
            pe.matmul(ps[:, 1, 64 * t + 16:64 * t + 32], GE[:], pre[:, 0, t, 16:32], start=True, stop=True)
            mm = pe.matmul(ps[:, 1, 64 * t + 32:64 * t + 64], ones[:], pre[:, 0, t, :], start=True, stop=True)
        mm.then_inc(*ab_pe.step("sums"))
        ab_pe.close()
        gd_pe.credit(pe)
        with pe.Fori(0, QKH) as n:
            gd_pe.begin(n)
            for s in (gd_dve, gd_act, gd_pool):
                pe.wait_ge(*s.end(n - 1))
            pe.wait_ge(*ab_dve.end())
            pe.wait_ge(*ab_pool.end())
            pe.wait_ge(*gd_in.at("in", n))
            for j in range(4):
                for k in range(ND):
                    mm = pe.matmul(ps[:, j, :], wg[:, k, j * P:(j + 1) * P], hT[:, k, :], start=(k == 0), stop=(k == ND - 1))
                mm.then_inc(*gd_pe.step(f"proj {j}"))
            for t in range(NT):
                for k in range(ND):
                    mm = pe.matmul(ps[:, 4 + t // 2, 256 * (t % 2):256 * (t % 2) + 256], hT[:, k, t * P:(t + 1) * P],
                                   wg[:, k, 4 * P:6 * P], start=(k == 0), stop=(k == ND - 1))
            mm.then_inc(*gd_pe.step("projected"))
            pe.wait_ge(*gd_pool.at("G", n))
            pe.wait_ge(*gd_act.at("raw 1", n))
            for c in range(2):
                for d in range(2):
                    cols = ps[:, c % 2, 256 * d:256 * d + 256]
                    pe.matmul(cols, (NLE, NGE)[d], fl(Gb[:, 4 * c + 2 * d:4 * c + 2 * d + 2, :]), start=True, stop=False)
                    for e in range(2):
                        mm = pe.matmul(cols[:, P * e:P * e + P], Gb[:, 4 * c + 2 * d + e, :], (LE, GE)[d][:], start=False,
                                       stop=(e == 1))
                mm.then_inc(*gd_pe.step(f"X {c}"))
            for j in range(2):
                pe.wait_ge(*gd_act.at(f"square {j}", n))
                pe.matmul(ps[:, 6 + j, :], ones[:], ctmp[:, j, :], start=True, stop=True).then_inc(*gd_pe.step(f"norm {j}"))
            for c in range(2, NT):
                pe.wait_ge(*gd_dve.at(f"X {c - 2}", n))
                for d in range(2):
                    cols = ps[:, c % 2, 256 * d:256 * d + 256]
                    pe.matmul(cols, (NLE, NGE)[d], fl(Gb[:, 4 * c + 2 * d:4 * c + 2 * d + 2, :]), start=True, stop=False)
                    for e in range(2):
                        mm = pe.matmul(cols[:, P * e:P * e + P], Gb[:, 4 * c + 2 * d + e, :], (LE, GE)[d][:], start=False,
                                       stop=(e == 1))
                mm.then_inc(*gd_pe.step(f"X {c}"))
            pe.wait_ge(*gd_pool.at("silu 3", n))
            pe.wait_ge(*gd_dve.at("unit 1", n))
            pe.wait_ge(*gd_act.at("z raw", n))
            for c in range(NT):
                cs = slice(c * P, c * P + P)
                for e in range(2):
                    mm = pe.transpose(ps[:, 3 + c // 2, 256 * (c % 2) + P * e:256 * (c % 2) + P * e + P], cv[:, 2 + e, cs], ident[:])
            mm.then_inc(*gd_pe.step("v tokens"))
            for c in range(NT):
                cs = slice(c * P, c * P + P)
                mm = pe.transpose(ps[:, 2, cs], cv[:, 1, cs], ident[:])
            mm.then_inc(*gd_pe.step("k tokens"))
            for c in range(NT):
                cs = slice(c * P, c * P + P)
                mm = pe.matmul(ps[:, 5, cs], cv[:, 1, cs], cv[:, 1, cs], start=True, stop=True)
            mm.then_inc(*gd_pe.step("k k"))
            pe.wait_ge(*gd_dve.at("unit 0", n))
            for c in range(NT):
                cs = slice(c * P, c * P + P)
                mm = pe.matmul(ps[:, 6, cs], cv[:, 1, cs], cv[:, 0, cs], start=True, stop=True)
            mm.then_inc(*gd_pe.step("k q"))
            pe.wait_ge(*gd_act.at("tokens", n))
            for g in range(NT):
                s3 = 3 * (g % 2)
                pe.wait_ge(*gd_dve.at(f"N {g}", n))
                if g >= 2:
                    pe.wait_ge(*gd_dve.at(f"T {g - 2} 0", n))
                for b in range(4):
                    mm = pe.transpose(ps[:, s3 + 2, b * P:(b + 1) * P], Nn[:, g, b, :], ident[:])
                mm.then_inc(*gd_pe.step(f"N^T {g}"))
            for lv in range(1, LEVELS):
                for st in range(NT + 1):
                    if st < NT:
                        g, s3 = st, 3 * (st % 2)
                        pe.wait_ge(*gd_dve.at(f"T {g} {lv - 1}", n))
                        for b in range(4):
                            mm = pe.matmul(ps[:, s3, b * P:(b + 1) * P], Nn[:, g, b, :], TTg[:, g, b, :], start=True, stop=True)
                        mm.then_inc(*gd_pe.step(f"V {g} {lv}"))
                    if st:
                        g, s3 = st - 1, 3 * ((st - 1) % 2)
                        pe.wait_ge(*gd_act.at(f"V {g} {lv}", n))
                        if g >= 2:
                            pe.wait_ge(*gd_dve.at(f"T {g - 2} {lv}", n))
                        elif lv > 1:
                            pe.wait_ge(*gd_dve.at(f"T {g + 2} {lv - 1}", n))
                        else:
                            pe.wait_ge(*gd_dve.at(f"T {g + 2} 0", n))
                        if lv < LEVELS - 1:
                            for b in range(4):
                                pe.matmul(ps[:, s3 + 1, b * P:(b + 1) * P], Vg[:, g % 2, b, :], Tg[:, g, b, :], start=True, stop=True)
                        for b in range(4):
                            mm = pe.matmul(ps[:, s3 + 2, b * P:(b + 1) * P], Tg[:, g, b, :], Vg[:, g % 2, b, :], start=True, stop=True)
                        mm.then_inc(*gd_pe.step(f"T {g} {lv}"))
            for st in range(NT):
                cc = (st, NT - 1 - st)
                pe.wait_ge(*gd_dve.at(f"S {st}", n))
                if st == 0:
                    pe.wait_ge(*gd_pool.at("T beta", n))
                for d in range(2):
                    cs = slice(cc[d] * P, cc[d] * P + P)
                    mm = pe.matmul(ps[:, 0, 256 * d:256 * d + 256], cv[:, 1, cs], fl(St[:, 2 * d:2 * d + 2, :]), start=True, stop=True)
                mm.then_inc(*gd_pe.step(f"kS {st}"))
                for d in range(2):
                    cs = slice(cc[d] * P, cc[d] * P + P)
                    mm = pe.matmul(ps[:, 1, 256 * d:256 * d + 256], cv[:, 0, cs], fl(St[:, 2 * d:2 * d + 2, :]), start=True, stop=True)
                mm.then_inc(*gd_pe.step(f"qS {st}"))
                pe.wait_ge(*gd_dve.at(f"R {st}", n))
                for b in range(4):
                    mm = pe.matmul(ps[:, 2, b * P:(b + 1) * P], TTg[:, cc[b // 2], b, :], Rr[:, b, :], start=True, stop=True)
                mm.then_inc(*gd_pe.step(f"v' {st}"))
                pe.wait_ge(*gd_dve.at(f"v'd {st}", n))
                for d in range(2):
                    mm = pe.matmul(ps[:, 4, 256 * d:256 * d + 256], ktok[:, cc[d], :], fl(vnd[:, 2 * d:2 * d + 2, :]), start=True, stop=True)
                mm.then_inc(*gd_pe.step(f"dS {st}"))
                pe.wait_ge(*gd_act.at(f"v' {st}", n))
                for b in range(4):
                    mm = pe.matmul(ps[:, 3, b * P:(b + 1) * P], attnT[:, cc[b // 2], b, :], vn[:, b, :], start=True, stop=True)
                mm.then_inc(*gd_pe.step(f"o {st}"))
            pe.wait_ge(*gd_dve.at("gated", n))
            for e in range(2):
                for c in range(NT):
                    mm = pe.transpose(ps[:, 5 + e, c * P:(c + 1) * P], oacc[:, c, e, :], ident[:])
                mm.then_inc(*gd_pe.step(f"o^T {e}"))
            gd_pe.close()

    @runs("scalar")
    def _(act):
        def link(ins, name=None):
            ins.then_inc(*S.step(name))
            act.wait_ge(*S.last())

        after(act, OUT1)
        S = ab_act
        act.wait_ge(*ab_pe.at("ab"))
        link(act.activation(ab.rearrange("p t c -> p (t c)"), ps[:, 0, 0:256], ACT.Copy), "ab")
        act.wait_ge(*ab_dve.at("arguments"))
        link(act.activation(abt[:, :, 0:32], abt[:, :, 0:32], ACT.Abs))
        link(act.activation(abt, abt, ACT.Exp, scale=-1.0))
        link(act.activation(abt, abt, ACT.Ln, bias=1.0))
        link(act.activation(abt[:, :, 32:64], abt[:, :, 32:64], ACT.Exp, scale=-1.0))
        act.wait_ge(ab_in, 64)
        link(act.activation(alog, alog, ACT.Exp), "logs")
        act.wait_ge(*ab_dve.at("sums"))
        for q, src in ((3, pre[:, 3, :, :]), (5, pre[:, 5, :, :]), (6, pre[:, 6, :, :])):
            link(act.activation(src, src, ACT.Exp), "exps")
        ab_act.close()
        S = gd_act
        gd_act.credit(act)
        with act.Fori(0, QKH) as n:
            gd_act.begin(n)
            for s in (gd_pe, gd_dve, gd_pool):
                act.wait_ge(*s.end(n - 1))
            act.wait_ge(*ab_pool.end())
            for j in range(4):
                act.wait_ge(*gd_pe.at(f"proj {j}", n))
                act.activation(raw[:, j, 2:2 + SEQ], ps[:, j, :], ACT.Copy).then_inc(*gd_act.step(f"raw {j}"))
            act.wait_ge(*gd_pe.at("projected", n))
            act.activation(zr.rearrange("p t c -> p (t c)").rearrange("p (b c) -> p b c", b=2), ps[:, 4:6, :], ACT.Copy)\
               .then_inc(*gd_act.step("z raw"))
            for j in range(4):
                act.wait_ge(*gd_dve.at(f"clamped {j}", n))
                link(act.activation(ctmp[:, j, :], ctmp[:, j, :], ACT.Exp, scale=-1.0))
                link(act.activation(ctmp[:, j, :], ctmp[:, j, :], ACT.Ln, bias=1.0))
                link(act.activation(ctmp[:, j, :], ctmp[:, j, :], ACT.Exp, scale=-1.0), f"sigmoid {j}")
            for j in range(2):
                act.wait_ge(*gd_pool.at(f"silu {j}", n))
                act.activation(ctmp[:, j, :], cv[:, j, :], ACT.Square).then_inc(*gd_act.step(f"square {j}"))
            act.wait_ge(*gd_dve.at("z clamped", n))
            link(act.activation(zg, zg, ACT.Exp, scale=-1.0))
            link(act.activation(zg, zg, ACT.Ln, bias=1.0))
            link(act.activation(zg, zg, ACT.Exp, scale=-1.0), "sigmoid z")
            for j in (0, 1):
                act.wait_ge(*gd_dve.at(f"norm eps {j}", n))
                link(act.activation(ctmp[:, j, :], ctmp[:, j, :], ACT.Ln))
                act.activation(ctmp[:, j, :], ctmp[:, j, :], ACT.Exp, scale=-0.5).then_inc(*gd_act.step(f"rsqrt {j}"))
            act.wait_ge(*gd_pe.at("v tokens", n))
            act.activation(vtk.rearrange("p c e t -> p (c e t)").rearrange("p (b t) -> p b t", b=2), ps[:, 3:5, :], ACT.Copy)\
               .then_inc(*gd_act.step())
            act.wait_ge(*gd_pe.at("k k", n))
            act.activation(ktok.rearrange("p c t -> p (c t)"), ps[:, 2, :], ACT.Copy).then_inc(*gd_act.step())
            act.activation(kkS.rearrange("p c t -> p (c t)"), ps[:, 5, :], ACT.Copy).then_inc(*gd_act.step())
            act.wait_ge(*gd_pe.at("k q", n))
            act.activation(qkS.rearrange("p c t -> p (c t)"), ps[:, 6, :], ACT.Copy).then_inc(*gd_act.step("tokens"))
            for c in range(NT):
                act.wait_ge(*gd_dve.at(f"X {c}", n))
                for k in range(2):
                    buf = XD[2 * (c % 2) + k]
                    act.activation(buf, buf, ACT.Exp, scale=(1.0, -1.0)[k]).then_inc(*gd_act.step(f"D {c}"))
            for lv in range(1, LEVELS):
                for g in range(NT):
                    act.wait_ge(*gd_pe.at(f"V {g} {lv}", n))
                    if g >= 2:
                        act.wait_ge(*gd_pe.at(f"T {g - 2} {lv}", n))
                    elif lv > 1:
                        act.wait_ge(*gd_pe.at(f"T {g + 2} {lv - 1}", n))
                    act.activation(Vg[:, g % 2, :, :].rearrange("p b t -> p (b t)"), ps[:, 3 * (g % 2), :], ACT.Copy)\
                       .then_inc(*gd_act.step(f"V {g} {lv}"))
            for st in range(NT):
                cc = (st, NT - 1 - st)
                act.wait_ge(*gd_pe.at(f"qS {st}", n))
                if st:
                    act.wait_ge(*gd_dve.at(f"o {st - 1}", n))
                for b in range(4):
                    act.activation(qs[:, b, :], ps[:, 1, b * P:(b + 1) * P], ACT.Copy, scale=pcg[:, 3, cc[b // 2], b:b + 1])\
                       .then_inc(*gd_act.step(f"qS {st}"))
                act.wait_ge(*gd_pe.at(f"v' {st}", n))
                act.wait_ge(*gd_dve.at(f"v'd {st}", n))
                act.activation(fl(vn), ps[:, 2, :], ACT.Copy).then_inc(*gd_act.step(f"v' {st}"))
            act.wait_ge(*gd_dve.at(f"o {NT - 1}", n))
            act.activation(osqr, oacc, ACT.Square).then_inc(*gd_act.step("o^2"))
            act.wait_ge(*gd_dve.at("o eps", n))
            link(act.activation(rsn, rsn, ACT.Ln))
            act.activation(rsn, rsn, ACT.Exp, scale=-0.5).then_inc(*gd_act.step("o rstd"))
            gd_act.close()

    @runs("gpsimd")
    def _(pool):
        def link(ins, name=None):
            ins.then_inc(*S.step(name))
            pool.wait_ge(*S.last())

        after(pool, OUT1)
        S = ab_pool
        for c0 in (0, SEQ + 2):
            pool.memset(raw[:, :, c0:c0 + 2], 0.0).then_inc(*ab_pool.step())
        pool.tensor_scalar(NLE, LE[:], -1.0, None, ALU.mult).then_inc(*ab_pool.step())
        pool.tensor_scalar(NGE, GE[:], -1.0, None, ALU.mult).then_inc(*ab_pool.step())
        ab_pool.close()
        S = gd_pool
        gd_pool.credit(pool)
        with pool.Fori(0, QKH) as n:
            gd_pool.begin(n)
            pool.wait_ge(*ab_pool.end())
            for s in (gd_pe, gd_dve, gd_act):
                pool.wait_ge(*s.end(n - 1))
            pool.wait_ge(*gd_dve.at("columns", n))
            pool.tensor_tensor(Gb, bcast(pcg[:, 0, :, :].rearrange("p c b -> p (c b)"), P), repeat(ones[:], 16), ALU.mult)\
                .then_inc(*gd_pool.step("G"))
            for t in (Tg, TTg):
                for g in range(NT):
                    pool.tensor_tensor(t[:, g, :, :], repeat(ident[:], 4), repeat(ones[:], 4), ALU.mult)\
                        .then_inc(*gd_pool.step("identity"))
            for j in range(4):
                pool.wait_ge(*gd_act.at(f"sigmoid {j}", n))
                pool.tensor_tensor(cv[:, j, :], cv[:, j, :], ctmp[:, j, :], ALU.mult).then_inc(*gd_pool.step(f"silu {j}"))
            pool.wait_ge(*gd_act.at("sigmoid z", n))
            pool.tensor_tensor(zg, zg, zr, ALU.mult).then_inc(*gd_pool.step("silu z"))
            pool.wait_ge(*gd_act.at("tokens", n))
            for d, m in ((0, LE), (1, GE)):
                pool.tensor_tensor(qkm[:, :, d, :], qkS, repeat(m[:], NT), ALU.mult).then_inc(*gd_pool.step())
            pool.wait_ge(*gd_pool.last())
            for c in range(NT):
                pool.wait_ge(*gd_act.at(f"D {c}", n))
                for d in range(2):
                    pool.tensor_tensor(attnT[:, c, 2 * d:2 * d + 2, :], XD[2 * (c % 2)].rearrange("p (b t) -> p b t", b=4)[:, 2 * d:2 * d + 2, :],
                                       repeat(qkm[:, c, d, :], 2), ALU.mult).then_inc(*gd_pool.step(f"attention {c}"))
            for g in range(NT):
                pool.wait_ge(*gd_dve.at(f"T {g} {LEVELS - 1}", n))
                pool.tensor_tensor(TTg[:, g, :, :], TTg[:, g, :, :], bcast(pcg[:, 1, g, :], P), ALU.mult).then_inc(*gd_pool.step("T beta"))
            gd_pool.close()

    @runs("vector")
    def _(dve):
        def link(ins, name=None):
            ins.then_inc(*S.step(name))
            dve.wait_ge(*S.last())

        after(dve, OUT1)
        S = ab_dve
        dve.wait_ge(ab_in, 64)
        dve.wait_ge(*ab_act.at("ab"))
        link(dve.tensor_tensor(ab[:, :, 0:32], ab[:, :, 0:32], repeat(dtb, NT), ALU.add))
        dve.tensor_copy(abt[:, :, 0:32], ab[:, :, 0:32]).then_inc(*ab_dve.step())
        link(dve.tensor_scalar(abt[:, :, 32:64], ab[:, :, 32:64], -LNCLAMP, None, ALU.max), "arguments")
        dve.wait_ge(*ab_act.at("logs"))
        link(dve.scalar_tensor_tensor(out=pre[:, 0, :, :], in0=ab[:, :, 0:32], scalar=0.0, in1=abt[:, :, 0:32], op0=ALU.max, op1=ALU.add))
        link(dve.scalar_tensor_tensor(out=pre[:, 0, :, :], in0=pre[:, 0, :, :], scalar=-1.0, in1=repeat(alog, NT),
                                      op0=ALU.mult, op1=ALU.mult), "g")
        link(dve.tensor_copy(pre[:, 1, :, :], abt[:, :, 32:64]))
        link(dve.tensor_scalar(pre[:, 2, :, :], pre[:, 1, :, :], -1.0, None, ALU.mult))
        dve.wait_ge(*ab_pe.at("sums"))
        sums = ps[:, 1, 0:256].rearrange("p (t c) -> p t c", t=NT)
        link(dve.tensor_copy(pre[:, 3, :, :], sums[:, :, 0:32]))
        link(dve.tensor_copy(pre[:, 6, :, :], sums[:, :, 32:64]))
        link(dve.tensor_tensor(pre[:, 5, :, :], pre[:, 6, :, :], pre[:, 3, :, :], ALU.subtract), "sums")
        dve.wait_ge(*ab_act.at("exps"))
        link(dve.tensor_scalar(pre[:, 4, :, :], pre[:, 3, :, :], -1.0, None, ALU.mult))
        ab_dve.close()
        S = gd_dve
        gd_dve.credit(dve)
        with dve.Fori(0, QKH) as n:
            gd_dve.begin(n)
            for s in (gd_pe, gd_act, gd_pool):
                dve.wait_ge(*s.end(n - 1))
            src = pre.rearrange("p q t (d h) -> p (q t d) h", d=2)[:, :, bass.ds(n * 2, 2)]
            link(dve.tensor_scalar(pcg.rearrange("p q t (d e) -> p (q t d) e", d=2), src, 1.0, None, ALU.mult), "columns")
            tcol = conv[:].rearrange("p (w c) -> p w c", w=TAPS)
            for j, c0, step in ((0, 0, 1), (1, 8, 1), (2, 16, 2), (3, 17, 2)):
                dve.tensor_scalar(taps[:, :, j], tcol[:, :, bass.ds(n * step + c0, 1)].rearrange("p w c -> p (w c)"), 1.0, None, ALU.mult).then_inc(*gd_dve.step())
            dve.wait_ge(*gd_dve.last())
            for j in range(4):
                dve.wait_ge(*gd_act.at(f"raw {j}", n))
                link(dve.tensor_scalar(cv[:, j, :], raw[:, j, 0:SEQ], taps[:, 0, j:j + 1], None, ALU.mult))
                for w in range(1, TAPS):
                    link(dve.scalar_tensor_tensor(out=cv[:, j, :], in0=raw[:, j, w:w + SEQ], scalar=taps[:, w, j:j + 1],
                                                  in1=cv[:, j, :], op0=ALU.mult, op1=ALU.add), f"conv {j}" if w == TAPS - 1 else None)
                dve.tensor_scalar(ctmp[:, j, :], cv[:, j, :], -LNCLAMP, None, ALU.max).then_inc(*gd_dve.step(f"clamped {j}"))
            dve.wait_ge(*gd_act.at("z raw", n))
            dve.tensor_scalar(zg, zr, -LNCLAMP, None, ALU.max).then_inc(*gd_dve.step("z clamped"))
            for j in range(2):
                dve.wait_ge(*gd_pe.at(f"norm {j}", n))
                link(dve.tensor_scalar(ctmp[:, j, :], ps[:, 6 + j, :], NORM_EPS, None, ALU.add), f"norm eps {j}")
                dve.wait_ge(*gd_act.at(f"rsqrt {j}", n))
                link(dve.scalar_tensor_tensor(out=cv[:, j, :], in0=cv[:, j, :], scalar=(P ** -0.5, 1.0)[j], in1=ctmp[:, j, :],
                                              op0=ALU.mult, op1=ALU.mult), f"unit {j}")
            for c in range(NT):
                dve.wait_ge(*gd_pe.at(f"X {c}", n))
                if c >= 2:
                    dve.wait_ge(*gd_pool.at(f"attention {c - 2}", n))
                    dve.wait_ge(*gd_dve.last())
                dve.tensor_scalar(XD[2 * (c % 2)], ps[:, c % 2, :], 0.0, None, ALU.min).then_inc(*gd_dve.step())
                dve.tensor_scalar(XD[2 * (c % 2) + 1], ps[:, c % 2, :], 0.0, None, ALU.max).then_inc(*gd_dve.step(f"X {c}"))
                if c:
                    triangle(dve, c - 1, n)
            triangle(dve, NT - 1, n)
            dve.wait_ge(*gd_pool.at("identity", n))
            for g in range(NT):
                dve.wait_ge(*gd_pe.at(f"N^T {g}", n))
                hold(dve).then_inc(*gd_dve.step())
                dve.copy_predicated(Tg[:, g, :, :], quad[:, 0, 0:4, :], Nn[:, g, :, :]).then_inc(*gd_dve.step())
                dve.copy_predicated(TTg[:, g, :, :], quad[:, 0, 2:6, :], ps[:, 3 * (g % 2) + 2, :].rearrange("p (b t) -> p b t", b=4))\
                   .then_inc(*gd_dve.step(f"T {g} 0"))
            for lv in range(1, LEVELS):
                for g in range(NT):
                    dve.wait_ge(*gd_pe.at(f"T {g} {lv}", n))
                    hold(dve).then_inc(*gd_dve.step())
                    if lv < LEVELS - 1:
                        dve.copy_predicated(Tg[:, g, :, :], quad[:, lv, 0:4, :], ps[:, 3 * (g % 2) + 1, :].rearrange("p (b t) -> p b t", b=4))\
                           .then_inc(*gd_dve.step())
                    dve.copy_predicated(TTg[:, g, :, :], quad[:, lv, 2:6, :], ps[:, 3 * (g % 2) + 2, :].rearrange("p (b t) -> p b t", b=4))\
                       .then_inc(*gd_dve.step(f"T {g} {lv}"))
            link(dve.memset(St, 0.0), "S 0")
            for st in range(NT):
                cc = (st, NT - 1 - st)
                dve.wait_ge(*gd_pe.at(f"kS {st}", n))
                for b in range(4):
                    dve.scalar_tensor_tensor(out=Rr[:, b, :], in0=ps[:, 0, b * P:(b + 1) * P], scalar=pcg[:, 4, cc[b // 2], b:b + 1],
                                             in1=vtk[:, cc[b // 2], b % 2, :], op0=ALU.mult, op1=ALU.add).then_inc(*gd_dve.step(f"R {st}"))
                dve.wait_ge(*gd_pe.at(f"v' {st}", n))
                for d in range(2):
                    dve.tensor_tensor(vnd[:, 2 * d:2 * d + 2, :], ps[:, 2, 256 * d:256 * d + 256].rearrange("p (e t) -> p e t", e=2),
                                      bcast(pcg[:, 5, cc[d], 2 * d:2 * d + 2], P), ALU.mult).then_inc(*gd_dve.step(f"v'd {st}"))
                dve.wait_ge(*gd_pe.at(f"dS {st}", n))
                dve.wait_ge(*gd_pe.at(f"qS {st}", n))
                for b in range(4):
                    dve.scalar_tensor_tensor(out=St[:, b, :], in0=St[:, b, :], scalar=pcg[:, 6, cc[b // 2], b:b + 1],
                                             in1=ps[:, 4, b * P:(b + 1) * P], op0=ALU.mult, op1=ALU.add).then_inc(*gd_dve.step(f"S {st + 1}"))
                dve.wait_ge(*gd_pe.at(f"o {st}", n))
                dve.wait_ge(*gd_act.at(f"qS {st}", n))
                dve.wait_ge(*gd_dve.last())
                for d in range(2):
                    o, pso, q = oacc[:, cc[d], :, :], ps[:, 3, 256 * d:256 * d + 256].rearrange("p (e t) -> p e t", e=2), qs[:, 2 * d:2 * d + 2, :]
                    if st < NT // 2:
                        dve.tensor_tensor(o, pso, q, ALU.add).then_inc(*gd_dve.step(f"o {st}"))
                    else:
                        link(dve.tensor_tensor(ob[:, 2 * d:2 * d + 2, :], pso, q, ALU.add))
                        dve.tensor_tensor(o, o, ob[:, 2 * d:2 * d + 2, :], ALU.add).then_inc(*gd_dve.step(f"o {st}"))
            dve.wait_ge(*gd_act.at("o^2", n))
            link(dve.tensor_reduce(rsn, osqr.rearrange("p c e t -> p (c e) t"), X_AXIS, ALU.add))
            link(dve.tensor_scalar(rsn, rsn, 1.0 / P, NORM_EPS, ALU.mult, ALU.add), "o eps")
            flat8 = oacc.rearrange("p c e t -> p (c e) t")
            dve.wait_ge(*gd_act.at("o rstd", n))
            link(dve.tensor_tensor(flat8, flat8, bcast(rsn, P), ALU.mult))
            link(dve.tensor_tensor(flat8, flat8, repeat(nw, 8), ALU.mult))
            dve.wait_ge(*gd_pool.at("silu z", n))
            link(dve.tensor_tensor(flat8, flat8, zg.rearrange("p c (e t) -> p (c e) t", e=2), ALU.mult), "gated")
            for e in range(2):
                dve.wait_ge(*gd_pe.at(f"o^T {e}", n))
                dve.tensor_scalar(yT[:, bass.ds(n * 2 + e, 1), :].rearrange("p a t -> p (a t)"), ps[:, 5 + e, :], 1.0, None, ALU.mult)\
                   .then_inc(*gd_dve.step())
            gd_dve.close()

    def triangle(dve, c, n):
        dve.wait_ge(*gd_act.at("tokens", n))
        dve.wait_ge(*gd_act.at(f"D {c}", n))
        buf = XD[2 * (c % 2) + 1].rearrange("p (b t) -> p b t", b=4)
        dve.tensor_tensor(buf, buf, repeat(kkS[:, c, :], 4), ALU.mult).then_inc(*gd_dve.step())
        dve.wait_ge(*gd_dve.last())
        dve.tensor_tensor(Nn[:, c, :, :], buf, bcast(pcg[:, 2, c, :], P), ALU.mult).then_inc(*gd_dve.step(f"N {c}"))

    GDN = [(s, None) for s in (ab_pe, ab_dve, ab_act, ab_pool)] + [(s, QKH) for s in (gd_pe, gd_dve, gd_act, gd_pool)]

    cut[0] = 0
    lng, lnb = take(2, D), take(2, D)
    stats = take(NT, 2, 6)
    mv = take(NT, 2)
    lrs = take(NT)
    wr = take(ND, NGRP + NEXP)
    rb = take(NGRP + NEXP)
    lg = take(NT, NGRP + NEXP)
    desc = take(EPG)
    ohg, gex, geq = take(NT, NGRP), take(NT, NGRP), take(NT, NGRP)
    prod = take(NT * NGRP, EPG)
    e8, e8b, eq8, oh1, oh2 = [take(NT, EPG) for _ in range(5)]
    gmax, gsum4, v1, v2, dd, wa, wb = [take(NT) for _ in range(7)]
    pick = take(2, NT, NEXP)
    both = take(NT, NEXP)
    rank = take(NT, NEXP)
    cnt, tiles, ends, starts, tmp32 = [take(NEXP) for _ in range(5)]
    iota = take(P)
    tokid = take(NT)
    rk, st_, qk_, pk_, sk_ = [take(2 * NT) for _ in range(5)]
    cmpt = take(NTAB, NEXP)
    etf = take(NTAB)
    gh = take(2, 2 * HID)
    hgT = take(2, 2, P)
    ptok = take(NT, PLE)
    pT = take(2, SEQ)
    yTall = yT[:].rearrange("p k t -> p (k t)")
    xg = yTall[:, 0:2 * D].rearrange("p (b d) -> p b d", b=2)
    xgT = yTall[:, 2 * D:4 * D].rearrange("p (b k t) -> p b k t", b=2, k=ND)
    yrow = yTall[:, 4 * D:6 * D].rearrange("p (b d) -> p b d", b=2)
    Ak = yTall[:, 6 * D:7 * D].rearrange("p (j r) -> p j r", j=2 * NT)
    Bk = yTall[:, 7 * D:7 * D + 2 * NT * NTAB].rearrange("p (j n) -> p j n", j=2 * NT)
    sgate = yrow
    idxu = sb("idxu", [P, NTAB], U32)
    slotu = sb("slotu", [P, 2 * NT], U32)
    etab = sb("etab", [1, 64], I32)
    nit = sb("nit", [1, 1], I32)
    spare2 = sb("spare2", [P, 4])
    icol = sb("icol", [P, 2], U32)
    x2d = nc.dram_tensor("x2_rows", (SEQ, D), F32, kind="Internal").ap()
    Wall = W[:].rearrange("p h n -> p (h n)")
    ring = [Wall[:, 4096 * s:4096 * s + 4096].rearrange("p (k n) -> p k n", k=4) for s in range(3)]
    w_out2 = a["gdn_w_out_2"][0].rearrange("(k p) n -> p k n", p=P)
    o2_pe, o2_dve, o2_act, o2_pool = steps("out2_products"), steps("out2_vector"), steps("out2_scalar"), steps("out2_pool")
    o2_in = [sem(f"out2_weights_in{s}") for s in range(3)]
    ln_in, rt_in, x2_out = sem("layernorm_in"), sem("router_in"), sem("x2_rows_out")

    def layernorm(dve, act_steps, S, t, which, name):
        def link(ins, n=None):
            ins.then_inc(*S.step(n))
            dve.wait_ge(*S.last())
        for h in range(2):
            dve.bn_stats(stats[:, t, h, :], xtok[:, t, 512 * h:512 * h + 512]).then_inc(*S.step())
        dve.wait_ge(*S.last())
        link(dve.bn_aggr(mv[:, t, :], stats[:, t, :, :]))
        link(dve.tensor_scalar(lrs[:, t:t + 1], mv[:, t, 1:2], LN_EPS, None, ALU.add), f"{name} eps {t}")
        dve.wait_ge(*act_steps.at(f"{name} rstd {t}"))
        link(dve.tensor_scalar(xtok[:, t, :], xtok[:, t, :], mv[:, t, 0:1], lrs[:, t:t + 1], ALU.subtract, ALU.mult))
        link(dve.tensor_tensor(xtok[:, t, :], xtok[:, t, :], lng[:, which, :], ALU.mult))
        link(dve.tensor_tensor(xtok[:, t, :], xtok[:, t, :], lnb[:, which, :], ALU.add), f"{name} {t}")

    def rsqrt_of(act, dve_steps, S, t, name):
        act.wait_ge(*dve_steps.at(f"{name} eps {t}"))
        act.activation(lrs[:, t:t + 1], lrs[:, t:t + 1], ACT.Ln).then_inc(*S.step())
        act.wait_ge(*S.last())
        act.activation(lrs[:, t:t + 1], lrs[:, t:t + 1], ACT.Exp, scale=-0.5).then_inc(*S.step(f"{name} rstd {t}"))

    @runs("sync")
    def _(sp):
        after(sp, GDN)
        for c in range(4):
            if c == 3:
                sp.wait_ge(*o2_pe.at("y 0"))
            sp.dma_start(ring[c % 3], w_out2[:, 4 * c:4 * c + 4, :]).then_inc(o2_in[c % 3], 16)
        for w in range(2):
            for dst, name in ((lng, "ln_g_2"), (lnb, "ln_b_2")):
                sp.dma_start(dst[:, w, :], flat(name)[:, w * D:(w + 1) * D].to_broadcast([P, D])).then_inc(ln_in, 16)
        for dst, name, c0, n in ((wr, "moe_w_group_2", 0, NGRP), (wr, "moe_w_router_2", NGRP, NEXP)):
            sp.dma_start(dst[:, :, c0:c0 + n], a[name][0].rearrange("(k p) n -> p k n", p=P)).then_inc(rt_in, 16)
        for name, c0, n in (("moe_b_group_2", 0, NGRP), ("moe_b_router_2", NGRP, NEXP)):
            sp.dma_start(rb[:, c0:c0 + n], flat(name).to_broadcast([P, n])).then_inc(rt_in, 16)
        sp.dma_start(ptok, a["p_2"][0, 0].rearrange("(t p) c -> p t c", p=P)).then_inc(rt_in, 16)
        for t in range(NT):
            sp.wait_ge(*o2_dve.at(f"x2 {t}"))
            sp.dma_start(x2d[t * P:(t + 1) * P, :], xtok[:, t, :]).then_inc(x2_out, 16)

    @runs("tensor")
    def _(pe):
        after(pe, GDN)
        for c in range(4):
            pe.wait_ge(o2_in[c % 3], 16 * (c // 3 + 1))
            for t in range(NT):
                for h in range(2):
                    for k in range(4):
                        mm = pe.matmul(ps[:, 2 * t + h, :], yT[:, 4 * c + k, t * P:(t + 1) * P],
                                       ring[c % 3][:, k, 512 * h:512 * h + 512], start=(c == 0 and k == 0),
                                       stop=(c == 3 and k == 3))
                if c == 3:
                    mm.then_inc(*o2_pe.step(f"h {t}"))
            if c < 3:
                mm.then_inc(*o2_pe.step(f"y {c}"))
        for t in range(NT):
            pe.wait_ge(*o2_dve.at(f"x2 {t}"))
        for k in range(ND):
            for t in range(NT):
                mm = pe.transpose(ps[:, k, t * P:(t + 1) * P], xtok[:, t, k * P:(k + 1) * P], ident[:])
            mm.then_inc(*o2_pe.step(f"x^T {k}"))
        pe.wait_ge(*o2_act.at(f"hT {ND - 1}"))
        pe.wait_ge(rt_in, 80)
        NL = NGRP + NEXP
        for t in range(NT):
            for k in range(ND):
                mm = pe.matmul(ps[:, 0, NL * t:NL * t + NL], hT[:, k, t * P:(t + 1) * P], wr[:, k, :], start=(k == 0), stop=(k == ND - 1))
        mm.then_inc(*o2_pe.step("logits"))
        for k in range(2):
            for t in range(NT):
                mm = pe.transpose(ps[:, 1 + k, t * P:(t + 1) * P], ptok[:, t, k * P:(k + 1) * P], ident[:])
        mm.then_inc(*o2_pe.step("p^T"))
        pe.wait_ge(*o2_dve.at("picks"))
        for t in range(NT):
            for u in range(t):
                pe.matmul(ps[:, 3, NEXP * t:NEXP * t + NEXP], ones[:], both[:, u, :], start=(u == 0), stop=False)
            pe.matmul(ps[:, 3, NEXP * t:NEXP * t + NEXP], LT[:], both[:, t, :], start=(t == 0), stop=True)
        for t in range(NT):
            mm = pe.matmul(ps[:, 4, 0:NEXP], ones[:], both[:, t, :], start=(t == 0), stop=(t == NT - 1))
        mm.then_inc(*o2_pe.step("counts"))
        pe.wait_ge(*o2_dve.at("rows"))
        for j in range(2 * NT):
            mm = pe.matmul(ps[:, 5, 0:NTAB], Ak[:, j, :], Bk[:, j, :], start=(j == 0), stop=(j == 2 * NT - 1))
        mm.then_inc(*o2_pe.step("indices"))
        o2_pe.close()

    @runs("scalar")
    def _(act):
        after(act, GDN)
        for t in range(NT):
            rsqrt_of(act, o2_dve, o2_act, t, "x2")
        for k in range(ND):
            act.wait_ge(*o2_pe.at(f"x^T {k}"))
            act.activation(hT[:, k, :], ps[:, k, :], ACT.Copy).then_inc(*o2_act.step(f"hT {k}"))
        act.wait_ge(*o2_pe.at("p^T"))
        act.activation(pT, ps[:, 1:3, :], ACT.Copy).then_inc(*o2_act.step())
        act.wait_ge(*o2_dve.at("shifted groups"))
        act.activation(gex, gex, ACT.Exp).then_inc(*o2_act.step("exp groups"))
        act.wait_ge(*o2_dve.at("v2 - v1"))
        act.activation(dd, dd, ACT.Exp).then_inc(*o2_act.step("exp experts"))
        o2_act.close()

    @runs("gpsimd")
    def _(pool):
        after(pool, GDN)
        for j in range(EPG):
            pool.memset(desc[:, j:j + 1], float(EPG - j)).then_inc(*o2_pool.step())
        pool.iota(iota, [[1, P]], base=0, channel_multiplier=0, allow_small_or_imprecise_dtypes=True).then_inc(*o2_pool.step())
        pool.iota(tokid, [[P, NT]], base=0, channel_multiplier=1, allow_small_or_imprecise_dtypes=True).then_inc(*o2_pool.step())
        o2_pool.close()

    @runs("vector")
    def _(dve):
        def link(ins, name=None):
            ins.then_inc(*o2_dve.step(name))
            dve.wait_ge(*o2_dve.last())

        def first_max(onehot, x, m, eq, n):
            link(dve.tensor_reduce(m, x, X_AXIS, ALU.max))
            link(dve.tensor_tensor(eq, x, bcast(m, n), ALU.is_equal))
            link(dve.tensor_tensor(eq, eq, repeat(desc[:, 0:n], NT), ALU.mult))
            link(dve.tensor_reduce(wa, eq, X_AXIS, ALU.max))
            link(dve.tensor_tensor(onehot, eq, bcast(wa, n), ALU.is_equal))

        after(dve, GDN)
        dve.wait_ge(ln_in, 64)
        for t in range(NT):
            dve.wait_ge(*o2_pe.at(f"h {t}"))
            for h in range(2):
                hs = slice(512 * h, 512 * h + 512)
                dve.scalar_tensor_tensor(out=xtok[:, t, hs], in0=xtok[:, t, hs], scalar=ALPHA, in1=ps[:, 2 * t + h, :],
                                         op0=ALU.mult, op1=ALU.add).then_inc(*o2_dve.step())
            dve.wait_ge(*o2_dve.last())
            layernorm(dve, o2_act, o2_dve, t, 0, "x2")
        dve.wait_ge(*o2_pe.at("logits"))
        dve.wait_ge(rt_in, 80)
        dve.wait_ge(*o2_pool.end())
        link(dve.tensor_tensor(lg, ps[:, 0, 0:NT * (NGRP + NEXP)].rearrange("p (t c) -> p t c", t=NT), repeat(rb, NT), ALU.add))
        gl, el = lg[:, :, 0:NGRP], lg[:, :, NGRP:NGRP + NEXP]
        first_max(ohg, gl, gmax, geq, NGRP)
        link(dve.tensor_tensor(gex, gl, bcast(gmax, NGRP), ALU.subtract), "shifted groups")
        for t in range(NT):
            dve.tensor_tensor(prod[:, NGRP * t:NGRP * t + NGRP, :], el[:, t, :].rearrange("p (g j) -> p g j", g=NGRP),
                              bcast(ohg[:, t, :], EPG), ALU.mult).then_inc(*o2_dve.step())
        dve.wait_ge(*o2_dve.last())
        link(dve.tensor_reduce(e8, prod.rearrange("p (t g) j -> p t j g", t=NT), X_AXIS, ALU.add))
        first_max(oh1, e8, v1, eq8, EPG)
        link(dve.scalar_tensor_tensor(out=e8b, in0=oh1, scalar=-1e30, in1=e8, op0=ALU.mult, op1=ALU.add))
        first_max(oh2, e8b, v2, eq8, EPG)
        link(dve.tensor_tensor(dd, v2, v1, ALU.subtract), "v2 - v1")
        dve.wait_ge(*o2_act.at("exp groups"))
        link(dve.tensor_reduce(gsum4, gex, X_AXIS, ALU.add))
        dve.wait_ge(*o2_act.at("exp experts"))
        link(dve.tensor_scalar(wb, dd, 1.0, None, ALU.add))
        link(dve.tensor_tensor(wb, wb, gsum4, ALU.mult))
        link(dve.reciprocal(wa, wb))
        link(dve.tensor_tensor(wb, wa, dd, ALU.mult))
        for k, oh in ((0, oh1), (1, oh2)):
            for t in range(NT):
                dve.tensor_tensor(pick[:, k, t, :].rearrange("p (g j) -> p g j", g=NGRP), bcast(ohg[:, t, :], EPG),
                                  repeat(oh[:, t, :], NGRP), ALU.mult).then_inc(*o2_dve.step())
        dve.wait_ge(*o2_dve.last())
        link(dve.tensor_tensor(both, pick[:, 0, :, :], pick[:, 1, :, :], ALU.add), "picks")
        dve.wait_ge(*o2_pe.at("counts"))
        link(dve.tensor_copy(cnt, ps[:, 4, 0:NEXP]))
        link(dve.tensor_copy(rank, ps[:, 3, 0:NT * NEXP].rearrange("p (t e) -> p t e", t=NT)))
        link(dve.tensor_scalar(tiles, cnt, 0.0, None, ALU.is_gt))
        for j in range(1, NT):
            link(dve.scalar_tensor_tensor(out=tiles, in0=cnt, scalar=float(P * j), in1=tiles, op0=ALU.is_gt, op1=ALU.add))
        link(dve.tensor_tensor_scan(ends, ones[:, 0:NEXP], tiles, 0.0, ALU.mult, ALU.add))
        link(dve.tensor_tensor(starts, ends, tiles, ALU.subtract))
        for k in range(2):
            ks = slice(NT * k, NT * k + NT)
            link(dve.tensor_tensor(both, pick[:, k, :, :], rank, ALU.mult))
            link(dve.tensor_reduce(rk[:, ks], both, X_AXIS, ALU.add))
            link(dve.tensor_tensor(both, pick[:, k, :, :], repeat(starts, NT), ALU.mult))
            link(dve.tensor_reduce(st_[:, ks], both, X_AXIS, ALU.add))
        link(dve.tensor_scalar(qk_, rk, float(P), None, ALU.is_ge))
        for j in range(2, NT):
            link(dve.scalar_tensor_tensor(out=qk_, in0=rk, scalar=float(P * j), in1=qk_, op0=ALU.is_ge, op1=ALU.add))
        link(dve.scalar_tensor_tensor(out=pk_, in0=qk_, scalar=-float(P), in1=rk, op0=ALU.mult, op1=ALU.add))
        link(dve.tensor_tensor(st_, st_, qk_, ALU.add))
        link(dve.scalar_tensor_tensor(out=sk_, in0=st_, scalar=float(P), in1=pk_, op0=ALU.mult, op1=ALU.add))
        link(dve.tensor_copy(slotu[:], sk_))
        for j in range(2 * NT):
            dve.tensor_scalar(Ak[:, j, :], iota, pk_[:, j:j + 1], None, ALU.is_equal).then_inc(*o2_dve.step())
            dve.tensor_scalar(Bk[:, j, :], iota[:, 0:NTAB], st_[:, j:j + 1], tokid[:, j % NT:j % NT + 1], ALU.is_equal, ALU.mult)\
               .then_inc(*o2_dve.step("rows"))
        link(dve.tensor_tensor(cmpt, bcast(iota[:, 0:NTAB], NEXP), repeat(ends, NTAB), ALU.is_ge))
        link(dve.tensor_reduce(etf, cmpt, X_AXIS, ALU.add))
        link(dve.tensor_scalar(etf, etf, float(NEXP - 1), None, ALU.min))
        link(dve.tensor_copy(etab[:, 0:NTAB], etf[0:1, :]))
        link(dve.tensor_scalar(tmp32[0:1, 0:NTAB // 2], iota[0:1, 0:NTAB // 2], 2.0, ends[0:1, NEXP - 1:NEXP], ALU.mult, ALU.is_lt))
        link(dve.tensor_reduce(etf[0:1, 0:1], tmp32[0:1, 0:NTAB // 2], X_AXIS, ALU.add))
        link(dve.tensor_copy(nit[:], etf[0:1, 0:1]), "tables")
        dve.wait_ge(*o2_pe.at("indices"))
        link(dve.tensor_copy(idxu[:], ps[:, 5, 0:NTAB]))
        o2_dve.close()

    OUT2 = [(s, None) for s in (o2_pe, o2_dve, o2_act, o2_pool)]

    KW = ND * HID
    ex = {e: steps(f"experts_{n}") for e, n in (("pe", "products"), ("dve", "vector"), ("act", "scalar"), ("pool", "pool"))}
    ex0 = {e: steps(f"first_tile_{n}") for e, n in (("pe", "products"), ("dve", "vector"), ("act", "scalar"), ("pool", "pool"))}
    ex_gu = [steps(f"experts_gate_up_in{b}", 16) for b in range(2)]
    ex_dn = [steps(f"experts_down_in{b}", 16) for b in range(2)]
    ex_g = [sem(f"experts_tokens_in{b}") for b in range(2)]
    ex_y = [steps(f"experts_rows_out{b}", 16) for b in range(2)]
    gu0_in, dn0_in, g0_in = sem("first_gate_up_in"), sem("first_down_in"), sem("first_tokens_in")

    def wview(b, j):
        v = W[:, b, KW * j:KW * j + KW]
        return v.rearrange("p (k n) -> p k n", k=ND) if j < 2 else v.rearrange("p (k n) -> p k n", k=2)

    def expert_rows(name, e):
        return a[name][0].rearrange("g e (k p) n -> (g e) p k n", p=P)[bass.ds(e, 1)].rearrange("a p k n -> p (a k) n")

    def iterations(eng):
        eng.wait_ge(*o2_dve.end())
        return eng.value_load(nit[0:1, 0:1], min_val=1, max_val=NTAB // 2)

    @runs("sync")
    def _(sp):
        def load(tile, b, gu, dn, free_gu, free_dn):
            e = sp.value_load(etab[0:1, bass.ds(tile, 1)] if not isinstance(tile, int) else etab[0:1, tile:tile + 1], min_val=0,
                              max_val=NEXP - 1)
            for s in free_gu:
                sp.wait_ge(*s)
            for j, name in enumerate(("moe_w_gate_2", "moe_w_up_2")):
                sp.dma_start(wview(b, j), expert_rows(name, e)).then_inc(*gu())
            for s in free_dn:
                sp.wait_ge(*s)
            sp.dma_start(wview(b, 2), expert_rows("moe_w_down_2", e)).then_inc(*dn())

        n_it = iterations(sp)
        after(sp, OUT2)
        load(0, 0, lambda: (gu0_in, 16), lambda: (dn0_in, 16), (), ())
        for s in ex_gu + ex_dn:
            s.credit(sp)
        with sp.Fori(0, n_it) as i:
            for b in (1, 0):
                ex_gu[b].begin(i)
                ex_dn[b].begin(i)
                load(2 * i + 2 - b, b, lambda: ex_gu[b].step("in"), lambda: ex_dn[b].step("in"),
                     [ex["pe"].at(f"up {b}", i - 1)] + ([ex0["pe"].end()] if b == 0 else []),
                     [ex["pe"].at(f"down {b}", i if b == 0 else i - 1)])
                ex_gu[b].close()
                ex_dn[b].close()

    @runs("gpsimd")
    def _(pool):
        def gather(tile, b, S, then):
            pool.tensor_tensor(spare2[:, 0:1], ones[:, 0:1], ones[:, 0:1], ALU.mult).then_inc(*S.step())
            pool.tensor_copy(icol[:, b:b + 1], idxu[:, bass.ds(tile, 1)] if not isinstance(tile, int) else idxu[:, tile:tile + 1])\
                .then_inc(*S.step())
            pool.wait_ge(*S.last())
            pool.tensor_tensor(spare2[:, 1:2], ones[:, 0:1], ones[:, 0:1], ALU.mult).then_inc(*S.step())
            pool.indirect_dma_start(out=xg[:, b, :], out_offset=None, in_=x2d,
                                    in_offset=bass.IndirectOffsetOnAxis(ap=icol[:, b:b + 1], axis=0)).then_inc(*then)

        n_it = iterations(pool)
        after(pool, OUT2)
        pool.wait_ge(x2_out, 16 * NT)
        gather(0, 0, ex0["pool"], (g0_in, 16))
        ex0["pool"].close()
        S = ex["pool"]
        S.credit(pool)
        pool.wait_ge(g0_in, 16)
        with pool.Fori(0, n_it) as i:
            S.begin(i)
            for b in (1, 0):
                pool.wait_ge(*ex["pe"].at(f"xg^T {b}", i - 1))
                pool.wait_ge(*ex0["pe"].at("xg^T"))
                pool.wait_ge(*S.last())
                gather(2 * i + 2 - b, b, S, (ex_g[b], 16))
            S.close()

    @runs("tensor")
    def _(pe):
        def turn(b):
            for k in range(ND):
                mm = pe.transpose(ps[:, k // 4, P * (k % 4):P * (k % 4) + P], xg[:, b, k * P:(k + 1) * P], ident[:])
            return mm

        def gate_up(b, S, name):
            for j in range(2):
                for k in range(ND):
                    mm = pe.matmul(ps[:, 2 + b, HID * j:HID * j + HID], xgT[:, b, k, :], wview(b, j)[:, k, :], start=(k == 0),
                                   stop=(k == ND - 1))
            mm.then_inc(*S.step(name))

        n_it = iterations(pe)
        after(pe, OUT2)
        S = ex0["pe"]
        pe.wait_ge(g0_in, 16)
        turn(0).then_inc(*S.step("xg^T"))
        pe.wait_ge(*ex0["act"].at("xg^T"))
        pe.wait_ge(gu0_in, 32)
        gate_up(0, S, "up")
        S.close()
        S = ex["pe"]
        S.credit(pe)
        with pe.Fori(0, n_it) as i:
            S.begin(i)
            for b in (1, 0):
                o = 1 - b
                pe.wait_ge(ex_g[b], 16 * (i + 1))
                pe.wait_ge(*ex["act"].at(f"xg^T {o}", i if o else i - 1))
                turn(b).then_inc(*S.step(f"xg^T {b}"))
                pe.wait_ge(*ex["dve"].at(f"hidden {o}", i if o else i - 1))
                pe.wait_ge(*ex0["dve"].end())
                for f in range(2):
                    mm = pe.transpose(ps[:, 4, f * P:(f + 1) * P], gh[:, o, f * P:(f + 1) * P], ident[:])
                mm.then_inc(*S.step(f"h^T {o}"))
                pe.wait_ge(*ex["act"].at(f"xg^T {b}", i))
                pe.wait_ge(*ex_gu[b].at("in", i))
                gate_up(b, S, f"up {b}")
                pe.wait_ge(*ex["act"].at(f"h^T {o}", i))
                pe.wait_ge(*ex_dn[o].at("in", i if o else i - 1))
                pe.wait_ge(dn0_in, 16)
                pe.wait_ge(*ex["dve"].at(f"y {b}", i - 1 if b else i))
                for h in range(2):
                    for f in range(2):
                        mm = pe.matmul(ps[:, 5 + h, :], hgT[:, o, f, :], wview(o, 2)[:, f, 512 * h:512 * h + 512], start=(f == 0),
                                       stop=(f == 1))
                mm.then_inc(*S.step(f"down {o}"))
            S.close()

    @runs("scalar")
    def _(act):
        def turned(b, S, name):
            for c in range(2):
                act.activation(xgT[:, b, 4 * c:4 * c + 4, :].rearrange("p k t -> p (k t)"), ps[:, c, :], ACT.Copy).then_inc(*S.step(name))

        def sigmoid(b, S, name):
            for func, kw in ((ACT.Exp, dict(scale=-1.0)), (ACT.Ln, dict(bias=1.0)), (ACT.Exp, dict(scale=-1.0))):
                act.activation(gh[:, b, 0:HID], gh[:, b, 0:HID], func, **kw).then_inc(*S.step(name))
                act.wait_ge(*S.last())

        n_it = iterations(act)
        after(act, OUT2)
        S = ex0["act"]
        act.wait_ge(*ex0["pe"].at("xg^T"))
        turned(0, S, "xg^T")
        act.wait_ge(*ex0["dve"].at("clamped"))
        sigmoid(0, S, "sigmoid")
        S.close()
        S = ex["act"]
        S.credit(act)
        for s in ex_y:
            s.credit(act)
        act.wait_ge(zeroed, 16)
        with act.Fori(0, n_it) as i:
            S.begin(i)
            for b in (1, 0):
                o = 1 - b
                act.wait_ge(*ex["pe"].at(f"xg^T {b}", i))
                act.wait_ge(*ex["pe"].at(f"up {b}", i - 1))
                act.wait_ge(*S.last())
                turned(b, S, f"xg^T {b}")
                act.wait_ge(*ex["pe"].at(f"h^T {o}", i))
                act.wait_ge(*ex["pe"].at(f"down {o}", i - 1))
                act.activation(hgT[:, o, :, :].rearrange("p f t -> p (f t)"), ps[:, 4, 0:2 * P], ACT.Copy).then_inc(*S.step(f"h^T {o}"))
                act.wait_ge(*ex["dve"].at(f"clamped {b}", i))
                sigmoid(b, S, f"sigmoid {b}")
                act.wait_ge(*ex["dve"].at(f"y {o}", i))
                ex_y[o].begin(i)
                act.dma_start(yd[bass.ds((2 * i + o) * P, P), :], yrow[:, o, :]).then_inc(*ex_y[o].step("out"))
                ex_y[o].close()
            S.close()

    @runs("vector")
    def _(dve):
        def clamp(b, S, name):
            dve.tensor_scalar(gh[:, b, 0:HID], ps[:, 2 + b, 0:HID], -LNCLAMP, None, ALU.max).then_inc(*S.step(name))

        def hidden(b, S, name):
            dve.tensor_tensor(gh[:, b, 0:HID], gh[:, b, 0:HID], ps[:, 2 + b, 0:HID], ALU.mult).then_inc(*S.step())
            dve.wait_ge(*S.last())
            dve.tensor_tensor(gh[:, b, 0:HID], gh[:, b, 0:HID], ps[:, 2 + b, HID:2 * HID], ALU.mult).then_inc(*S.step(name))

        n_it = iterations(dve)
        after(dve, OUT2)
        S = ex0["dve"]
        dve.wait_ge(*ex0["pe"].at("up"))
        clamp(0, S, "clamped")
        dve.wait_ge(*ex0["act"].at("sigmoid"))
        hidden(0, S, "hidden")
        for t in range(NT):
            dve.tensor_scalar(xtok[:, t, :], xtok[:, t, :], ALPHA, None, ALU.mult).then_inc(*S.step())
        S.close()
        S = ex["dve"]
        S.credit(dve)
        with dve.Fori(0, n_it) as i:
            S.begin(i)
            for b in (1, 0):
                o = 1 - b
                dve.wait_ge(*ex["pe"].at(f"up {b}", i))
                dve.wait_ge(*ex["pe"].at(f"h^T {b}", i - 1 if b else i))
                dve.wait_ge(*S.last())
                clamp(b, S, f"clamped {b}")
                dve.wait_ge(*ex["act"].at(f"sigmoid {b}", i))
                hidden(b, S, f"hidden {b}")
                dve.wait_ge(*ex["pe"].at(f"down {o}", i))
                dve.wait_ge(*ex_y[o].end(i - 1))
                for h in range(2):
                    dve.tensor_copy(yrow[:, o, 512 * h:512 * h + 512], ps[:, 5 + h, :]).then_inc(*S.step(f"y {o}"))
            S.close()

    def after_experts(eng, n_it):
        for s in ex.values():
            eng.wait_ge(*s.end(n_it - 1))
        for s in ex_gu + ex_dn + ex_y:
            eng.wait_ge(*s.end(n_it - 1))
        for s in ex_g:
            eng.wait_ge(s, 16 * n_it)

    yg = xg
    co_pool, co_dve = steps("combine_pool"), steps("combine_vector")
    co_in = [sem(f"combine_in{b}") for b in range(2)]

    @runs("gpsimd")
    def _(pool):
        after_experts(pool, iterations(pool))
        for j in range(2 * NT):
            t, k = j // 2, j % 2
            if j >= 2:
                pool.wait_ge(*co_dve.at(f"added {j - 2}"))
            pool.tensor_tensor(spare2[:, 2:3], ones[:, 0:1], ones[:, 0:1], ALU.mult).then_inc(*co_pool.step())
            pool.wait_ge(*co_pool.last())
            pool.indirect_dma_start(out=yg[:, k, :], out_offset=None, in_=yd,
                                    in_offset=bass.IndirectOffsetOnAxis(ap=slotu[:, NT * k + t:NT * k + t + 1], axis=0))\
                .then_inc(co_in[k], 16)
        co_pool.close()

    @runs("vector")
    def _(dve):
        after_experts(dve, iterations(dve))
        for j in range(2 * NT):
            t, k = j // 2, j % 2
            dve.wait_ge(co_in[k], 16 * (t + 1))
            dve.scalar_tensor_tensor(out=xtok[:, t, :], in0=yg[:, k, :], scalar=(wa, wb)[k][:, t:t + 1], in1=xtok[:, t, :],
                                     op0=ALU.mult, op1=ALU.add).then_inc(*co_dve.step(f"added {j}"))
            dve.wait_ge(*co_dve.last())
        co_dve.close()

    MOE = [(co_pool, None), (co_dve, None)]

    wpg = Wall[:, 0:ND * D].rearrange("p (k n) -> p k n", k=ND)
    wpp = Wall[:, ND * D:ND * D + 2 * D].rearrange("p (k n) -> p k n", k=2)
    fin_pe, fin_dve, fin_act = steps("last_products"), steps("last_vector"), steps("last_scalar")
    fin_in = sem("last_weights_in")

    @runs("sync")
    def _(sp):
        after(sp, MOE)
        sp.dma_start(wpg, a["pe_w_gate_2"][0].rearrange("(k p) n -> p k n", p=P)).then_inc(fin_in, 16)
        sp.dma_start(wpp, a["pe_w_proj_2"][0].rearrange("(k p) n -> p k n", p=P)).then_inc(fin_in, 16)
        for t in range(NT):
            sp.wait_ge(*fin_dve.at(f"out {t}"))
            sp.dma_start(out[0, t * P:(t + 1) * P, :], xtok[:, t, :]).then_inc(stores, 16)
        sp.wait_ge(stores, 16 * NT)

    @runs("tensor")
    def _(pe):
        after(pe, MOE)
        for t in range(NT):
            pe.wait_ge(*fin_dve.at(f"x3 {t}"))
        for k in range(ND):
            for t in range(NT):
                mm = pe.transpose(ps[:, k, t * P:(t + 1) * P], xtok[:, t, k * P:(k + 1) * P], ident[:])
            mm.then_inc(*fin_pe.step(f"x^T {k}"))
        pe.wait_ge(*fin_act.at(f"hT {ND - 1}"))
        pe.wait_ge(fin_in, 32)
        for t in range(NT):
            b0 = 4 * (t % 2)
            if t >= 2:
                pe.wait_ge(*fin_dve.at(f"out {t - 2}"))
            for h in range(2):
                for k in range(ND):
                    mm = pe.matmul(ps[:, b0 + h, :], hT[:, k, t * P:(t + 1) * P], wpg[:, k, 512 * h:512 * h + 512], start=(k == 0),
                                   stop=(k == ND - 1))
            mm.then_inc(*fin_pe.step(f"gate {t}"))
            for h in range(2):
                for k in range(2):
                    mm = pe.matmul(ps[:, b0 + 2 + h, :], pT[:, k, t * P:(t + 1) * P], wpp[:, k, 512 * h:512 * h + 512], start=(k == 0),
                                   stop=(k == 1))
            mm.then_inc(*fin_pe.step(f"proj {t}"))
        fin_pe.close()

    @runs("scalar")
    def _(act):
        def link(ins, name=None):
            ins.then_inc(*fin_act.step(name))
            act.wait_ge(*fin_act.last())

        after(act, MOE)
        for t in range(NT):
            rsqrt_of(act, fin_dve, fin_act, t, "x3")
        for k in range(ND):
            act.wait_ge(*fin_pe.at(f"x^T {k}"))
            act.activation(hT[:, k, :], ps[:, k, :], ACT.Copy).then_inc(*fin_act.step(f"hT {k}"))
        for t in range(NT):
            act.wait_ge(*fin_dve.at(f"clamped {t}"))
            s = sgate[:, t % 2, :]
            link(act.activation(s, s, ACT.Exp, scale=-1.0))
            link(act.activation(s, s, ACT.Ln, bias=1.0))
            link(act.activation(s, s, ACT.Exp, scale=-1.0), f"sigmoid {t}")
        fin_act.close()

    @runs("vector")
    def _(dve):
        def link(ins, name=None):
            ins.then_inc(*fin_dve.step(name))
            dve.wait_ge(*fin_dve.last())

        after(dve, MOE)
        for t in range(NT):
            layernorm(dve, fin_act, fin_dve, t, 1, "x3")
        for t in range(NT):
            b0 = 4 * (t % 2)
            s = sgate[:, t % 2, :]
            dve.wait_ge(*fin_pe.at(f"gate {t}"))
            link(dve.tensor_scalar(s.rearrange("p (h c) -> p h c", h=2), ps[:, b0:b0 + 2, :], -LNCLAMP, None, ALU.max), f"clamped {t}")
            dve.wait_ge(*fin_act.at(f"sigmoid {t}"))
            dve.wait_ge(*fin_pe.at(f"proj {t}"))
            link(dve.tensor_tensor(s.rearrange("p (h c) -> p h c", h=2), s.rearrange("p (h c) -> p h c", h=2), ps[:, b0 + 2:b0 + 4, :], ALU.mult))
            link(dve.tensor_tensor(xtok[:, t, :], xtok[:, t, :], s, ALU.add), f"out {t}")
        fin_dve.close()

    block = ctx.enter_context(nc.Block())

    @block.sync
    def _(sp):
        for part in progs["sync"]:
            part(sp)

    @block.tensor
    def _(pe):
        for part in progs["tensor"]:
            part(pe)

    @block.vector
    def _(dve):
        for part in progs["vector"]:
            part(dve)

    @block.scalar
    def _(act):
        for part in progs["scalar"]:
            part(act)

    @block.gpsimd
    def _(pool):
        for part in progs["gpsimd"]:
            part(pool)

    ctx.close()


def compose(nc, names, shapes, dtypes):
    args = {n: nc.dram_tensor(f"in_{n}_dram", s, d, kind="ExternalInput").ap() for n, s, d in zip(names, shapes, dtypes)}
    return args, nc.dram_tensor("out_0_dram", (1, SEQ, D), F32, kind="ExternalOutput").ap()


_INS = ["x", "c", "norm_g", "ada_w", "ada_b", "w_in", "w_out", "tshift_mu", "decay_w0", "decay_w2", "iclr_a0", "iclr_a2",
        "k_k", "k_a", "r_k", "rwkv_ln_w", "rwkv_ln_b", "sb_norm_g", "final_g", "p_2", "gdn_w_in_2", "gdn_conv_w_2",
        "gdn_a_log_2", "gdn_dt_bias_2", "gdn_norm_w_2", "gdn_w_out_2", "ln_g_2", "ln_b_2", "moe_w_group_2",
        "moe_b_group_2", "moe_w_router_2", "moe_b_router_2", "moe_w_gate_2", "moe_w_up_2", "moe_w_down_2",
        "pe_w_gate_2", "pe_w_proj_2"]


def kernel(**inputs):
    import numpy as _np
    import concourse.bacc as _bacc
    from concourse import mybir as _mybir
    from concourse.bass_utils import run_bass_kernel_spmd as _run

    arrays = {f"in_{n}_dram": _np.ascontiguousarray(inputs[n]) for n in _INS}
    shapes = [arrays[f"in_{n}_dram"].shape for n in _INS]
    dtypes = [_mybir.dt.from_np(arrays[f"in_{n}_dram"].dtype) for n in _INS]
    book = {}
    for _ in range(2):
        nc = _bacc.Bacc("TRN2", target_bir_lowering=False, num_devices=1)
        args, out = compose(nc, _INS, shapes, dtypes)
        build(nc, args, out, book)
    r = _run(nc, [arrays], core_ids=[0])
    return r.results[0]["out_0_dram"]
```

```python
from contextlib import ExitStack
import math

import numpy as np
import concourse.bass as bass
from concourse import mybir

F32 = mybir.dt.float32
U8 = mybir.dt.uint8
U32 = mybir.dt.uint32
I32 = mybir.dt.int32
ALU = mybir.AluOpType
ACT = mybir.ActivationFunctionType
X_AXIS = mybir.AxisListType.X

P = 128
SEQ, D = 512, 1024
NT = SEQ // P
ND = D // P
HD = 64
RW = D // 2
NPAIR = RW // P
SHIFT = 3 * RW + 2 * HD
SB0 = SHIFT + RW
NORM_EPS, GN_EPS, LN_EPS = 1e-6, 64e-5, 1e-5
DECAY = math.exp(-0.5)
QKH, VH = 8, 16
TAPS = 5
GDN_CONV = 4096
ALPHA = 2.0 ** 0.25
NEXP, NGRP, EPG, HID = 32, 4, 8, 256
PLE = 256
LEVELS = 7
CLAMP = 80.0
LNCLAMP = 44.0


class Steps:

    def __init__(self, book, sem, name, unit=1):
        self.names = book.setdefault(name, {})
        self.sem, self.unit, self.k, self.i = sem, unit, 0, None
        self.per = self.names.get("per iteration")

    def step(self, name=None):
        self.k += 1
        if name is not None:
            self.names[name] = self.k
        return self.sem, self.unit

    def value(self, k, i):
        k = k * self.unit
        return k if i is None else (i + 1) * (self.unit * (self.per or 1)) + k

    def at(self, name, i=None):
        return self.sem, self.value(self.names.get(name, 1), i)

    def last(self):
        return self.sem, self.value(self.k, self.i)

    def end(self, i=None):
        if i is None:
            return self.sem, self.unit * self.names.get("steps", 1)
        return self.sem, (i + 2) * (self.unit * (self.per or 1))

    def final(self, n):
        return self.end(n - 1)

    def credit(self, eng):
        eng.nop().then_inc(self.sem, self.unit * (self.per or 1))

    def begin(self, i):
        self.k, self.i = 0, i

    def close(self):
        self.names["per iteration" if self.i is not None else "steps"] = self.k


def bcast(ap, n):
    return ap.unsqueeze(2).to_broadcast([ap.shape[0], ap.shape[1], n])


def repeat(ap, n):
    return ap.unsqueeze(1).to_broadcast([ap.shape[0], n, ap.shape[1]])


def build(nc, a, out, book):
    ctx = ExitStack()

    def sb(name, shape, dt=F32):
        return ctx.enter_context(nc.sbuf_tensor(name, shape, dt))

    def sem(name):
        return ctx.enter_context(nc.semaphore(name))

    def steps(name, unit=1):
        return Steps(book, sem(name), name, unit)

    xtok = sb("xtok", [P, NT, D])
    hT = sb("hT", [P, ND, SEQ])
    yT = sb("yT", [P, 2 * ND, SEQ])
    W = sb("W", [P, 2, 6 * D])
    ident = sb("ident", [P, P])
    ones = sb("ones", [P, P])
    pairs = sb("pairs", [P, P])
    LE = sb("LE", [P, P])
    GE = sb("GE", [P, P])
    LT = sb("LT", [P, P])
    GT = sb("GT", [P, P])
    quad = sb("quad", [P, LEVELS, 6, P], U8)
    par = sb("par", [P, 61])
    conv = sb("conv", [P, 160])
    small = sb("small", [P, 64])
    lnshift = sb("lnshift", [P, 1])
    spare = sb("spare", [P, 32])
    arena = sb("arena", [P, 20480])
    zeros = sb("zeros", [P, 256])
    ps = ctx.enter_context(nc.psum_tensor("ps", [P, 8, 512], F32))
    MAXT = (2 * SEQ - NEXP) // P + NEXP
    MAXIT = (MAXT + 1) // 2
    NTAB = 2 * MAXIT + 2
    assert NTAB <= 64
    yd = nc.dram_tensor("expert_rows", (NTAB * P, D), F32, kind="Internal").ap()
    zeroed = sem("expert_rows_zeroed")
    cut = [0]

    def take(*shape):
        n = math.prod(shape)
        ap = arena[:, cut[0]:cut[0] + n]
        cut[0] += n
        assert cut[0] <= arena.shape[1], cut[0]
        if len(shape) == 2:
            return ap.rearrange("p (a b) -> p a b", a=shape[0])
        if len(shape) == 3:
            return ap.rearrange("p (a b c) -> p a b c", a=shape[0], b=shape[1])
        if len(shape) == 4:
            return ap.rearrange("p (a b c d) -> p a b c d", a=shape[0], b=shape[1], c=shape[2])
        return ap

    held = [0]

    def hold(dve):
        held[0] += 1
        k = held[0] % 32
        return dve.tensor_copy(spare[:, k:k + 1], ones[:, 0:1])

    def rows(name):
        return a[name].flatten().rearrange("(r c) -> r c", c=P)

    def flat(name):
        return a[name].flatten().rearrange("(a n) -> a n", a=1)

    stores = sem("stores")
    progs = {"sync": [], "tensor": [], "vector": [], "scalar": [], "gpsimd": []}

    def runs(engine):
        return progs[engine].append

    PAR_G, PAR_C, PAR_MU, PAR_PAIR, PAR_SBG, PAR_MULORA = 0, 8, 16, 16, 56, 60
    PARAMS = [("norm_g", PAR_G, 8), ("c", PAR_C, 8), ("decay_w0", 28, 4), ("iclr_a0", 32, 4), ("k_k", 36, 4),
              ("k_a", 40, 4), ("r_k", 44, 4), ("rwkv_ln_w", 48, 4), ("rwkv_ln_b", 52, 4), ("sb_norm_g", 56, 4)]

    cut[0] = 0
    prm = take(P)
    cnv = take(2, P)
    adab = take(3 * D)
    acc = take(3 * D)
    xs = take(NT, D)
    gate = sb("gate", [P, D])
    modc = take(24)
    ct = take(4, 8)
    gs = take(8)
    sq = take(D)
    qtmp = take(2 * P)
    ssum = take(4)
    rstd = take(4)

    su_pe, su_dve, su_act, su_pool = steps("setup_products"), steps("setup_vector"), steps("setup_scalar"), steps("setup_pool")
    x_in, par_in, ada_in = sem("x_in"), sem("par_in"), [sem(f"ada_in{q}") for q in range(4)]
    adab_in = sem("adab_in")
    CH = 3 * D // 4
    ada = [W[:, 0, :], W[:, 1, :], yT[:].rearrange("p k t -> p (k t)")[:, 0:ND * CH], take(ND * CH)]

    @runs("sync")
    def _(sp):
        sp.wait_ge(par_in, 16 * (len(PARAMS) + 4))
        for q in range(4):
            src = a["ada_w"][0].rearrange("(k p) n -> p k n", p=P)[:, :, q * CH:(q + 1) * CH]
            sp.dma_start(ada[q].rearrange("p (k n) -> p k n", k=ND), src).then_inc(ada_in[q], 16)
            if q == 1:
                sp.dma_start(xtok[:], a["x"][0].rearrange("(t p) d -> p t d", p=P)).then_inc(x_in, 16)

    @runs("scalar")
    def _(act):
        act.preload_act_table_set("natural_log_exp_and_others")
        for name, at, n in PARAMS:
            act.dma_start(prm[at:at + n, :], rows(name)).then_inc(par_in, 16)
        act.dma_start(prm[16:28, :], rows("tshift_mu")[0:12, :]).then_inc(par_in, 16)
        act.dma_start(prm[60:61, :], rows("tshift_mu")[12:13, :]).then_inc(par_in, 16)
        for h in range(2):
            act.dma_start(cnv[0:80, h, :], rows("gdn_conv_w_2")[80 * h:80 * h + 80, :]).then_inc(par_in, 16)
        act.wait_ge(*su_pool.at("ada_b zeros"))
        act.dma_start(adab[0:1, :], flat("ada_b")).then_inc(adab_in, 16)
        act.wait_ge(*su_dve.at("c clamped"))
        act.activation(ct[:, 1, :], ct[:, 0, :], ACT.Exp, scale=-1.0).then_inc(*su_act.step("exp c"))
        act.wait_ge(x_in, 16)
        for t in range(NT):
            act.wait_ge(*su_act.last())
            act.activation(sq, xtok[:, t, :], ACT.Square, accum_out=ssum[:, t:t + 1]).then_inc(*su_act.step())
        act.wait_ge(*su_dve.at("ssum eps"))
        act.activation(rstd, rstd, ACT.Ln).then_inc(*su_act.step())
        act.wait_ge(*su_act.last())
        act.activation(rstd, rstd, ACT.Exp, scale=-0.5).then_inc(*su_act.step("rstd"))
        act.wait_ge(*su_dve.at("scales"))
        for k in range(ND):
            act.wait_ge(*su_pe.at(f"x^T {k}"))
            act.activation(hT[:, k, :], ps[:, k, :], ACT.Identity, scale=gs[:, k:k + 1],
                           bias=modc[:, k:k + 1]).then_inc(*su_act.step(f"h {k}"))
        su_act.close()

    @runs("gpsimd")
    def _(pool):
        def link(ins, name=None):
            ins.then_inc(*su_pool.step(name))
            pool.wait_ge(*su_pool.last())

        def keep(out_, in_, pattern, op, base, mult):
            link(pool.affine_select(out=out_, in_=in_, pattern=pattern, compare_op=op, fill=0.0, base=base,
                                    channel_multiplier=mult))

        link(pool.memset(ones[:], 1.0))
        keep(GE[:], ones[:], [[-1, P]], ALU.is_ge, 0, 1)
        keep(ident[:], GE[:], [[1, P]], ALU.is_ge, 0, -1)
        pool.nop().then_inc(*su_pool.step("ident"))
        link(pool.memset(adab, 0.0), "ada_b zeros")
        pool.memset(zeros[:], 0.0).then_inc(*su_pool.step("zeros"))
        keep(LE[:], ones[:], [[1, P]], ALU.is_ge, 0, -1)
        keep(LT[:], ones[:], [[1, P]], ALU.is_gt, 0, -1)
        keep(GT[:], ones[:], [[-1, P]], ALU.is_gt, 0, 1)
        keep(pairs[:, 0:HD], ones[:, 0:HD], [[0, HD]], ALU.is_gt, HD, -1)
        keep(pairs[:, HD:P], ones[:, HD:P], [[0, HD]], ALU.is_ge, -HD, 1)
        q0, q1 = qtmp[:, 0:P], qtmp[:, P:2 * P]
        for lv in range(LEVELS):
            half = 1 << lv
            blocks = P // (2 * half)
            pool.memset(q0, 0.0).then_inc(*su_pool.step())
            link(pool.memset(q1, 0.0))
            low = q0.rearrange("p (b h r) -> p b h r", h=2, r=half)[:, :, 0, :]
            up = q1.rearrange("p (b h r) -> p b h r", h=2, r=half)[:, :, 1, :]
            src = ones[:].rearrange("p (b h r) -> p b h r", h=2, r=half)[:, :, 0, :]
            pat = [[-2 * half, blocks], [0, half]]
            neg = [[2 * half, blocks], [0, half]]
            keep(low, src, pat, ALU.is_ge, -half, 1)
            keep(low, low, neg, ALU.is_gt, 2 * half, -1)
            keep(up, src, pat, ALU.is_ge, 0, 1)
            keep(up, up, neg, ALU.is_gt, half, -1)
            for s, q in ((0, q0), (1, q0), (2, q1), (3, q1), (4, q0), (5, q0)):
                pool.tensor_copy(quad[:, lv, s, :], q).then_inc(*su_pool.step())
            pool.wait_ge(*su_pool.last())
        su_pool.close()

    @runs("tensor")
    def _(pe):
        pe.wait_ge(*su_pool.at("ident"))
        pe.wait_ge(par_in, 16 * (len(PARAMS) + 4))
        pe.transpose(ps[:, 0, 0:61], prm[0:61, :], ident[0:61, 0:61])
        for h in range(2):
            pe.transpose(ps[:, 0, P + 80 * h:P + 80 * h + 80], cnv[0:80, h, :], ident[0:80, 0:80])\
              .then_inc(*su_pe.step("columns"))
        pe.wait_ge(*su_dve.at("ada_b"))
        for j in range(24):
            mm = pe.matmul(ps[:, 1, j:j + 1], acc[:, j * P:(j + 1) * P], ones[:, 0:1], start=True, stop=True)
        mm.then_inc(*su_pe.step("mod columns"))
        for h in range(2):
            pe.matmul(ps[:, 2 + h, :], ones[:], acc[:, 2 * D + 512 * h:2 * D + 512 * h + 512], start=True, stop=True)\
              .then_inc(*su_pe.step("gate rows"))
        pe.wait_ge(*su_dve.at("gate"))
        pe.wait_ge(*su_dve.at("xs"))
        for k in range(ND):
            for t in range(NT):
                mm = pe.transpose(ps[:, k, t * P:(t + 1) * P], xs[:, t, k * P:(k + 1) * P], ident[:])
            mm.then_inc(*su_pe.step(f"x^T {k}"))
        su_pe.close()

    @runs("vector")
    def _(dve):
        def link(ins, name=None):
            ins.then_inc(*su_dve.step(name))
            dve.wait_ge(*su_dve.last())

        dve.wait_ge(*su_pe.at("columns"))
        dve.tensor_copy(par[:], ps[:, 0, 0:61]).then_inc(*su_dve.step())
        link(dve.tensor_copy(conv[:], ps[:, 0, P:P + 160]))
        link(dve.tensor_scalar(ct[:, 0, :], par[:, PAR_C:PAR_C + 8], -CLAMP, None, ALU.max), "c clamped")
        dve.wait_ge(*su_act.at("exp c"))
        link(dve.tensor_scalar(ct[:, 1, :], ct[:, 1, :], 1.0, None, ALU.add))
        link(dve.reciprocal(ct[:, 2, :], ct[:, 1, :]))
        link(dve.tensor_tensor(ct[:, 3, :], ct[:, 2, :], par[:, PAR_C:PAR_C + 8], ALU.mult))
        dve.wait_ge(adab_in, 16)
        for q in range(4):
            dve.wait_ge(ada_in[q], 16)
            w = ada[q].rearrange("p (k n) -> p k n", k=ND)
            part = acc[:, q * CH:(q + 1) * CH]
            for k in range(ND):
                link(dve.scalar_tensor_tensor(out=part, in0=w[:, k, :], scalar=ct[:, 3, k:k + 1],
                                              in1=adab[:, q * CH:(q + 1) * CH] if k == 0 else part,
                                              op0=ALU.mult, op1=ALU.add), f"ada {q}" if k == ND - 1 else None)
        dve.nop().then_inc(*su_dve.step("ada_b"))
        dve.wait_ge(x_in, 16)
        dve.wait_ge(*su_act.at("exp c"))
        dve.wait_ge(*su_act_sums())
        link(dve.tensor_scalar(rstd, ssum, 1.0 / D, NORM_EPS, ALU.mult, ALU.add), "ssum eps")
        dve.wait_ge(*su_pe.at("mod columns"))
        link(dve.tensor_copy(modc, ps[:, 1, 0:24]))
        link(dve.scalar_tensor_tensor(out=gs, in0=modc[:, 8:16], scalar=1.0, in1=par[:, PAR_G:PAR_G + 8],
                                      op0=ALU.add, op1=ALU.mult), "scales")
        dve.wait_ge(*su_pe.at("gate rows"))
        dve.tensor_copy(gate[:, 0:512], ps[:, 2, :]).then_inc(*su_dve.step())
        link(dve.tensor_copy(gate[:, 512:D], ps[:, 3, :]), "gate")
        dve.wait_ge(*su_act.at("rstd"))
        for t in range(NT):
            dve.tensor_scalar(xs[:, t, :], xtok[:, t, :], rstd[:, t:t + 1], None, ALU.mult)\
               .then_inc(*su_dve.step("xs"))
        su_dve.close()

    def su_act_sums():
        return su_act.sem, su_act.names.get("exp c", 1) + NT

    SETUP = [su_pe, su_dve, su_act, su_pool]
    SETUP = [(s, None) for s in SETUP]

    def after(eng, done):
        for s, n in done:
            eng.wait_ge(*(s.end() if n is None else s.final(n)))

    cut[0] = 0
    mixraw = take(3, SEQ + 1)
    loraraw = take(SEQ + 1)
    gpair = take(SEQ)
    lora = take(SEQ)
    rkv = take(3, SEQ)
    sg = take(SEQ)
    sig = take(2, SEQ)
    tmp2 = take(2, SEQ)
    gsum = take(SEQ)
    E1 = take(SEQ)
    E2 = take(SEQ)
    E3 = take(SEQ)
    kk = take(SEQ)
    AR = take(NT, 2, P)
    BK = take(2, SEQ)
    tok = take(NT, 3, P)
    pc = take(16)
    mid = take(4)
    fac = take(2, 4)
    S0 = take(HD)
    S1 = take(HD)
    RU = take(P)
    U = take(P)
    bonus = take(SEQ)
    maskQ = take(4, P)
    pairTS = cut[0]
    N_ = take(2, NT, P)
    T_ = take(2, NT, P)
    TT_ = take(2, NT, P)
    wq = W[:, 0, 0:4096].rearrange("p (k j c) -> p k j c", k=ND, j=4)
    w2a2 = W[:, 0, 4096:4096 + P]
    wlora = W[:, 0, 5120:6144].rearrange("p (k c) -> p k c", k=ND)
    Vs = W[:, 1, 4096:5120].rearrange("p (h c t) -> p h c t", h=2, c=NT)
    ysb, ysq = W[:, 1, 5120:5632], W[:, 1, 5632:6144]
    Q = yT[:, ND:2 * ND, :].rearrange("p k n -> p (k n)").rearrange("p (h c j t) -> p h c j t", h=2, c=NT, j=4)

    lo_pe, lo_dve, lo_act, lo_pool = steps("lora_products"), steps("lora_vector"), steps("lora_scalar"), steps("lora_pool")
    rw_pe, rw_dve, rw_act, rw_pool = steps("rwkv_products"), steps("rwkv_vector"), steps("rwkv_scalar"), steps("rwkv_pool")
    lora_in, rw0_in, rw_in = sem("lora_in"), sem("rwkv_first_weights_in"), steps("rwkv_weights_in", 16)
    rw2_in = steps("rwkv_second_factors_in", 16)
    wq_cols = (0, RW, 2 * RW, SHIFT)
    assert max(wq_cols) + (NPAIR + 1) * P <= a["w_in"].shape[-1]
    w_in = a["w_in"][0].rearrange("(k p) n -> p k n", p=P)

    @runs("sync")
    def _(sp):
        sp.wait_ge(*su_dve.at("ada 0"))
        sp.dma_start(wlora, w_in[:, :, 3 * RW:SHIFT]).then_inc(lora_in, 16)
        for j, c0 in enumerate(wq_cols):
            sp.dma_start(wq[:, :, j, :], w_in[:, :, c0:c0 + P]).then_inc(rw0_in, 16)
        rw_in.credit(sp)
        rw2_in.credit(sp)
        sp.wait_ge(*lo_pe.end())
        with sp.Fori(0, NPAIR) as n:
            rw_in.begin(n)
            rw2_in.begin(n)
            sp.wait_ge(*rw_pe.at("decay a", n - 1))
            for r, name in ((slice(0, HD), "decay_w2"), (slice(HD, P), "iclr_a2")):
                sp.dma_start(w2a2[r, :], a[name][0][:, bass.ds(n * P, P)]).then_inc(*rw2_in.step("in"))
            rw2_in.close()
            sp.wait_ge(*rw_pe.at("projected", n - 1))
            for j, c0 in enumerate(wq_cols):
                sp.dma_start(wq[:, :, j, :], w_in[:, :, bass.ds(n * P + (c0 + P), P)]).then_inc(*rw_in.step("in"))
            rw_in.close()

    @runs("tensor")
    def _(pe):
        after(pe, SETUP)
        pe.wait_ge(lora_in, 16)
        for k in range(ND):
            mm = pe.matmul(ps[:, 0, :], wlora[:, k, :], hT[:, k, :], start=(k == 0), stop=(k == ND - 1))
        mm.then_inc(*lo_pe.step("z"))
        pe.wait_ge(rw0_in, 64)
        for j in range(4):
            for k in range(ND):
                mm = pe.matmul(ps[:, 1 + j, :], wq[:, k, j, :], hT[:, k, :], start=(k == 0), stop=(k == ND - 1))
            mm.then_inc(*lo_pe.step(f"proj {j}"))
        lo_pe.close()

        def project_next(j, part):
            for k in range(2 * part, 2 * part + 2):
                mm = pe.matmul(ps[:, 5 + j % 2, :], wq[:, k, j, :], hT[:, k, :], start=(k == 0), stop=(k == ND - 1))
            if part == 3:
                mm.then_inc(*rw_pe.step("projected" if j == 3 else f"proj {j}"))

        rw_pe.credit(pe)
        with pe.Fori(0, NPAIR) as n:
            rw_pe.begin(n)
            for s in (rw_dve, rw_act, rw_pool):
                pe.wait_ge(*s.end(n - 1))
            pe.wait_ge(*lo_act.end())
            pe.wait_ge(*lo_dve.end())
            pe.wait_ge(*rw2_in.at("in", n))
            for j in range(2):
                r = slice(j * HD, j * HD + HD)
                mm = pe.matmul(ps[:, 4 + j, :], w2a2[r, :], lora[r, :], start=True, stop=True)
                mm.then_inc(*rw_pe.step("decay a"))
            pe.wait_ge(*rw_act.at("kk^2", n))
            pe.matmul(ps[:, 6, :], pairs[:], tmp2[:, 0, :], start=True, stop=True).then_inc(*rw_pe.step("kk sums"))
            pe.wait_ge(*rw_dve.at("rkr", n))
            pe.matmul(ps[:, 7, :], pairs[:], tmp2[:, 1, :], start=True, stop=True).then_inc(*rw_pe.step("bonus sums"))
            pe.wait_ge(*rw_dve.at("factors", n))
            pe.wait_ge(*rw_pool.at("factors", n))
            for c in range(NT):
                cs = slice(c * P, c * P + P)
                if c:
                    pe.wait_ge(*rw_act.at(f"tok {c - 1}", n))
                for j, src in enumerate((BK[:, 0, cs], BK[:, 1, cs], rkv[:, 2, cs])):
                    mm = pe.transpose(ps[:, 0, j * P:(j + 1) * P], src, ident[:])
                mm.then_inc(*rw_pe.step(f"tok {c}"))
            pe.wait_ge(*rw_dve.at("bonus", n))
            pe.wait_ge(*rw_act.at(f"tok {NT - 1}", n))
            for h in range(2):
                r = slice(h * HD, h * HD + HD)
                for c in range(NT):
                    cs = slice(c * P, c * P + P)
                    if h:
                        pe.wait_ge(*rw_dve.at(f"Q 0 {c}", n))
                    ar = AR[r, c, :, :].rearrange("p j t -> p (j t)")
                    pe.matmul(ps[:, 1 + c, 0:256], BK[r, 0, cs], ar, start=True, stop=True)
                    pe.matmul(ps[:, 1 + c, 256:512], BK[r, 1, cs], ar, start=True, stop=True)\
                      .then_inc(*rw_pe.step(f"Q {h} {c}"))
                    mm = pe.matmul(ps[:, 5 + h, cs], AR[r, c, 0, :], BK[r, 0, cs], start=True, stop=True)
                mm.then_inc(*rw_pe.step(f"A {h}"))
            pe.wait_ge(*rw_dve.at(f"Q 1 {NT - 1}", n))
            for lv in range(1, LEVELS):
                for h in range(2):
                    pe.wait_ge(*rw_dve.at(f"T {h} {lv - 1}", n))
                    for c in range(NT):
                        mm = pe.matmul(ps[:, 1 + 3 * h, c * P:(c + 1) * P], N_[:, h, c, :], TT_[:, h, c, :], start=True, stop=True)
                    mm.then_inc(*rw_pe.step(f"V {h} {lv}"))
                for h in range(2):
                    pe.wait_ge(*rw_act.at(f"V {h} {lv}", n))
                    if lv < LEVELS - 1:
                        for c in range(NT):
                            mm = pe.matmul(ps[:, 2 + 3 * h, c * P:(c + 1) * P], Vs[:, h, c, :], T_[:, h, c, :], start=True, stop=True)
                        mm.then_inc(*rw_pe.step(f"T {h} {lv}"))
                    for c in range(NT):
                        mm = pe.matmul(ps[:, 3 + 3 * h, c * P:(c + 1) * P], T_[:, h, c, :], Vs[:, h, c, :], start=True, stop=True)
                    mm.then_inc(*rw_pe.step(f"TT {h} {lv}"))
            for h in range(2):
                pe.wait_ge(*rw_dve.at(f"T {h} {LEVELS - 1}", n))
            for c in range(NT):
                cs = slice(c * P, c * P + P)
                pe.wait_ge(*rw_dve.at(f"S0 {c}", n))
                for h in range(2):
                    r = slice(h * HD, h * HD + HD)
                    pe.matmul(ps[:, 4 * h, 0:HD], AR[r, c, 0, :], S0[r, :], start=True, stop=False)
                    mm = pe.matmul(ps[:, 4 * h, 0:HD], Q[:, h, c, 2, :], tok[:, c, 2, r], start=False, stop=True)
                mm.then_inc(*rw_pe.step(f"RU {c}"))
                if c == 0:
                    pe.wait_ge(*rw_in.at("in", n))
                if c >= 2:
                    pe.wait_ge(*rw_act.at(f"raw {c - 2}", n))
                project_next(c, 0)
                pe.wait_ge(*rw_act.at(f"RU {c}", n))
                for h in range(2):
                    r = slice(h * HD, h * HD + HD)
                    mm = pe.matmul(ps[:, 1, r], TT_[:, h, c, :], RU[:, r], start=True, stop=True)
                mm.then_inc(*rw_pe.step(f"U {c}"))
                project_next(c, 1)
                pe.wait_ge(*rw_act.at(f"U {c}", n))
                for h in range(2):
                    r = slice(h * HD, h * HD + HD)
                    pe.matmul(ps[r, 2, 0:HD], tok[:, c, 0, r], U[:, r], start=True, stop=False)
                    mm = pe.matmul(ps[r, 2, 0:HD], tok[:, c, 1, r], tok[:, c, 2, r], start=False, stop=True)
                mm.then_inc(*rw_pe.step(f"S1 {c}"))
                if c < NT - 1:
                    project_next(c, 2)
                for h in range(2):
                    r = slice(h * HD, h * HD + HD)
                    pe.matmul(ps[r, 7, cs], U[:, r], Q[:, h, c, 1, :], start=True, stop=False)
                    pe.matmul(ps[r, 7, cs], tok[:, c, 2, r], Q[:, h, c, 3, :], start=False, stop=False)
                    mm = pe.matmul(ps[r, 7, cs], S0[r, :], AR[r, c, 1, :], start=False, stop=True)
                mm.then_inc(*rw_pe.step(f"Y {c}"))
                if c < NT - 1:
                    project_next(c, 3)
            pe.wait_ge(*rw_act.at("Y", n))
            pe.matmul(ps[:, 3, :], pairs[:], ysb, start=True, stop=True).then_inc(*rw_pe.step("mean"))
            project_next(NT - 1, 2)
            pe.wait_ge(*rw_act.at("Y dev^2", n))
            pe.matmul(ps[:, 4, :], pairs[:], ysq, start=True, stop=True).then_inc(*rw_pe.step("var"))
            project_next(NT - 1, 3)
            rw_pe.close()

    @runs("scalar")
    def _(act):
        def link(ins, name=None):
            ins.then_inc(*S.step(name))
            act.wait_ge(*S.last())

        after(act, SETUP)
        S = lo_act
        act.wait_ge(*lo_pool.end())
        act.wait_ge(*lo_pe.at("z"))
        link(act.activation(loraraw[:, 1:SEQ + 1], ps[:, 0, :], ACT.Copy), "z")
        act.wait_ge(*lo_dve.at("clamped"))
        link(act.activation(tmp2[0:HD, 0, :], tmp2[0:HD, 0, :], ACT.Exp, scale=-2.0))
        link(act.activation(tmp2[0:HD, 0, :], tmp2[0:HD, 0, :], ACT.Ln, bias=1.0))
        link(act.activation(tmp2[0:HD, 0, :], tmp2[0:HD, 0, :], ACT.Exp, scale=-1.0), "exp")
        for j in range(4):
            act.wait_ge(*lo_pe.at(f"proj {j}"))
            act.activation(mixraw[:, j, 1:SEQ + 1] if j < 3 else gpair, ps[:, 1 + j, :], ACT.Copy).then_inc(*lo_act.step())
        lo_act.close()
        S = rw_act
        rw_act.credit(act)
        with act.Fori(0, NPAIR) as n:
            rw_act.begin(n)
            act.wait_ge(*lo_dve.end())
            for s in (rw_pe, rw_dve, rw_pool):
                act.wait_ge(*s.end(n - 1))
            act.wait_ge(*rw_dve.at("sig clamped", n))
            link(act.activation(sig, sig, ACT.Exp, scale=-1.0))
            link(act.activation(sig, sig, ACT.Ln, bias=1.0))
            link(act.activation(sig, sig, ACT.Exp, scale=-1.0), "sigmoids")
            act.wait_ge(*rw_dve.at("k", n))
            act.activation(tmp2[:, 0, :], rkv[:, 1, :], ACT.Square, scale=pc[:, 5:6]).then_inc(*rw_act.step("kk^2"))
            act.wait_ge(*rw_dve.at("g clamped", n))
            link(act.activation(sg, sg, ACT.Exp, scale=-1.0))
            link(act.activation(sg, sg, ACT.Ln, bias=1.0))
            link(act.activation(sg, sg, ACT.Exp, scale=-1.0), "sigmoid g")
            act.wait_ge(*rw_dve.at("kk clamped", n))
            link(act.activation(kk, kk, ACT.Ln, scale=2.0 ** 24))
            act.activation(kk, kk, ACT.Exp, scale=-0.5, bias=lnshift[:, 0:1]).then_inc(*rw_act.step("kk rsqrt"))
            act.wait_ge(*rw_dve.at("centred", n))
            act.activation(fac[:, 0, :], mid, ACT.Exp, scale=-DECAY).then_inc(*rw_act.step())
            act.activation(E1, gsum, ACT.Exp, scale=-DECAY).then_inc(*rw_act.step())
            act.activation(E2, gsum, ACT.Exp, scale=DECAY).then_inc(*rw_act.step())
            act.activation(E3, E3, ACT.Exp, scale=-DECAY).then_inc(*rw_act.step("decays"))
            for c in range(NT):
                act.wait_ge(*rw_pe.at(f"tok {c}", n))
                act.activation(tok[:, c, :, :].rearrange("p j t -> p (j t)"), ps[:, 0, 0:3 * P], ACT.Copy)\
                   .then_inc(*rw_act.step(f"tok {c}"))
            for h in range(2):
                act.wait_ge(*rw_pe.at(f"A {h}", n))
                act.activation(N_[:, h, :, :].rearrange("p c t -> p (c t)"), ps[:, 5 + h, :], ACT.Copy)\
                   .then_inc(*rw_act.step(f"N {h}"))
            for lv in range(1, LEVELS):
                for h in range(2):
                    act.wait_ge(*rw_pe.at(f"V {h} {lv}", n))
                    act.activation(Vs[:, h, :, :].rearrange("p c t -> p (c t)"), ps[:, 1 + 3 * h, :], ACT.Copy)\
                       .then_inc(*rw_act.step(f"V {h} {lv}"))
            for c in range(NT):
                act.wait_ge(*rw_pe.at(f"RU {c}", n))
                act.activation(RU.rearrange("p (h t) -> p h t", h=2), ps[:, 0:5:4, 0:HD], ACT.Copy).then_inc(*rw_act.step(f"RU {c}"))
                act.wait_ge(*rw_pe.at(f"U {c}", n))
                if c:
                    act.wait_ge(*rw_pe.at(f"Y {c - 1}", n))
                act.activation(U, ps[:, 1, 0:P], ACT.Copy).then_inc(*rw_act.step(f"U {c}"))
                if c < NT - 1:
                    act.wait_ge(*rw_pe.at(f"proj {c}", n))
                    act.wait_ge(*rw_dve.at("silu g", n))
                    act.activation(mixraw[:, c, 1:SEQ + 1], ps[:, 5 + c % 2, :], ACT.Copy).then_inc(*rw_act.step(f"raw {c}"))
            act.wait_ge(*rw_pe.at(f"Y {NT - 1}", n))
            act.activation(ysb, ps[:, 7, :], ACT.Copy).then_inc(*rw_act.step("Y"))
            act.wait_ge(*rw_dve.at("Y dev", n))
            act.activation(ysq, ysb, ACT.Square).then_inc(*rw_act.step("Y dev^2"))
            act.wait_ge(*rw_dve.at("var eps", n))
            link(act.activation(ysq, ysq, ACT.Ln))
            act.activation(ysq, ysq, ACT.Exp, scale=-0.5).then_inc(*rw_act.step("rstd"))
            act.wait_ge(*rw_pe.at("projected", n))
            act.activation(gpair, ps[:, 6, :], ACT.Copy).then_inc(*rw_act.step("raw 3"))
            rw_act.close()

    @runs("gpsimd")
    def _(pool):
        def link(ins, name=None):
            ins.then_inc(*S.step(name))
            pool.wait_ge(*S.last())

        after(pool, SETUP)
        S = lo_pool
        pool.memset(mixraw[:, :, 0:1], 0.0).then_inc(*lo_pool.step())
        pool.memset(loraraw[:, 0:1], 0.0).then_inc(*lo_pool.step())
        pool.memset(lnshift[:], 12.0 * math.log(2.0)).then_inc(*lo_pool.step())
        for j, m in enumerate((LT, LE, LT, LE)):
            pool.tensor_copy(maskQ[:, j, :], m[:]).then_inc(*lo_pool.step())
        lo_pool.close()
        S = rw_pool
        rw_pool.credit(pool)
        with pool.Fori(0, NPAIR) as n:
            rw_pool.begin(n)
            pool.wait_ge(*lo_pool.last())
            for s in (rw_pe, rw_dve, rw_act):
                pool.wait_ge(*s.end(n - 1))
            for h in range(2):
                for t in (T_, TT_):
                    pool.tensor_tensor(t[:, h, :, :], repeat(ident[:], NT), repeat(ones[:], NT), ALU.mult)\
                        .then_inc(*rw_pool.step("identity"))
            pool.wait_ge(*rw_dve.at("k'", n))
            pool.wait_ge(*rw_act.at("decays", n))
            pool.tensor_tensor(BK[:, 1, :], rkv[:, 1, :], E2, ALU.mult).then_inc(*rw_pool.step())
            pool.tensor_tensor(AR[:, :, 1, :], rkv[:, 0, :].rearrange("p (c t) -> p c t", c=NT),
                               E1.rearrange("p (c t) -> p c t", c=NT), ALU.mult).then_inc(*rw_pool.step("factors"))
            rw_pool.close()

    @runs("vector")
    def _(dve):
        def link(ins, name=None):
            ins.then_inc(*S.step(name))
            dve.wait_ge(*S.last())

        def chunks(ap):
            return ap.rearrange("p (c t) -> p c t", c=NT)

        after(dve, SETUP)
        S = lo_dve
        dve.wait_ge(*lo_act.at("z"))
        mu = par[:, PAR_MULORA:PAR_MULORA + 1]
        link(dve.tensor_tensor(lora, loraraw[:, 0:SEQ], loraraw[:, 1:SEQ + 1], ALU.subtract))
        link(dve.scalar_tensor_tensor(out=lora, in0=lora, scalar=mu, in1=loraraw[:, 1:SEQ + 1], op0=ALU.mult, op1=ALU.add))
        link(dve.tensor_scalar(tmp2[0:HD, 0, :], lora[0:HD, :], -CLAMP / 2, None, ALU.max), "clamped")
        dve.wait_ge(*lo_act.at("exp"))
        link(dve.tensor_scalar(lora[0:HD, :], tmp2[0:HD, 0, :], 2.0, -1.0, ALU.mult, ALU.add))
        lo_dve.close()
        S = rw_dve
        rw_dve.credit(dve)
        with dve.Fori(0, NPAIR) as n:
            rw_dve.begin(n)
            for s in (rw_pe, rw_act, rw_pool):
                dve.wait_ge(*s.end(n - 1))
            dve.wait_ge(*lo_pool.end())
            link(dve.tensor_scalar(pc[:, 0:10], par[:, bass.ds(n + PAR_PAIR, 10, 4)], 1.0, None, ALU.mult))
            dve.wait_ge(*rw_pe.at("decay a", n))
            for j in range(2):
                dve.tensor_scalar(sig[:, j, :], ps[:, 4 + j, :], pc[:, 3 + j:4 + j], -LNCLAMP, ALU.add, ALU.max)\
                   .then_inc(*rw_dve.step("sig clamped"))
            for j in (1, 0, 2):
                if j == 1:
                    dve.wait_ge(*lo_act.end())
                dve.wait_ge(*rw_act.at(f"raw {j}", n - 1))
                link(dve.tensor_tensor(rkv[:, j, :], mixraw[:, j, 0:SEQ], mixraw[:, j, 1:SEQ + 1], ALU.subtract))
                link(dve.scalar_tensor_tensor(out=rkv[:, j, :], in0=rkv[:, j, :], scalar=pc[:, j:j + 1],
                                              in1=mixraw[:, j, 1:SEQ + 1], op0=ALU.mult, op1=ALU.add),
                     "k" if j == 1 else None)
            dve.wait_ge(*rw_act.at("raw 3", n - 1))
            dve.tensor_scalar(sg, gpair, -LNCLAMP, None, ALU.max).then_inc(*rw_dve.step("g clamped"))
            dve.wait_ge(*rw_act.at("sigmoids", n))
            for c in range(NT):
                cs = slice(c * P, c * P + P)
                dve.tensor_tensor_scan(gsum[:, cs], ones[:], sig[:, 0, cs], 0.0, ALU.mult, ALU.add).then_inc(*rw_dve.step())
            dve.wait_ge(*rw_dve.last())
            link(dve.tensor_copy(mid, chunks(gsum)[:, :, HD - 1]))
            link(dve.tensor_tensor(chunks(gsum), chunks(gsum), bcast(mid, P), ALU.subtract))
            link(dve.tensor_tensor(E3, gsum, sig[:, 0, :], ALU.subtract), "centred")
            dve.wait_ge(*rw_pe.at("kk sums", n))
            link(dve.tensor_scalar(kk, ps[:, 6, :], 1e-24, None, ALU.max), "kk clamped")
            dve.wait_ge(*rw_act.at("kk rsqrt", n))
            link(dve.scalar_tensor_tensor(out=kk, in0=rkv[:, 1, :], scalar=pc[:, 5:6], in1=kk, op0=ALU.mult, op1=ALU.mult))
            link(dve.tensor_scalar(tmp2[:, 0, :], sig[:, 1, :], -1.0, pc[:, 6:7], ALU.add, ALU.mult))
            link(dve.scalar_tensor_tensor(out=rkv[:, 1, :], in0=tmp2[:, 0, :], scalar=1.0, in1=rkv[:, 1, :],
                                          op0=ALU.add, op1=ALU.mult), "k'")
            link(dve.scalar_tensor_tensor(out=tmp2[:, 1, :], in0=rkv[:, 0, :], scalar=pc[:, 7:8], in1=rkv[:, 1, :],
                                          op0=ALU.mult, op1=ALU.mult), "rkr")
            dve.wait_ge(*rw_act.at("decays", n))
            dve.scalar_tensor_tensor(out=AR[:, :, 0, :], in0=chunks(kk), scalar=-1.0, in1=chunks(E3),
                                     op0=ALU.mult, op1=ALU.mult).then_inc(*rw_dve.step())
            link(dve.tensor_tensor(BK[:, 0, :], kk, sig[:, 1, :], ALU.mult))
            dve.tensor_tensor(BK[:, 0, :], BK[:, 0, :], E2, ALU.mult).then_inc(*rw_dve.step("factors"))
            link(dve.tensor_tensor(fac[:, 1, 0:3], chunks(E1)[:, 0:3, P - 1], fac[:, 0, 1:4], ALU.mult))
            dve.wait_ge(*rw_pe.at("bonus sums", n))
            link(dve.tensor_tensor(bonus, ps[:, 7, :], rkv[:, 2, :], ALU.mult), "bonus")
            dve.wait_ge(*rw_act.at("sigmoid g", n))
            link(dve.tensor_tensor(sg, sg, gpair, ALU.mult), "silu g")
            for h in range(2):
                for c in range(NT):
                    dve.wait_ge(*rw_pe.at(f"Q {h} {c}", n))
                    dve.tensor_tensor(Q[:, h, c, :, :].rearrange("p j t -> p (j t)"), ps[:, 1 + c, :],
                                      maskQ.rearrange("p j t -> p (j t)"), ALU.mult).then_inc(*rw_dve.step(f"Q {h} {c}"))
            dve.wait_ge(*rw_pool.at("identity", n))
            dve.wait_ge(*rw_dve.last())
            for h in range(2):
                dve.wait_ge(*rw_act.at(f"N {h}", n))
                hold(dve).then_inc(*rw_dve.step())
                dve.copy_predicated(T_[:, h, :, :], repeat(quad[:, 0, 0, :], NT), N_[:, h, :, :]).then_inc(*rw_dve.step())
                dve.copy_predicated(TT_[:, h, :, :], repeat(quad[:, 0, 2, :], NT), Q[:, h, :, 0, :])\
                   .then_inc(*rw_dve.step(f"T {h} 0"))
            for lv in range(1, LEVELS):
                for h in range(2):
                    dve.wait_ge(*rw_pe.at(f"TT {h} {lv}", n))
                    hold(dve).then_inc(*rw_dve.step())
                    if lv < LEVELS - 1:
                        dve.copy_predicated(T_[:, h, :, :], repeat(quad[:, lv, 0, :], NT), chunks(ps[:, 2 + 3 * h, :]))\
                           .then_inc(*rw_dve.step())
                    dve.copy_predicated(TT_[:, h, :, :], repeat(quad[:, lv, 2, :], NT), chunks(ps[:, 3 + 3 * h, :]))\
                       .then_inc(*rw_dve.step(f"T {h} {lv}"))
            link(dve.memset(S0, 0.0), "S0 0")
            for c in range(NT - 1):
                dve.wait_ge(*rw_pe.at(f"S1 {c}", n))
                link(dve.tensor_tensor(S1, ps[:, 2, 0:HD], S0, ALU.add))
                dve.wait_ge(*rw_pe.at(f"Y {c}", n))
                link(dve.tensor_scalar(S0, S1, fac[:, 1, c:c + 1], None, ALU.mult), f"S0 {c + 1}")
            dve.wait_ge(*rw_pe.at("mean", n))
            link(dve.scalar_tensor_tensor(out=ysb, in0=ps[:, 3, :], scalar=-1.0 / HD, in1=ysb, op0=ALU.mult, op1=ALU.add),
                 "Y dev")
            dve.wait_ge(*rw_pe.at("var", n))
            link(dve.tensor_scalar(ysq, ps[:, 4, :], 1.0 / HD, GN_EPS, ALU.mult, ALU.add), "var eps")
            dve.wait_ge(*rw_act.at("rstd", n))
            link(dve.tensor_tensor(ysb, ysb, ysq, ALU.mult))
            link(dve.tensor_scalar(ysb, ysb, pc[:, 8:9], pc[:, 9:10], ALU.mult, ALU.add))
            link(dve.tensor_tensor(ysb, ysb, bonus, ALU.add))
            dve.tensor_tensor(yT[:, bass.ds(n, 1), :].rearrange("p a t -> p (a t)"), ysb, sg, ALU.mult).then_inc(*rw_dve.step())
            rw_dve.close()

    RWKV = [(s, None) for s in (lo_pe, lo_dve, lo_act, lo_pool)] + [(s, NPAIR) for s in (rw_pe, rw_dve, rw_act, rw_pool)]

    cut[0] = 0
    qk = take(2, SEQ)
    vtok = take(NT, P)
    graw = take(SEQ)
    sgs = take(SEQ)
    WID = [SEQ - j * P for j in range(NT)]
    OFF = [sum(WID[:j]) for j in range(NT)]
    TRI = sum(WID)
    zs = take(2, TRI)
    spl = take(2, TRI)
    wt = take(2, TRI)
    osb, osq = take(SEQ), take(SEQ)
    sbg = take(1)
    wsb = W[:, 0, 0:4096].rearrange("p (k j c) -> p k j c", k=ND, j=4)
    sb_pe, sb_dve, sb_act = steps("stick_products"), steps("stick_vector"), steps("stick_scalar")
    sb0_in, sb_in = sem("stick_first_weights_in"), steps("stick_weights_in", 16)
    st_pe, st_act = steps("stick_first_products"), steps("stick_first_scalar")
    SB_BANK = (7, 3, 7, 7)
    wo1 = W[:].rearrange("p h n -> p (h n)")[:, 4096:4096 + ND * D].rearrange("p (k n) -> p k n", k=ND)
    o1_in = sem("out1_weights_in")
    ZB = [[(4, 0), (5, 0), (6, 0), (6, WID[2])], [(0, 0), (1, 0), (2, 0), (2, WID[2])]]
    SPANS = [(0, 0, WID[0]), (1, OFF[1], WID[1]), (2, OFF[2], WID[2] + WID[3])]

    @runs("sync")
    def _(sp):
        sp.wait_ge(*rw_pe.at("projected", NPAIR - 1))
        last = SB0 + (NPAIR - 1) * P
        for j in range(4):
            sp.dma_start(wsb[:, :, j, :], w_in[:, :, last + j * RW:last + j * RW + P]).then_inc(sb0_in, 16)
        sb_in.credit(sp)
        sp.wait_ge(*st_pe.end())
        with sp.Fori(0, NPAIR) as n:
            sb_in.begin(n)
            sp.wait_ge(*sb_pe.at("projected", n - 1))
            for j in range(4):
                sp.dma_start(wsb[:, :, j, :], w_in[:, :, bass.ds(n * -P + (last - P + j * RW), P)]).then_inc(*sb_in.step("in"))
            sb_in.close()
        after(sp, RWKV)
        sp.dma_start(wo1, a["w_out"][0].rearrange("(k p) n -> p k n", p=P)).then_inc(o1_in, 16)

    @runs("tensor")
    def _(pe):
        after(pe, RWKV)

        def project(j, bank):
            if j == 2:
                for t in range(NT):
                    for k in range(ND):
                        mm = pe.matmul(ps[:, bank, t * P:(t + 1) * P], hT[:, k, t * P:(t + 1) * P], wsb[:, k, 2, :],
                                       start=(k == 0), stop=(k == ND - 1))
                return mm
            for k in range(ND):
                mm = pe.matmul(ps[:, bank, :], wsb[:, k, j, :], hT[:, k, :], start=(k == 0), stop=(k == ND - 1))
            return mm

        pe.wait_ge(sb0_in, 64)
        for j in (0, 1, 3, 2):
            project(j, j).then_inc(*st_pe.step(f"proj {j}"))
        st_pe.close()
        sb_pe.credit(pe)
        with pe.Fori(0, NPAIR) as n:
            sb_pe.begin(n)
            for s in (sb_dve, sb_act):
                pe.wait_ge(*s.end(n - 1))
            pe.wait_ge(*st_act.end())
            for h in range(2):
                r = slice(h * HD, h * HD + HD)
                for j in range(NT):
                    b, c = ZB[h][j]
                    pe.matmul(ps[:, b, c:c + WID[j]], qk[r, 1, j * P:(j + 1) * P], qk[r, 0, j * P:SEQ], start=True, stop=True)\
                      .then_inc(*sb_pe.step(f"z {h} {j}"))
            pe.wait_ge(*sb_in.at("in", n))
            project(0, 7).then_inc(*sb_pe.step("proj 0"))
            for h in range(2):
                pe.wait_ge(*sb_dve.at(f"sp {h}", n))
                for j in range(NT):
                    b, c = ZB[h][j]
                    mm = pe.matmul(ps[:, b, c:c + WID[j]], GE[:], spl[:, h, OFF[j]:OFF[j] + WID[j]], start=True,
                                   stop=(j == NT - 1))
                    for i in range(j + 1, NT):
                        mm = pe.matmul(ps[:, b, c + (i - j) * P:c + WID[j]], ones[:], spl[:, h, OFF[i]:OFF[i] + WID[i]],
                                       start=False, stop=(i == NT - 1))
                mm.then_inc(*sb_pe.step(f"R {h}"))
                if h == 0:
                    project(1, 3).then_inc(*sb_pe.step("proj 1"))
            pe.wait_ge(*sb_act.at("next 0", n))
            project(3, 7).then_inc(*sb_pe.step("proj 3"))
            pe.wait_ge(*sb_act.at("next 1", n))
            for h in range(2):
                r = slice(h * HD, h * HD + HD)
                pe.wait_ge(*sb_dve.at(f"weights {h}", n))
                for j in range(NT):
                    mm = pe.matmul(ps[r, 3, j * P:SEQ], vtok[:, j, r], wt[:, h, OFF[j]:OFF[j] + WID[j]], start=(j == 0),
                                   stop=(j == NT - 1))
                mm.then_inc(*sb_pe.step("O"))
            pe.wait_ge(*sb_act.at("next 3", n))
            project(2, 7).then_inc(*sb_pe.step("projected"))
            pe.wait_ge(*sb_act.at("O^2", n))
            pe.matmul(ps[:, 0, :], pairs[:], osq, start=True, stop=True).then_inc(*sb_pe.step("O sums"))
            sb_pe.close()

    @runs("scalar")
    def _(act):
        after(act, RWKV)
        sb_act.credit(act)
        NEXT = {0: (qk[:, 0, :], HD ** -0.5), 1: (qk[:, 1, :], 1.0), 2: (vtok.rearrange("p t c -> p (t c)"), 1.0), 3: (graw, 1.0)}
        for j in (0, 1, 3, 2):
            act.wait_ge(*st_pe.at(f"proj {j}"))
            act.activation(NEXT[j][0], ps[:, j, :], ACT.Copy, scale=NEXT[j][1]).then_inc(*st_act.step())
        st_act.close()
        first = 2 * SEQ // P
        act.wait_ge(*su_pool.at("zeros"))
        act.wait_ge(*sb_in.at("in", 0))
        act.dma_start(yd[first * P:, :].rearrange("(p n) (c d) -> p (n c) d", p=P, d=256),
                      zeros[:].unsqueeze(1).to_broadcast([P, (NTAB - first) * (D // 256), 256])).then_inc(zeroed, 16)

        def keep_next(j, n):
            act.wait_ge(*sb_pe.at("projected" if j == 2 else f"proj {j}", n))
            act.activation(NEXT[j][0], ps[:, SB_BANK[j], :], ACT.Copy, scale=NEXT[j][1]).then_inc(*sb_act.step(f"next {j}"))

        with act.Fori(0, NPAIR) as n:
            def link(ins, name=None):
                ins.then_inc(*sb_act.step(name))
                act.wait_ge(*sb_act.last())

            sb_act.begin(n)
            for s in (sb_pe, sb_dve):
                act.wait_ge(*s.end(n - 1))
            for h in range(2):
                act.wait_ge(*sb_pe.at(f"z {h} {NT - 1}", n))
                for b, c, w in SPANS:
                    act.activation(zs[:, h, c:c + w], ps[:, ZB[h][b][0], 0:w], ACT.Copy).then_inc(*sb_act.step())
                act.wait_ge(*sb_act.last())
                link(act.activation(wt[:, h, :], zs[:, h, :], ACT.Abs), f"zs {h}")
                link(act.activation(wt[:, h, :], wt[:, h, :], ACT.Exp, scale=-1.0))
                link(act.activation(wt[:, h, :], wt[:, h, :], ACT.Ln, bias=1.0), f"ln {h}")
            act.wait_ge(*sb_dve.at("g clamped", n))
            link(act.activation(sgs, sgs, ACT.Exp, scale=-1.0))
            link(act.activation(sgs, sgs, ACT.Ln, bias=1.0))
            link(act.activation(sgs, sgs, ACT.Exp, scale=-1.0), "sigmoid g")
            keep_next(0, n)
            for h in range(2):
                act.wait_ge(*sb_dve.at(f"logs {h}", n))
                act.activation(wt[:, h, :], wt[:, h, :], ACT.Exp).then_inc(*sb_act.step(f"exp {h}"))
                if h == 0:
                    keep_next(1, n)
            act.wait_ge(*sb_dve.at("silu g", n))
            keep_next(3, n)
            act.wait_ge(*sb_pe.at("O", n))
            link(act.activation(osb, ps[:, 3, :], ACT.Copy))
            link(act.activation(osq, osb, ACT.Square), "O^2")
            keep_next(2, n)
            act.wait_ge(*sb_dve.at("sums eps", n))
            link(act.activation(osq, osq, ACT.Ln))
            act.activation(osq, osq, ACT.Exp, scale=-0.5).then_inc(*sb_act.step("rstd"))
            sb_act.close()

    @runs("vector")
    def _(dve):
        after(dve, RWKV)
        sb_dve.credit(dve)
        with dve.Fori(0, NPAIR) as n:
            def link(ins, name=None):
                ins.then_inc(*sb_dve.step(name))
                dve.wait_ge(*sb_dve.last())

            sb_dve.begin(n)
            for s in (sb_pe, sb_act):
                dve.wait_ge(*s.end(n - 1))
            dve.tensor_scalar(sbg, par[:, bass.ds(n * -1 + (PAR_SBG + NPAIR - 1), 1)], 1.0, None, ALU.mult).then_inc(*sb_dve.step())
            dve.wait_ge(*st_act.end())
            dve.wait_ge(*sb_dve.end(n - 1))
            link(dve.tensor_scalar(sgs, graw, -LNCLAMP, None, ALU.max), "g clamped")
            for h in range(2):
                dve.wait_ge(*sb_act.at(f"ln {h}", n))
                link(dve.scalar_tensor_tensor(out=spl[:, h, :], in0=zs[:, h, :], scalar=0.0, in1=wt[:, h, :],
                                              op0=ALU.max, op1=ALU.add))
                for j in range(NT):
                    d = spl[:, h, OFF[j]:OFF[j] + P]
                    dve.tensor_tensor(d, d, LT[:], ALU.mult).then_inc(*sb_dve.step(f"sp {h}"))
            dve.wait_ge(*sb_act.at("sigmoid g", n))
            dve.tensor_tensor(sgs, sgs, graw, ALU.mult).then_inc(*sb_dve.step("silu g"))
            for h in range(2):
                dve.wait_ge(*sb_pe.at(f"R {h}", n))
                for b, c, w in SPANS:
                    dve.tensor_tensor(wt[:, h, c:c + w], zs[:, h, c:c + w], ps[:, ZB[h][b][0], 0:w], ALU.subtract)\
                       .then_inc(*sb_dve.step())
                dve.wait_ge(*sb_dve.last())
                for j in range(NT):
                    d = wt[:, h, OFF[j]:OFF[j] + P]
                    dve.tensor_scalar(d, d, 0.0, None, ALU.min).then_inc(*sb_dve.step(f"logs {h}"))
            for h in range(2):
                dve.wait_ge(*sb_act.at(f"exp {h}", n))
                for j in range(NT):
                    d = wt[:, h, OFF[j]:OFF[j] + P]
                    dve.tensor_tensor(d, d, LT[:], ALU.mult).then_inc(*sb_dve.step(f"weights {h}"))
            dve.wait_ge(*sb_pe.at("O sums", n))
            dve.wait_ge(*sb_act.at("O^2", n))
            link(dve.tensor_scalar(osq, ps[:, 0, :], 1.0 / HD, NORM_EPS, ALU.mult, ALU.add), "sums eps")
            dve.wait_ge(*sb_act.at("rstd", n))
            link(dve.scalar_tensor_tensor(out=osb, in0=osb, scalar=sbg, in1=osq, op0=ALU.mult, op1=ALU.mult))
            dve.tensor_tensor(yT[:, bass.ds(n * -1 + (2 * NPAIR - 1), 1), :].rearrange("p a (i b) -> p (a i) b", b=NT),
                              osb.rearrange("p (b i) -> p i b", b=NT), sgs.rearrange("p (i b) -> p i b", b=NT), ALU.mult)\
               .then_inc(*sb_dve.step())
            sb_dve.close()

    STICK = [(s, NPAIR) for s in (sb_pe, sb_dve, sb_act)]

    cut[0] = 0
    grow = take(D)
    xsq = take(D)
    mixed = take(8, SEQ)
    fs = take(NT)
    o1_pe, o1_dve, o1_act = steps("out1_products"), steps("out1_vector"), steps("out1_scalar")
    o1_g = sem("out1_g_in")

    @runs("sync")
    def _(sp):
        after(sp, STICK)
        sp.dma_start(grow, flat("final_g").to_broadcast([P, D])).then_inc(o1_g, 16)

    @runs("tensor")
    def _(pe):
        after(pe, STICK)
        pe.wait_ge(o1_in, 16)
        for t in range(NT):
            for h in range(2):
                for k in range(ND):
                    mm = pe.matmul(ps[:, 2 * t + h, :], yT[:, k, t * P:(t + 1) * P], wo1[:, k, 512 * h:512 * h + 512],
                                   start=(k == 0), stop=(k == ND - 1))
                mm.then_inc(*o1_pe.step(f"y {t} {h}"))
        for t in range(NT):
            pe.wait_ge(*o1_dve.at(f"x {t}"))
        for k in range(ND):
            for t in range(NT):
                mm = pe.transpose(ps[:, k, t * P:(t + 1) * P], xtok[:, t, k * P:(k + 1) * P], ident[:])
            mm.then_inc(*o1_pe.step(f"x^T {k}"))
        o1_pe.close()

    @runs("scalar")
    def _(act):
        after(act, STICK)
        for t in range(NT):
            act.wait_ge(*o1_dve.at(f"sum {t}"))
            act.wait_ge(*o1_act.last()) if t else None
            act.activation(xsq, xtok[:, t, :], ACT.Square, accum_out=fs[:, t:t + 1]).then_inc(*o1_act.step(f"ss {t}"))
            act.wait_ge(*o1_dve.at(f"eps {t}"))
            act.activation(fs[:, t:t + 1], fs[:, t:t + 1], ACT.Ln).then_inc(*o1_act.step())
            act.wait_ge(*o1_act.last())
            act.activation(fs[:, t:t + 1], fs[:, t:t + 1], ACT.Exp, scale=-0.5).then_inc(*o1_act.step(f"rstd {t}"))
        for k in range(ND):
            act.wait_ge(*o1_pe.at(f"x^T {k}"))
            act.activation(hT[:, k, :], ps[:, k, :], ACT.Copy).then_inc(*o1_act.step(f"hT {k}"))
        o1_act.close()

    @runs("vector")
    def _(dve):
        def link(ins, name=None):
            ins.then_inc(*o1_dve.step(name))
            dve.wait_ge(*o1_dve.last())

        after(dve, STICK)
        dve.wait_ge(o1_g, 16)
        for t in range(NT):
            for h in range(2):
                hs = slice(512 * h, 512 * h + 512)
                dve.wait_ge(*o1_pe.at(f"y {t} {h}"))
                link(dve.tensor_tensor(mixed[:, 2 * t + h, :], ps[:, 2 * t + h, :], gate[:, hs], ALU.mult))
                link(dve.tensor_tensor(xtok[:, t, hs], xtok[:, t, hs], mixed[:, 2 * t + h, :], ALU.add), f"sum {t}")
            dve.wait_ge(*o1_act.at(f"ss {t}"))
            link(dve.tensor_scalar(fs[:, t:t + 1], fs[:, t:t + 1], 1.0 / D, NORM_EPS, ALU.mult, ALU.add), f"eps {t}")
            dve.wait_ge(*o1_act.at(f"rstd {t}"))
            link(dve.scalar_tensor_tensor(out=xtok[:, t, :], in0=xtok[:, t, :], scalar=fs[:, t:t + 1], in1=grow,
                                          op0=ALU.mult, op1=ALU.mult), f"x {t}")
        o1_dve.close()

    OUT1 = [(s, None) for s in (o1_pe, o1_dve, o1_act)]

    cut[0] = 0
    raw = take(4, SEQ + TAPS - 1)
    cv = take(4, SEQ)
    Nn = take(NT, 4, P)
    zr, zg = take(NT, 2 * P), take(NT, 2 * P)
    ktok, vtk = take(NT, P), take(NT, 2, P)
    kkS, qkS, qkm = take(NT, P), take(NT, P), take(NT, 2, P)
    Gb = take(NT * 4, P)
    attnT = take(NT, 4, P)
    Tg = take(NT, 4, P)
    QUANT = 7
    pre = take(QUANT, NT, 32)
    pcg = take(QUANT, NT, 4)
    NLE, NGE = take(P), take(P)
    nw = take(P)
    ab = take(NT, 64)
    abt = take(NT, 64)
    alog, dtb = take(32), take(32)
    rsn = take(8)
    taps = take(TAPS, 4)
    half2 = W[:, 1, :]
    TTg = half2[:, 0:2048].rearrange("p (g b t) -> p g b t", g=NT, b=4)
    Vg = half2[:, 2048:3072].rearrange("p (s b t) -> p s b t", s=2, b=4)
    St = half2[:, 3072:3584].rearrange("p (b t) -> p b t", b=4)
    ob = half2[:, 3584:4096].rearrange("p (b t) -> p b t", b=4)
    oacc = half2[:, 4096:5120].rearrange("p (c e t) -> p c e t", c=NT, e=2)
    osqr = half2[:, 5120:6144].rearrange("p (c e t) -> p c e t", c=NT, e=2)
    ctmp = Nn.rearrange("p c b t -> p (c b t)").rearrange("p (j t) -> p j t", j=4)
    XD = [raw[:, k, 2:2 + SEQ] for k in range(4)]
    Rr, vn, vnd, qs = [Gb[:, 4 * k:4 * k + 4, :] for k in range(4)]
    wg = W[:, 0, :].rearrange("p (k n) -> p k n", k=ND)
    wab = W[:, 1, 0:512].rearrange("p (k n) -> p k n", k=ND)
    g_in = a["gdn_w_in_2"][0].rearrange("(k p) n -> p k n", p=P)
    GDN_AB = GDN_CONV + 2 * D

    ab_pe, ab_dve, ab_act, ab_pool = steps("gates_products"), steps("gates_vector"), steps("gates_scalar"), steps("gates_pool")
    gd_pe, gd_dve, gd_act, gd_pool = steps("gdn_products"), steps("gdn_vector"), steps("gdn_scalar"), steps("gdn_pool")
    ab_in, gd_in, gz_in = sem("gates_in"), steps("gdn_weights_in", 16), steps("gdn_z_weights_in", 16)
    gq0_in = sem("gdn_first_weights_in")
    assert 2 * D + 2 * P * (QKH + 1) <= GDN_CONV + 2 * D

    def fl(ap):
        return ap.rearrange("p b t -> p (b t)")

    @runs("sync")
    def _(sp):
        sp.wait_ge(*o1_pe.at("y 3 1"))
        sp.dma_start(wab, g_in[:, :, GDN_AB:GDN_AB + 64]).then_inc(ab_in, 16)
        qkv_cols = ((0, 0, P), (P, D, P), (2 * P, 2 * D, 2 * P))
        for dst, c0, each in qkv_cols:
            sp.dma_start(wg[:, :, dst:dst + each], g_in[:, :, c0:c0 + each]).then_inc(gq0_in, 16)
        after(sp, OUT1)
        sp.dma_start(alog, flat("gdn_a_log_2").to_broadcast([P, 32])).then_inc(ab_in, 16)
        sp.dma_start(dtb, flat("gdn_dt_bias_2").to_broadcast([P, 32])).then_inc(ab_in, 16)
        sp.dma_start(nw, flat("gdn_norm_w_2").to_broadcast([P, P])).then_inc(ab_in, 16)
        gd_in.credit(sp)
        gz_in.credit(sp)
        with sp.Fori(0, QKH) as n:
            gd_in.begin(n)
            gz_in.begin(n)
            sp.wait_ge(*gd_pe.at("z", n - 1))
            sp.dma_start(wg[:, :, 4 * P:6 * P], g_in[:, :, bass.ds(n * 2 * P + GDN_CONV, 2 * P)]).then_inc(*gz_in.step("in"))
            sp.wait_ge(*gd_pe.at("projected", n - 1))
            sp.wait_ge(*ab_pe.end())
            for dst, c0, each in qkv_cols:
                sp.dma_start(wg[:, :, dst:dst + each], g_in[:, :, bass.ds(n * each + (c0 + each), each)]).then_inc(*gd_in.step("in"))
            gd_in.close()
            gz_in.close()

    @runs("tensor")
    def _(pe):
        after(pe, OUT1)
        pe.wait_ge(ab_in, 64)
        for t in range(NT):
            for k in range(ND):
                mm = pe.matmul(ps[:, 0, 64 * t:64 * t + 64], hT[:, k, t * P:(t + 1) * P], wab[:, k, :], start=(k == 0),
                               stop=(k == ND - 1))
        mm.then_inc(*ab_pe.step("ab"))
        pe.wait_ge(gq0_in, 48)
        for j in range(4):
            for k in range(ND):
                mm = pe.matmul(ps[:, 2 + j, :], wg[:, k, j * P:(j + 1) * P], hT[:, k, :], start=(k == 0), stop=(k == ND - 1))
            mm.then_inc(*ab_pe.step(f"proj {j}"))
        pe.wait_ge(*ab_dve.at("g"))
        for t in range(NT):
            pe.matmul(ps[:, 1, 64 * t:64 * t + 16], LE[:], pre[:, 0, t, 0:16], start=True, stop=True)
            pe.matmul(ps[:, 1, 64 * t + 16:64 * t + 32], GE[:], pre[:, 0, t, 16:32], start=True, stop=True)
            mm = pe.matmul(ps[:, 1, 64 * t + 32:64 * t + 64], ones[:], pre[:, 0, t, :], start=True, stop=True)
        mm.then_inc(*ab_pe.step("sums"))
        ab_pe.close()

        def z_half(pe, half, bank):
            for t in (2 * half, 2 * half + 1):
                for k in range(ND):
                    mm = pe.matmul(ps[:, bank, 256 * (t % 2):256 * (t % 2) + 256], hT[:, k, t * P:(t + 1) * P],
                                   wg[:, k, 4 * P:6 * P], start=(k == 0), stop=(k == ND - 1))
            mm.then_inc(*gd_pe.step("z half" if half == 0 else "z"))

        def project_next(pe, j, part):
            for k in range(2 * part, 2 * part + 2):
                mm = pe.matmul(ps[:, 6 + j % 2, :], wg[:, k, j * P:(j + 1) * P], hT[:, k, :], start=(k == 0), stop=(k == ND - 1))
            if part == 3:
                mm.then_inc(*gd_pe.step("projected" if j == 3 else f"proj {j}"))

        gd_pe.credit(pe)
        with pe.Fori(0, QKH) as n:
            gd_pe.begin(n)
            for s in (gd_dve, gd_act, gd_pool):
                pe.wait_ge(*s.end(n - 1))
            pe.wait_ge(*ab_dve.end())
            pe.wait_ge(*ab_pool.end())
            pe.wait_ge(*ab_act.end())
            pe.wait_ge(*gz_in.at("in", n))
            z_half(pe, 0, 3)
            pe.wait_ge(*gd_pool.at("G", n))
            for c in range(2):
                for d in range(2):
                    cols = ps[:, c % 2, 256 * d:256 * d + 256]
                    pe.matmul(cols, (NLE, NGE)[d], fl(Gb[:, 4 * c + 2 * d:4 * c + 2 * d + 2, :]), start=True, stop=False)
                    for e in range(2):
                        mm = pe.matmul(cols[:, P * e:P * e + P], Gb[:, 4 * c + 2 * d + e, :], (LE, GE)[d][:], start=False,
                                       stop=(e == 1))
                mm.then_inc(*gd_pe.step(f"X {c}"))
            for j in range(2):
                pe.wait_ge(*gd_act.at(f"square {j}", n))
                pe.matmul(ps[:, 6 + j, :], ones[:], ctmp[:, j, :], start=True, stop=True).then_inc(*gd_pe.step(f"norm {j}"))
            for c in range(2, NT):
                pe.wait_ge(*gd_dve.at(f"X {c - 2}", n))
                for d in range(2):
                    cols = ps[:, c % 2, 256 * d:256 * d + 256]
                    pe.matmul(cols, (NLE, NGE)[d], fl(Gb[:, 4 * c + 2 * d:4 * c + 2 * d + 2, :]), start=True, stop=False)
                    for e in range(2):
                        mm = pe.matmul(cols[:, P * e:P * e + P], Gb[:, 4 * c + 2 * d + e, :], (LE, GE)[d][:], start=False,
                                       stop=(e == 1))
                mm.then_inc(*gd_pe.step(f"X {c}"))
            pe.wait_ge(*gd_pool.at("silu 3", n))
            pe.wait_ge(*gd_dve.at("unit 1", n))
            pe.wait_ge(*gd_act.at("z raw 0", n))
            for c in range(NT):
                cs = slice(c * P, c * P + P)
                for e in range(2):
                    mm = pe.transpose(ps[:, 3 + c // 2, 256 * (c % 2) + P * e:256 * (c % 2) + P * e + P], cv[:, 2 + e, cs], ident[:])
            mm.then_inc(*gd_pe.step("v tokens"))
            for c in range(NT):
                cs = slice(c * P, c * P + P)
                mm = pe.transpose(ps[:, 2, cs], cv[:, 1, cs], ident[:])
            mm.then_inc(*gd_pe.step("k tokens"))
            for c in range(NT):
                cs = slice(c * P, c * P + P)
                mm = pe.matmul(ps[:, 5, cs], cv[:, 1, cs], cv[:, 1, cs], start=True, stop=True)
            mm.then_inc(*gd_pe.step("k k"))
            pe.wait_ge(*gd_dve.at("unit 0", n))
            for c in range(NT):
                cs = slice(c * P, c * P + P)
                mm = pe.matmul(ps[:, 6, cs], cv[:, 1, cs], cv[:, 0, cs], start=True, stop=True)
            mm.then_inc(*gd_pe.step("k q"))
            z_half(pe, 1, 7)
            pe.wait_ge(*gd_act.at("tokens", n))
            for g in range(NT):
                s3 = 3 * (g % 2)
                pe.wait_ge(*gd_dve.at(f"N {g}", n))
                if g >= 2:
                    pe.wait_ge(*gd_dve.at(f"T {g - 2} 0", n))
                for b in range(4):
                    mm = pe.transpose(ps[:, s3 + 2, b * P:(b + 1) * P], Nn[:, g, b, :], ident[:])
                mm.then_inc(*gd_pe.step(f"N^T {g}"))
            for lv in range(1, LEVELS):
                for st in range(NT + 1):
                    if st < NT:
                        g, s3 = st, 3 * (st % 2)
                        pe.wait_ge(*gd_dve.at(f"T {g} {lv - 1}", n))
                        for b in range(4):
                            mm = pe.matmul(ps[:, s3, b * P:(b + 1) * P], Nn[:, g, b, :], TTg[:, g, b, :], start=True, stop=True)
                        mm.then_inc(*gd_pe.step(f"V {g} {lv}"))
                    if st:
                        g, s3 = st - 1, 3 * ((st - 1) % 2)
                        pe.wait_ge(*gd_act.at(f"V {g} {lv}", n))
                        if g >= 2:
                            pe.wait_ge(*gd_dve.at(f"T {g - 2} {lv}", n))
                        elif lv > 1:
                            pe.wait_ge(*gd_dve.at(f"T {g + 2} {lv - 1}", n))
                        else:
                            pe.wait_ge(*gd_dve.at(f"T {g + 2} 0", n))
                        if lv < LEVELS - 1:
                            for b in range(4):
                                pe.matmul(ps[:, s3 + 1, b * P:(b + 1) * P], Vg[:, g % 2, b, :], Tg[:, g, b, :], start=True, stop=True)
                        for b in range(4):
                            mm = pe.matmul(ps[:, s3 + 2, b * P:(b + 1) * P], Tg[:, g, b, :], Vg[:, g % 2, b, :], start=True, stop=True)
                        mm.then_inc(*gd_pe.step(f"T {g} {lv}"))
            for st in range(NT):
                cc = (st, NT - 1 - st)
                pe.wait_ge(*gd_dve.at(f"S {st}", n))
                for d in range(2):
                    cs = slice(cc[d] * P, cc[d] * P + P)
                    mm = pe.matmul(ps[:, 0, 256 * d:256 * d + 256], cv[:, 1, cs], fl(St[:, 2 * d:2 * d + 2, :]), start=True, stop=True)
                mm.then_inc(*gd_pe.step(f"kS {st}"))
                for d in range(2):
                    cs = slice(cc[d] * P, cc[d] * P + P)
                    mm = pe.matmul(ps[:, 1, 256 * d:256 * d + 256], cv[:, 0, cs], fl(St[:, 2 * d:2 * d + 2, :]), start=True, stop=True)
                mm.then_inc(*gd_pe.step(f"qS {st}"))
                if st == 0:
                    pe.wait_ge(*gd_in.at("in", n))
                    pe.wait_ge(*gd_act.at("z raw 1", n))
                if st >= 2:
                    pe.wait_ge(*gd_act.at(f"raw {st - 2}", n))
                project_next(pe, st, 0)
                pe.wait_ge(*gd_dve.at(f"R {st}", n))
                if st == 0:
                    pe.wait_ge(*gd_pool.at("T beta", n))
                for b in range(4):
                    mm = pe.matmul(ps[:, 2, b * P:(b + 1) * P], TTg[:, cc[b // 2], b, :], Rr[:, b, :], start=True, stop=True)
                mm.then_inc(*gd_pe.step(f"v' {st}"))
                if st < NT - 1:
                    project_next(pe, st, 1)
                pe.wait_ge(*gd_dve.at(f"v'd {st}", n))
                for d in range(2):
                    mm = pe.matmul(ps[:, 4, 256 * d:256 * d + 256], ktok[:, cc[d], :], fl(vnd[:, 2 * d:2 * d + 2, :]), start=True, stop=True)
                mm.then_inc(*gd_pe.step(f"dS {st}"))
                if st < NT - 1:
                    project_next(pe, st, 2)
                pe.wait_ge(*gd_act.at(f"v' {st}", n))
                for b in range(4):
                    mm = pe.matmul(ps[:, 3, b * P:(b + 1) * P], attnT[:, cc[b // 2], b, :], vn[:, b, :], start=True, stop=True)
                mm.then_inc(*gd_pe.step(f"o {st}"))
                for part in ((3,) if st < NT - 1 else (1, 2, 3)):
                    project_next(pe, st, part)
            pe.wait_ge(*gd_dve.at("gated", n))
            for e in range(2):
                for c in range(NT):
                    mm = pe.transpose(ps[:, 4 + e, c * P:(c + 1) * P], oacc[:, c, e, :], ident[:])
                mm.then_inc(*gd_pe.step(f"o^T {e}"))
            gd_pe.close()

    @runs("scalar")
    def _(act):
        def link(ins, name=None):
            ins.then_inc(*S.step(name))
            act.wait_ge(*S.last())

        after(act, OUT1)
        S = ab_act
        act.wait_ge(*ab_pe.at("ab"))
        link(act.activation(ab.rearrange("p t c -> p (t c)"), ps[:, 0, 0:256], ACT.Copy), "ab")
        act.wait_ge(*ab_dve.at("arguments"))
        link(act.activation(abt[:, :, 0:32], abt[:, :, 0:32], ACT.Abs))
        link(act.activation(abt, abt, ACT.Exp, scale=-1.0))
        link(act.activation(abt, abt, ACT.Ln, bias=1.0))
        link(act.activation(abt[:, :, 32:64], abt[:, :, 32:64], ACT.Exp, scale=-1.0))
        act.wait_ge(ab_in, 64)
        link(act.activation(alog, alog, ACT.Exp), "logs")
        act.wait_ge(*ab_dve.at("sums"))
        for q, src in ((3, pre[:, 3, :, :]), (5, pre[:, 5, :, :]), (6, pre[:, 6, :, :])):
            link(act.activation(src, src, ACT.Exp), "exps")
        for j in range(4):
            act.wait_ge(*ab_pe.at(f"proj {j}"))
            act.activation(raw[:, j, 2:2 + SEQ], ps[:, 2 + j, :], ACT.Copy).then_inc(*ab_act.step("raw"))
        ab_act.close()
        S = gd_act
        gd_act.credit(act)
        with act.Fori(0, QKH) as n:
            gd_act.begin(n)
            for s in (gd_pe, gd_dve, gd_pool):
                act.wait_ge(*s.end(n - 1))
            act.wait_ge(*ab_pool.end())
            def decay(c):
                act.wait_ge(*gd_dve.at(f"X {c}", n))
                for k in range(2):
                    buf = XD[2 * (c % 2) + k]
                    act.activation(buf, buf, ACT.Exp, scale=(1.0, -1.0)[k]).then_inc(*gd_act.step(f"D {c}"))

            act.wait_ge(*gd_pe.at("z half", n))
            act.activation(zr[:, 0:2, :].rearrange("p t c -> p (t c)"), ps[:, 3, :], ACT.Copy).then_inc(*gd_act.step("z raw 0"))
            for j in range(4):
                act.wait_ge(*gd_dve.at(f"clamped {j}", n))
                link(act.activation(ctmp[:, j, :], ctmp[:, j, :], ACT.Exp, scale=-1.0))
                link(act.activation(ctmp[:, j, :], ctmp[:, j, :], ACT.Ln, bias=1.0))
                link(act.activation(ctmp[:, j, :], ctmp[:, j, :], ACT.Exp, scale=-1.0), f"sigmoid {j}")
            for j in range(2):
                act.wait_ge(*gd_pool.at(f"silu {j}", n))
                act.activation(ctmp[:, j, :], cv[:, j, :], ACT.Square).then_inc(*gd_act.step(f"square {j}"))
            for c in (0, 1):
                decay(c)
            for j in (0, 1):
                act.wait_ge(*gd_dve.at(f"norm eps {j}", n))
                link(act.activation(ctmp[:, j, :], ctmp[:, j, :], ACT.Ln))
                act.activation(ctmp[:, j, :], ctmp[:, j, :], ACT.Exp, scale=-0.5).then_inc(*gd_act.step(f"rsqrt {j}"))
            act.wait_ge(*gd_pe.at("v tokens", n))
            act.activation(vtk.rearrange("p c e t -> p (c e t)").rearrange("p (b t) -> p b t", b=2), ps[:, 3:5, :], ACT.Copy)\
               .then_inc(*gd_act.step())
            act.wait_ge(*gd_pe.at("k k", n))
            act.activation(ktok.rearrange("p c t -> p (c t)"), ps[:, 2, :], ACT.Copy).then_inc(*gd_act.step())
            act.activation(kkS.rearrange("p c t -> p (c t)"), ps[:, 5, :], ACT.Copy).then_inc(*gd_act.step())
            act.wait_ge(*gd_pe.at("k q", n))
            act.activation(qkS.rearrange("p c t -> p (c t)"), ps[:, 6, :], ACT.Copy).then_inc(*gd_act.step("tokens"))
            for c in (2, 3):
                decay(c)
            act.wait_ge(*gd_pe.at("z", n))
            act.activation(zr[:, 2:4, :].rearrange("p t c -> p (t c)"), ps[:, 7, :], ACT.Copy).then_inc(*gd_act.step("z raw 1"))
            for lv in range(1, LEVELS):
                if 2 <= lv < 5:
                    if lv == 2:
                        act.wait_ge(*gd_dve.at("z clamped", n))
                    else:
                        act.wait_ge(*gd_act.at("z exp" if lv == 3 else "z ln", n))
                    if lv == 3:
                        act.activation(zg, zg, ACT.Ln, bias=1.0).then_inc(*gd_act.step("z ln"))
                    else:
                        act.activation(zg, zg, ACT.Exp, scale=-1.0).then_inc(*gd_act.step("z exp" if lv == 2 else "sigmoid z"))
                for g in range(NT):
                    act.wait_ge(*gd_pe.at(f"V {g} {lv}", n))
                    if g >= 2:
                        act.wait_ge(*gd_pe.at(f"T {g - 2} {lv}", n))
                    elif lv > 1:
                        act.wait_ge(*gd_pe.at(f"T {g + 2} {lv - 1}", n))
                    act.activation(Vg[:, g % 2, :, :].rearrange("p b t -> p (b t)"), ps[:, 3 * (g % 2), :], ACT.Copy)\
                       .then_inc(*gd_act.step(f"V {g} {lv}"))
            for st in range(NT):
                cc = (st, NT - 1 - st)
                act.wait_ge(*gd_pe.at(f"qS {st}", n))
                if st:
                    act.wait_ge(*gd_dve.at(f"o {st - 1}", n))
                for b in range(4):
                    act.activation(qs[:, b, :], ps[:, 1, b * P:(b + 1) * P], ACT.Copy, scale=pcg[:, 3, cc[b // 2], b:b + 1])\
                       .then_inc(*gd_act.step(f"qS {st}"))
                act.wait_ge(*gd_pe.at(f"v' {st}", n))
                act.wait_ge(*gd_dve.at(f"v'd {st}", n))
                act.activation(fl(vn), ps[:, 2, :], ACT.Copy).then_inc(*gd_act.step(f"v' {st}"))
                if st == NT - 1:
                    break
                act.wait_ge(*gd_pe.at(f"proj {st}", n))
                if st == 0:
                    act.wait_ge(*gd_pool.at(f"attention {NT - 1}", n))
                    act.wait_ge(*gd_dve.at(f"N {NT - 1}", n))
                act.activation(raw[:, st, 2:2 + SEQ], ps[:, 6 + st % 2, :], ACT.Copy).then_inc(*gd_act.step(f"raw {st}"))
            act.wait_ge(*gd_dve.at(f"o {NT - 1}", n))
            act.activation(osqr, oacc, ACT.Square).then_inc(*gd_act.step("o^2"))
            act.wait_ge(*gd_dve.at("o eps", n))
            link(act.activation(rsn, rsn, ACT.Ln))
            act.activation(rsn, rsn, ACT.Exp, scale=-0.5).then_inc(*gd_act.step("o rstd"))
            act.wait_ge(*gd_pe.at("projected", n))
            act.activation(raw[:, 3, 2:2 + SEQ], ps[:, 7, :], ACT.Copy).then_inc(*gd_act.step("raw 3"))
            gd_act.close()

    @runs("gpsimd")
    def _(pool):
        def link(ins, name=None):
            ins.then_inc(*S.step(name))
            pool.wait_ge(*S.last())

        after(pool, OUT1)
        S = ab_pool
        for c0 in (0, SEQ + 2):
            pool.memset(raw[:, :, c0:c0 + 2], 0.0).then_inc(*ab_pool.step())
        pool.tensor_scalar(NLE, LE[:], -1.0, None, ALU.mult).then_inc(*ab_pool.step())
        pool.tensor_scalar(NGE, GE[:], -1.0, None, ALU.mult).then_inc(*ab_pool.step())
        ab_pool.close()
        S = gd_pool
        gd_pool.credit(pool)
        with pool.Fori(0, QKH) as n:
            gd_pool.begin(n)
            pool.wait_ge(*ab_pool.end())
            for s in (gd_pe, gd_dve, gd_act):
                pool.wait_ge(*s.end(n - 1))
            pool.wait_ge(*gd_dve.at("columns", n))
            pool.tensor_tensor(Gb, bcast(pcg[:, 0, :, :].rearrange("p c b -> p (c b)"), P), repeat(ones[:], 16), ALU.mult)\
                .then_inc(*gd_pool.step("G"))
            for t in (Tg, TTg):
                for g in range(NT):
                    pool.tensor_tensor(t[:, g, :, :], repeat(ident[:], 4), repeat(ones[:], 4), ALU.mult)\
                        .then_inc(*gd_pool.step("identity"))
            for j in range(4):
                pool.wait_ge(*gd_act.at(f"sigmoid {j}", n))
                pool.tensor_tensor(cv[:, j, :], cv[:, j, :], ctmp[:, j, :], ALU.mult).then_inc(*gd_pool.step(f"silu {j}"))
            pool.wait_ge(*gd_act.at("tokens", n))
            for d, m in ((0, LE), (1, GE)):
                pool.tensor_tensor(qkm[:, :, d, :], qkS, repeat(m[:], NT), ALU.mult).then_inc(*gd_pool.step())
            pool.wait_ge(*gd_pool.last())
            for c in range(NT):
                pool.wait_ge(*gd_act.at(f"D {c}", n))
                for d in range(2):
                    pool.tensor_tensor(attnT[:, c, 2 * d:2 * d + 2, :], XD[2 * (c % 2)].rearrange("p (b t) -> p b t", b=4)[:, 2 * d:2 * d + 2, :],
                                       repeat(qkm[:, c, d, :], 2), ALU.mult).then_inc(*gd_pool.step(f"attention {c}"))
            pool.wait_ge(*gd_act.at("sigmoid z", n))
            pool.tensor_tensor(zg, zg, zr, ALU.mult).then_inc(*gd_pool.step("silu z"))
            for g in range(NT):
                pool.wait_ge(*gd_dve.at(f"T {g} {LEVELS - 1}", n))
                pool.tensor_tensor(TTg[:, g, :, :], TTg[:, g, :, :], bcast(pcg[:, 1, g, :], P), ALU.mult).then_inc(*gd_pool.step("T beta"))
            gd_pool.close()

    @runs("vector")
    def _(dve):
        def link(ins, name=None):
            ins.then_inc(*S.step(name))
            dve.wait_ge(*S.last())

        after(dve, OUT1)
        S = ab_dve
        dve.wait_ge(ab_in, 64)
        dve.wait_ge(*ab_act.at("ab"))
        link(dve.tensor_tensor(ab[:, :, 0:32], ab[:, :, 0:32], repeat(dtb, NT), ALU.add))
        dve.tensor_copy(abt[:, :, 0:32], ab[:, :, 0:32]).then_inc(*ab_dve.step())
        link(dve.tensor_scalar(abt[:, :, 32:64], ab[:, :, 32:64], -LNCLAMP, None, ALU.max), "arguments")
        dve.wait_ge(*ab_act.at("logs"))
        link(dve.scalar_tensor_tensor(out=pre[:, 0, :, :], in0=ab[:, :, 0:32], scalar=0.0, in1=abt[:, :, 0:32], op0=ALU.max, op1=ALU.add))
        link(dve.scalar_tensor_tensor(out=pre[:, 0, :, :], in0=pre[:, 0, :, :], scalar=-1.0, in1=repeat(alog, NT),
                                      op0=ALU.mult, op1=ALU.mult), "g")
        link(dve.tensor_copy(pre[:, 1, :, :], abt[:, :, 32:64]))
        link(dve.tensor_scalar(pre[:, 2, :, :], pre[:, 1, :, :], -1.0, None, ALU.mult))
        dve.wait_ge(*ab_pe.at("sums"))
        sums = ps[:, 1, 0:256].rearrange("p (t c) -> p t c", t=NT)
        link(dve.tensor_copy(pre[:, 3, :, :], sums[:, :, 0:32]))
        link(dve.tensor_copy(pre[:, 6, :, :], sums[:, :, 32:64]))
        link(dve.tensor_tensor(pre[:, 5, :, :], pre[:, 6, :, :], pre[:, 3, :, :], ALU.subtract), "sums")
        dve.wait_ge(*ab_act.at("exps"))
        link(dve.tensor_scalar(pre[:, 4, :, :], pre[:, 3, :, :], -1.0, None, ALU.mult))
        ab_dve.close()
        S = gd_dve
        gd_dve.credit(dve)
        with dve.Fori(0, QKH) as n:
            gd_dve.begin(n)
            for s in (gd_pe, gd_act, gd_pool):
                dve.wait_ge(*s.end(n - 1))
            src = pre.rearrange("p q t (d h) -> p (q t d) h", d=2)[:, :, bass.ds(n * 2, 2)]
            link(dve.tensor_scalar(pcg.rearrange("p q t (d e) -> p (q t d) e", d=2), src, 1.0, None, ALU.mult), "columns")
            tcol = conv[:].rearrange("p (w c) -> p w c", w=TAPS)
            for j, c0, step in ((0, 0, 1), (1, 8, 1), (2, 16, 2), (3, 17, 2)):
                dve.tensor_scalar(taps[:, :, j], tcol[:, :, bass.ds(n * step + c0, 1)].rearrange("p w c -> p (w c)"), 1.0, None, ALU.mult).then_inc(*gd_dve.step())
            dve.wait_ge(*gd_dve.last())
            dve.wait_ge(*ab_act.end())
            dve.wait_ge(*ab_pool.end())
            for j in range(4):
                dve.wait_ge(*gd_act.at(f"raw {j}", n - 1))
                link(dve.tensor_scalar(cv[:, j, :], raw[:, j, 0:SEQ], taps[:, 0, j:j + 1], None, ALU.mult))
                for w in range(1, TAPS):
                    link(dve.scalar_tensor_tensor(out=cv[:, j, :], in0=raw[:, j, w:w + SEQ], scalar=taps[:, w, j:j + 1],
                                                  in1=cv[:, j, :], op0=ALU.mult, op1=ALU.add), f"conv {j}" if w == TAPS - 1 else None)
                dve.tensor_scalar(ctmp[:, j, :], cv[:, j, :], -LNCLAMP, None, ALU.max).then_inc(*gd_dve.step(f"clamped {j}"))
            differences(dve, 0, n)
            differences(dve, 1, n)
            for j in range(2):
                dve.wait_ge(*gd_pe.at(f"norm {j}", n))
                link(dve.tensor_scalar(ctmp[:, j, :], ps[:, 6 + j, :], NORM_EPS, None, ALU.add), f"norm eps {j}")
                dve.wait_ge(*gd_act.at(f"rsqrt {j}", n))
                link(dve.scalar_tensor_tensor(out=cv[:, j, :], in0=cv[:, j, :], scalar=(P ** -0.5, 1.0)[j], in1=ctmp[:, j, :],
                                              op0=ALU.mult, op1=ALU.mult), f"unit {j}")
            for c in (0, 2):
                if c:
                    differences(dve, c, n)
                    differences(dve, c + 1, n)
                triangle(dve, c, n)
                triangle(dve, c + 1, n)
            dve.wait_ge(*gd_pool.at("identity", n))
            for g in range(NT):
                dve.wait_ge(*gd_pe.at(f"N^T {g}", n))
                hold(dve).then_inc(*gd_dve.step())
                dve.copy_predicated(Tg[:, g, :, :], quad[:, 0, 0:4, :], Nn[:, g, :, :]).then_inc(*gd_dve.step())
                dve.copy_predicated(TTg[:, g, :, :], quad[:, 0, 2:6, :], ps[:, 3 * (g % 2) + 2, :].rearrange("p (b t) -> p b t", b=4))\
                   .then_inc(*gd_dve.step(f"T {g} 0"))
            dve.wait_ge(*gd_act.at("z raw 1", n))
            dve.tensor_scalar(zg, zr, -LNCLAMP, None, ALU.max).then_inc(*gd_dve.step("z clamped"))
            for lv in range(1, LEVELS):
                for g in range(NT):
                    dve.wait_ge(*gd_pe.at(f"T {g} {lv}", n))
                    hold(dve).then_inc(*gd_dve.step())
                    if lv < LEVELS - 1:
                        dve.copy_predicated(Tg[:, g, :, :], quad[:, lv, 0:4, :], ps[:, 3 * (g % 2) + 1, :].rearrange("p (b t) -> p b t", b=4))\
                           .then_inc(*gd_dve.step())
                    dve.copy_predicated(TTg[:, g, :, :], quad[:, lv, 2:6, :], ps[:, 3 * (g % 2) + 2, :].rearrange("p (b t) -> p b t", b=4))\
                       .then_inc(*gd_dve.step(f"T {g} {lv}"))
            link(dve.memset(St, 0.0), "S 0")
            for st in range(NT):
                cc = (st, NT - 1 - st)
                dve.wait_ge(*gd_pe.at(f"kS {st}", n))
                for b in range(4):
                    dve.scalar_tensor_tensor(out=Rr[:, b, :], in0=ps[:, 0, b * P:(b + 1) * P], scalar=pcg[:, 4, cc[b // 2], b:b + 1],
                                             in1=vtk[:, cc[b // 2], b % 2, :], op0=ALU.mult, op1=ALU.add).then_inc(*gd_dve.step(f"R {st}"))
                dve.wait_ge(*gd_pe.at(f"v' {st}", n))
                for d in range(2):
                    dve.tensor_tensor(vnd[:, 2 * d:2 * d + 2, :], ps[:, 2, 256 * d:256 * d + 256].rearrange("p (e t) -> p e t", e=2),
                                      bcast(pcg[:, 5, cc[d], 2 * d:2 * d + 2], P), ALU.mult).then_inc(*gd_dve.step(f"v'd {st}"))
                dve.wait_ge(*gd_pe.at(f"dS {st}", n))
                dve.wait_ge(*gd_pe.at(f"qS {st}", n))
                for b in range(4):
                    dve.scalar_tensor_tensor(out=St[:, b, :], in0=St[:, b, :], scalar=pcg[:, 6, cc[b // 2], b:b + 1],
                                             in1=ps[:, 4, b * P:(b + 1) * P], op0=ALU.mult, op1=ALU.add).then_inc(*gd_dve.step(f"S {st + 1}"))
                dve.wait_ge(*gd_pe.at(f"o {st}", n))
                dve.wait_ge(*gd_act.at(f"qS {st}", n))
                dve.wait_ge(*gd_dve.last())
                for d in range(2):
                    o, pso, q = oacc[:, cc[d], :, :], ps[:, 3, 256 * d:256 * d + 256].rearrange("p (e t) -> p e t", e=2), qs[:, 2 * d:2 * d + 2, :]
                    if st < NT // 2:
                        dve.tensor_tensor(o, pso, q, ALU.add).then_inc(*gd_dve.step(f"o {st}"))
                    else:
                        link(dve.tensor_tensor(ob[:, 2 * d:2 * d + 2, :], pso, q, ALU.add))
                        dve.tensor_tensor(o, o, ob[:, 2 * d:2 * d + 2, :], ALU.add).then_inc(*gd_dve.step(f"o {st}"))
            dve.wait_ge(*gd_act.at("o^2", n))
            link(dve.tensor_reduce(rsn, osqr.rearrange("p c e t -> p (c e) t"), X_AXIS, ALU.add))
            link(dve.tensor_scalar(rsn, rsn, 1.0 / P, NORM_EPS, ALU.mult, ALU.add), "o eps")
            flat8 = oacc.rearrange("p c e t -> p (c e) t")
            dve.wait_ge(*gd_act.at("o rstd", n))
            link(dve.tensor_tensor(flat8, flat8, bcast(rsn, P), ALU.mult))
            link(dve.tensor_tensor(flat8, flat8, repeat(nw, 8), ALU.mult))
            dve.wait_ge(*gd_pool.at("silu z", n))
            link(dve.tensor_tensor(flat8, flat8, zg.rearrange("p c (e t) -> p (c e) t", e=2), ALU.mult), "gated")
            for e in range(2):
                dve.wait_ge(*gd_pe.at(f"o^T {e}", n))
                dve.tensor_scalar(yT[:, bass.ds(n * 2 + e, 1), :].rearrange("p a t -> p (a t)"), ps[:, 4 + e, :], 1.0, None, ALU.mult)\
                   .then_inc(*gd_dve.step())
            gd_dve.close()

    def differences(dve, c, n):
        dve.wait_ge(*gd_pe.at(f"X {c}", n))
        if c >= 2:
            dve.wait_ge(*gd_pool.at(f"attention {c - 2}", n))
        dve.wait_ge(*gd_dve.last())
        dve.tensor_scalar(XD[2 * (c % 2)], ps[:, c % 2, :], 0.0, None, ALU.min).then_inc(*gd_dve.step())
        dve.tensor_scalar(XD[2 * (c % 2) + 1], ps[:, c % 2, :], 0.0, None, ALU.max).then_inc(*gd_dve.step(f"X {c}"))

    def triangle(dve, c, n):
        dve.wait_ge(*gd_act.at("tokens", n))
        dve.wait_ge(*gd_act.at(f"D {c}", n))
        buf = XD[2 * (c % 2) + 1].rearrange("p (b t) -> p b t", b=4)
        dve.tensor_tensor(buf, buf, repeat(kkS[:, c, :], 4), ALU.mult).then_inc(*gd_dve.step())
        dve.wait_ge(*gd_dve.last())
        dve.tensor_tensor(Nn[:, c, :, :], buf, bcast(pcg[:, 2, c, :], P), ALU.mult).then_inc(*gd_dve.step(f"N {c}"))

    GDN = [(s, None) for s in (ab_pe, ab_dve, ab_act, ab_pool)] + [(s, QKH) for s in (gd_pe, gd_dve, gd_act, gd_pool)]

    cut[0] = 0
    lng, lnb = take(2, D), take(2, D)
    stats = take(NT, 2, 6)
    mv = take(NT, 2)
    lrs = take(NT)
    wr = take(ND, NGRP + NEXP)
    rb = take(NGRP + NEXP)
    lg = take(NT, NGRP + NEXP)
    desc = take(EPG)
    ohg, gex, geq = take(NT, NGRP), take(NT, NGRP), take(NT, NGRP)
    prod = take(NT * NGRP, EPG)
    e8, e8b, eq8, oh1, oh2 = [take(NT, EPG) for _ in range(5)]
    gmax, gsum4, v1, v2, dd, wa, wb = [take(NT) for _ in range(7)]
    pick = take(2, NT, NEXP)
    both = take(NT, NEXP)
    rank = take(NT, NEXP)
    cnt, tiles, ends, starts, tmp32 = [take(NEXP) for _ in range(5)]
    iota = take(P)
    tokid = take(NT)
    rk, st_, qk_, pk_, sk_ = [take(2 * NT) for _ in range(5)]
    cmpt = take(NTAB, NEXP)
    etf = take(NTAB)
    gh = take(2, 2 * HID)
    hgT = take(2, 2, P)
    ptok = take(NT, PLE)
    pT = take(2, SEQ)
    yTall = yT[:].rearrange("p k t -> p (k t)")
    xg = yTall[:, 0:2 * D].rearrange("p (b d) -> p b d", b=2)
    xgT = yTall[:, 2 * D:4 * D].rearrange("p (b k t) -> p b k t", b=2, k=ND)
    yrow = yTall[:, 4 * D:6 * D].rearrange("p (b d) -> p b d", b=2)
    Ak = yTall[:, 6 * D:7 * D].rearrange("p (j r) -> p j r", j=2 * NT)
    Bk = yTall[:, 7 * D:7 * D + 2 * NT * NTAB].rearrange("p (j n) -> p j n", j=2 * NT)
    sgate = xgT.rearrange("p b k t -> p b (k t)")
    idxu = sb("idxu", [P, NTAB], U32)
    slotu = sb("slotu", [P, 2 * NT], U32)
    etab = sb("etab", [1, 64], I32)
    nit = sb("nit", [1, 1], I32)
    spare2 = sb("spare2", [P, 4])
    icol = sb("icol", [P, 2], U32)
    x2d = nc.dram_tensor("x2_rows", (SEQ, D), F32, kind="Internal").ap()
    Wall = W[:].rearrange("p h n -> p (h n)")
    ring = [Wall[:, 4096 * s:4096 * s + 4096].rearrange("p (k n) -> p k n", k=4) for s in range(3)]
    w_out2 = a["gdn_w_out_2"][0].rearrange("(k p) n -> p k n", p=P)
    o2_pe, o2_dve, o2_act, o2_pool = steps("out2_products"), steps("out2_vector"), steps("out2_scalar"), steps("out2_pool")
    o2_in = [sem(f"out2_weights_in{s}") for s in range(3)]
    ln_in, rt_in, x2_out = sem("layernorm_in"), sem("router_in"), sem("x2_rows_out")

    def layernorm(dve, act_steps, S, t, which, name):
        def link(ins, n=None):
            ins.then_inc(*S.step(n))
            dve.wait_ge(*S.last())
        for h in range(2):
            dve.bn_stats(stats[:, t, h, :], xtok[:, t, 512 * h:512 * h + 512]).then_inc(*S.step())
        dve.wait_ge(*S.last())
        link(dve.bn_aggr(mv[:, t, :], stats[:, t, :, :]))
        link(dve.tensor_scalar(lrs[:, t:t + 1], mv[:, t, 1:2], LN_EPS, None, ALU.add), f"{name} eps {t}")
        dve.wait_ge(*act_steps.at(f"{name} rstd {t}"))
        link(dve.tensor_scalar(xtok[:, t, :], xtok[:, t, :], mv[:, t, 0:1], lrs[:, t:t + 1], ALU.subtract, ALU.mult))
        link(dve.tensor_tensor(xtok[:, t, :], xtok[:, t, :], lng[:, which, :], ALU.mult))
        link(dve.tensor_tensor(xtok[:, t, :], xtok[:, t, :], lnb[:, which, :], ALU.add), f"{name} {t}")

    def rsqrt_of(act, dve_steps, S, t, name):
        act.wait_ge(*dve_steps.at(f"{name} eps {t}"))
        act.activation(lrs[:, t:t + 1], lrs[:, t:t + 1], ACT.Ln).then_inc(*S.step())
        act.wait_ge(*S.last())
        act.activation(lrs[:, t:t + 1], lrs[:, t:t + 1], ACT.Exp, scale=-0.5).then_inc(*S.step(f"{name} rstd {t}"))

    @runs("sync")
    def _(sp):
        sp.wait_ge(*gd_pe.at("projected", QKH - 1))
        for c in range(4):
            if c == 1:
                after(sp, GDN)
            if c == 3:
                sp.wait_ge(*o2_pe.at("y 0"))
            sp.dma_start(ring[c % 3], w_out2[:, 4 * c:4 * c + 4, :]).then_inc(o2_in[c % 3], 16)
        for w in range(2):
            for dst, name in ((lng, "ln_g_2"), (lnb, "ln_b_2")):
                sp.dma_start(dst[:, w, :], flat(name)[:, w * D:(w + 1) * D].to_broadcast([P, D])).then_inc(ln_in, 16)
        for dst, name, c0, n in ((wr, "moe_w_group_2", 0, NGRP), (wr, "moe_w_router_2", NGRP, NEXP)):
            sp.dma_start(dst[:, :, c0:c0 + n], a[name][0].rearrange("(k p) n -> p k n", p=P)).then_inc(rt_in, 16)
        for name, c0, n in (("moe_b_group_2", 0, NGRP), ("moe_b_router_2", NGRP, NEXP)):
            sp.dma_start(rb[:, c0:c0 + n], flat(name).to_broadcast([P, n])).then_inc(rt_in, 16)
        sp.dma_start(ptok, a["p_2"][0, 0].rearrange("(t p) c -> p t c", p=P)).then_inc(rt_in, 16)
        for t in range(NT):
            sp.wait_ge(*o2_dve.at(f"x2 {t}"))
            sp.dma_start(x2d[t * P:(t + 1) * P, :], xtok[:, t, :]).then_inc(x2_out, 16)

    @runs("tensor")
    def _(pe):
        after(pe, GDN)
        for c in range(4):
            pe.wait_ge(o2_in[c % 3], 16 * (c // 3 + 1))
            for t in range(NT):
                for h in range(2):
                    for k in range(4):
                        mm = pe.matmul(ps[:, 2 * t + h, :], yT[:, 4 * c + k, t * P:(t + 1) * P],
                                       ring[c % 3][:, k, 512 * h:512 * h + 512], start=(c == 0 and k == 0),
                                       stop=(c == 3 and k == 3))
                if c == 3:
                    mm.then_inc(*o2_pe.step(f"h {t}"))
            if c < 3:
                mm.then_inc(*o2_pe.step(f"y {c}"))
        pe.wait_ge(rt_in, 80)
        NL = NGRP + NEXP
        for t in range(NT + 1):
            if t < NT:
                pe.wait_ge(*o2_dve.at(f"x2 {t}"))
                for k in range(ND):
                    mm = pe.transpose(ps[:, 2 * t + k // 4, P * (k % 4):P * (k % 4) + P], xtok[:, t, k * P:(k + 1) * P], ident[:])
                mm.then_inc(*o2_pe.step(f"x^T {t}"))
            if t:
                u = t - 1
                pe.wait_ge(*o2_act.at(f"hT {u}"))
                for k in range(ND):
                    mm = pe.matmul(ps[:, 0, NL * u:NL * u + NL], hT[:, k, u * P:(u + 1) * P], wr[:, k, :], start=(k == 0), stop=(k == ND - 1))
        mm.then_inc(*o2_pe.step("logits"))
        for k in range(2):
            for t in range(NT):
                mm = pe.transpose(ps[:, 1 + k, t * P:(t + 1) * P], ptok[:, t, k * P:(k + 1) * P], ident[:])
        mm.then_inc(*o2_pe.step("p^T"))
        pe.wait_ge(*o2_dve.at("picks"))
        for t in range(NT):
            for u in range(t):
                pe.matmul(ps[:, 3, NEXP * t:NEXP * t + NEXP], ones[:], both[:, u, :], start=(u == 0), stop=False)
            pe.matmul(ps[:, 3, NEXP * t:NEXP * t + NEXP], LT[:], both[:, t, :], start=(t == 0), stop=True)
        for t in range(NT):
            mm = pe.matmul(ps[:, 4, 0:NEXP], ones[:], both[:, t, :], start=(t == 0), stop=(t == NT - 1))
        mm.then_inc(*o2_pe.step("counts"))
        pe.wait_ge(*o2_dve.at("rows"))
        for j in range(2 * NT):
            mm = pe.matmul(ps[:, 5, 0:NTAB], Ak[:, j, :], Bk[:, j, :], start=(j == 0), stop=(j == 2 * NT - 1))
        mm.then_inc(*o2_pe.step("indices"))
        o2_pe.close()

    @runs("scalar")
    def _(act):
        after(act, GDN)
        for t in range(NT + 1):
            if t < NT:
                rsqrt_of(act, o2_dve, o2_act, t, "x2")
            if t:
                u = t - 1
                act.wait_ge(*o2_pe.at(f"x^T {u}"))
                act.activation(hT[:, :, u * P:(u + 1) * P], ps[:, 2 * u:2 * u + 2, :].rearrange("p b (k c) -> p (b k) c", k=4), ACT.Copy)\
                   .then_inc(*o2_act.step(f"hT {u}"))
        act.wait_ge(*o2_pe.at("p^T"))
        act.activation(pT, ps[:, 1:3, :], ACT.Copy).then_inc(*o2_act.step())
        act.wait_ge(*o2_dve.at("shifted groups"))
        act.activation(gex, gex, ACT.Exp).then_inc(*o2_act.step("exp groups"))
        act.wait_ge(*o2_dve.at("v2 - v1"))
        act.activation(dd, dd, ACT.Exp).then_inc(*o2_act.step("exp experts"))
        o2_act.close()

    @runs("gpsimd")
    def _(pool):
        after(pool, GDN)
        for j in range(EPG):
            pool.memset(desc[:, j:j + 1], float(EPG - j)).then_inc(*o2_pool.step())
        pool.iota(iota, [[1, P]], base=0, channel_multiplier=0, allow_small_or_imprecise_dtypes=True).then_inc(*o2_pool.step())
        pool.iota(tokid, [[P, NT]], base=0, channel_multiplier=1, allow_small_or_imprecise_dtypes=True).then_inc(*o2_pool.step())
        o2_pool.close()

    @runs("vector")
    def _(dve):
        def link(ins, name=None):
            ins.then_inc(*o2_dve.step(name))
            dve.wait_ge(*o2_dve.last())

        def first_max(onehot, x, m, eq, n):
            link(dve.tensor_reduce(m, x, X_AXIS, ALU.max))
            link(dve.tensor_tensor(eq, x, bcast(m, n), ALU.is_equal))
            link(dve.tensor_tensor(eq, eq, repeat(desc[:, 0:n], NT), ALU.mult))
            link(dve.tensor_reduce(wa, eq, X_AXIS, ALU.max))
            link(dve.tensor_tensor(onehot, eq, bcast(wa, n), ALU.is_equal))

        after(dve, GDN)
        dve.wait_ge(ln_in, 64)
        for t in range(NT):
            dve.wait_ge(*o2_pe.at(f"h {t}"))
            for h in range(2):
                hs = slice(512 * h, 512 * h + 512)
                dve.scalar_tensor_tensor(out=xtok[:, t, hs], in0=xtok[:, t, hs], scalar=ALPHA, in1=ps[:, 2 * t + h, :],
                                         op0=ALU.mult, op1=ALU.add).then_inc(*o2_dve.step())
            dve.wait_ge(*o2_dve.last())
            layernorm(dve, o2_act, o2_dve, t, 0, "x2")
        dve.wait_ge(*o2_pe.at("logits"))
        dve.wait_ge(rt_in, 80)
        dve.wait_ge(*o2_pool.end())
        link(dve.tensor_tensor(lg, ps[:, 0, 0:NT * (NGRP + NEXP)].rearrange("p (t c) -> p t c", t=NT), repeat(rb, NT), ALU.add))
        gl, el = lg[:, :, 0:NGRP], lg[:, :, NGRP:NGRP + NEXP]
        first_max(ohg, gl, gmax, geq, NGRP)
        link(dve.tensor_tensor(gex, gl, bcast(gmax, NGRP), ALU.subtract), "shifted groups")
        for t in range(NT):
            dve.tensor_tensor(prod[:, NGRP * t:NGRP * t + NGRP, :], el[:, t, :].rearrange("p (g j) -> p g j", g=NGRP),
                              bcast(ohg[:, t, :], EPG), ALU.mult).then_inc(*o2_dve.step())
        dve.wait_ge(*o2_dve.last())
        link(dve.tensor_reduce(e8, prod.rearrange("p (t g) j -> p t j g", t=NT), X_AXIS, ALU.add))
        first_max(oh1, e8, v1, eq8, EPG)
        link(dve.scalar_tensor_tensor(out=e8b, in0=oh1, scalar=-1e30, in1=e8, op0=ALU.mult, op1=ALU.add))
        first_max(oh2, e8b, v2, eq8, EPG)
        link(dve.tensor_tensor(dd, v2, v1, ALU.subtract), "v2 - v1")
        dve.wait_ge(*o2_act.at("exp groups"))
        link(dve.tensor_reduce(gsum4, gex, X_AXIS, ALU.add))
        dve.wait_ge(*o2_act.at("exp experts"))
        link(dve.tensor_scalar(wb, dd, 1.0, None, ALU.add))
        link(dve.tensor_tensor(wb, wb, gsum4, ALU.mult))
        link(dve.reciprocal(wa, wb))
        link(dve.tensor_tensor(wb, wa, dd, ALU.mult))
        for k, oh in ((0, oh1), (1, oh2)):
            for t in range(NT):
                dve.tensor_tensor(pick[:, k, t, :].rearrange("p (g j) -> p g j", g=NGRP), bcast(ohg[:, t, :], EPG),
                                  repeat(oh[:, t, :], NGRP), ALU.mult).then_inc(*o2_dve.step())
        dve.wait_ge(*o2_dve.last())
        link(dve.tensor_tensor(both, pick[:, 0, :, :], pick[:, 1, :, :], ALU.add), "picks")
        dve.wait_ge(*o2_pe.at("counts"))
        link(dve.tensor_copy(cnt, ps[:, 4, 0:NEXP]))
        link(dve.tensor_copy(rank, ps[:, 3, 0:NT * NEXP].rearrange("p (t e) -> p t e", t=NT)))
        link(dve.tensor_scalar(tiles, cnt, 0.0, None, ALU.is_gt))
        for j in range(1, NT):
            link(dve.scalar_tensor_tensor(out=tiles, in0=cnt, scalar=float(P * j), in1=tiles, op0=ALU.is_gt, op1=ALU.add))
        link(dve.tensor_tensor_scan(ends, ones[:, 0:NEXP], tiles, 0.0, ALU.mult, ALU.add))
        link(dve.tensor_tensor(starts, ends, tiles, ALU.subtract))
        for k in range(2):
            ks = slice(NT * k, NT * k + NT)
            link(dve.tensor_tensor(both, pick[:, k, :, :], rank, ALU.mult))
            link(dve.tensor_reduce(rk[:, ks], both, X_AXIS, ALU.add))
            link(dve.tensor_tensor(both, pick[:, k, :, :], repeat(starts, NT), ALU.mult))
            link(dve.tensor_reduce(st_[:, ks], both, X_AXIS, ALU.add))
        link(dve.tensor_scalar(qk_, rk, float(P), None, ALU.is_ge))
        for j in range(2, NT):
            link(dve.scalar_tensor_tensor(out=qk_, in0=rk, scalar=float(P * j), in1=qk_, op0=ALU.is_ge, op1=ALU.add))
        link(dve.scalar_tensor_tensor(out=pk_, in0=qk_, scalar=-float(P), in1=rk, op0=ALU.mult, op1=ALU.add))
        link(dve.tensor_tensor(st_, st_, qk_, ALU.add))
        link(dve.scalar_tensor_tensor(out=sk_, in0=st_, scalar=float(P), in1=pk_, op0=ALU.mult, op1=ALU.add))
        link(dve.tensor_copy(slotu[:], sk_))
        for j in range(2 * NT):
            dve.tensor_scalar(Ak[:, j, :], iota, pk_[:, j:j + 1], None, ALU.is_equal).then_inc(*o2_dve.step())
            dve.tensor_scalar(Bk[:, j, :], iota[:, 0:NTAB], st_[:, j:j + 1], tokid[:, j % NT:j % NT + 1], ALU.is_equal, ALU.mult)\
               .then_inc(*o2_dve.step("rows"))
        link(dve.tensor_tensor(cmpt, bcast(iota[:, 0:NTAB], NEXP), repeat(ends, NTAB), ALU.is_ge))
        link(dve.tensor_reduce(etf, cmpt, X_AXIS, ALU.add))
        link(dve.tensor_scalar(etf, etf, float(NEXP - 1), None, ALU.min))
        link(dve.tensor_copy(etab[:, 0:NTAB], etf[0:1, :]))
        link(dve.tensor_scalar(tmp32[0:1, 0:MAXIT], iota[0:1, 0:MAXIT], 2.0, ends[0:1, NEXP - 1:NEXP], ALU.mult, ALU.is_lt))
        link(dve.tensor_reduce(etf[0:1, 0:1], tmp32[0:1, 0:MAXIT], X_AXIS, ALU.add))
        link(dve.tensor_copy(nit[:], etf[0:1, 0:1]), "tables")
        dve.wait_ge(*o2_pe.at("indices"))
        link(dve.tensor_copy(idxu[:], ps[:, 5, 0:NTAB]))
        o2_dve.close()

    OUT2 = [(s, None) for s in (o2_pe, o2_dve, o2_act, o2_pool)]

    KW = ND * HID
    ex = {e: steps(f"experts_{n}") for e, n in (("pe", "products"), ("dve", "vector"), ("act", "scalar"), ("pool", "pool"))}
    ex0 = {e: steps(f"first_tile_{n}") for e, n in (("pe", "products"), ("dve", "vector"), ("act", "scalar"), ("pool", "pool"))}
    ex_gu = [steps(f"experts_gate_up_in{b}", 16) for b in range(2)]
    ex_dn = [steps(f"experts_down_in{b}", 16) for b in range(2)]
    ex_g = [sem(f"experts_tokens_in{b}") for b in range(2)]
    ex_y = [steps(f"experts_rows_out{b}", 16) for b in range(2)]
    gu0_in, g0_in = sem("first_gate_up_in"), [sem(f"first_tokens_in{b}") for b in range(2)]

    def wview(b, j):
        v = W[:, b, KW * j:KW * j + KW]
        return v.rearrange("p (k n) -> p k n", k=ND) if j < 2 else v.rearrange("p (k n) -> p k n", k=2)

    def expert_rows(name, e):
        return a[name][0].rearrange("g e (k p) n -> (g e) p k n", p=P)[bass.ds(e, 1)].rearrange("a p k n -> p (a k) n")

    def iterations(eng):
        eng.wait_ge(*o2_dve.end())
        return eng.value_load(nit[0:1, 0:1], min_val=1, max_val=MAXIT)

    @runs("sync")
    def _(sp):
        def expert(tile):
            place = etab[0:1, tile:tile + 1] if isinstance(tile, int) else etab[0:1, bass.ds(tile, 1)]
            return sp.value_load(place, min_val=0, max_val=NEXP - 1)

        def load(e, b, js, then):
            for j in js:
                sp.dma_start(wview(b, j), expert_rows(("moe_w_gate_2", "moe_w_up_2", "moe_w_down_2")[j], e)).then_inc(*then())

        n_it = iterations(sp)
        after(sp, OUT2)
        sp.dma_start(wpp, a["pe_w_proj_2"][0].rearrange("(k p) n -> p k n", p=P)).then_inc(fin_p_in, 16)
        load(expert(0), 0, (0, 1), lambda: (gu0_in, 16))
        for s in ex_gu + ex_dn:
            s.credit(sp)
        with sp.Fori(0, n_it) as i:
            for s in ex_gu + ex_dn:
                s.begin(i)
            e0, e1, e2 = expert(2 * i), expert(2 * i + 1), expert(2 * i + 2)
            sp.wait_ge(*ex["pe"].at("up 1", i - 1))
            load(e1, 1, (0, 1), lambda: ex_gu[1].step("in"))
            sp.wait_ge(*ex["pe"].at("down 0", i - 1))
            load(e0, 0, (2,), lambda: ex_dn[0].step("in"))
            sp.wait_ge(*ex0["pe"].end())
            sp.wait_ge(*ex["pe"].at("up 0", i - 1))
            load(e2, 0, (0, 1), lambda: ex_gu[0].step("in"))
            sp.wait_ge(*ex["pe"].at("down 1", i - 1))
            load(e1, 1, (2,), lambda: ex_dn[1].step("in"))
            for s in ex_gu + ex_dn:
                s.close()

    @runs("gpsimd")
    def _(pool):
        def gather(tile, b, S, then):
            pool.tensor_tensor(spare2[:, 0:1], ones[:, 0:1], ones[:, 0:1], ALU.mult).then_inc(*S.step())
            pool.tensor_copy(icol[:, b:b + 1], idxu[:, bass.ds(tile, 1)] if not isinstance(tile, int) else idxu[:, tile:tile + 1])\
                .then_inc(*S.step())
            pool.wait_ge(*S.last())
            pool.tensor_tensor(spare2[:, 1:2], ones[:, 0:1], ones[:, 0:1], ALU.mult).then_inc(*S.step())
            pool.indirect_dma_start(out=xg[:, b, :], out_offset=None, in_=x2d,
                                    in_offset=bass.IndirectOffsetOnAxis(ap=icol[:, b:b + 1], axis=0)).then_inc(*then)

        n_it = iterations(pool)
        after(pool, OUT2)
        pool.wait_ge(x2_out, 16 * NT)
        for b in range(2):
            gather(b, b, ex0["pool"], (g0_in[b], 16))
        ex0["pool"].close()
        S = ex["pool"]
        S.credit(pool)
        pool.wait_ge(g0_in[0], 16)
        pool.wait_ge(g0_in[1], 16)
        with pool.Fori(0, n_it) as i:
            S.begin(i)
            for b in range(2):
                pool.wait_ge(*ex["pe"].at(f"xg^T {b}", i - 1))
                pool.wait_ge(*ex0["pe"].end())
                pool.wait_ge(*S.last())
                gather(2 * i + 2 + b, b, S, (ex_g[b], 16))
            S.close()

    @runs("tensor")
    def _(pe):
        def turn(b):
            for k in range(ND):
                mm = pe.transpose(ps[:, k // 4, P * (k % 4):P * (k % 4) + P], xg[:, b, k * P:(k + 1) * P], ident[:])
            return mm

        def gate_up(b, S, name):
            for j in range(2):
                for k in range(ND):
                    mm = pe.matmul(ps[:, 2 + b, HID * j:HID * j + HID], xgT[:, b, k, :], wview(b, j)[:, k, :], start=(k == 0),
                                   stop=(k == ND - 1))
            mm.then_inc(*S.step(name))

        n_it = iterations(pe)
        after(pe, OUT2)
        S = ex0["pe"]
        pe.wait_ge(g0_in[0], 16)
        turn(0).then_inc(*S.step("xg^T 0"))
        pe.wait_ge(*ex0["act"].at("xg^T 0"))
        pe.wait_ge(gu0_in, 32)
        gate_up(0, S, "up")
        pe.wait_ge(g0_in[1], 16)
        turn(1).then_inc(*S.step("xg^T 1"))
        S.close()
        S = ex["pe"]
        S.credit(pe)
        with pe.Fori(0, n_it) as i:
            S.begin(i)
            for b in (1, 0):
                o = 1 - b
                pe.wait_ge(*ex["dve"].at(f"hidden {o}", i if o else i - 1))
                pe.wait_ge(*ex0["dve"].end())
                for f in range(2):
                    mm = pe.transpose(ps[:, 4, f * P:(f + 1) * P], gh[:, o, f * P:(f + 1) * P], ident[:])
                mm.then_inc(*S.step(f"h^T {o}"))
                pe.wait_ge(*ex["act"].at(f"xg^T {b}", i - 1 if b else i))
                pe.wait_ge(*ex0["act"].end())
                pe.wait_ge(*ex_gu[b].at("in", i))
                gate_up(b, S, f"up {b}")
                pe.wait_ge(ex_g[o], 16 * (i + 1))
                turn(o).then_inc(*S.step(f"xg^T {o}"))
                pe.wait_ge(*ex["act"].at(f"h^T {o}", i))
                pe.wait_ge(*ex_dn[o].at("in", i))
                pe.wait_ge(*ex["dve"].at(f"y {b}", i - 1 if b else i))
                for h in range(2):
                    for f in range(2):
                        mm = pe.matmul(ps[:, 5 + h, :], hgT[:, o, f, :], wview(o, 2)[:, f, 512 * h:512 * h + 512], start=(f == 0),
                                       stop=(f == 1))
                mm.then_inc(*S.step(f"down {o}"))
            S.close()

    @runs("scalar")
    def _(act):
        def turned(b, S, name):
            for c in range(2):
                act.activation(xgT[:, b, 4 * c:4 * c + 4, :].rearrange("p k t -> p (k t)"), ps[:, c, :], ACT.Copy).then_inc(*S.step(name))

        def sigmoid(b, S, name):
            for func, kw in ((ACT.Exp, dict(scale=-1.0)), (ACT.Ln, dict(bias=1.0)), (ACT.Exp, dict(scale=-1.0))):
                act.activation(gh[:, b, 0:HID], gh[:, b, 0:HID], func, **kw).then_inc(*S.step(name))
                act.wait_ge(*S.last())

        n_it = iterations(act)
        after(act, OUT2)
        S = ex0["act"]
        act.wait_ge(*ex0["pe"].at("xg^T 0"))
        turned(0, S, "xg^T 0")
        act.wait_ge(*ex0["dve"].at("clamped"))
        sigmoid(0, S, "sigmoid")
        act.wait_ge(*ex0["pe"].at("xg^T 1"))
        turned(1, S, "xg^T 1")
        S.close()
        S = ex["act"]
        S.credit(act)
        for s in ex_y:
            s.credit(act)
        act.wait_ge(zeroed, 16)
        with act.Fori(0, n_it) as i:
            S.begin(i)
            for b in (1, 0):
                o = 1 - b
                act.wait_ge(*ex["pe"].at(f"h^T {o}", i))
                act.wait_ge(*ex["pe"].at(f"down {o}", i - 1))
                act.activation(hgT[:, o, :, :].rearrange("p f t -> p (f t)"), ps[:, 4, 0:2 * P], ACT.Copy).then_inc(*S.step(f"h^T {o}"))
                act.wait_ge(*ex["dve"].at(f"clamped {b}", i))
                sigmoid(b, S, f"sigmoid {b}")
                act.wait_ge(*ex["pe"].at(f"xg^T {o}", i))
                turned(o, S, f"xg^T {o}")
                act.wait_ge(*ex["dve"].at(f"y {o}", i))
                ex_y[o].begin(i)
                act.dma_start(yd[bass.ds((2 * i + o) * P, P), :], yrow[:, o, :]).then_inc(*ex_y[o].step("out"))
                ex_y[o].close()
            S.close()

    @runs("vector")
    def _(dve):
        def clamp(b, S, name):
            dve.tensor_scalar(gh[:, b, 0:HID], ps[:, 2 + b, 0:HID], -LNCLAMP, None, ALU.max).then_inc(*S.step(name))

        def hidden(b, S, name):
            dve.tensor_tensor(gh[:, b, 0:HID], gh[:, b, 0:HID], ps[:, 2 + b, 0:HID], ALU.mult).then_inc(*S.step())
            dve.wait_ge(*S.last())
            dve.tensor_tensor(gh[:, b, 0:HID], gh[:, b, 0:HID], ps[:, 2 + b, HID:2 * HID], ALU.mult).then_inc(*S.step(name))

        n_it = iterations(dve)
        after(dve, OUT2)
        S = ex0["dve"]
        dve.wait_ge(*ex0["pe"].at("up"))
        clamp(0, S, "clamped")
        dve.wait_ge(*ex0["act"].at("sigmoid"))
        hidden(0, S, "hidden")
        for t in range(NT):
            dve.tensor_scalar(xtok[:, t, :], xtok[:, t, :], ALPHA, None, ALU.mult).then_inc(*S.step())
        S.close()
        S = ex["dve"]
        S.credit(dve)
        with dve.Fori(0, n_it) as i:
            S.begin(i)
            for b in (1, 0):
                o = 1 - b
                dve.wait_ge(*ex["pe"].at(f"up {b}", i))
                dve.wait_ge(*ex["pe"].at(f"h^T {b}", i - 1 if b else i))
                dve.wait_ge(*S.last())
                clamp(b, S, f"clamped {b}")
                dve.wait_ge(*ex["act"].at(f"sigmoid {b}", i))
                hidden(b, S, f"hidden {b}")
                dve.wait_ge(*ex["pe"].at(f"down {o}", i))
                dve.wait_ge(*ex_y[o].end(i - 1))
                for h in range(2):
                    dve.tensor_copy(yrow[:, o, 512 * h:512 * h + 512], ps[:, 5 + h, :]).then_inc(*S.step(f"y {o}"))
            S.close()

    def after_experts(eng, n_it):
        for s in ex.values():
            eng.wait_ge(*s.end(n_it - 1))
        for s in ex_gu + ex_dn + ex_y:
            eng.wait_ge(*s.end(n_it - 1))
        for s in ex_g:
            eng.wait_ge(s, 16 * n_it)

    yg = xg
    co_pool, co_dve = steps("combine_pool"), steps("combine_vector")
    co_in = [sem(f"combine_in{b}") for b in range(2)]

    @runs("gpsimd")
    def _(pool):
        after_experts(pool, iterations(pool))
        for j in range(2 * NT):
            t, k = j // 2, j % 2
            if j >= 2:
                pool.wait_ge(*co_dve.at(f"added {j - 2}"))
            pool.tensor_tensor(spare2[:, 2:3], ones[:, 0:1], ones[:, 0:1], ALU.mult).then_inc(*co_pool.step())
            pool.wait_ge(*co_pool.last())
            pool.indirect_dma_start(out=yg[:, k, :], out_offset=None, in_=yd,
                                    in_offset=bass.IndirectOffsetOnAxis(ap=slotu[:, NT * k + t:NT * k + t + 1], axis=0))\
                .then_inc(co_in[k], 16)
        co_pool.close()

    wpg = Wall[:, 0:ND * D].rearrange("p (k n) -> p k n", k=ND)
    pproj = Wall[:, ND * D:ND * D + NT * D].rearrange("p (t n) -> p t n", t=NT)
    wpp = hT[:].rearrange("p k t -> p (k t)")[:, 0:2 * D].rearrange("p (k n) -> p k n", k=2)
    xT = yTall[:, 4 * D:8 * D].rearrange("p (t k c) -> p t k c", t=NT, k=ND)
    fin_pe, fin_dve, fin_act = steps("last_products"), steps("last_vector"), steps("last_scalar")
    fin_in, fin_p_in = sem("last_weights_in"), sem("last_projection_in")

    @runs("sync")
    def _(sp):
        sp.wait_ge(*fin_pe.at("proj 0"))
        sp.dma_start(wpg, a["pe_w_gate_2"][0].rearrange("(k p) n -> p k n", p=P)).then_inc(fin_in, 16)
        for t in range(NT):
            sp.wait_ge(*fin_dve.at(f"out {t}"))
            sp.dma_start(out[0, t * P:(t + 1) * P, :], xtok[:, t, :]).then_inc(stores, 16)
        sp.wait_ge(stores, 16 * NT)

    @runs("tensor")
    def _(pe):
        after_experts(pe, iterations(pe))
        pe.wait_ge(fin_p_in, 16)
        for t in range(NT):
            for h in range(2):
                for k in range(2):
                    mm = pe.matmul(ps[:, 2 * t + h, :], pT[:, k, t * P:(t + 1) * P], wpp[:, k, 512 * h:512 * h + 512], start=(k == 0),
                                   stop=(k == 1))
            mm.then_inc(*fin_pe.step(f"proj {t}"))
        def turn_x(t):
            pe.wait_ge(*fin_dve.at(f"x3 {t}"))
            pe.wait_ge(*fin_act.at(f"xT {t - 1}" if t else f"proj {NT - 1}"))
            for k in range(ND):
                mm = pe.transpose(ps[:, 6 + k // 4, P * (k % 4):P * (k % 4) + P], xtok[:, t, k * P:(k + 1) * P], ident[:])
            mm.then_inc(*fin_pe.step(f"x^T {t}"))

        turn_x(0)
        pe.wait_ge(fin_in, 16)
        for t in range(NT):
            b0 = 2 * (t % 3)
            pe.wait_ge(*fin_act.at(f"xT {t}"))
            if t >= 3:
                pe.wait_ge(*fin_dve.at(f"clamped {t - 3}"))
            for h in range(2):
                for k in range(ND):
                    mm = pe.matmul(ps[:, b0 + h, :], xT[:, t, k, :], wpg[:, k, 512 * h:512 * h + 512], start=(k == 0),
                                   stop=(k == ND - 1))
                if h == 1:
                    mm.then_inc(*fin_pe.step(f"gate {t}"))
                elif t < NT - 1:
                    turn_x(t + 1)
        fin_pe.close()

    @runs("scalar")
    def _(act):
        def link(ins, name=None):
            ins.then_inc(*fin_act.step(name))
            act.wait_ge(*fin_act.last())

        after_experts(act, iterations(act))
        for t in range(NT):
            act.wait_ge(*fin_pe.at(f"proj {t}"))
            act.activation(pproj[:, t, :].rearrange("p (h c) -> p h c", h=2), ps[:, 2 * t:2 * t + 2, :], ACT.Copy)\
               .then_inc(*fin_act.step(f"proj {t}"))

        def keep_x(t):
            act.wait_ge(*fin_pe.at(f"x^T {t}"))
            act.activation(xT[:, t, :, :].rearrange("p k c -> p (k c)").rearrange("p (h c) -> p h c", h=2), ps[:, 6:8, :], ACT.Copy)\
               .then_inc(*fin_act.step(f"xT {t}"))

        def sigmoid_x(t):
            act.wait_ge(*fin_dve.at(f"clamped {t}"))
            s = sgate[:, t % 2, :]
            link(act.activation(s, s, ACT.Exp, scale=-1.0))
            link(act.activation(s, s, ACT.Ln, bias=1.0))
            link(act.activation(s, s, ACT.Exp, scale=-1.0), f"sigmoid {t}")

        for t in range(NT):
            rsqrt_of(act, fin_dve, fin_act, t, "x3")
            if t == 0:
                keep_x(0)
        for t in range(NT):
            if t:
                sigmoid_x(t - 1)
            if t < NT - 1:
                keep_x(t + 1)
        sigmoid_x(NT - 1)
        fin_act.close()

    @runs("vector")
    def _(dve):
        def link(ins, name=None):
            ins.then_inc(*fin_dve.step(name))
            dve.wait_ge(*fin_dve.last())

        def clamp_gate(t):
            b0 = 2 * (t % 3)
            s = sgate[:, t % 2, :]
            dve.wait_ge(*fin_pe.at(f"gate {t}"))
            link(dve.tensor_scalar(s.rearrange("p (h c) -> p h c", h=2), ps[:, b0:b0 + 2, :], -LNCLAMP, None, ALU.max), f"clamped {t}")

        def add_gated(t):
            s = sgate[:, t % 2, :]
            dve.wait_ge(*fin_act.at(f"sigmoid {t}"))
            link(dve.tensor_tensor(s, s, pproj[:, t, :], ALU.mult))
            link(dve.tensor_tensor(xtok[:, t, :], xtok[:, t, :], s, ALU.add), f"out {t}")

        after_experts(dve, iterations(dve))
        for t in range(NT):
            for k in range(2):
                dve.wait_ge(co_in[k], 16 * (t + 1))
                dve.scalar_tensor_tensor(out=xtok[:, t, :], in0=yg[:, k, :], scalar=(wa, wb)[k][:, t:t + 1], in1=xtok[:, t, :],
                                         op0=ALU.mult, op1=ALU.add).then_inc(*co_dve.step(f"added {2 * t + k}"))
                dve.wait_ge(*co_dve.last())
            layernorm(dve, fin_act, fin_dve, t, 1, "x3")
        co_dve.close()
        for t in range(NT):
            clamp_gate(t)
            add_gated(t)
        fin_dve.close()

    block = ctx.enter_context(nc.Block())

    @block.sync
    def _(sp):
        for part in progs["sync"]:
            part(sp)

    @block.tensor
    def _(pe):
        for part in progs["tensor"]:
            part(pe)

    @block.vector
    def _(dve):
        for part in progs["vector"]:
            part(dve)

    @block.scalar
    def _(act):
        for part in progs["scalar"]:
            part(act)

    @block.gpsimd
    def _(pool):
        for part in progs["gpsimd"]:
            part(pool)

    ctx.close()


def compose(nc, names, shapes, dtypes):
    args = {n: nc.dram_tensor(f"in_{n}_dram", s, d, kind="ExternalInput").ap() for n, s, d in zip(names, shapes, dtypes)}
    return args, nc.dram_tensor("out_0_dram", (1, SEQ, D), F32, kind="ExternalOutput").ap()


_INS = ["x", "c", "norm_g", "ada_w", "ada_b", "w_in", "w_out", "tshift_mu", "decay_w0", "decay_w2", "iclr_a0", "iclr_a2",
        "k_k", "k_a", "r_k", "rwkv_ln_w", "rwkv_ln_b", "sb_norm_g", "final_g", "p_2", "gdn_w_in_2", "gdn_conv_w_2",
        "gdn_a_log_2", "gdn_dt_bias_2", "gdn_norm_w_2", "gdn_w_out_2", "ln_g_2", "ln_b_2", "moe_w_group_2",
        "moe_b_group_2", "moe_w_router_2", "moe_b_router_2", "moe_w_gate_2", "moe_w_up_2", "moe_w_down_2",
        "pe_w_gate_2", "pe_w_proj_2"]


def kernel(**inputs):
    import numpy as _np
    import concourse.bacc as _bacc
    from concourse import mybir as _mybir
    from concourse.bass_utils import run_bass_kernel_spmd as _run

    arrays = {f"in_{n}_dram": _np.ascontiguousarray(inputs[n]) for n in _INS}
    shapes = [arrays[f"in_{n}_dram"].shape for n in _INS]
    dtypes = [_mybir.dt.from_np(arrays[f"in_{n}_dram"].dtype) for n in _INS]
    book = {}
    for _ in range(2):
        nc = _bacc.Bacc("TRN2", target_bir_lowering=False, num_devices=1)
        args, out = compose(nc, _INS, shapes, dtypes)
        build(nc, args, out, book)
    r = _run(nc, [arrays], core_ids=[0])
    return r.results[0]["out_0_dram"]
```
